# Optimizing a Trainium2 kernel written in Bass

```python
import jax, jax.numpy as jnp
from jax import lax
import numpy as np
import math

D_MODEL = 1024
BATCH = 1
SEQ = 512
DEPTH = 2

N_A_LAYERS = DEPTH // 2
N_B_LAYERS = DEPTH - N_A_LAYERS
HEAD_DIM = 64
SB_HEADS = D_MODEL // HEAD_DIM
NSA_HEADS = D_MODEL // HEAD_DIM
NSA_KV_GROUPS = 4
NSA_HPG = NSA_HEADS // NSA_KV_GROUPS
CMP_LEN = 32
CMP_STRIDE = 16
CMP_HIDDEN = 256
SEL_LEN = 64
SEL_TOPK = 16
WINDOW = 512
D_FF = 4 * D_MODEL
ROPE_THETA = 500000.0
ROT_DIM = HEAD_DIM // 4
Q_BLOCK = 128
NORM_EPS = 1e-5
NEG = -1e30
FORCED_SCORE = 1e6


def rms_norm(x, g):
    xf = x.astype(jnp.float32)
    y = xf * lax.rsqrt(jnp.mean(xf * xf, axis=-1, keepdims=True) + NORM_EPS)
    return (y * g.astype(jnp.float32)).astype(x.dtype)

def partial_rope(x):
    s = x.shape[1]
    half = ROT_DIM // 2
    inv_freq = ROPE_THETA ** (-jnp.arange(half, dtype=jnp.float32) * 2.0 / ROT_DIM)
    ang = jnp.arange(s, dtype=jnp.float32)[:, None] * inv_freq[None, :]
    cos = jnp.cos(ang)[None, :, None, :]
    sin = jnp.sin(ang)[None, :, None, :]
    xr = x[..., :ROT_DIM].astype(jnp.float32)
    x1, x2 = xr[..., :half], xr[..., half:]
    rot = jnp.concatenate([x1 * cos - x2 * sin, x2 * cos + x1 * sin], axis=-1).astype(x.dtype)
    return jnp.concatenate([rot, x[..., ROT_DIM:]], axis=-1)

def to_qblocks(a):
    b, s = a.shape[0], a.shape[1]
    return jnp.moveaxis(a.reshape((b, s // Q_BLOCK, Q_BLOCK) + a.shape[2:]), 1, 0)

def from_qblocks(a):
    a = jnp.moveaxis(a, 0, 1)
    return a.reshape((a.shape[0], a.shape[1] * a.shape[2]) + a.shape[3:])

def sqrelu_mlp(x, w1, w2):
    h = jax.nn.relu(x @ w1)
    return (h * h) @ w2

def stick_breaking_attention(h, w_qkv, w_o):
    b, s, _ = h.shape
    n_qb = s // Q_BLOCK
    qkv = (h @ w_qkv).reshape(b, s, 3, SB_HEADS, HEAD_DIM)
    q, k, v = qkv[:, :, 0], qkv[:, :, 1], qkv[:, :, 2]
    scale = HEAD_DIM ** -0.5
    key_pos = jnp.arange(s)

    def block(args):
        qi, q_blk = args
        t = qi * Q_BLOCK + jnp.arange(Q_BLOCK)
        z = jnp.einsum('bqhd,bshd->bhqs', q_blk, k).astype(jnp.float32) * scale
        causal = key_pos[None, :] < t[:, None]
        log_1m = jnp.where(causal, jax.nn.log_sigmoid(-z), 0.0)
        excl = lax.cumsum(log_1m, axis=3, reverse=True) - log_1m
        a = jnp.where(causal, jnp.exp(jax.nn.log_sigmoid(z) + excl), 0.0)
        return jnp.einsum('bhqs,bshd->bqhd', a.astype(v.dtype), v)

    o = lax.map(block, (jnp.arange(n_qb), to_qblocks(q)))
    return from_qblocks(o).reshape(b, s, SB_HEADS * HEAD_DIM) @ w_o

def nsa_shared_kv(h, kv_norm, w_kv, cmp_pos, cmp_w1, cmp_w2):
    b, s, _ = h.shape
    hn = rms_norm(h, kv_norm)
    kv = (hn @ w_kv).reshape(b, s, 3, 2, NSA_KV_GROUPS, HEAD_DIM)
    n_cmp = (s - CMP_LEN) // CMP_STRIDE + 1
    idx = jnp.arange(n_cmp)[:, None] * CMP_STRIDE + jnp.arange(CMP_LEN)[None, :]
    blk = kv[:, :, 0][:, idx]
    blk = blk + jnp.transpose(cmp_pos, (1, 0, 2))[None, None, :, :, None, :]
    blk = jnp.transpose(blk, (0, 1, 3, 4, 2, 5)).reshape(b, n_cmp, 2, NSA_KV_GROUPS, CMP_LEN * HEAD_DIM)
    hid = jax.nn.gelu(jnp.einsum('bncgf,cfe->bncge', blk, cmp_w1))
    cmp = jnp.einsum('bncge,ced->bncgd', hid, cmp_w2)
    k_cmp, v_cmp = cmp[:, :, 0], cmp[:, :, 1]
    k_slc, v_slc = partial_rope(kv[:, :, 1, 0]), kv[:, :, 1, 1]
    k_win, v_win = partial_rope(kv[:, :, 2, 0]), kv[:, :, 2, 1]
    return (k_cmp, v_cmp, k_slc, v_slc, k_win, v_win)

def nsa_attention(h, w_q, gate_b, w_o, shared):
    k_cmp, v_cmp, k_slc, v_slc, k_win, v_win = shared
    b, s, _ = h.shape
    G, HPG, DH = NSA_KV_GROUPS, NSA_HPG, HEAD_DIM
    n_cmp = k_cmp.shape[1]
    n_sel = s // SEL_LEN
    n_qb = s // Q_BLOCK
    topk = min(SEL_TOPK, n_sel)
    scale = DH ** -0.5

    proj = h @ w_q
    q = proj[..., :NSA_HEADS * DH].reshape(b, s, NSA_HEADS, DH)
    gates = jax.nn.sigmoid((proj[..., NSA_HEADS * DH:] + gate_b).astype(jnp.float32)).reshape(b, s, 3, NSA_HEADS)
    q_rot = partial_rope(q)

    cmp_start = jnp.arange(n_cmp) * CMP_STRIDE
    cmp_end = cmp_start + CMP_LEN - 1
    sel_ids = jnp.arange(n_sel)
    sel_start = sel_ids * SEL_LEN
    overlap = ((cmp_start[:, None] < sel_start[None, :] + SEL_LEN)
               & (cmp_start[:, None] + CMP_LEN > sel_start[None, :])).astype(jnp.float32)
    k_sel_blocks = jnp.transpose(k_slc.reshape(b, n_sel, SEL_LEN, G, DH), (0, 3, 1, 2, 4))
    v_sel_blocks = jnp.transpose(v_slc.reshape(b, n_sel, SEL_LEN, G, DH), (0, 3, 1, 2, 4))
    pad = ((0, 0), (WINDOW, 0), (0, 0), (0, 0))
    k_win_p = jnp.pad(k_win, pad)
    v_win_p = jnp.pad(v_win, pad)
    gather = jax.vmap(jax.vmap(lambda blocks, ids: blocks[ids]))

    def block(args):
        qi, q_blk, qr_blk = args
        q0 = qi * Q_BLOCK
        t = q0 + jnp.arange(Q_BLOCK)
        qg = q_blk.reshape(b, Q_BLOCK, G, HPG, DH)
        qrg = qr_blk.reshape(b, Q_BLOCK, G, HPG, DH)

        sc = jnp.einsum('bqghd,bngd->bghqn', qg, k_cmp).astype(jnp.float32) * scale
        valid_c = cmp_end[None, :] <= t[:, None]
        p_cmp = jax.nn.softmax(jnp.where(valid_c, sc, NEG), axis=-1)
        p_cmp = p_cmp * jnp.any(valid_c, axis=-1)[:, None]
        o_cmp = jnp.einsum('bghqn,bngd->bqghd', p_cmp.astype(v_cmp.dtype), v_cmp)

        imp = jnp.einsum('bghqn,nm->bgqm', p_cmp, overlap)
        blk_t = t // SEL_LEN
        forced = (sel_ids[None, :] == 0) | (sel_ids[None, :] == blk_t[:, None]) | (sel_ids[None, :] == blk_t[:, None] - 1)
        causal_b = sel_ids[None, :] <= blk_t[:, None]
        imp = jnp.where(causal_b, jnp.where(forced, FORCED_SCORE, imp), -jnp.inf)
        _, top_idx = lax.top_k(imp, topk)
        k_sel = gather(k_sel_blocks, top_idx)
        v_sel = gather(v_sel_blocks, top_idx)
        ss = jnp.einsum('bqghd,bgqkld->bghqkl', qrg, k_sel).astype(jnp.float32) * scale
        key_pos = top_idx[..., None] * SEL_LEN + jnp.arange(SEL_LEN)
        valid_s = key_pos <= t[None, None, :, None, None]
        ss = jnp.where(valid_s[:, :, None], ss, NEG)
        p_sel = jax.nn.softmax(ss.reshape(b, G, HPG, Q_BLOCK, topk * SEL_LEN), axis=-1).reshape(ss.shape)
        o_sel = jnp.einsum('bghqkl,bgqkld->bqghd', p_sel.astype(v_sel.dtype), v_sel)

        k_w = lax.dynamic_slice_in_dim(k_win_p, q0, WINDOW + Q_BLOCK, axis=1)
        v_w = lax.dynamic_slice_in_dim(v_win_p, q0, WINDOW + Q_BLOCK, axis=1)
        sw = jnp.einsum('bqghd,bsgd->bghqs', qrg, k_w).astype(jnp.float32) * scale
        kpos = q0 - WINDOW + jnp.arange(WINDOW + Q_BLOCK)
        diff = t[:, None] - kpos[None, :]
        valid_w = (diff >= 0) & (diff < WINDOW) & (kpos[None, :] >= 0)
        p_w = jax.nn.softmax(jnp.where(valid_w, sw, NEG), axis=-1)
        o_win = jnp.einsum('bghqs,bsgd->bqghd', p_w.astype(v_w.dtype), v_w)

        return jnp.stack([o_cmp, o_sel, o_win], axis=2).reshape(b, Q_BLOCK, 3, NSA_HEADS, DH)

    o = from_qblocks(lax.map(block, (jnp.arange(n_qb), to_qblocks(q), to_qblocks(q_rot))))
    out = jnp.einsum('bsch,bschd->bshd', gates.astype(o.dtype), o).reshape(b, s, NSA_HEADS * DH)
    return out @ w_o

def first_inputs(seed: int = 0) -> dict:
    key = jax.random.key(seed)
    ks = jax.random.split(key, 16)
    f32 = jnp.float32

    def w(k, shape, fan_in):
        return jax.random.normal(k, shape, f32) * fan_in ** -0.5

    x = jax.random.normal(ks[0], (BATCH, SEQ, D_MODEL), f32)
    norm_gain = 1.0 + 0.02 * jax.random.normal(ks[1], (DEPTH, 2, D_MODEL), f32)
    sb_w_qkv = w(ks[2], (N_A_LAYERS, D_MODEL, 3 * SB_HEADS * HEAD_DIM), D_MODEL)
    sb_w_o = w(ks[3], (N_A_LAYERS, SB_HEADS * HEAD_DIM, D_MODEL), SB_HEADS * HEAD_DIM)
    kv_norm = 1.0 + 0.02 * jax.random.normal(ks[4], (D_MODEL,), f32)
    nsa_w_kv = w(ks[5], (D_MODEL, 3 * 2 * NSA_KV_GROUPS * HEAD_DIM), D_MODEL)
    cmp_pos = 0.1 * jax.random.normal(ks[6], (2, CMP_LEN, HEAD_DIM), f32)
    cmp_w1 = w(ks[7], (2, CMP_LEN * HEAD_DIM, CMP_HIDDEN), CMP_LEN * HEAD_DIM)
    cmp_w2 = w(ks[8], (2, CMP_HIDDEN, HEAD_DIM), CMP_HIDDEN)
    nsa_w_q = w(ks[9], (N_B_LAYERS, D_MODEL, NSA_HEADS * HEAD_DIM + 3 * NSA_HEADS), D_MODEL)
    nsa_gate_b = 0.1 * jax.random.normal(ks[10], (N_B_LAYERS, 3 * NSA_HEADS), f32)
    nsa_w_o = w(ks[11], (N_B_LAYERS, NSA_HEADS * HEAD_DIM, D_MODEL), NSA_HEADS * HEAD_DIM)
    mlp_w1 = w(ks[12], (DEPTH, D_MODEL, D_FF), D_MODEL)
    mlp_w2 = w(ks[13], (DEPTH, D_FF, D_MODEL), D_FF)
    final_norm = 1.0 + 0.02 * jax.random.normal(ks[14], (D_MODEL,), f32)
    return {"x": x, "norm_gain": norm_gain, "sb_w_qkv": sb_w_qkv, "sb_w_o": sb_w_o,
            "kv_norm": kv_norm, "nsa_w_kv": nsa_w_kv, "cmp_pos": cmp_pos, "cmp_w1": cmp_w1,
            "cmp_w2": cmp_w2, "nsa_w_q": nsa_w_q, "nsa_gate_b": nsa_gate_b, "nsa_w_o": nsa_w_o,
            "mlp_w1": mlp_w1, "mlp_w2": mlp_w2, "final_norm": final_norm}

def first_block(x, norm_gain, sb_w_qkv, sb_w_o, kv_norm, nsa_w_kv, cmp_pos, cmp_w1, cmp_w2,
              nsa_w_q, nsa_gate_b, nsa_w_o, mlp_w1, mlp_w2, final_norm):
    h = x
    shared = None
    for layer in range(DEPTH):
        hn = rms_norm(h, norm_gain[layer, 0])
        if layer < N_A_LAYERS:
            h = h + stick_breaking_attention(hn, sb_w_qkv[layer], sb_w_o[layer])
        else:
            j = layer - N_A_LAYERS
            h = h + nsa_attention(hn, nsa_w_q[j], nsa_gate_b[j], nsa_w_o[j], shared)
        h = h + sqrelu_mlp(rms_norm(h, norm_gain[layer, 1]), mlp_w1[layer], mlp_w2[layer])
        if layer == N_A_LAYERS - 1:
            shared = nsa_shared_kv(h, kv_norm, nsa_w_kv, cmp_pos, cmp_w1, cmp_w2)
    return rms_norm(h, final_norm)


DEPTH_2 = 1

N_META = 16
GRID_W = 64
EPS = 1e-6

A_HEADS = 8
A_HEAD_DIM = 64
A_QK_WIDTH = A_HEADS * 2 * A_HEAD_DIM
A_V_WIDTH = A_HEADS * 2 * A_HEAD_DIM

B_HEADS = 8
B_KV_HEADS = 2
B_GROUP = B_HEADS // B_KV_HEADS
B_HEAD_DIM = 128
B_Q_WIDTH = B_HEADS * B_HEAD_DIM
B_KV_WIDTH = B_KV_HEADS * B_HEAD_DIM
ROPE_THETA_2 = 10000.0

SPLITS = (A_QK_WIDTH, A_QK_WIDTH, A_V_WIDTH, B_Q_WIDTH, B_KV_WIDTH, B_KV_WIDTH, D_MODEL, D_MODEL)
IN_WIDTH = sum(SPLITS)

N_EXPERTS = 16
EXPERT_FF = 512
CAPACITY_FACTOR = 2


def rms_norm_2(x, g):
    xf = x.astype(jnp.float32)
    y = xf * lax.rsqrt(jnp.mean(xf * xf, axis=-1, keepdims=True) + EPS)
    return (y * g.astype(jnp.float32)).astype(x.dtype)

def sweep_queries(block_fn, *qs):
    out_meta = block_fn(*[a[:, :N_META] for a in qs])

    def to_blocks(a):
        r = a[:, N_META:]
        n = r.shape[1] // Q_BLOCK
        r = r.reshape((r.shape[0], n, Q_BLOCK) + r.shape[2:])
        return jnp.moveaxis(r, 1, 0)

    out_real = lax.map(lambda args: block_fn(*args), tuple(to_blocks(a) for a in qs))
    out_real = jnp.moveaxis(out_real, 0, 1)
    out_real = out_real.reshape((out_real.shape[0], -1) + out_real.shape[3:])
    return jnp.concatenate([out_meta, out_real], axis=1)

def alibi_slopes(n_heads):
    return jnp.exp2(-8.0 * jnp.arange(1, n_heads + 1, dtype=jnp.float32) / n_heads)

def diff_attention(q, k, v, pos, slopes, lam):
    scale = A_HEAD_DIM ** -0.5
    k_meta = pos < N_META

    def block(qb, pb):
        qp = pb[0]
        s = jnp.einsum('bqhmd,bkhmd->bhmqk', qb, k).astype(jnp.float32) * scale
        dist = jnp.abs(qp[:, None] - pos[None, :]).astype(jnp.float32)
        dist = jnp.where((qp[:, None] < N_META) | k_meta[None, :], 0.0, dist)
        s = s - slopes[None, :, None, None, None] * dist
        p = jax.nn.softmax(s, axis=-1)
        w = p[:, :, 0] - lam * p[:, :, 1]
        return jnp.einsum('bhqk,bkhe->bqhe', w.astype(v.dtype), v)

    return sweep_queries(block, q, pos[None])

def gqa_attention(q, k, v):
    scale = B_HEAD_DIM ** -0.5

    def block(qb):
        s = jnp.einsum('bqngd,bknd->bngqk', qb, k).astype(jnp.float32) * scale
        p = jax.nn.softmax(s, axis=-1)
        return jnp.einsum('bngqk,bknd->bqngd', p.astype(v.dtype), v)

    return sweep_queries(block, q)

def axial_angles(total_len):
    n_tok = total_len - N_META
    rows = n_tok // GRID_W
    row_id = jnp.repeat(jnp.arange(rows, dtype=jnp.int32), GRID_W)
    col_id = jnp.tile(jnp.arange(GRID_W, dtype=jnp.int32), rows)
    zeros = jnp.zeros((N_META,), jnp.int32)
    row_id = jnp.concatenate([zeros, row_id])
    col_id = jnp.concatenate([zeros, col_id])
    half = B_HEAD_DIM // 2
    inv_freq = ROPE_THETA_2 ** (-jnp.arange(0, half, 2, dtype=jnp.float32) / half)
    return (row_id.astype(jnp.float32)[:, None] * inv_freq[None, :],
            col_id.astype(jnp.float32)[:, None] * inv_freq[None, :])

def rotate(x, ang):
    m = ang.shape[-1]
    cos = jnp.cos(ang)[None, :, None, :].astype(x.dtype)
    sin = jnp.sin(ang)[None, :, None, :].astype(x.dtype)
    x1, x2 = x[..., :m], x[..., m:]
    return jnp.concatenate([x1 * cos - x2 * sin, x2 * cos + x1 * sin], axis=-1)

def axial_rope(x, ang_row, ang_col):
    half = x.shape[-1] // 2
    return jnp.concatenate([rotate(x[..., :half], ang_row), rotate(x[..., half:], ang_col)], axis=-1)

def expert_choice_ffn(u, w_router, w_gate, w_up, w_down):
    b, L, d = u.shape
    cap = CAPACITY_FACTOR * L // N_EXPERTS
    logits = jnp.einsum('bld,de->ble', u, w_router).astype(jnp.float32)
    aff = jax.nn.softmax(logits, axis=-1)
    top_aff, top_idx = lax.top_k(jnp.swapaxes(aff, 1, 2), cap)
    xs = jax.vmap(lambda ub, ib: ub[ib])(u, top_idx)
    hid = jax.nn.silu(jnp.einsum('becd,edf->becf', xs, w_gate)) * jnp.einsum('becd,edf->becf', xs, w_up)
    y = jnp.einsum('becf,efd->becd', hid, w_down) * top_aff[..., None].astype(u.dtype)
    return jax.vmap(lambda yb, ib: jnp.zeros((L, d), yb.dtype).at[ib.reshape(-1)].add(yb.reshape(-1, d)))(y, top_idx)

def second_inputs(seed: int = 0) -> dict:
    key = jax.random.key(seed)
    ks = jax.random.split(key, 24)
    f32 = jnp.float32

    def nrm(k, shape, scale):
        return jax.random.normal(k, shape, f32) * scale

    def gain(k, shape):
        return 1.0 + 0.02 * jax.random.normal(k, shape, f32)

    return {
        'x': nrm(ks[0], (BATCH, SEQ, D_MODEL), 1.0),
        'meta_tokens': nrm(ks[1], (N_META, D_MODEL), 1.0),
        'g_mix': gain(ks[2], (DEPTH_2, D_MODEL)),
        'w_in': nrm(ks[3], (DEPTH_2, D_MODEL, IN_WIDTH), D_MODEL ** -0.5),
        'lambda_q1': nrm(ks[4], (DEPTH_2, A_HEAD_DIM), 0.1),
        'lambda_k1': nrm(ks[5], (DEPTH_2, A_HEAD_DIM), 0.1),
        'lambda_q2': nrm(ks[6], (DEPTH_2, A_HEAD_DIM), 0.1),
        'lambda_k2': nrm(ks[7], (DEPTH_2, A_HEAD_DIM), 0.1),
        'g_subln': gain(ks[8], (DEPTH_2, 2 * A_HEAD_DIM)),
        'g_qnorm': gain(ks[9], (DEPTH_2, B_HEAD_DIM)),
        'g_knorm': gain(ks[10], (DEPTH_2, B_HEAD_DIM)),
        'w_branch_a': nrm(ks[11], (DEPTH_2, A_V_WIDTH, D_MODEL), A_V_WIDTH ** -0.5),
        'w_branch_b': nrm(ks[12], (DEPTH_2, B_Q_WIDTH, D_MODEL), B_Q_WIDTH ** -0.5),
        'w_out': nrm(ks[13], (DEPTH_2, D_MODEL, D_MODEL), D_MODEL ** -0.5),
        'g_ffn': gain(ks[14], (DEPTH_2, D_MODEL)),
        'w_router': nrm(ks[15], (DEPTH_2, D_MODEL, N_EXPERTS), D_MODEL ** -0.5),
        'w_gate': nrm(ks[16], (DEPTH_2, N_EXPERTS, D_MODEL, EXPERT_FF), D_MODEL ** -0.5),
        'w_up': nrm(ks[17], (DEPTH_2, N_EXPERTS, D_MODEL, EXPERT_FF), D_MODEL ** -0.5),
        'w_down': nrm(ks[18], (DEPTH_2, N_EXPERTS, EXPERT_FF, D_MODEL), EXPERT_FF ** -0.5),
        'g_final': gain(ks[19], (D_MODEL,)),
    }

def second_block(x, meta_tokens, g_mix, w_in, lambda_q1, lambda_k1, lambda_q2, lambda_k2,
              g_subln, g_qnorm, g_knorm, w_branch_a, w_branch_b, w_out, g_ffn,
              w_router, w_gate, w_up, w_down, g_final):
    b = x.shape[0]
    meta = jnp.broadcast_to(meta_tokens[None].astype(x.dtype), (b, N_META, x.shape[-1]))
    h = jnp.concatenate([meta, x], axis=1)
    L = h.shape[1]
    pos = jnp.arange(L, dtype=jnp.int32)
    ang_row, ang_col = axial_angles(L)
    slopes = alibi_slopes(A_HEADS)
    cut = list(np.cumsum(SPLITS)[:-1])

    for layer in range(DEPTH_2):
        u = rms_norm_2(h, g_mix[layer])
        z = jnp.einsum('bld,df->blf', u, w_in[layer])
        qa, ka, va, qb, kb, vb, ga, gb = jnp.split(z, cut, axis=-1)

        lam_init = 0.8 - 0.6 * math.exp(-0.3 * layer)
        lam = (jnp.exp(jnp.sum(lambda_q1[layer].astype(jnp.float32) * lambda_k1[layer].astype(jnp.float32)))
               - jnp.exp(jnp.sum(lambda_q2[layer].astype(jnp.float32) * lambda_k2[layer].astype(jnp.float32)))
               + lam_init)
        oa = diff_attention(qa.reshape(b, L, A_HEADS, 2, A_HEAD_DIM),
                            ka.reshape(b, L, A_HEADS, 2, A_HEAD_DIM),
                            va.reshape(b, L, A_HEADS, 2 * A_HEAD_DIM), pos, slopes, lam)
        oa = (rms_norm_2(oa, g_subln[layer]) * (1.0 - lam_init)).reshape(b, L, A_V_WIDTH)

        qh = axial_rope(rms_norm_2(qb.reshape(b, L, B_HEADS, B_HEAD_DIM), g_qnorm[layer]), ang_row, ang_col)
        kh = axial_rope(rms_norm_2(kb.reshape(b, L, B_KV_HEADS, B_HEAD_DIM), g_knorm[layer]), ang_row, ang_col)
        ob = gqa_attention(qh.reshape(b, L, B_KV_HEADS, B_GROUP, B_HEAD_DIM), kh,
                           vb.reshape(b, L, B_KV_HEADS, B_HEAD_DIM)).reshape(b, L, B_Q_WIDTH)

        ya = jnp.einsum('blf,fd->bld', oa, w_branch_a[layer])
        yb = jnp.einsum('blf,fd->bld', ob, w_branch_b[layer])
        merged = jax.nn.sigmoid(ga) * ya + jax.nn.sigmoid(gb) * yb
        h = h + jnp.einsum('bld,de->ble', merged, w_out[layer])

        h = h + expert_choice_ffn(rms_norm_2(h, g_ffn[layer]), w_router[layer], w_gate[layer],
                                  w_up[layer], w_down[layer])

    return rms_norm_2(h, g_final)[:, N_META:]


def setup_inputs(seed=0):
    out = dict(first_inputs(seed))
    for name, value in second_inputs(seed + 1).items():
        if name != "x":
            out[name + "_2"] = value
    return out


def reference(
    x, norm_gain, sb_w_qkv, sb_w_o, kv_norm, nsa_w_kv, cmp_pos, cmp_w1, cmp_w2, nsa_w_q,
    nsa_gate_b, nsa_w_o, mlp_w1, mlp_w2, final_norm, meta_tokens_2, g_mix_2, w_in_2,
    lambda_q1_2, lambda_k1_2, lambda_q2_2, lambda_k2_2, g_subln_2, g_qnorm_2, g_knorm_2,
    w_branch_a_2, w_branch_b_2, w_out_2, g_ffn_2, w_router_2, w_gate_2, w_up_2, w_down_2,
    g_final_2,
):
    x = first_block(
        x, norm_gain, sb_w_qkv, sb_w_o, kv_norm, nsa_w_kv, cmp_pos, cmp_w1, cmp_w2, nsa_w_q,
        nsa_gate_b, nsa_w_o, mlp_w1, mlp_w2, final_norm,
    )
    return second_block(
        x, meta_tokens_2, g_mix_2, w_in_2, lambda_q1_2, lambda_k1_2, lambda_q2_2, lambda_k2_2,
        g_subln_2, g_qnorm_2, g_knorm_2, w_branch_a_2, w_branch_b_2, w_out_2, g_ffn_2,
        w_router_2, w_gate_2, w_up_2, w_down_2, g_final_2,
    )


_drawn_inputs = setup_inputs


def setup_inputs(seed=0):
    import zlib

    import numpy as np

    out = dict(_drawn_inputs(seed))
    spreads = {}
    factors = {'kv_norm': 8.0,
     'nsa_gate_b': 3.86,
     'g_mix_2': 3.503,
     'lambda_q1_2': 8.0,
     'lambda_k1_2': 3.312,
     'lambda_q2_2': 2.902,
     'g_subln_2': 5.089,
     'g_qnorm_2': 8.0,
     'g_knorm_2': 8.0,
     'g_ffn_2': 3.475}
    for name, (base, spread) in spreads.items():
        noise = np.random.default_rng([zlib.crc32(name.encode()), seed]).standard_normal(out[name].shape)
        drawn = base * np.exp(spread * noise) if base else spread * noise
        out[name] = __import__('jax').numpy.asarray(drawn.astype(out[name].dtype))
    for name, factor in factors.items():
        out[name] = (out[name] * factor).astype(out[name].dtype)
    return out
```

```python
from contextlib import ExitStack, contextmanager

import numpy as np
import concourse.bass as bass
from concourse import mybir

F32, F32R, BF16, F16, U32 = mybir.dt.float32, mybir.dt.float32r, mybir.dt.bfloat16, mybir.dt.float16, mybir.dt.uint32
ACT, ALU, AX = mybir.ActivationFunctionType, mybir.AluOpType, mybir.AxisListType

P = 128
D = 1024
KT = D // P
SEQ = 512
QT = SEQ // P
META = 16
L2 = SEQ + META
T2 = QT + 1
CH2 = L2 // 2
HD = 64
PAIRS = 8
D_FF = 4096
FF_PARTS = 4
FF_TILES = D_FF // FF_PARTS // P
SPLITS = 4
EPS1, EPS2 = 1e-5, 1e-6
RING = 8
CAUSAL_COLS = [QT * P - P * i for i in range(QT)]
CAUSAL_AT = [sum(CAUSAL_COLS[:i]) for i in range(QT)]
CAUSAL = sum(CAUSAL_COLS)
GROUPS = 4
BRANCHES = 3
UNITS = 4 * BRANCHES
CMP_LEN, CMP_STRIDE, CMP_HID = 32, 16, 256
N_CMP = (SEQ - CMP_LEN) // CMP_STRIDE + 1
CMP_KT = CMP_LEN * HD // P
N_GATES = 48
SCORE_AT = [(1, 384), (2, 0), (1, 0), (0, 0)]
PROB_AT = [0, P, 3 * P, 6 * P]
PT_AT = [(3, 0, 0), (4, 0, SEQ), (5, 0, 2 * SEQ), (4, 384, SEQ + 384)]
GELU_C, GELU_K = 0.044715, (2.0 / np.pi) ** 0.5


HEADS2 = 8
KV2 = 2
Q_PER_KV = HEADS2 // KV2
USES = 8 + 6 * Q_PER_KV
LAM_INIT = 0.8 - 0.6
O_TAIL = 128
EXPERTS, CAP, EXPERT_FF = 16, 2 * L2 // 16, 512
FT = EXPERT_FF // P
W_IN = {"qa": 0, "ka": 8, "va": 16, "qb": 24, "kb": 32, "vb": 34, "ga": 36, "gb": 44}


def rows_of(t):
    return P if t < QT else META


class Tally:

    def __init__(self, sem):
        self.sem, self.n, self.turn, self.per, self.start = sem, 0, None, 0, 0

    def inc(self, ins):
        ins.then_inc(self.sem, 1)
        self.n += 1

    def value(self):
        return self.n if self.turn is None else self.turn * self.per + self.n


@contextmanager
def loop(eng, count, **per):
    tallies = per.pop("tallies", [])
    with eng.Fori(0, count) as turn:
        for t, k in tallies:
            t.turn, t.per, t.start = turn, k, t.n
        yield turn
        for t, k in tallies:
            assert t.n - t.start == k, (t.n - t.start, k)
            t.n, t.turn = t.start + k * count, None


class Ring:

    def __init__(self, tile, loaded, free):
        self.tile, self.loaded, self.free = tile, loaded, free
        self.at, self.loads, self.plan = 0, [0] * RING, {}

    def load(self, sp, name, sources, turns=1):
        n = len(sources)
        assert turns == 1 or n % RING == 0, (name, n)
        per = [0] * RING
        waits = []
        for j, s in enumerate(sources):
            slot = (self.at + j) % RING
            waits.append((slot, self.loads[slot], per[slot] + 1))
            per[slot] += s is not None
        self.plan[name] = [(slot, base, k, per[slot]) for slot, base, k in waits]

        def turn_loads(turn):
            for j, s in enumerate(sources):
                if s is None:
                    continue
                slot = (self.at + j) % RING
                sp.wait_ge(self.free, self.at + turn * n + j + 1)
                dst, src = s(self.tile[:, slot, :], turn)
                sp.dma_start(dst, src).then_inc(self.loaded[slot], 16)

        if turns == 1:
            turn_loads(0)
        else:
            with sp.Fori(0, turns) as turn:
                turn_loads(turn)
        self.at += n * turns
        for slot in range(RING):
            self.loads[slot] += per[slot] * turns

    def wait(self, pe, name, j, turn=0):
        slot, base, k, per = self.plan[name][j]
        pe.wait_ge(self.loaded[slot], (turn * per + base + k) * 16)
        return self.tile[:, slot, :]


def cols_tile(w, n_tile):
    def source(slot, turn):
        return (slot.rearrange("p (k n) -> p k n", n=P),
                w[:, bass.ds(n_tile(turn) * P, P)].rearrange("(k p) n -> p k n", p=P))
    return source


def rows_tiles(w, row_tile, col, width=512):
    k = D // width

    def source(slot, turn):
        return (slot.rearrange("p (k n) -> p k n", n=width),
                w[bass.ds(row_tile(turn) * P, k * P), bass.ds(col(turn), width)].rearrange("(k p) n -> p k n", p=P))
    return source


def build_program(nc, A, C, out):
    ctx = ExitStack()
    with ctx:
        def sb(name, shape, dt=F32, stack=ctx):
            return stack.enter_context(nc.sbuf_tensor(name, shape, dt))

        def sem(name):
            return ctx.enter_context(nc.semaphore(name))

        h = sb("h", [P, T2, D])
        xT = sb("xT", [P, KT, L2])
        ring_tile = sb("ring_tile", [P, RING, D])
        ident = sb("ident", [P, P])
        ident_bf = sb("ident_bf", [P, P], BF16)
        gain_rows = sb("gain_rows", [7 * KT, P])
        gains = sb("gains", [P, 7, KT])
        ssq = sb("ssq", [P, T2])
        rstd = sb("rstd", [P, T2])
        xn = sb("xn", [P, 2, D])
        oT = sb("oT", [P, KT, L2])

        one = sb("one", [P, 1])
        gain_bc = sb("gain_bc", [P, D])

        psum = ctx.enter_context(nc.psum_tensor("psum", [P, 8, 512], F32))
        bank = [psum[:, k, :] for k in range(8)]

        st = ExitStack()
        qT = sb("qT", [P, 2, SEQ], stack=st)
        kT = sb("kT", [P, 2, SEQ], stack=st)
        vN = sb("vN", [P, 2, QT, P], stack=st)
        absz = sb("absz", [P, CAUSAL], stack=st)
        softp = sb("softp", [P, CAUSAL], stack=st)
        stick = sb("stick", [P, CAUSAL], stack=st)
        tri_neg = sb("tri_neg", [P, P], stack=st)
        ones_neg = sb("ones_neg", [P, P], stack=st)
        past01 = sb("past01", [P, P], stack=st)
        past_neg = sb("past_neg", [P, P], stack=st)
        past_neg_bf = sb("past_neg_bf", [P, P], BF16, stack=st)
        st.close()
        st = ExitStack()
        x_hi = sb("x_hi", [P, KT, SEQ], F32R, stack=st)
        x_lo = sb("x_lo", [P, KT, SEQ], F32R, stack=st)
        w_hi = sb("w_hi", [P, SPLITS, D], F32R, stack=st)
        w_lo = sb("w_lo", [P, SPLITS, D], F32R, stack=st)
        hid_hi = sb("hid_hi", [P, FF_TILES, SEQ], F32R, stack=st)
        hid_lo = sb("hid_lo", [P, FF_TILES, SEQ], F32R, stack=st)
        relu = sb("relu", [P, 2, SEQ], stack=st)
        hid_sq = sb("hid_sq", [P, 2, SEQ], stack=st)
        st.close()

        st = ExitStack()
        kv_pairs = sb("kv_pairs", [P, 2, GROUPS, SEQ], stack=st)
        blocks = sb("blocks", [P, 2, CMP_KT, GROUPS * N_CMP], stack=st)
        pos_rows = sb("pos_rows", [2 * CMP_KT, P], stack=st)
        pos_off = sb("pos_off", [P, 2 * CMP_KT], stack=st)
        cmp_w2 = sb("cmp_out_w", [P, 2, 2, HD], stack=st)
        cmp_x = sb("cmp_x", [P, 2, GROUPS * N_CMP], stack=st)
        cmp_u = sb("cmp_u", [P, 2, GROUPS * N_CMP], stack=st)
        cmp_h = sb("cmp_h", [P, 2, 2, GROUPS * N_CMP], stack=st)
        k_cmp = sb("k_cmp", [P, GROUPS, N_CMP], stack=st)
        v_cmp = sb("v_cmp", [N_CMP, GROUPS, HD], stack=st)
        k_all = sb("k_all", [P, 2, GROUPS, SEQ], stack=st)
        v_all = sb("v_all", [P, 2, QT, GROUPS, HD], stack=st)
        k_grp = sb("k_grp", [P, 2, SEQ], stack=st)
        v_grp = sb("v_grp", [P, 2, QT, HD], stack=st)
        kc_grp = sb("kc_grp", [P, N_CMP], stack=st)
        vc_grp = sb("vc_grp", [N_CMP, HD], stack=st)
        q_raw = sb("q_raw", [P, 2, SEQ], stack=st)
        q_rot = sb("q_rot", [P, 2, SEQ], stack=st)
        rope_a = sb("rope_a", [P, SEQ], stack=st)
        rope_b = sb("rope_b", [P, SEQ], stack=st)
        cos1 = sb("cos1", [P, SEQ], stack=st)
        sin1 = sb("sin1", [P, SEQ], stack=st)
        rot1 = sb("rot1", [P, P], stack=st)
        probs = sb("probs", [P, 2, CAUSAL], stack=st)
        probs_T = sb("probs_T", [P, 2, CAUSAL], stack=st)
        gate_w = sb("gate_w", [P, KT, N_GATES], stack=st)
        gate_b = sb("gate_b", [P, N_GATES], stack=st)
        gates = sb("gates", [P, QT, N_GATES], stack=st)
        future_neg = sb("future_neg", [P, P], stack=st)
        future_neg_bf = sb("future_neg_bf", [P, P], BF16, stack=st)
        cmp_neg = sb("cmp_neg", [P, QT, N_CMP], stack=st)
        cmp_any = sb("cmp_any", [P, QT], stack=st)
        top = sb("top", [P, 2, QT], stack=st)
        rsum = sb("rsum", [P, 2, QT], stack=st)
        factor = sb("factor", [P, 2, QT], stack=st)
        st.close()
        st = ExitStack()
        merged = sb("merged", [P, KT, L2], stack=st)
        sig = sb("sig", [P, 2, L2], stack=st)
        q2 = sb("q2", [P, 2, L2], stack=st)
        k2 = sb("k2", [P, 2, L2], stack=st)
        v2 = sb("v2", [P, 2, T2, P], stack=st)
        prob_a = sb("prob_a", [P, 2, L2], stack=st)
        prob_b = sb("prob_b", [P, 2, L2], stack=st)
        w_T = sb("w_T", [P, 2, T2, P], stack=st)
        dist = sb("dist", [P, T2, L2], F16, stack=st)
        slope = sb("slope", [P, 2, P], F16, stack=st)
        lam_in = sb("lam_in", [P, 4, HD], stack=st)
        lam_prod = sb("lam_prod", [P, HD], stack=st)
        lam = sb("lam", [P, 2], stack=st)
        neg_lam = sb("neg_lam", [P, 1], stack=st)
        head_gain_rows = sb("head_gain_rows", [3, P], stack=st)
        head_gain = sb("head_gain", [P, 3], stack=st)
        mean_w = sb("mean_w", [P, P], stack=st)
        sq2 = sb("sq2", [P, L2], stack=st)
        var2 = sb("var2", [P, L2], stack=st)
        raw2 = sb("raw2", [P, L2], stack=st)
        norm2 = sb("norm2", [P, L2], stack=st)
        rope_c = sb("rope_c", [P, L2], stack=st)
        cos2 = sb("cos2", [P, L2], stack=st)
        sin2 = sb("sin2", [P, L2], stack=st)
        rot2 = sb("rot2", [P, P], stack=st)
        top2 = sb("top2", [P, 2], stack=st)
        rsum2 = sb("rsum2", [P, 2], stack=st)
        rinv2 = sb("rinv2", [P, 2], stack=st)
        st.close()
        st = ExitStack()
        u_rows = sb("u_rows", [P, 2, D], stack=st)
        router_w = sb("router_w", [P, KT, EXPERTS], stack=st)
        logits = sb("logits", [P, T2, EXPERTS], stack=st)
        lmax = sb("lmax", [P, T2], stack=st)
        token_aff = sb("token_aff", [P, T2, EXPERTS, 2], stack=st)
        aff_T = sb("aff_T", [EXPERTS, L2], stack=st)
        work = sb("work", [EXPERTS, L2], stack=st)
        best8 = sb("best8", [EXPERTS, 8], stack=st)
        above = sb("above", [EXPERTS, L2], stack=st)
        equal = sb("equal", [EXPERTS, L2], stack=st)
        count = sb("count", [EXPERTS, L2], stack=st)
        ones_row = sb("ones_row", [EXPERTS, L2], stack=st)
        n_above = sb("n_above", [EXPERTS, 2], stack=st)
        slot_T = sb("slot_T", [P, T2, EXPERTS], stack=st)
        slot_no = sb("slot_no", [P, CAP], stack=st)
        token_no = sb("token_no", [P, T2], stack=st)
        one_hot = sb("one_hot", [P, 2, T2, CAP], stack=st)
        pick = sb("pick", [CAP, EXPERTS, 2], stack=st)
        pick_no = sb("pick_no", [CAP, EXPERTS], U32, stack=st)
        no_get = sb("no_get", [CAP, 2, 1], U32, stack=st)
        no_put = sb("no_put", [CAP, 2, 1], U32, stack=st)
        aff_now = sb("aff_now", [CAP, 2, 1], stack=st)
        xs = sb("xs", [CAP, 2, D], stack=st)
        xs_T = sb("xs_T", [P, 2, KT, CAP], stack=st)
        act_sig = sb("act_sig", [CAP, EXPERT_FF], stack=st)
        act_hid = sb("act_hid", [CAP, 2, EXPERT_FF], stack=st)
        hid_T = sb("hid_T", [P, 2, FT, CAP], stack=st)
        ys = sb("ys", [CAP, 2, D], stack=st)
        st.close()
        u_dram = nc.dram_tensor("u_dram", [L2, D], F32).ap()
        y_dram = nc.dram_tensor("y_dram", [L2, D], F32).ap()

        one_in, ff_freed = sem("one_in"), sem("ff_freed")
        const_in, gains_T, gains_in = sem("const_in"), sem("gains_T"), sem("gains_in")
        loaded = [sem(f"slot{k}_loaded") for k in range(RING)]
        slot_free = sem("slot_free")
        h_upd = sem("h_upd")
        dve_step, act_step = sem("dve_step"), sem("act_step")
        norm_sq, norm_ms, norm_sd, norm_xn, norm_tp, norm_ev = (sem(f"norm_{s}") for s in ("sq", "ms", "sd", "xn", "tp", "ev"))
        sb_pj, sb_pe, sb_z, sb_l, sb_sp, sb_zi, sb_a, sb_o, sb_oe = (
            sem(f"sb_{s}") for s in ("pj", "pe", "z", "l", "sp", "zi", "a", "o", "oe"))
        acc_done = sem("acc_done")
        ff_mm, ff_relu, ff_hid, ff_w2 = sem("ff_mm"), sem("ff_relu"), sem("ff_hid"), sem("ff_w2")
        split_x_hi, split_x, split_w_hi, split_w = sem("split_x_hi"), sem("split_x"), sem("split_w_hi"), sem("split_w")
        out_sem = sem("out_sem")
        nsa_in, gain_in = sem("nsa_in"), sem("gain_in")
        kv_mm, kv_ev, kv_rot, kv_k, pos_T, pos_in = (sem(s) for s in ("kv_mm", "kv_ev", "kv_rot", "kv_k", "pos_T", "pos_in"))
        cmp_blk, cmp_mm, cmp_uu, cmp_ee, cmp_hh, cmp_kv, cmp_out = (
            sem(f"cmp_{s}") for s in ("blk", "mm", "uu", "ee", "hh", "kv", "out"))
        gate_mm, gate_x, gate_in = (sem(f"gate_{s}") for s in ("mm", "x", "in"))
        ns_grp, ns_q, ns_qe, ns_s, ns_m, ns_p, ns_f, ns_tt, ns_t, ns_o, ns_oe = (
            sem(f"ns_{s}") for s in ("grp", "q", "qe", "s", "m", "p", "f", "tt", "t", "o", "oe"))

        b2_in, b2_T, b2_ready = sem("b2_in"), sem("b2_T"), sem("b2_ready")
        lam_d, lam_e = sem("lam_d"), sem("lam_e")
        df_pj, df_pe, df_s, df_m, df_p, df_f, df_tt, df_t, df_o, df_sq, df_ms, df_v, df_sd, df_oe = (
            sem(f"df_{s}") for s in ("pj", "pe", "s", "m", "p", "f", "tt", "t", "o", "sq", "ms", "v", "sd", "oe"))
        br_mm, br_sig, br_m = (sem(f"br_{s}") for s in ("mm", "sig", "m"))
        gq_b, gq_br, gq_x, gq_sd, gq_s, gq_m, gq_p, gq_f, gq_tt, gq_t, gq_o, gq_oe = (
            sem(f"gq_{s}") for s in ("b", "br", "x", "sd", "s", "m", "p", "f", "tt", "t", "o", "oe"))
        moe_in, u_row, h_out, y_in = (sem(s) for s in ("moe_in", "u_row", "h_out", "y_in"))
        ex_done = sem("ex_done")
        u_out = [sem(f"u_out{k}") for k in range(2)]
        ex_x = [sem(f"ex_x{k}") for k in range(2)]
        rt_l, rt_x, rt_e, rt_a, rt_at, rt_s, rt_st, rt_oh, rt_pk, rt_in = (
            sem(f"rt_{s}") for s in ("l", "x", "e", "a", "at", "s", "st", "oh", "pk", "in"))
        ex_no, ex_xt, ex_xe, ex_gu, ex_sg, ex_h, ex_ht, ex_he, ex_y, ex_ye, ex_out = (
            sem(f"ex_{s}") for s in ("no", "xt", "xe", "gu", "sg", "h", "ht", "he", "y", "ye", "out"))

        ring = Ring(ring_tile, loaded, slot_free)
        NSA_CONST = 16 * 10
        B2_CONST, MOE_CONST = 16 * 12, 16 * 3
        NORM_TILES = [QT] * 6 + [T2] * 2 + [QT]
        PLAIN = (5, 8)
        GAIN = {**{u: u for u in range(5)}, 6: 5, 7: 6}
        UPD = 2 * QT
        FF_UPD = FF_PARTS * UPD
        H_BEFORE = [0, UPD, UPD + FF_UPD, UPD + FF_UPD, 2 * UPD + FF_UPD]
        H_ALL = 2 * UPD + 2 * FF_UPD
        H_X2 = H_ALL + QT
        H_FFN = H_X2 + 2 * T2

        block = ctx.enter_context(nc.Block())

        def load_ff(sp, m):
            w1, w2 = A["mlp_w1"][m], A["mlp_w2"][m]
            ring.load(sp, f"ff{m}",
                      [cols_tile(w1, lambda t, j=j: t * FF_TILES + j) for j in range(FF_TILES)]
                      + [rows_tiles(w2, lambda t, k=k: t * FF_TILES + 2 * k, lambda t, n=n: 512 * n)
                         for n in range(2) for k in range(FF_TILES // 2)], FF_PARTS)

        def finish(sp):
            sp.wait_ge(h_upd, H_FFN + QT)
            sp.dma_start(out[0].rearrange("(t p) d -> p t d", p=P), h[:, 0:QT, :]).then_inc(out_sem, 16)
            sp.wait_ge(out_sem, 16)

        ALL_CONST = 16 * (QT + 4 + 7)

        @block.sync
        def _(sp):
            n_const = 0
            for t in range(QT):
                sp.dma_start(h[:, t, :], A["x"][0, t * P:(t + 1) * P, :]).then_inc(const_in, 16)
            for dst, src in ((ident, C["ident"]), (tri_neg, C["tri_neg"]), (past01, C["past01"]), (past_neg, C["past_neg"])):
                sp.dma_start(dst[:, :], src[:, :]).then_inc(const_in, 16)
            for k, g in enumerate((A["norm_gain"][0, 0], A["norm_gain"][0, 1], A["kv_norm"], A["norm_gain"][1, 0],
                                   A["norm_gain"][1, 1], A["g_mix_2"][0], A["g_ffn_2"][0])):
                sp.dma_start(gain_rows[k * KT:(k + 1) * KT, :], g.rearrange("(k p) -> k p", p=P)).then_inc(const_in, 16)

            wq = A["sb_w_qkv"][0]

            def pair(p):
                return [cols_tile(wq, lambda t: p(t)), cols_tile(wq, lambda t: KT + p(t)),
                        cols_tile(wq, lambda t: 2 * KT + p(t)), None]
            ring.load(sp, "sb_first", pair(lambda t: 0))
            ring.load(sp, "sb_loop", pair(lambda t: t * 2 + 1) + pair(lambda t: t * 2 + 2), PAIRS // 2 - 1)
            ring.load(sp, "sb_last", pair(lambda t: PAIRS - 1))
            ring.load(sp, "sb_o", [rows_tiles(A["sb_w_o"][0], lambda t, k=k: 2 * k, lambda t, n=n: 512 * n)
                                   for n in range(2) for k in range(KT // 2)])
            load_ff(sp, 0)

            sp.wait_ge(h_upd, H_BEFORE[2])
            for dst, src in ((pos_rows[:, :], A["cmp_pos"].rearrange("c (k l) d -> (c k) (l d)", l=2)),
                             (cmp_w2[:, :, :, :], A["cmp_w2"].rearrange("c (e p) d -> p c e d", p=P)),
                             (gate_w[:, :, :], A["nsa_w_q"][0][:, D:D + N_GATES].rearrange("(k p) n -> p k n", p=P)),
                             (gate_b[:, :], A["nsa_gate_b"][0].partition_broadcast(P)),
                             (cos1[:, :], C["cos1"]), (sin1[:, :], C["sin1"]), (rot1[:, :], C["rot1"]),
                             (future_neg[:, :], C["future_neg"]), (cmp_neg[:, :, :], C["cmp_neg"]), (cmp_any[:, :], C["cmp_any"])):
                sp.dma_start(dst, src).then_inc(nsa_in, 16)
            sp.dma_start(gain_bc[:, :], A["final_norm"].partition_broadcast(P)).then_inc(gain_in, 16)
            ring.load(sp, "kv", [cols_tile(A["nsa_w_kv"], lambda t, j=j: j) for j in range(12)])
            ring.load(sp, "cmp", [rows_tiles(A["cmp_w1"][c], lambda t, k=k: 4 * k, lambda t: 0, CMP_HID)
                                  for c in range(2) for k in range(CMP_KT // 4)])
            wq = A["nsa_w_q"][0]
            ring.load(sp, "nsa", [cols_tile(wq, lambda t: t * 2), None, None, None,
                                  cols_tile(wq, lambda t: t * 2 + 1), None, None, None], GROUPS)
            ring.load(sp, "nsa_o", [rows_tiles(A["nsa_w_o"][0], lambda t, k=k: 2 * k, lambda t, n=n: 512 * n)
                                    for n in range(2) for k in range(KT // 2)])
            load_ff(sp, 1)

            sp.dma_start(h[0:META, QT, :], A["meta_tokens_2"][:, :]).then_inc(b2_in, 16)
            sp.wait_ge(h_upd, H_ALL)
            for dst, src in ((dist[:, :, :], C["dist"]), (cos2[:, :], C["cos2"]), (sin2[:, :], C["sin2"]), (rot2[:, :], C["rot2"]),
                             (head_gain_rows[0:1, :], A["g_subln_2"]), (head_gain_rows[1:2, :], A["g_qnorm_2"]),
                             (head_gain_rows[2:3, :], A["g_knorm_2"]),
                             (lam_in[:, 0, :], A["lambda_q1_2"][0].partition_broadcast(P)),
                             (lam_in[:, 1, :], A["lambda_k1_2"][0].partition_broadcast(P)),
                             (lam_in[:, 2, :], A["lambda_q2_2"][0].partition_broadcast(P)),
                             (lam_in[:, 3, :], A["lambda_k2_2"][0].partition_broadcast(P))):
                sp.dma_start(dst, src).then_inc(b2_in, 16)
            w = A["w_in_2"][0]

            def head(p):
                return [cols_tile(w, lambda t, c=c: c + p(t)) for c in (W_IN["qa"], W_IN["ka"], W_IN["va"])] + [None]

            def branch(name, gate, out_w):
                pairs = [(cols_tile(w, lambda t, n=n: gate + t * 4 + n), cols_tile(out_w, lambda t, n=n: t * 4 + n)) for n in range(4)]
                ring.load(sp, name, [s for p in pairs for s in p], 2)

            ring.load(sp, "df_first", head(lambda t: 0))
            ring.load(sp, "df_loop", head(lambda t: t * 2 + 1) + head(lambda t: t * 2 + 2), HEADS2 // 2 - 1)
            ring.load(sp, "df_last", head(lambda t: HEADS2 - 1))
            branch("br0", W_IN["ga"], A["w_branch_a_2"][0])
            ring.load(sp, "gqa", [cols_tile(w, lambda t: W_IN["kb"] + t), cols_tile(w, lambda t: W_IN["vb"] + t)]
                      + [cols_tile(w, lambda t, j=j: W_IN["qb"] + t * Q_PER_KV + j) for j in range(Q_PER_KV)] + [None, None], KV2)
            branch("br1", W_IN["gb"], A["w_branch_b_2"][0])
            ring.load(sp, "w_out", [rows_tiles(A["w_out_2"][0], lambda t, k=k: 2 * k, lambda t, n=n: 512 * n)
                                    for n in range(2) for k in range(KT // 2)])

            sp.wait_ge(h_upd, H_FFN)
            for dst, src in ((router_w[:, :, :], A["w_router_2"][0].rearrange("(k p) n -> p k n", p=P)),
                             (slot_no[:, :], C["slot_no"]), (token_no[:, :], C["token_no"])):
                sp.dma_start(dst, src).then_inc(moe_in, 16)
            sp.wait_ge(gain_in, 16)
            sp.dma_start(gain_bc[:, :], A["g_ffn_2"][0].partition_broadcast(P)).then_inc(gain_in, 16)
            wg, wu, wd = (A[n][0].rearrange("e r c -> (e r) c") for n in ("w_gate_2", "w_up_2", "w_down_2"))

            def gate_up(e):
                return [rows_tiles(m, lambda t, k=k: e(t) * KT + 2 * k, lambda t: 0) for m in (wg, wu) for k in range(KT // 2)]

            def down(e):
                return [rows_tiles(wd, lambda t, k=k: e(t) * FT + k, lambda t: 0, D) for k in range(FT)]

            ring.load(sp, "ex_first", gate_up(lambda t: 0))
            ring.load(sp, "ex_loop", gate_up(lambda t: t * 2 + 1) + down(lambda t: t * 2)
                      + gate_up(lambda t: t * 2 + 2) + down(lambda t: t * 2 + 1), EXPERTS // 2 - 1)
            ring.load(sp, "ex_last", gate_up(lambda t: EXPERTS - 1) + down(lambda t: EXPERTS - 2) + down(lambda t: EXPERTS - 1))
            sp.wait_ge(u_row, T2)
            sp.dma_start(gain_bc[:, :], A["g_final_2"].partition_broadcast(P)).then_inc(gain_in, 16)
            finish(sp)

        def norm_base(u):
            return sum(n for v, n in enumerate(NORM_TILES[:u]) if v not in PLAIN)

        def norm_act(act, u, eps_rows=None):
            for t in range(NORM_TILES[u]):
                r = P if t < QT else META
                act_t.inc(act.activation(sq_junk(r), h[0:r, t, :], ACT.Square, accum_out=ssq[0:r, t:t + 1]))
                act.wait_ge(act_step, act_t.value())
            act.sem_inc(norm_sq, 1)
            act.wait_ge(norm_ms, u + 1)
            act.activation(rstd[:, :], rstd[:, :], ACT.Sqrt).then_inc(norm_sd, 1)

        def sq_junk(r):
            return xn[0:r, 1, :]

        def norm_dve(dve, u, eps):
            base = norm_base(u)
            dve.wait_ge(norm_sq, u + 1)
            dve.tensor_scalar(rstd[:, :], ssq[:, :], 1.0 / D, eps, ALU.mult, ALU.add).then_inc(norm_ms, 1)
            dve.wait_ge(norm_sd, u + 1)
            step(dve, dve.reciprocal(rstd[:, :], rstd[:, :]))

            def scale(t):
                r = P if t < QT else META
                if t >= 2:
                    dve.wait_ge(norm_tp, 2 * (base + t - 1))
                dve.tensor_scalar(xn[0:r, t % 2, :], h[0:r, t, :], rstd[0:r, t:t + 1], None, ALU.mult).then_inc(norm_xn, 1)

            scale(0)
            for t in range(NORM_TILES[u]):
                if t + 1 < NORM_TILES[u]:
                    scale(t + 1)
                r = P if t < QT else META
                for c in range(2):
                    dve.wait_ge(norm_tp, 2 * (base + t) + c + 1)
                    src = bank[2 * (t % 2) + c][:, :].rearrange("p (k n) -> p k n", k=4)[:, :, 0:r]
                    dve.tensor_tensor(xT[:, 4 * c:4 * c + 4, t * P:t * P + r], src,
                                      gains[:, GAIN[u], 4 * c:4 * c + 4].unsqueeze(2).broadcast_to([P, 4, r]), ALU.mult).then_inc(norm_ev, 1)
                if u in SPLIT_NORMS and t:
                    split_x_dve(dve, u, t - 1)
            if u in SPLIT_NORMS:
                split_x_dve(dve, u, QT - 1)

        SPLIT_NORMS = (1, 4)

        def x_part(x, t, c):
            return x[:, 4 * c:4 * c + 4, t * P:(t + 1) * P]

        def split_x_act(act, u):
            for t in range(QT):
                for c in range(2):
                    act.wait_ge(norm_ev, 2 * (norm_base(u) + t) + c + 1)
                    act.activation(x_part(x_hi, t, c), x_part(xT, t, c), ACT.Copy).then_inc(split_x_hi, 1)

        def split_x_dve(dve, u, t):
            for c in range(2):
                dve.wait_ge(norm_ev, 2 * (norm_base(u) + t) + c + 1)
                dve.wait_ge(split_x_hi, 2 * (SPLIT_NORMS.index(u) * QT + t) + c + 1)
                dve.tensor_tensor(x_part(x_lo, t, c), x_part(xT, t, c), x_part(x_hi, t, c).bitcast(F32), ALU.subtract).then_inc(split_x, 1)

        def norm_pe(pe, u):
            base = norm_base(u)
            for t in range(NORM_TILES[u]):
                r = P if t < QT else META
                pe.wait_ge(norm_xn, base + t + 1)
                if t >= 2:
                    pe.wait_ge(norm_ev, 2 * (base + t - 1))
                for c in range(2):
                    for k in range(4):
                        last = pe.transpose(bank[2 * (t % 2) + c][:, k * P:k * P + r],
                                            xn[0:r, t % 2, (4 * c + k) * P:(4 * c + k + 1) * P], ident[0:r, 0:r])
                    last.then_inc(norm_tp, 1)
            pe.wait_ge(norm_ev, 2 * (base + NORM_TILES[u]))

        def plain_norm_dve(dve, u, eps, tiles):
            dve.wait_ge(norm_sq, u + 1)
            dve.tensor_scalar(rstd[:, :], ssq[:, :], 1.0 / D, eps, ALU.mult, ALU.add).then_inc(norm_ms, 1)
            dve.wait_ge(norm_sd, u + 1)
            step(dve, dve.reciprocal(rstd[:, :], rstd[:, :]))
            for t in range(tiles):
                dve.scalar_tensor_tensor(h[:, t, :], h[:, t, :], rstd[:, t:t + 1], gain_bc[:, :], ALU.mult, ALU.mult).then_inc(h_upd, 1)

        KV_ROT = {4: 0, 5: 1, 8: 2, 9: 3}

        def kv_pe(pe):
            pe.wait_ge(nsa_in, NSA_CONST)
            pe.transpose(bank[7][:, 0:2 * CMP_KT], pos_rows[:, :], ident[0:2 * CMP_KT, 0:2 * CMP_KT]).then_inc(pos_T, 1)

            def tile(n):
                slot = ring.wait(pe, "kv", n)
                if n >= 4:
                    pe.wait_ge(kv_ev, n - 3)
                if n in (6, 7, 10, 11):
                    for t in range(QT):
                        last = mm_N(pe, bank[n % 4][:, t * P:(t + 1) * P], slot, t)
                else:
                    last = mm_T(pe, bank[n % 4][:, :], slot, xT[:, :, 0:SEQ])
                last.then_inc(kv_mm, 1)
                pe.wait_ge(kv_mm, n + 1)
                pe.sem_inc(slot_free, 1)

            def rotate(n):
                pe.wait_ge(kv_ev, n + 1)
                pe.matmul(bank[4 + n % 2][:, :], rot1[:, :], (rope_a if n % 2 == 0 else rope_b)[:, :],
                          start=True, stop=True).then_inc(kv_rot, 1)

            for n in range(4):
                tile(n)
            for n in (4, 8):
                tile(n)
                tile(n + 1)
                rotate(n)
                tile(n + 2)
                rotate(n + 1)
                tile(n + 3)
            pe.wait_ge(kv_k, 4)
            for c in range(2):
                for k in range(CMP_KT):
                    w = ring.wait(pe, "cmp", c * 4 + k // 4).rearrange("p (k n) -> p k n", n=CMP_HID)
                    if k == 0:
                        pe.wait_ge(cmp_blk, c + 1)
                    for e in range(2):
                        last = pe.matmul(bank[4 + 2 * c + e][:, 0:GROUPS * N_CMP], w[:, k % 4, e * P:(e + 1) * P], blocks[:, c, k, :],
                                         start=(k == 0), stop=(k == CMP_KT - 1))
                    if k == CMP_KT - 1:
                        last.then_inc(cmp_mm, 1)
                        pe.wait_ge(cmp_mm, c + 1)
                        pe.sem_inc(slot_free, 1)
                    elif k % 4 == 3:
                        last.then_inc(slot_free, 1)
            pe.wait_ge(cmp_hh, 2)
            for half in range(2):
                for e in range(2):
                    pe.matmul(bank[0][HD * half:HD * half + HD, 0:GROUPS * N_CMP], cmp_w2[:, 0, e, :], cmp_h[:, 0, e, :],
                              start=(e == 0), stop=(e == 1))
            for g in range(GROUPS):
                for e in range(2):
                    last = pe.matmul(bank[1][0:N_CMP, g * HD:(g + 1) * HD], cmp_h[:, 1, e, g * N_CMP:(g + 1) * N_CMP],
                                     cmp_w2[:, 1, e, :], start=(e == 0), stop=(e == 1))
            last.then_inc(cmp_kv, 1)

        def kv_dve(dve):
            dve.wait_ge(nsa_in, NSA_CONST)
            dve.tensor_copy(future_neg_bf[:, :], future_neg[:, :])
            dve.wait_ge(pos_T, 1)
            step(dve, dve.tensor_copy(pos_off[:, :], bank[7][:, 0:2 * CMP_KT]))
            for n in range(4):
                c, gp = n // 2, n % 2
                dve.wait_ge(kv_mm, n + 1)
                for gi in range(2):
                    src = bank[n % 4][HD * gi:HD * gi + HD, :]
                    dve.tensor_copy(kv_pairs[0:HD, c, 2 * gp + gi, :], src)
                    last = dve.tensor_copy(kv_pairs[HD:P, c, 2 * gp + gi, 0:SEQ - 1], src[:, 1:SEQ])
                last.then_inc(kv_ev, 1)
            def take_blocks(c, k0, k1):
                dve.wait_ge(kv_ev, 2 * c + 2)
                for k in range(k0, k1):
                    last = dve.tensor_scalar(blocks[:, c, k, :].rearrange("p (g n) -> p g n", g=GROUPS),
                                             kv_pairs[:, c, :, bass.ds(2 * k, N_CMP, CMP_STRIDE)],
                                             pos_off[:, c * CMP_KT + k:c * CMP_KT + k + 1], None, ALU.add)
                if k1 == CMP_KT:
                    last.then_inc(cmp_blk, 1)

            for br, n0 in ((0, 4), (1, 8)):
                for n in (n0, n0 + 1):
                    dve.wait_ge(kv_mm, n + 1)
                    raw = (rope_a if n % 2 == 0 else rope_b)
                    dve.tensor_copy(raw[:, :], bank[n % 4][:, :]).then_inc(kv_ev, 1)
                for n in (n0, n0 + 1):
                    raw = (rope_a if n % 2 == 0 else rope_b)
                    dve.wait_ge(kv_rot, KV_ROT[n] + 1)
                    dve_t.inc(dve.tensor_tensor(q_raw[:, 0, :], raw[:, :], cos1[:, :], ALU.mult))
                    step(dve, dve.tensor_tensor(q_raw[:, 1, :], bank[4 + n % 2][:, :], sin1[:, :], ALU.mult))
                    for gi in range(2):
                        r = slice(HD * gi, HD * gi + HD)
                        for half in range(2):
                            last = dve.tensor_tensor(k_all[HD * half:HD * half + HD, br, 2 * (n - n0) + gi, :],
                                                     q_raw[r, 0, :], q_raw[r, 1, :], ALU.add)
                    last.then_inc(kv_k, 1)
                    dve.wait_ge(kv_k, KV_ROT[n] + 1)
                    dve.wait_ge(kv_mm, n + 3)
                    dve.tensor_copy(v_all[:, br, :, 2 * (n - n0):2 * (n - n0) + 2, :],
                                    bank[(n + 2) % 4][:, :].rearrange("p (t g d) -> p t g d", t=QT, g=2)).then_inc(kv_ev, 1)
                take_blocks(br, 0, CMP_KT)
            for c in range(2):
                dve.wait_ge(cmp_mm, c + 1)
                for e in range(2):
                    last = dve.tensor_copy(cmp_x[:, e, :], bank[4 + 2 * c + e][:, 0:GROUPS * N_CMP])
                step(dve, last)
                step(dve, dve.tensor_tensor(cmp_u[:, :, :], cmp_x[:, :, :], cmp_x[:, :, :], ALU.mult))
                step(dve, dve.tensor_scalar(cmp_u[:, :, :], cmp_u[:, :, :], GELU_C, 1.0, ALU.mult, ALU.add))
                dve.tensor_tensor(cmp_u[:, :, :], cmp_u[:, :, :], cmp_x[:, :, :], ALU.mult).then_inc(cmp_uu, 1)
                dve.wait_ge(cmp_ee, c + 1)
                step(dve, dve.tensor_scalar(cmp_u[:, :, :], cmp_u[:, :, :], 0.5, 0.5, ALU.mult, ALU.add))
                dve.tensor_tensor(cmp_h[:, c, :, :], cmp_u[:, :, :], cmp_x[:, :, :], ALU.mult).then_inc(cmp_hh, 1)
                dve.wait_ge(cmp_hh, c + 1)
            dve.wait_ge(cmp_kv, 1)
            dve.tensor_copy(k_cmp[:, :, :].rearrange("p g n -> p (g n)"), bank[0][:, 0:GROUPS * N_CMP])
            dve.tensor_copy(v_cmp[:, :, :].rearrange("p g d -> p (g d)"), bank[1][0:N_CMP, 0:GROUPS * HD]).then_inc(cmp_out, 1)

        def kv_act(act):
            for c in range(2):
                act.wait_ge(cmp_uu, c + 1)
                act.activation(cmp_u[:, :, :], cmp_u[:, :, :], ACT.Tanh, scale=GELU_K).then_inc(cmp_ee, 1)

        def gates_pe(pe):
            for t in range(QT):
                for k in range(KT):
                    last = pe.matmul(bank[4][:, t * N_GATES:(t + 1) * N_GATES], xT[:, k, t * P:(t + 1) * P], gate_w[:, k, :],
                                     start=(k == 0), stop=(k == KT - 1))
            last.then_inc(gate_mm, 1)

        def gates_dve(dve):
            dve.wait_ge(gate_mm, 1)
            dve.tensor_tensor(gates[:, :, :], bank[4][:, 0:QT * N_GATES].rearrange("p (t n) -> p t n", t=QT),
                              gate_b[:, :].unsqueeze(1).broadcast_to([P, QT, N_GATES]), ALU.add).then_inc(gate_x, 1)
            dve.wait_ge(gate_in, 1)

        def gates_act(act):
            act.wait_ge(gate_x, 1)
            act.activation(gates[:, :, :], gates[:, :, :], ACT.Sigmoid).then_inc(gate_in, 1)

        def unit(n):
            head, br = n // BRANCHES, n % BRANCHES
            return head // 2, slice(HD * (head % 2), HD * (head % 2) + HD), br

        PIECES = ((3,), (2, 0), (1,))
        PER_HEAD = 1 + 2 * len(PIECES)

        def piece(n, k):
            head, br = n // BRANCHES, n % BRANCHES
            return head * PER_HEAD + (3 * br - 2 + k if br else 0)

        def piece_before(n, k):
            head, br = n // BRANCHES, n % BRANCHES
            return piece(n, 0) + (-1, (-4, -3, -1)[k], k - 3)[br]

        PER_GROUP = 4 * PER_HEAD

        def pieces(br):
            return PIECES if br else (range(QT),)

        def score_bank(i, br):
            if br == 0:
                return bank[2][:, 256 + 32 * i:256 + 32 * i + N_CMP]
            b, at = SCORE_AT[i]
            return bank[b][:, at:at + P * (i + 1)]

        def nsa_pe(pe, g):
            def project(u):
                slot = ring.wait(pe, "nsa", 4 * u, g)
                mm_T(pe, bank[7 - u][:, :], slot, xT[:, :, 0:SEQ]).then_inc(ns_q, 1)
                pe.wait_ge(ns_q, g * 4 + u + 1)
                pe.sem_inc(slot_free, 4)

            def rotate(u):
                pe.wait_ge(ns_qe, g * 4 + u + 1)
                pe.matmul(bank[7 - u][:, :], rot1[:, :], q_raw[:, u, :], start=True, stop=True).then_inc(ns_q, 1)

            def scores(n):
                u, r, br = unit(n)
                if n == 0:
                    pe.wait_ge(ns_grp, g + 1)
                if n in (1, 7):
                    pe.wait_ge(ns_qe, g * 4 + 3 + u)
                for k, tiles in enumerate(pieces(br)):
                    pe.wait_ge(ns_p, g * PER_GROUP + piece_before(n, k) + 4)
                    for i in tiles:
                        q, dst = slice(i * P, (i + 1) * P), score_bank(i, br)
                        if br == 0:
                            last = pe.matmul(dst, q_raw[r, u, q], kc_grp[r, :], start=True, stop=True)
                            continue
                        pe.matmul(dst, q_rot[r, u, q], k_grp[r, br - 1, 0:P * (i + 1)], start=True, stop=False, skip_group_check=True)
                        last = pe.matmul(dst[:, i * P:(i + 1) * P], ident_bf[:, :], future_neg_bf[:, :], start=False, stop=True,
                                         skip_group_check=True)
                    last.then_inc(ns_s, 1)

            def transposes(n):
                _, _, br = unit(n)
                pe.wait_ge(ns_f, g * UNITS + n + 1)
                pe.wait_ge(ns_t, g * UNITS + n + 1)
                if br == 0:
                    for i in range(QT):
                        last = pe.transpose(bank[3][0:N_CMP, i * P:(i + 1) * P], probs[:, n % 2, i * N_CMP:(i + 1) * N_CMP], ident[:, :])
                else:
                    for j in range(QT):
                        b, at, _ = PT_AT[j]
                        for i in range(j, QT):
                            last = pe.transpose(bank[b][:, at + (i - j) * P:at + (i - j + 1) * P],
                                                probs[:, n % 2, PROB_AT[i] + j * P:PROB_AT[i] + (j + 1) * P], ident[:, :])
                last.then_inc(ns_tt, 1)

            def weigh(n):
                u, r, br = unit(n)
                pe.wait_ge(ns_t, g * UNITS + n + 2)
                if br == 0:
                    pe.wait_ge(ns_oe, g * 4 + n // BRANCHES + 1)
                    pe.matmul(bank[6][0:HD, :], vc_grp[:, :], probs_T[0:N_CMP, n % 2, 0:SEQ], start=True, stop=False, skip_group_check=True)
                    return
                for j in range(QT):
                    at = PT_AT[j][2]
                    last = pe.matmul(bank[6][0:HD, j * P:SEQ], v_grp[:, br - 1, j, :], probs_T[:, n % 2, at:at + CAUSAL_COLS[j]],
                                     start=False, stop=(br == 2 and j == QT - 1), skip_group_check=True)
                if br == 2:
                    last.then_inc(ns_o, 1)

            pe.wait_ge(ns_oe, g * 4 + 1)
            project(0)
            project(1)
            rotate(0)
            rotate(1)
            scores(0)
            for n in range(UNITS):
                if n + 1 < UNITS:
                    scores(n + 1)
                if n:
                    weigh(n - 1)
                transposes(n)
            weigh(UNITS - 1)

        def nsa_act(act, g):
            def exps(n):
                _, _, br = unit(n)
                for k, tiles in enumerate(pieces(br)):
                    act.wait_ge(ns_m, g * PER_GROUP + piece(n, k) + 1)
                    if br == 0:
                        act.activation(probs[:, n % 2, 0:QT * N_CMP], probs[:, n % 2, 0:QT * N_CMP], ACT.Exp).then_inc(ns_p, 1)
                        return
                    for i in tiles:
                        last = act.activation(probs[:, n % 2, PROB_AT[i]:PROB_AT[i] + P * (i + 1)], score_bank(i, br), ACT.Exp,
                                              bias=top[:, n % 2, i:i + 1], accum_out=rsum[:, n % 2, i:i + 1])
                    last.then_inc(ns_p, 1)

            def take(n):
                _, _, br = unit(n)
                act.wait_ge(ns_tt, g * UNITS + n + 1)
                if br == 0:
                    act.activation(probs_T[0:N_CMP, n % 2, 0:SEQ], bank[3][0:N_CMP, :], ACT.Copy).then_inc(ns_t, 1)
                    return
                act.activation(probs_T[:, n % 2, 0:SEQ], bank[3][:, :], ACT.Copy)
                act.activation(probs_T[:, n % 2, SEQ:2 * SEQ], bank[4][:, :], ACT.Copy)
                act.activation(probs_T[:, n % 2, 2 * SEQ:CAUSAL], bank[5][:, 0:256], ACT.Copy).then_inc(ns_t, 1)

            exps(0)
            for n in range(UNITS):
                if n + 1 < UNITS:
                    exps(n + 1)
                take(n)

        def nsa_dve(dve, g):
            def one(ap):
                return ap.rearrange("p a n -> p (a n)")

            for br in range(2):
                dve.tensor_copy(k_grp[:, br, :], one(k_all[:, br, bass.ds(g, 1), :]))
                dve.tensor_copy(v_grp[:, br, :, :], v_all[:, br, :, bass.ds(g, 1), :].rearrange("p t a d -> p t (a d)"))
            dve.tensor_copy(kc_grp[:, :], one(k_cmp[:, bass.ds(g, 1), :]))
            dve.tensor_copy(vc_grp[:, :], one(v_cmp[:, bass.ds(g, 1), :])).then_inc(ns_grp, 1)
            for u in range(2):
                dve.wait_ge(ns_q, g * 4 + u + 1)
                dve.tensor_scalar(q_raw[:, u, :], bank[7 - u][:, :], HD ** -0.5, None, ALU.mult).then_inc(ns_qe, 1)
            for u in range(2):
                dve.wait_ge(ns_q, g * 4 + 3 + u)
                dve_t.inc(dve.tensor_tensor(rope_a[:, :], q_raw[:, u, :], cos1[:, :], ALU.mult))
                step(dve, dve.tensor_tensor(rope_b[:, :], bank[7 - u][:, :], sin1[:, :], ALU.mult))
                dve.tensor_tensor(q_rot[:, u, :], rope_a[:, :], rope_b[:, :], ALU.add).then_inc(ns_qe, 1)
                dve.wait_ge(ns_qe, g * 4 + 3 + u)
            def cmp_probs(n):
                return probs[:, n % 2, 0:QT * N_CMP].rearrange("p (t n) -> p t n", t=QT)

            def maxima(n):
                br, p = n % BRANCHES, cmp_probs(n)
                for k, tiles in enumerate(pieces(br)):
                    dve.wait_ge(ns_s, g * PER_GROUP + piece(n, k) + 1)
                    if br == 0:
                        s = bank[2][:, 256:384].rearrange("p (t n) -> p t n", t=QT)[:, :, 0:N_CMP]
                        step(dve, dve.tensor_tensor(p, s, cmp_neg[:, :, :], ALU.add))
                        step(dve, dve.reduce_max(top[:, n % 2, :], p, AX.X))
                        dve.tensor_tensor(p, p, top[:, n % 2, :].unsqueeze(2).broadcast_to([P, QT, N_CMP]), ALU.subtract).then_inc(ns_m, 1)
                        return
                    for i in tiles:
                        last = dve.reduce_max(top[:, n % 2, i:i + 1], score_bank(i, br), AX.X, negate=True)
                    last.then_inc(ns_m, 1)

            maxima(0)
            for n in range(UNITS):
                head, br = n // BRANCHES, n % BRANCHES
                p = cmp_probs(n)
                if n + 1 < UNITS:
                    maxima(n + 1)
                dve.wait_ge(ns_p, g * PER_GROUP + piece(n, len(pieces(br)) - 1) + 4)
                sums = rsum[:, n % 2, :]
                if br == 0:
                    step(dve, dve.reduce_sum(sums, p, AX.X))
                step(dve, dve.reciprocal(factor[:, n % 2, :], sums))
                gate = gates[:, :, bass.ds(g * 4 + (br * 16 + head), 1)].rearrange("p t a -> p (t a)")
                step(dve, dve.tensor_tensor(factor[:, n % 2, :], factor[:, n % 2, :], gate, ALU.mult))
                if br == 0:
                    step(dve, dve.tensor_tensor(factor[:, n % 2, :], factor[:, n % 2, :], cmp_any[:, :], ALU.mult))
                    dve.tensor_tensor(p, p, factor[:, n % 2, :].unsqueeze(2).broadcast_to([P, QT, N_CMP]), ALU.mult).then_inc(ns_f, 1)
                else:
                    for i in range(QT):
                        rows = probs[:, n % 2, PROB_AT[i]:PROB_AT[i] + P * (i + 1)]
                        last = dve.tensor_scalar(rows, rows, factor[:, n % 2, i:i + 1], None, ALU.mult)
                    last.then_inc(ns_f, 1)
                if br == 0 and head:
                    nsa_out(dve, g, head - 1)
            nsa_out(dve, g, 3)

        def nsa_out(dve, g, head):
            dve.wait_ge(ns_o, g * 4 + head + 1)
            r = slice(HD * (head % 2), HD * (head % 2) + HD)
            dve.tensor_copy(oT[r, bass.ds(g * 2 + head // 2, 1), 0:SEQ].rearrange("p a n -> p (a n)"), bank[6][0:HD, :]).then_inc(ns_oe, 1)

        def two(b, r=P):
            return psum[0:r, b:b + 2, 0:CH2]

        def halves(ap):
            return ap.rearrange("p (c n) -> p c n", c=2)

        def half(c):
            return slice(c * CH2, (c + 1) * CH2)

        def project2(pe, name, j, turn, made, taken, no):
            slot = ring.wait(pe, name, j, turn)
            for c in range(2):
                pe.wait_ge(taken, no + c + 1)
                mm_T(pe, bank[7][:, 0:CH2], slot, xT[:, :, half(c)]).then_inc(made, 1)
                if c:
                    pe.wait_ge(made, no + 2)
                    pe.sem_inc(slot_free, 1)
                yield

        def project_v2(pe, name, j, turn, made, taken, no, slots):
            slot = ring.wait(pe, name, j, turn)
            pe.wait_ge(taken, no + 1)
            for t in range(QT):
                last = mm_N(pe, bank[7][:, t * P:(t + 1) * P], slot, t)
            last.then_inc(made, 1)
            yield
            pe.wait_ge(taken, no + 2)
            mm_N(pe, bank[7][0:META, 0:P], slot, QT, META).then_inc(made, 1)
            pe.wait_ge(made, no + 2)
            pe.sem_inc(slot_free, slots)
            yield

        def take2(dve, dst, c, taken):
            dve.tensor_copy(dst[:, half(c)], bank[7][:, 0:CH2]).then_inc(taken, 1)

        def take_v2(dve, u, c, taken):
            if c == 0:
                dve.tensor_copy(v2[:, u, 0:QT, :], bank[7][:, :].rearrange("p (t n) -> p t n", n=P)).then_inc(taken, 1)
            else:
                dve.tensor_copy(v2[0:META, u, QT, :], bank[7][0:META, 0:P]).then_inc(taken, 1)

        def transposes2(pe, src):
            for j in range(QT):
                pe.transpose(bank[4][:, j * P:(j + 1) * P], src[:, j * P:(j + 1) * P], ident[:, :])
            return pe.transpose(bank[5][0:META, 0:P], src[:, SEQ:L2], ident[:, :])

        def take_T2(act, n, r):
            act.activation(w_T[:, n % 2, 0:QT, 0:r], bank[4][:, :].rearrange("p (j q) -> p j q", q=P)[:, :, 0:r], ACT.Copy)
            return act.activation(w_T[0:META, n % 2, QT, 0:r], bank[5][0:META, 0:r], ACT.Copy)

        def weigh2(pe, n, t, u):
            r = rows_of(t)
            dst = bank[6][:, t * P:(t + 1) * P] if t < QT else bank[5][:, O_TAIL:O_TAIL + META]
            for j in range(T2):
                k = rows_of(j)
                last = pe.matmul(dst, v2[0:k, u, j, :], w_T[0:k, n % 2, j, 0:r], start=(j == 0), stop=(j == T2 - 1))
            return last

        def df_parts(pe, name, j, turn, hd):
            for n in range(2):
                yield from project2(pe, name, j + n, turn, df_pj, df_pe, hd * 6 + 2 * n)
            yield from project_v2(pe, name, j + 2, turn, df_pj, df_pe, hd * 6 + 4, 2)

        def df_pe_head(pe, hd, u, parts):
            parts = iter(parts)

            def scores(t):
                r = rows_of(t)
                if t < QT:
                    pe.wait_ge(df_p, hd * T2 + t + 1)
                if t == 0:
                    pe.wait_ge(df_v, hd + 1)
                for m in range(2):
                    f = slice(HD * m, HD * m + HD)
                    for c in range(2):
                        dst, k = bank[2 * m + c][0:r, 0:CH2], slice(c * CH2, (c + 1) * CH2)
                        last = pe.matmul(dst, q2[f, u, t * P:t * P + r], k2[f, u, k], start=True, stop=(t == QT), skip_group_check=True)
                        if t < QT:
                            last = pe.matmul(dst, slope[:, u, :], dist[:, t, k], start=False, stop=True, skip_group_check=True)
                last.then_inc(df_s, 1)

            pe.wait_ge(df_pe, hd * 6 + 7)
            scores(0)
            for t in range(T2):
                if t < QT - 1:
                    scores(t + 1)
                if t:
                    df_weigh(pe, hd, u, t - 1)
                if t == QT - 1:
                    scores(QT)
                next(parts, None)
                pe.wait_ge(df_f, hd * T2 + t + 1)
                pe.wait_ge(df_t, hd * T2 + t + 1)
                transposes2(pe, prob_a[:, t % 2, :]).then_inc(df_tt, 1)
            df_weigh(pe, hd, u, QT)
            for _ in parts:
                pass
            pe.wait_ge(df_sq, hd + 1)
            pe.wait_ge(df_p, hd * T2 + T2 + 1)
            for c in range(2):
                last = pe.matmul(bank[c][:, 0:CH2], mean_w[:, :], sq2[:, c * CH2:(c + 1) * CH2], start=True, stop=True)
            last.then_inc(df_ms, 1)

        def df_weigh(pe, hd, u, t):
            pe.wait_ge(df_t, hd * T2 + t + 2)
            if t == 0:
                pe.wait_ge(df_oe, hd + 1)
            last = weigh2(pe, t, t, u)
            if t == QT:
                last.then_inc(df_o, 1)

        def df_act_head(act, hd):
            def exps(t):
                r = rows_of(t)
                act.wait_ge(df_m, hd * T2 + t + 1)
                for m, dst in enumerate((prob_a, prob_b)):
                    last = act.activation(halves(dst[0:r, t % 2, :]), two(2 * m, r), ACT.Exp, bias=top2[0:r, m:m + 1],
                                          scale=HD ** -0.5, accum_out=rsum2[0:r, m:m + 1])
                last.then_inc(df_p, 1)

            exps(0)
            for t in range(T2):
                if t < QT:
                    exps(t + 1)
                act.wait_ge(df_tt, hd * T2 + t + 1)
                take_T2(act, t, rows_of(t)).then_inc(df_t, 1)
            act.wait_ge(df_o, hd + 1)
            act.activation(sq2[:, 0:SEQ], bank[6][:, :], ACT.Square)
            act.activation(sq2[:, SEQ:L2], bank[5][:, O_TAIL:O_TAIL + META], ACT.Square).then_inc(df_sq, 1)
            act.wait_ge(df_v, hd + 2)
            act.activation(var2[:, :], var2[:, :], ACT.Sqrt).then_inc(df_sd, 1)

        def df_dve_head(dve, hd, u, take):
            def maxima(t):
                r = rows_of(t)
                dve.wait_ge(df_s, hd * T2 + t + 1)
                for m in range(2):
                    last = dve.reduce_max(top2[0:r, m:m + 1], two(2 * m, r), AX.XY)
                step(dve, last)
                dve.tensor_scalar(top2[0:r, :], top2[0:r, :], -HD ** -0.5, None, ALU.mult).then_inc(df_m, 1)

            maxima(0)
            for t in range(T2):
                r = rows_of(t)
                dve.wait_ge(df_p, hd * T2 + t + 2)
                step(dve, dve.reciprocal(rinv2[0:r, :], rsum2[0:r, :]))
                dve_t.inc(dve.tensor_tensor(rinv2[0:r, 1:2], rinv2[0:r, 1:2], neg_lam[0:r, :], ALU.mult))
                a, b = prob_a[0:r, t % 2, :], prob_b[0:r, t % 2, :]
                step(dve, dve.tensor_scalar(a, a, rinv2[0:r, 0:1], None, ALU.mult))
                dve.scalar_tensor_tensor(a, b, rinv2[0:r, 1:2], a, ALU.mult, ALU.add).then_inc(df_f, 1)
                if t < QT:
                    maxima(t + 1)
                if take:
                    df_take(dve, t, hd + 1, 1 - u)
            if take:
                df_take(dve, T2, hd + 1, 1 - u)
            step(dve, dve.tensor_scalar(slope[:, u, :], slope[:, u, :], 0.25, None, ALU.mult))
            dve.wait_ge(df_ms, hd + 1)
            dve.tensor_scalar(halves(var2[:, :]), two(0), EPS2, None, ALU.add).then_inc(df_v, 1)
            dve.wait_ge(df_sd, hd + 1)
            step(dve, dve.reciprocal(var2[:, :], var2[:, :]))
            o = oT[:, bass.ds(hd, 1), :].rearrange("p a n -> p (a n)")
            dve.scalar_tensor_tensor(o[:, 0:SEQ], bank[6][:, :], head_gain[:, 0:1], var2[:, 0:SEQ], ALU.mult, ALU.mult)
            dve.scalar_tensor_tensor(o[:, SEQ:L2], bank[5][:, O_TAIL:O_TAIL + META], head_gain[:, 0:1], var2[:, SEQ:L2],
                                     ALU.mult, ALU.mult).then_inc(df_oe, 1)

        def ready2_dve(dve):
            dve.wait_ge(b2_T, 1)
            dve.tensor_scalar(head_gain[:, 0:1], bank[7][:, 0:1], 1.0 - LAM_INIT, None, ALU.mult)
            dve.tensor_copy(head_gain[:, 1:3], bank[7][:, 1:3])
            dve.memset(mean_w[:, :], 1.0 / P)
            for u in range(2):
                dve_t.inc(dve.tensor_scalar(slope[:, u, :], ident[:, :], -(HD ** 0.5) * 0.5 ** (u + 1), None, ALU.mult))
            for m in range(2):
                step(dve, dve.tensor_tensor(lam_prod[:, :], lam_in[:, 2 * m, :], lam_in[:, 2 * m + 1, :], ALU.mult))
                last = dve.reduce_sum(lam[:, m:m + 1], lam_prod[:, :], AX.X)
                if m:
                    last.then_inc(lam_d, 1)
                else:
                    step(dve, last)
            dve.wait_ge(lam_e, 1)
            step(dve, dve.tensor_tensor(neg_lam[:, :], lam[:, 1:2], lam[:, 0:1], ALU.subtract))
            dve.tensor_scalar(neg_lam[:, :], neg_lam[:, :], -LAM_INIT, None, ALU.add).then_inc(b2_ready, 1)
            dve.wait_ge(b2_ready, 1)

        def df_take(dve, n, hd, u):
            dve.wait_ge(df_pj, hd * 6 + n + 1)
            if n >= 4:
                take_v2(dve, u, n % 2, df_pe)
            else:
                take2(dve, (q2, k2)[n // 2][:, u, :], n % 2, df_pe)

        def branch_pe(pe, b):
            with loop(pe, 2) as turn:
                for n in range(4):
                    i = turn * 4 + (b * KT + n)
                    for m, src in enumerate((xT, oT)):
                        slot = ring.wait(pe, f"br{b}", 2 * n + m, turn)
                        if m == 0:
                            pe.wait_ge(br_m, i + 1)
                        for c in range(2):
                            last = mm_T(pe, bank[4 * (n % 2) + 2 * m + c][:, 0:CH2], slot, src[:, :, c * CH2:(c + 1) * CH2])
                        last.then_inc(br_mm, 1)
                        pe.wait_ge(br_mm, i * 2 + m + 1)
                        pe.sem_inc(slot_free, 1)

        def branch_act(act, b):
            with loop(act, 2) as turn:
                for n in range(4):
                    i = turn * 4 + (b * KT + n)
                    act.wait_ge(br_mm, i * 2 + 1)
                    act.wait_ge(br_m, i + 1)
                    act.activation(halves(sig[:, n % 2, :]), two(4 * (n % 2)), ACT.Sigmoid).then_inc(br_sig, 1)

        def branch_dve(dve, b, per):
            with loop(dve, 2, tallies=[(dve_t, per)]) as turn:
                for n in range(4):
                    i = turn * 4 + (b * KT + n)
                    dve.wait_ge(br_mm, i * 2 + 2)
                    dve.wait_ge(br_sig, i + 1)
                    m = merged[:, bass.ds(turn * 4 + n, 1), :].rearrange("p a n -> p (a n)")
                    if b == 0:
                        dve.tensor_tensor(halves(m), halves(sig[:, n % 2, :]), two(4 * (n % 2) + 2), ALU.mult).then_inc(br_m, 1)
                    else:
                        gated = sig[:, n % 2, :]
                        step(dve, dve.tensor_tensor(halves(gated), halves(gated), two(4 * (n % 2) + 2), ALU.mult))
                        dve.tensor_tensor(m, m, gated, ALU.add).then_inc(br_m, 1)

        def use_no(tile, what):
            if tile == 0:
                return {"proj": 0, "mean": 2, "value": 4, "rot": 6}[what]
            return 8 + 6 * (tile - 1) + {"proj": 0, "mean": 2, "rot": 4}[what]

        UN = Q_PER_KV * T2

        def gq_pe_turn(pe, kv):
            def project(tile):
                for _ in project2(pe, "gqa", tile + (tile > 0), kv, gq_b, gq_br, kv * USES + use_no(tile, "proj")):
                    pass

            def small(tile, what, weight, src):
                pe.wait_ge(gq_x, kv * 3 * (Q_PER_KV + 1) + tile * 3 + (1 if what == "mean" else 2))
                for c in range(2):
                    pe.wait_ge(gq_br, kv * USES + use_no(tile, what) + c + 1)
                    pe.matmul(bank[7][:, 0:CH2], weight[:, :], src[:, half(c)], start=True, stop=True).then_inc(gq_b, 1)

            def mean(tile):
                small(tile, "mean", mean_w, sq2)

            def rotate(tile):
                small(tile, "rot", rot2, norm2)

            def prepare(tile):
                project(tile)
                yield
                mean(tile)
                yield
                yield
                rotate(tile)
                yield

            def scores(n):
                j, t = n // T2, n % T2
                r = rows_of(t)
                pe.wait_ge(gq_p, kv * UN + n + 1)
                if t == 0:
                    pe.wait_ge(gq_x, kv * 3 * (Q_PER_KV + 1) + (j + 1) * 3 + 3)
                for c in range(2):
                    last = pe.matmul(bank[2 * (n % 2) + c][0:r, 0:CH2], q2[:, j % 2, t * P:t * P + r], k2[:, 0, c * CH2:(c + 1) * CH2],
                                     start=True, stop=True)
                last.then_inc(gq_s, 1)

            def weigh(n):
                j, t = n // T2, n % T2
                pe.wait_ge(gq_t, kv * UN + n + 2)
                if t == 0:
                    pe.wait_ge(gq_oe, kv * Q_PER_KV + j + 1)
                last = weigh2(pe, n, t, 0)
                if t == QT:
                    last.then_inc(gq_o, 1)

            project(0)
            mean(0)
            for _ in project_v2(pe, "gqa", 1, kv, gq_b, gq_br, kv * USES + use_no(0, "value"), 1):
                pass
            rotate(0)
            for _ in prepare(1):
                pass
            scores(0)
            parts = iter(())
            for n in range(UN):
                j, t = n // T2, n % T2
                if t == 0:
                    parts = prepare(j + 2) if j + 1 < Q_PER_KV else iter(())
                if n + 1 < UN:
                    scores(n + 1)
                if n:
                    weigh(n - 1)
                next(parts, None)
                pe.wait_ge(gq_f, kv * UN + n + 1)
                pe.wait_ge(gq_t, kv * UN + n + 1)
                if t == 0:
                    pe.wait_ge(gq_oe, kv * Q_PER_KV + j + 1)
                transposes2(pe, prob_a[:, n % 2, :]).then_inc(gq_tt, 1)
            weigh(UN - 1)
            pe.sem_inc(slot_free, 2)

        def gq_act_turn(act, kv):
            def root(tile):
                act.wait_ge(gq_br, kv * USES + use_no(tile, "mean") + 3)
                act.activation(var2[:, :], var2[:, :], ACT.Sqrt).then_inc(gq_sd, 1)

            def exps(n):
                r = rows_of(n % T2)
                act.wait_ge(gq_m, kv * UN + n + 1)
                act.activation(halves(prob_a[0:r, n % 2, :]), two(2 * (n % 2), r), ACT.Exp, bias=top2[0:r, n % 2:n % 2 + 1],
                               scale=P ** -0.5, accum_out=rsum2[0:r, n % 2:n % 2 + 1]).then_inc(gq_p, 1)

            root(0)
            root(1)
            exps(0)
            for n in range(UN):
                j, t = n // T2, n % T2
                if n + 1 < UN:
                    exps(n + 1)
                act.wait_ge(gq_tt, kv * UN + n + 1)
                take_T2(act, n, rows_of(t)).then_inc(gq_t, 1)
                if t == 1 and j + 1 < Q_PER_KV:
                    root(j + 2)

        def gq_dve_turn(dve, kv):
            def piece(tile, what, c):
                dve.wait_ge(gq_b, kv * USES + use_no(tile, what) + c + 1)

            def x_done(k, tile):
                dve.wait_ge(gq_x, kv * 3 * (Q_PER_KV + 1) + tile * 3 + k)

            def square(tile, c):
                piece(tile, "proj", c)
                take2(dve, raw2, c, gq_br)
                if c:
                    dve.wait_ge(gq_br, kv * USES + use_no(tile, "proj") + 3)
                    dve.tensor_tensor(sq2[:, :], raw2[:, :], raw2[:, :], ALU.mult).then_inc(gq_x, 1)

            def variance(tile, c):
                piece(tile, "mean", c)
                dve.tensor_scalar(var2[:, half(c)], bank[7][:, 0:CH2], EPS2, None, ALU.add).then_inc(gq_br, 1)

            def normalise(tile):
                dve.wait_ge(gq_sd, kv * (Q_PER_KV + 1) + tile + 1)
                step(dve, dve.reciprocal(var2[:, :], var2[:, :]))
                g = 2 if tile == 0 else 1
                dve.scalar_tensor_tensor(norm2[:, :], raw2[:, :], head_gain[:, g:g + 1], var2[:, :], ALU.mult, ALU.mult).then_inc(gq_x, 1)
                x_done(2, tile)
                dve_t.inc(dve.tensor_tensor(raw2[:, :], norm2[:, :], cos2[:, :], ALU.mult))

            def rotated(tile, c):
                piece(tile, "rot", c)
                dve.tensor_tensor(rope_c[:, half(c)], bank[7][:, 0:CH2], sin2[:, half(c)], ALU.mult).then_inc(gq_br, 1)
                dve.wait_ge(gq_br, kv * USES + use_no(tile, "rot") + c + 2)
                dve.wait_ge(dve_step, dve_t.value())
                dst = k2[:, 0, half(c)] if tile == 0 else q2[:, (tile - 1) % 2, half(c)]
                last = dve.tensor_tensor(dst, raw2[:, half(c)], rope_c[:, half(c)], ALU.add)
                if c:
                    last.then_inc(gq_x, 1)
                    x_done(3, tile)

            for tile in range(2):
                for stage in (square, variance):
                    for c in range(2):
                        stage(tile, c)
                normalise(tile)
                for c in range(2):
                    if tile == 0:
                        piece(0, "value", c)
                        take_v2(dve, 0, c, gq_br)
                for c in range(2):
                    rotated(tile, c)
            def maxima(n):
                r, c = rows_of(n % T2), n % 2
                dve.wait_ge(gq_s, kv * UN + n + 1)
                step(dve, dve.reduce_max(top2[0:r, c:c + 1], two(2 * c, r), AX.XY))
                dve.tensor_scalar(top2[0:r, c:c + 1], top2[0:r, c:c + 1], -P ** -0.5, None, ALU.mult).then_inc(gq_m, 1)

            maxima(0)
            for n in range(UN):
                j, t = n // T2, n % T2
                r, more = rows_of(t), j + 1 < Q_PER_KV
                c = n % 2
                stage = {0: square, 1: variance, 3: rotated}.get(t) if more else None
                if stage:
                    stage(j + 2, 0)
                dve.wait_ge(gq_p, kv * UN + n + 3)
                step(dve, dve.reciprocal(rinv2[0:r, c:c + 1], rsum2[0:r, c:c + 1]))
                a = prob_a[0:r, c, :]
                dve.tensor_scalar(a, a, rinv2[0:r, c:c + 1], None, ALU.mult).then_inc(gq_f, 1)
                if n + 1 < UN:
                    maxima(n + 1)
                if t == 0 and j:
                    gq_out(dve, kv, j - 1)
                if stage:
                    stage(j + 2, 1)
                if more and t == 2:
                    normalise(j + 2)
            gq_out(dve, kv, Q_PER_KV - 1)

        def gq_out(dve, kv, j):
            dve.wait_ge(gq_o, kv * Q_PER_KV + j + 1)
            o = oT[:, bass.ds(kv * Q_PER_KV + j, 1), :].rearrange("p a n -> p (a n)")
            dve.tensor_copy(o[:, 0:SEQ], bank[6][:, :])
            dve.tensor_copy(o[:, SEQ:L2], bank[5][:, O_TAIL:O_TAIL + META]).then_inc(gq_oe, 1)

        def route_pe(pe):
            pe.wait_ge(moe_in, MOE_CONST)
            for t in range(T2):
                r = rows_of(t)
                for k in range(KT):
                    last = pe.matmul(bank[0][0:r, t * EXPERTS:(t + 1) * EXPERTS], xT[:, k, t * P:t * P + r], router_w[:, k, :],
                                     start=(k == 0), stop=(k == KT - 1))
            last.then_inc(rt_l, 1)
            pe.wait_ge(rt_a, 1)
            for t in range(T2):
                r = rows_of(t)
                dst = bank[1][0:EXPERTS, t * P:(t + 1) * P] if t < QT else bank[2][0:EXPERTS, 0:META]
                last = pe.transpose(dst, logits[0:r, t, :], ident[0:r, 0:r])
            last.then_inc(rt_at, 1)
            pe.wait_ge(rt_s, 1)
            for t in range(T2):
                r = rows_of(t)
                at = META + t * P if t < QT else 0
                last = pe.transpose(bank[3][0:r, t * EXPERTS:(t + 1) * EXPERTS], work[:, at:at + r], ident[0:EXPERTS, 0:EXPERTS])
            last.then_inc(rt_st, 1)
            for e in range(EXPERTS):
                pe.wait_ge(rt_oh, e + 1)
                for t in range(T2):
                    r = rows_of(t)
                    last = pe.matmul(bank[4][0:CAP, 2 * e:2 * e + 2], one_hot[0:r, e % 2, t, :], token_aff[0:r, t, e, :],
                                     start=(t == 0), stop=(t == QT))
                last.then_inc(rt_pk, 1)

        def route_act(act):
            act.wait_ge(rt_x, 1)
            act.activation(logits[:, :, :], logits[:, :, :], ACT.Exp).then_inc(rt_e, 1)

        def route_dve(dve):
            dve.wait_ge(moe_in, MOE_CONST)
            dve_t.inc(dve.memset(logits[:, :, :], 0.0))
            dve_t.inc(dve.memset(slot_T[:, :, :], -1.0))
            dve_t.inc(dve.memset(ones_row[:, :], 1.0))
            step(dve, dve.tensor_copy(token_aff[:, :, :, 0], token_no[:, :].unsqueeze(2).broadcast_to([P, T2, EXPERTS])))
            dve.wait_ge(rt_l, 1)
            dve_t.inc(dve.tensor_copy(logits[:, 0:QT, :], bank[0][:, 0:QT * EXPERTS].rearrange("p (t n) -> p t n", n=EXPERTS)))
            step(dve, dve.tensor_copy(logits[0:META, QT, :], bank[0][0:META, QT * EXPERTS:T2 * EXPERTS]))

            def wide(ap):
                return ap.unsqueeze(2).broadcast_to([P, T2, EXPERTS])

            step(dve, dve.reduce_max(lmax[:, :], logits[:, :, :], AX.X))
            dve.tensor_tensor(logits[:, :, :], logits[:, :, :], wide(lmax[:, :]), ALU.subtract).then_inc(rt_x, 1)
            dve.wait_ge(rt_e, 1)
            step(dve, dve.reduce_sum(lmax[:, :], logits[:, :, :], AX.X))
            step(dve, dve.reciprocal(lmax[:, :], lmax[:, :]))
            dve.tensor_tensor(logits[:, :, :], logits[:, :, :], wide(lmax[:, :]), ALU.mult).then_inc(rt_a, 1)
            dve.wait_ge(rt_a, 1)
            dve_t.inc(dve.tensor_copy(token_aff[:, :, :, 1], logits[:, :, :]))
            dve.wait_ge(rt_at, 1)
            dve_t.inc(dve.tensor_copy(aff_T[:, META:L2], bank[1][0:EXPERTS, :]))
            step(dve, dve.tensor_copy(aff_T[:, 0:META], bank[2][0:EXPERTS, 0:META]))
            src = aff_T
            for k in range((CAP - 1) // 8 + 1):
                step(dve, dve.max(best8[:, :], src[:, :]))
                if k < (CAP - 1) // 8:
                    step(dve, dve.match_replace(work[:, :], best8[:, :], src[:, :], -1.0))
                    src = work
            least = best8[:, (CAP - 1) % 8:(CAP - 1) % 8 + 1]
            step(dve, dve.tensor_scalar(above[:, :], aff_T[:, :], least, None, ALU.is_gt))
            dve_t.inc(dve.reduce_sum(n_above[:, 0:1], above[:, :], AX.X))
            step(dve, dve.tensor_scalar(equal[:, :], aff_T[:, :], least, None, ALU.is_equal))
            dve_t.inc(dve.tensor_scalar(n_above[:, 1:2], n_above[:, 0:1], -1.0, float(CAP), ALU.mult, ALU.add))
            step(dve, dve.tensor_tensor_scan(count[:, :], ones_row[:, :], equal[:, :], 0.0, ALU.mult, ALU.add))
            step(dve, dve.scalar_tensor_tensor(equal[:, :], count[:, :], n_above[:, 1:2], equal[:, :], ALU.is_le, ALU.mult))
            step(dve, dve.tensor_tensor(above[:, :], above[:, :], equal[:, :], ALU.add))
            step(dve, dve.tensor_tensor_scan(count[:, :], ones_row[:, :], above[:, :], 0.0, ALU.mult, ALU.add))
            step(dve, dve.tensor_tensor(work[:, :], count[:, :], above[:, :], ALU.mult))
            dve.tensor_scalar(work[:, :], work[:, :], -1.0, None, ALU.add).then_inc(rt_s, 1)
            dve.wait_ge(rt_st, 1)
            dve_t.inc(dve.tensor_copy(slot_T[:, 0:QT, :], bank[3][:, 0:QT * EXPERTS].rearrange("p (t n) -> p t n", n=EXPERTS)))
            step(dve, dve.tensor_copy(slot_T[0:META, QT, :], bank[3][0:META, QT * EXPERTS:T2 * EXPERTS]))
            for e in range(EXPERTS):
                if e >= 2:
                    dve.wait_ge(rt_pk, e - 1)
                dve.tensor_tensor(one_hot[:, e % 2, :, :], slot_no[:, :].unsqueeze(1).broadcast_to([P, T2, CAP]),
                                  slot_T[:, :, e:e + 1].broadcast_to([P, T2, CAP]), ALU.is_equal).then_inc(rt_oh, 1)
            dve.wait_ge(rt_pk, EXPERTS)
            step(dve, dve.tensor_copy(pick[:, :, :].rearrange("p e c -> p (e c)"), bank[4][0:CAP, 0:2 * EXPERTS]))
            dve.tensor_copy(pick_no[:, :], pick[:, :, 0]).then_inc(ex_no, 1)

        def tokens_dve(dve):
            dve.wait_ge(gain_in, 32)
            for t in range(T2):
                r = rows_of(t)
                if t >= 2:
                    dve.wait_ge(u_out[t % 2], 16 * (t // 2))
                dve.scalar_tensor_tensor(u_rows[0:r, t % 2, :], h[0:r, t, :], rstd[0:r, t:t + 1], gain_bc[0:r, :],
                                         ALU.mult, ALU.mult).then_inc(u_row, 1)

        def ex_up_pe(pe, name, j, turn, i, u):
            e = i * 2 + u
            pe.wait_ge(ex_x[u], i * 16 + 16)
            pe.wait_ge(ex_xe, e + 1)
            for k in range(KT):
                last = pe.transpose(bank[k // 4][:, (k % 4) * CAP:(k % 4 + 1) * CAP], xs[:, u, k * P:(k + 1) * P], ident[0:CAP, 0:CAP])
            last.then_inc(ex_xt, 1)
            pe.wait_ge(ex_xe, e + 2)
            pe.wait_ge(ex_h, e + 1)
            for m in range(2):
                for k in range(KT):
                    n = m * (KT // 2) + k // 2
                    w = ring.wait(pe, name, j + n, turn).rearrange("p (k n) -> p k n", n=512)
                    last = pe.matmul(bank[2 + m][0:CAP, :], xs_T[:, u, k, :], w[:, k % 2, :], start=(k == 0), stop=(k == KT - 1))
                    if k % 2 and not (m == 1 and k == KT - 1):
                        last.then_inc(slot_free, 1)
            last.then_inc(ex_gu, 1)
            pe.wait_ge(ex_gu, e + 1)
            pe.sem_inc(slot_free, 1)

        def ex_down_pe(pe, name, j, turn, i, u):
            e = i * 2 + u
            pe.wait_ge(ex_h, e + 2)
            pe.wait_ge(ex_he, e + 1)
            for k in range(FT):
                last = pe.transpose(bank[4][:, k * CAP:(k + 1) * CAP], act_hid[:, u, k * P:(k + 1) * P], ident[0:CAP, 0:CAP])
            last.then_inc(ex_ht, 1)
            pe.wait_ge(ex_he, e + 2)
            pe.wait_ge(ex_ye, e + 1)
            for k in range(FT):
                w = ring.wait(pe, name, j + k, turn)
                for n in range(2):
                    last = pe.matmul(bank[5 + n][0:CAP, :], hid_T[:, u, k, :], w[:, 512 * n:512 * n + 512], start=(k == 0), stop=(k == FT - 1))
                if k < FT - 1:
                    last.then_inc(slot_free, 1)
            last.then_inc(ex_y, 1)
            pe.wait_ge(ex_y, e + 1)
            pe.sem_inc(slot_free, 1)

        def ex_act(act, i, u):
            e = i * 2 + u
            act.wait_ge(ex_xt, e + 3)
            for c in range(2):
                last = act.activation(xs_T[:, u, 4 * c:4 * c + 4, :], bank[c][:, 0:4 * CAP].rearrange("p (k n) -> p k n", n=CAP), ACT.Copy)
            last.then_inc(ex_xe, 1)
            act.wait_ge(ex_gu, e + 1)
            act.wait_ge(ex_h, e + 1)
            act.activation(act_sig[:, :], bank[2][0:CAP, :], ACT.Sigmoid).then_inc(ex_sg, 1)

        def ex_hid_dve(dve, i, u):
            e = i * 2 + u
            dve.wait_ge(ex_sg, e + 1)
            step(dve, dve.tensor_tensor(act_hid[:, u, :], act_sig[:, :], bank[2][0:CAP, :], ALU.mult))
            dve.tensor_tensor(act_hid[:, u, :], act_hid[:, u, :], bank[3][0:CAP, :], ALU.mult).then_inc(ex_h, 1)

        def ex_out_dve(dve, i, u):
            e = i * 2 + u
            dve.wait_ge(ex_ht, e + 1)
            dve.tensor_copy(hid_T[:, u, :, :], bank[4][:, 0:FT * CAP].rearrange("p (k n) -> p k n", n=CAP)).then_inc(ex_he, 1)
            dve.wait_ge(ex_done, e + 1)
            step(dve, dve.tensor_copy(aff_now[:, u, :], pick[:, bass.ds(e, 1), 1]))
            dve.wait_ge(ex_y, e + 1)
            for n in range(2):
                last = dve.tensor_scalar(ys[:, u, 512 * n:512 * n + 512], bank[5 + n][0:CAP, :], aff_now[:, u, :], None, ALU.mult)
            last.then_inc(ex_ye, 1)

        def ex_put(pool, i, u):
            e = i * 2 + u
            pool.wait_ge(ex_ye, e + 2)
            pool.tensor_copy(no_put[:, u, :], pick_no[:, bass.ds(e, 1)])
            pool.drain()
            pool.indirect_dma_start(y_dram[:, :], bass.IndirectOffsetOnAxis(ap=no_put[:, u, :], axis=0), ys[:, u, :], None,
                                    compute_op=ALU.add).then_inc(ex_out, 16)
            pool.wait_ge(ex_out, e * 16 + 16)
            pool.sem_inc(ex_done, 1)
        def ex_get(pool, i, u):
            e = i * 2 + u
            pool.wait_ge(ex_xt, e + 1)
            pool.tensor_copy(no_get[:, u, :], pick_no[:, bass.ds(e, 1)])
            pool.drain()
            pool.indirect_dma_start(xs[:, u, :], None, u_dram[:, :], bass.IndirectOffsetOnAxis(ap=no_get[:, u, :], axis=0)).then_inc(ex_x[u], 16)

        def mm_T(pe, dst, slot, src, k0=0, k1=KT):
            w = slot.rearrange("p (k n) -> p k n", n=P)
            for k in range(k0, k1):
                last = pe.matmul(dst, w[:, k, :], src[:, k, :], start=(k == 0), stop=(k == KT - 1))
            return last

        def mm_N(pe, dst, slot, t, r=P):
            w = slot.rearrange("p (k n) -> p k n", n=P)
            for k in range(KT):
                last = pe.matmul(dst, xT[:, k, t * P:t * P + r], w[:, k, :], start=(k == 0), stop=(k == KT - 1))
            return last

        def sb_project(pe, name, j, turn, p):
            slot = None
            for n, b in ((0, 5), (1, 6)):
                for half in range(2):
                    if half == 0:
                        slot = ring.wait(pe, name, j + n, turn)
                        pe.wait_ge(sb_pe, p * 3 + n + 1)
                    last = mm_T(pe, bank[b][:, :], slot, xT[:, :, 0:SEQ], half * 4, half * 4 + 4)
                    if half:
                        last.then_inc(sb_pj, 1)
                        pe.wait_ge(sb_pj, p * 3 + n + 1)
                        pe.sem_inc(slot_free, 1)
                    yield
            slot = ring.wait(pe, name, j + 2, turn)
            pe.wait_ge(sb_pe, p * 3 + 3)
            for half in range(2):
                for t in (2 * half, 2 * half + 1):
                    last = mm_N(pe, bank[7][:, t * P:(t + 1) * P], slot, t)
                if half:
                    last.then_inc(sb_pj, 1)
                    pe.wait_ge(sb_pj, p * 3 + 3)
                    pe.sem_inc(slot_free, 2)
                yield

        def sb_pair_pe(pe, p, u, project):
            parts = iter(project)

            def fill(n):
                for _ in range(n):
                    next(parts, None)

            pe.wait_ge(sb_pe, p * 3 + 6)
            for hh in range(2):
                hd = p * 2 + hh
                r = slice(HD * hh, HD * hh + HD)
                for i in range(QT):
                    pe.matmul(bank[i][:, 0:CAUSAL_COLS[i]], kT[r, u, i * P:(i + 1) * P], qT[r, u, i * P:SEQ],
                              start=True, stop=True).then_inc(sb_z, 1)
                fill(2)
                pe.wait_ge(sb_sp, hd + 1)
                for i in range(QT):
                    n = CAUSAL_COLS[i]
                    for j in range(i, QT):
                        pe.matmul(bank[i][:, n - CAUSAL_COLS[j]:n], (tri_neg if j == i else ones_neg)[:, :],
                                  softp[:, CAUSAL_AT[j]:CAUSAL_AT[j] + CAUSAL_COLS[j]], start=False, stop=False,
                                  skip_group_check=True)
                    pe.matmul(bank[i][:, 0:P], ident_bf[:, :], past_neg_bf[:, :], start=False, stop=True,
                              skip_group_check=True).then_inc(sb_zi, 1)
                fill(1)
                pe.wait_ge(sb_oe, hd + 1)
                for i in range(QT):
                    pe.wait_ge(sb_a, hd * QT + i + 1)
                    last = pe.matmul(bank[4][0:HD, i * P:SEQ], vN[:, u, i, r], stick[:, CAUSAL_AT[i]:CAUSAL_AT[i] + CAUSAL_COLS[i]],
                                     start=(i == 0), stop=(i == QT - 1))
                last.then_inc(sb_o, 1)
            fill(6)

        def w_out_pe(pe):
            for n in range(2):
                for k in range(KT):
                    w = ring.wait(pe, "w_out", n * (KT // 2) + k // 2).rearrange("p (k n) -> p k n", n=512)
                    for t in range(T2):
                        r, i = rows_of(t), n * T2 + t
                        if k == 0 and i >= 8:
                            pe.wait_ge(h_upd, H_X2 + i - 7)
                        last = pe.matmul(bank[i % 8][0:r, :], merged[:, k, t * P:t * P + r], w[:, k % 2, :], start=(k == 0), stop=(k == KT - 1))
                        if k == KT - 1:
                            last.then_inc(acc_done, 1)
                    if k == KT - 1:
                        pe.wait_ge(acc_done, H_ALL + (n + 1) * T2)
                        pe.sem_inc(slot_free, 1)
                    elif k % 2:
                        last.then_inc(slot_free, 1)

        def accumulate_N(pe, name, lhs, kts, tiles, n_base, bank_wait, turn=0, j0=0, per=0):
            for n in range(2):
                for j in range(kts // 2):
                    w = ring.wait(pe, name, j0 + n * (kts // 2) + j, turn).rearrange("p (k n) -> p k n", n=512)
                    for kk in range(2):
                        k = 2 * j + kk
                        for t in range(tiles):
                            last = pe.matmul(bank[4 * (1 - n) + t][:, :], lhs[:, k, t * P:(t + 1) * P], w[:, kk, :],
                                             start=(k == 0), stop=(k == kts - 1))
                            if k == kts - 1:
                                last.then_inc(acc_done, 1)
                    if k == kts - 1:
                        pe.wait_ge(acc_done, turn * per + n_base + (n + 1) * tiles)
                        pe.sem_inc(slot_free, 1)
                    else:
                        last.then_inc(slot_free, 1)

        def mm3(pe, dst, a_hi, a_lo, b_hi, b_lo, first, final):
            pe.matmul(dst, a_hi, b_hi, start=first, stop=False)
            pe.matmul(dst, a_hi, b_lo, start=False, stop=False)
            return pe.matmul(dst, a_lo, b_hi, start=False, stop=final)

        FF_SLOTS = 2 * FF_TILES

        def ff_pe(pe, m, upd):
            def weights(f, j, width):
                pe.wait_ge(split_w, f * FF_SLOTS + (m * FF_PARTS * FF_SLOTS + j + 1))
                return [w[:, j % SPLITS, :].rearrange("p (k n) -> p k n", n=width) for w in (w_hi, w_lo)]

            pe.wait_ge(split_x, 2 * QT * (m + 1))
            with loop(pe, FF_PARTS) as f:
                for j in range(FF_TILES):
                    n = f * FF_TILES + (m * FF_PARTS * FF_TILES + j)
                    hi, lo = weights(f, j, P)
                    pe.wait_ge(ff_relu, n + 1)
                    if j < QT:
                        pe.wait_ge(h_upd, f * UPD + (upd - UPD + QT + j + 1))
                    for k in range(KT):
                        last = mm3(pe, bank[j % 4][:, :], hi[:, k, :], lo[:, k, :], x_hi[:, k, :], x_lo[:, k, :], k == 0, k == KT - 1)
                    last.then_inc(ff_mm, 1)
                pe.wait_ge(ff_hid, f * FF_TILES + ((m * FF_PARTS + 1) * FF_TILES + 2))
                for n in range(2):
                    for k in range(FF_TILES):
                        if k % 2 == 0:
                            hi, lo = weights(f, FF_TILES + n * (FF_TILES // 2) + k // 2, 512)
                        for t in range(QT):
                            rows = slice(t * P, (t + 1) * P)
                            last = mm3(pe, bank[4 * (1 - n) + t][:, :], hid_hi[:, k, rows], hid_lo[:, k, rows],
                                       hi[:, k % 2, :], lo[:, k % 2, :], k == 0, k == FF_TILES - 1)
                            if k == FF_TILES - 1:
                                last.then_inc(acc_done, 1)
                        if k % 2 and k < FF_TILES - 1:
                            last.then_inc(ff_w2, 1)

        def ff_pool(pool, m, upd):
            w2_frees = FF_TILES // 2 - 1
            with loop(pool, FF_PARTS) as f:
                for j in range(FF_SLOTS):
                    n = f * FF_SLOTS + (m * FF_PARTS * FF_SLOTS + j)
                    was = (j - SPLITS) % FF_SLOTS
                    half, k = (was - FF_TILES) // (FF_TILES // 2), (was - FF_TILES) % (FF_TILES // 2)
                    part = 0 if j < SPLITS else 1
                    if was < FF_TILES:
                        pool.wait_ge(ff_mm, f * FF_TILES + (m * FF_PARTS * FF_TILES + was + 1))
                    elif k < w2_frees:
                        pool.wait_ge(ff_w2, f * (2 * w2_frees) + ((m * FF_PARTS + part) * 2 * w2_frees + half * w2_frees + k + 1))
                    else:
                        pool.wait_ge(acc_done, f * UPD + (upd + (part - 1) * UPD + (half + 1) * QT))
                    raw = ring.wait(pool, f"ff{m}", j, f)
                    hi, lo = w_hi[:, j % SPLITS, :], w_lo[:, j % SPLITS, :]
                    pool.tensor_tensor(hi, raw, one[:, :].broadcast_to([P, D]), ALU.mult).then_inc(split_w_hi, 1)
                    pool.wait_ge(split_w_hi, n + 1)
                    pool.tensor_tensor(lo, raw, hi.bitcast(F32), ALU.subtract).then_inc(split_w, 1)
                    pool.wait_ge(split_w, n + 1)
                    pool.sem_inc(slot_free, 1)

        @block.tensor
        def _(pe):
            pe.sem_inc(slot_free, RING)
            pe.sem_inc(ex_xt, 2)
            pe.wait_ge(const_in, ALL_CONST)
            pe.transpose(bank[0][:, 0:7 * KT], gain_rows[:, :], ident[0:7 * KT, 0:7 * KT]).then_inc(gains_T, 1)
            pe.wait_ge(gains_in, 1)
            norm_pe(pe, 0)
            for _ in sb_project(pe, "sb_first", 0, 0, 0):
                pass
            with loop(pe, PAIRS // 2 - 1) as turn:
                sb_pair_pe(pe, turn * 2, 0, sb_project(pe, "sb_loop", 0, turn, turn * 2 + 1))
                sb_pair_pe(pe, turn * 2 + 1, 1, sb_project(pe, "sb_loop", 4, turn, turn * 2 + 2))
            sb_pair_pe(pe, PAIRS - 2, 0, sb_project(pe, "sb_last", 0, 0, PAIRS - 1))
            sb_pair_pe(pe, PAIRS - 1, 1, ())
            pe.wait_ge(sb_oe, 2 * PAIRS + 1)
            accumulate_N(pe, "sb_o", oT, KT, QT, 0, None)
            norm_pe(pe, 1)
            ff_pe(pe, 0, UPD)
            norm_pe(pe, 2)
            pe.wait_ge(ff_freed, 1)
            ring.wait(pe, "kv", RING - 1)
            kv_pe(pe)
            norm_pe(pe, 3)
            gates_pe(pe)
            pe.wait_ge(gate_in, 1)
            with loop(pe, GROUPS) as g:
                nsa_pe(pe, g)
            pe.wait_ge(ns_oe, 4 * GROUPS + 1)
            accumulate_N(pe, "nsa_o", oT, KT, QT, H_BEFORE[3], None)
            norm_pe(pe, 4)
            ff_pe(pe, 1, H_BEFORE[4])

            pe.wait_ge(b2_in, B2_CONST)
            pe.transpose(bank[7][:, 0:3], head_gain_rows[:, :], ident[0:3, 0:3]).then_inc(b2_T, 1)
            pe.wait_ge(b2_ready, 1)
            norm_pe(pe, 6)
            pe.wait_ge(ff_freed, 2)
            ring.wait(pe, "df_loop", 2)
            for _ in df_parts(pe, "df_first", 0, 0, 0):
                pass
            with loop(pe, HEADS2 // 2 - 1) as turn:
                df_pe_head(pe, turn * 2, 0, df_parts(pe, "df_loop", 0, turn, turn * 2 + 1))
                df_pe_head(pe, turn * 2 + 1, 1, df_parts(pe, "df_loop", 4, turn, turn * 2 + 2))
            df_pe_head(pe, HEADS2 - 2, 0, df_parts(pe, "df_last", 0, 0, HEADS2 - 1))
            df_pe_head(pe, HEADS2 - 1, 1, ())
            pe.wait_ge(df_oe, HEADS2 + 1)
            branch_pe(pe, 0)
            pe.wait_ge(br_m, KT + 2)
            with loop(pe, KV2) as kv:
                gq_pe_turn(pe, kv)
            pe.wait_ge(gq_oe, HEADS2 + 1)
            branch_pe(pe, 1)
            pe.wait_ge(br_m, 2 * KT + 2)
            w_out_pe(pe)
            norm_pe(pe, 7)
            route_pe(pe)
            ex_up_pe(pe, "ex_first", 0, 0, 0, 0)
            with loop(pe, EXPERTS // 2 - 1) as turn:
                ex_up_pe(pe, "ex_loop", 0, turn, turn, 1)
                ex_down_pe(pe, "ex_loop", 8, turn, turn, 0)
                ex_up_pe(pe, "ex_loop", 12, turn, turn + 1, 0)
                ex_down_pe(pe, "ex_loop", 20, turn, turn, 1)
            ex_up_pe(pe, "ex_last", 0, 0, EXPERTS // 2 - 1, 1)
            ex_down_pe(pe, "ex_last", 8, 0, EXPERTS // 2 - 1, 0)
            ex_down_pe(pe, "ex_last", 12, 0, EXPERTS // 2 - 1, 1)

        def sb_pair_act(act, p):
            for hh in range(2):
                hd = p * 2 + hh
                for i in range(QT):
                    act.wait_ge(sb_z, hd * QT + i + 1)
                    act_t.inc(act.activation(absz[:, CAUSAL_AT[i]:CAUSAL_AT[i] + CAUSAL_COLS[i]], bank[i][:, 0:CAUSAL_COLS[i]], ACT.Abs))
                act.wait_ge(act_step, act_t.value())
                act_t.inc(act.activation(absz[:, :], absz[:, :], ACT.Exp, scale=-1.0))
                act.wait_ge(act_step, act_t.value())
                act.activation(absz[:, :], absz[:, :], ACT.Ln, bias=1.0).then_inc(sb_l, 1)
                for i in range(QT):
                    act.wait_ge(sb_zi, hd * QT + i + 1)
                    act.activation(stick[:, CAUSAL_AT[i]:CAUSAL_AT[i] + CAUSAL_COLS[i]], bank[i][:, 0:CAUSAL_COLS[i]], ACT.Exp).then_inc(sb_a, 1)

        def ff_act(act, m):
            with loop(act, FF_PARTS) as f:
                for j in range(FF_TILES):
                    n = f * FF_TILES + (m * FF_PARTS * FF_TILES + j)
                    act.wait_ge(ff_mm, n + 1)
                    act.wait_ge(ff_hid, n + 1)
                    act.activation(relu[:, j % 2, :], bank[j % 4][:, :], ACT.Relu).then_inc(ff_relu, 1)

        act_t, dve_t = Tally(act_step), Tally(dve_step)

        @block.scalar
        def _(act):
            act.sem_inc(ff_relu, 4)
            act.sem_inc(ns_p, 3)
            act.sem_inc(ns_t, 1)
            act.sem_inc(df_p, 1)
            act.sem_inc(df_t, 1)
            act.sem_inc(gq_p, 2)
            act.sem_inc(gq_t, 1)
            act.sem_inc(ex_xe, 1)
            act.wait_ge(const_in, ALL_CONST)
            act.wait_ge(gains_in, 1)
            norm_act(act, 0)
            with loop(act, PAIRS // 2 - 1, tallies=[(act_t, 4 * (QT + 1))]) as turn:
                sb_pair_act(act, turn * 2)
                sb_pair_act(act, turn * 2 + 1)
            sb_pair_act(act, PAIRS - 2)
            sb_pair_act(act, PAIRS - 1)
            act.wait_ge(h_upd, H_BEFORE[1])
            norm_act(act, 1)
            split_x_act(act, 1)
            ff_act(act, 0)
            act.wait_ge(h_upd, H_BEFORE[2])
            norm_act(act, 2)
            kv_act(act)
            norm_act(act, 3)
            gates_act(act)
            with loop(act, GROUPS) as g:
                nsa_act(act, g)
            act.wait_ge(h_upd, H_BEFORE[4])
            norm_act(act, 4)
            split_x_act(act, 4)
            ff_act(act, 1)
            act.wait_ge(h_upd, H_ALL)
            norm_act(act, 5)

            act.wait_ge(lam_d, 1)
            act.activation(lam[:, :], lam[:, :], ACT.Exp).then_inc(lam_e, 1)
            act.wait_ge(b2_in, B2_CONST)
            act.wait_ge(h_upd, H_X2)
            norm_act(act, 6)
            with loop(act, HEADS2) as hd:
                df_act_head(act, hd)
            branch_act(act, 0)
            with loop(act, KV2) as kv:
                gq_act_turn(act, kv)
            branch_act(act, 1)
            act.wait_ge(h_upd, H_FFN)
            norm_act(act, 7)
            route_act(act)
            ex_act(act, 0, 0)
            with loop(act, EXPERTS // 2 - 1) as turn:
                ex_act(act, turn, 1)
                ex_act(act, turn + 1, 0)
            ex_act(act, EXPERTS // 2 - 1, 1)
            act.wait_ge(y_in, 16)
            norm_act(act, 8)

        def step(dve, ins):
            dve_t.inc(ins)
            dve.wait_ge(dve_step, dve_t.value())

        def sb_take(dve, n, p, u):
            dve.wait_ge(sb_pj, p * 3 + n + 1)
            if n == 0:
                dve.tensor_scalar(qT[:, u, :], bank[5][:, :], HD ** -0.5, None, ALU.mult).then_inc(sb_pe, 1)
            elif n == 1:
                dve.tensor_copy(kT[:, u, :], bank[6][:, :]).then_inc(sb_pe, 1)
            else:
                dve.tensor_copy(vN[:, u, :, :], bank[7][:, :].rearrange("p (t n) -> p t n", n=P)).then_inc(sb_pe, 1)

        def sb_pair_dve(dve, p, u, take):
            for hh in range(2):
                hd = p * 2 + hh
                dve.wait_ge(sb_l, hd + 1)
                for i in range(QT):
                    s = slice(CAUSAL_AT[i], CAUSAL_AT[i] + CAUSAL_COLS[i])
                    dve_t.inc(dve.scalar_tensor_tensor(softp[:, s], bank[i][:, 0:CAUSAL_COLS[i]], 0.0, absz[:, s], ALU.max, ALU.add))
                dve.wait_ge(dve_step, dve_t.value())
                for i in range(QT):
                    d = softp[:, CAUSAL_AT[i]:CAUSAL_AT[i] + P]
                    last = dve.tensor_tensor(d, d, past01[:, :], ALU.mult)
                    if i == QT - 1:
                        last.then_inc(sb_sp, 1)
                if take and hh == 0:
                    sb_take(dve, 0, p + 1, 1 - u)
                if take and hh == 1:
                    sb_take(dve, 1, p + 1, 1 - u)
                    sb_take(dve, 2, p + 1, 1 - u)
                dve.wait_ge(sb_o, hd + 1)
                dve.tensor_copy(oT[HD * hh:HD * hh + HD, bass.ds(p, 1), 0:SEQ].rearrange("p a n -> p (a n)"),
                                bank[4][0:HD, :]).then_inc(sb_oe, 1)

        def w_out_dve(dve):
            for n in range(2):
                for t in range(T2):
                    r = rows_of(t)
                    dve.wait_ge(acc_done, H_ALL + n * T2 + t + 1)
                    hs = h[0:r, t, 512 * n:512 * n + 512]
                    dve.tensor_tensor(hs, bank[(n * T2 + t) % 8][0:r, :], hs, ALU.add).then_inc(h_upd, 1)

        def residual_dve(dve, done):
            for n in range(2):
                for t in range(QT):
                    dve.wait_ge(acc_done, done + n * QT + t + 1)
                    hs = h[:, t, 512 * n:512 * n + 512]
                    dve.tensor_tensor(hs, bank[4 * (1 - n) + t][:, :], hs, ALU.add).then_inc(h_upd, 1)

        def ff_dve(dve, m, upd):
            with loop(dve, FF_PARTS, tallies=[(dve_t, 2 * FF_TILES)]) as f:
                for j in range(FF_TILES):
                    n = f * FF_TILES + (m * FF_PARTS * FF_TILES + j)
                    dve.wait_ge(ff_relu, n + 5)
                    r, sq = relu[:, j % 2, :], hid_sq[:, j % 2, :]
                    dve_t.inc(dve.tensor_tensor(sq, r, r, ALU.mult))
                    step(dve, dve.tensor_tensor(hid_hi[:, j, :], r, r, ALU.mult))
                    dve.tensor_tensor(hid_lo[:, j, :], sq, hid_hi[:, j, :].bitcast(F32), ALU.subtract).then_inc(ff_hid, 1)
                residual_dve(dve, f * UPD + upd)

        @block.vector
        def _(dve):
            dve.sem_inc(sb_pe, 3)
            dve.sem_inc(sb_oe, 1)
            dve.sem_inc(ff_hid, 2)
            dve.sem_inc(ns_oe, 1)
            dve.sem_inc(df_pe, 1)
            dve.sem_inc(df_v, 1)
            dve.sem_inc(df_oe, 1)
            dve.sem_inc(br_m, 2)
            dve.sem_inc(gq_br, 1)
            dve.sem_inc(gq_oe, 1)
            dve.sem_inc(ex_h, 1)
            dve.sem_inc(ex_he, 1)
            dve.sem_inc(ex_ye, 1)
            dve.sem_inc(ex_done, 2)
            dve_t.inc(dve.memset(ssq[:, :], 0.0))
            dve.memset(ones_neg[:, :], -1.0)
            dve.wait_ge(const_in, ALL_CONST)
            dve.tensor_copy(ident_bf[:, :], ident[:, :])
            dve.tensor_copy(past_neg_bf[:, :], past_neg[:, :])
            dve.wait_ge(gains_T, 1)
            dve.tensor_copy(gains[:, :, :].rearrange("p g k -> p (g k)"), bank[0][:, 0:7 * KT]).then_inc(gains_in, 1)
            norm_dve(dve, 0, EPS1)
            for n in range(3):
                sb_take(dve, n, 0, 0)
            with loop(dve, PAIRS // 2 - 1, tallies=[(dve_t, 4 * QT)]) as turn:
                sb_pair_dve(dve, turn * 2, 0, True)
                sb_pair_dve(dve, turn * 2 + 1, 1, True)
            sb_pair_dve(dve, PAIRS - 2, 0, True)
            sb_pair_dve(dve, PAIRS - 1, 1, False)
            residual_dve(dve, 0)
            norm_dve(dve, 1, EPS1)
            ff_dve(dve, 0, UPD)
            norm_dve(dve, 2, EPS1)
            kv_dve(dve)
            norm_dve(dve, 3, EPS1)
            gates_dve(dve)
            with loop(dve, GROUPS, tallies=[(dve_t, 44)]) as g:
                nsa_dve(dve, g)
            residual_dve(dve, H_BEFORE[3])
            norm_dve(dve, 4, EPS1)
            ff_dve(dve, 1, H_BEFORE[4])
            dve.wait_ge(gain_in, 16)
            plain_norm_dve(dve, 5, EPS1, QT)

            ready2_dve(dve)
            norm_dve(dve, 6, EPS2)
            for n in range(6):
                df_take(dve, n, 0, 0)
            with loop(dve, HEADS2 // 2 - 1, tallies=[(dve_t, 2 * (4 * T2 + 2))]) as turn:
                df_dve_head(dve, turn * 2, 0, True)
                df_dve_head(dve, turn * 2 + 1, 1, True)
            df_dve_head(dve, HEADS2 - 2, 0, True)
            df_dve_head(dve, HEADS2 - 1, 1, False)
            branch_dve(dve, 0, 0)
            with loop(dve, KV2, tallies=[(dve_t, 50)]) as kv:
                gq_dve_turn(dve, kv)
            branch_dve(dve, 1, 4)
            w_out_dve(dve)
            norm_dve(dve, 7, EPS2)
            tokens_dve(dve)
            route_dve(dve)
            ex_hid_dve(dve, 0, 0)
            with loop(dve, EXPERTS // 2 - 1, tallies=[(dve_t, 4)]) as turn:
                ex_hid_dve(dve, turn, 1)
                ex_out_dve(dve, turn, 0)
                ex_hid_dve(dve, turn + 1, 0)
                ex_out_dve(dve, turn, 1)
            ex_hid_dve(dve, EXPERTS // 2 - 1, 1)
            ex_out_dve(dve, EXPERTS // 2 - 1, 0)
            ex_out_dve(dve, EXPERTS // 2 - 1, 1)
            dve.wait_ge(gain_in, 48)
            plain_norm_dve(dve, 8, EPS2, QT)

        @block.gpsimd
        def _(pool):
            pool.sem_inc(ff_w2, 2 * (FF_TILES // 2 - 1))
            pool.memset(one[:, :], 1.0).then_inc(one_in, 1)
            pool.wait_ge(one_in, 1)
            for m in range(2):
                pool.wait_ge(norm_tp, 2 * norm_base(SPLIT_NORMS[m]) + 1)
                ff_pool(pool, m, UPD if m == 0 else H_BEFORE[4])
                pool.sem_inc(ff_freed, 1)
            pool.wait_ge(h_upd, H_FFN)
            pool.dma_start(y_dram[0:SEQ, :].rearrange("(t p) d -> p t d", p=P), h[:, 0:QT, :]).then_inc(h_out, 16)
            pool.dma_start(y_dram[SEQ:L2, :], h[0:META, QT, :]).then_inc(h_out, 16)
            for t in range(T2):
                r = rows_of(t)
                pool.wait_ge(u_row, t + 1)
                pool.dma_start(u_dram[t * P:t * P + r, :], u_rows[0:r, t % 2, :]).then_inc(u_out[t % 2], 16)
            pool.wait_ge(ex_no, 1)
            pool.wait_ge(h_out, 32)
            pool.wait_ge(u_out[0], 16 * (T2 - T2 // 2))
            pool.wait_ge(u_out[1], 16 * (T2 // 2))
            ex_get(pool, 0, 0)
            ex_get(pool, 0, 1)
            with loop(pool, EXPERTS // 2 - 1) as turn:
                ex_get(pool, turn + 1, 0)
                ex_put(pool, turn, 0)
                ex_get(pool, turn + 1, 1)
                ex_put(pool, turn, 1)
            ex_put(pool, EXPERTS // 2 - 1, 0)
            ex_put(pool, EXPERTS // 2 - 1, 1)
            pool.dma_start(h[:, 0:QT, :], y_dram[0:SEQ, :].rearrange("(t p) d -> p t d", p=P)).then_inc(y_in, 16)


def rope_tables_1():
    f, half = np.float32, 8
    inv = f(500000.0) ** (-np.arange(half, dtype=f) * f(2.0) / f(16))
    ang = np.arange(SEQ, dtype=f)[None, :] * inv[:, None]
    cos, sin, rot = np.ones((P, SEQ), f), np.zeros((P, SEQ), f), np.zeros((P, P), f)
    for base in (0, HD):
        for d in range(half):
            for x, y, sign in ((d, d + half, -1), (d + half, d, 1)):
                cos[base + x], sin[base + x] = np.cos(ang[d]), np.sin(ang[d])
                rot[base + y, base + x] = sign
    return cos, sin, rot


def rope_tables_2():
    f, half, grid_w = np.float32, HD // 2, 64
    inv = f(10000.0) ** (-np.arange(0, HD, 2, dtype=f) / f(HD))
    i = np.arange(SEQ)
    cos, sin, rot = np.ones((P, L2), f), np.zeros((P, L2), f), np.zeros((P, P), f)
    for base, place in ((0, i // grid_w), (HD, i % grid_w)):
        ang = place.astype(f)[None, :] * inv[:, None]
        for d in range(half):
            for x, y, sign in ((d, d + half, -1), (d + half, d, 1)):
                cos[base + x, 0:SEQ], sin[base + x, 0:SEQ] = np.cos(ang[d]), np.sin(ang[d])
                rot[base + y, base + x] = sign
    return cos, sin, rot


def distances():
    pos = np.arange(T2 * P)
    d = np.abs(pos[:, None] - pos[None, :L2])
    d[(pos >= SEQ), :] = 0
    d[:, SEQ:] = 0
    return np.ascontiguousarray(d.reshape(T2, P, L2).transpose(1, 0, 2)).astype(np.float16)


def constants():
    f = np.float32
    i = np.arange(P)
    tok = i[:, None] + P * np.arange(QT)[None, :]
    cmp_ok = (CMP_STRIDE * np.arange(N_CMP) + CMP_LEN - 1)[None, None, :] <= tok[:, :, None]
    cos1, sin1, rot1 = rope_tables_1()
    cos2, sin2, rot2 = rope_tables_2()
    return {
        "ident": np.eye(P, dtype=f),
        "tri_neg": -(i[:, None] >= i[None, :]).astype(f),
        "past01": (i[:, None] < i[None, :]).astype(f),
        "future_neg": np.where(i[:, None] >= i[None, :], f(0), f(-1e30)).astype(f),
        "cmp_neg": np.where(cmp_ok, f(0), f(-1e30)).astype(f),
        "cmp_any": cmp_ok.any(-1).astype(f),
        "cos1": cos1, "sin1": sin1, "rot1": rot1,
        "cos2": cos2, "sin2": sin2, "rot2": rot2, "dist": distances(),
        "slot_no": np.tile(np.arange(CAP, dtype=f), (P, 1)),
        "token_no": (i[:, None] + P * np.arange(T2)[None, :]).astype(f),
        "past_neg": np.where(i[:, None] < i[None, :], f(0), f(-1e30)).astype(f),
    }


def kernel(**inputs):
    import concourse.bacc as _bacc
    from concourse.bass_utils import run_bass_kernel_spmd as _run

    nc = _bacc.Bacc("TRN2", target_bir_lowering=False, num_devices=1)
    arrays, A, C = {}, {}, {}
    for kind, into, values in (("in", A, inputs), ("c", C, constants())):
        for name, value in values.items():
            a = np.ascontiguousarray(value)
            arrays[f"{kind}_{name}"] = a
            into[name] = nc.dram_tensor(f"{kind}_{name}", a.shape, mybir.dt.from_np(a.dtype), kind="ExternalInput").ap()
    out = nc.dram_tensor("out", (1, SEQ, D), F32, kind="ExternalOutput").ap()
    build_program(nc, A, C, out)
    return _run(nc, [arrays], core_ids=[0]).results[0]["out"]
```

```python
from contextlib import ExitStack, contextmanager

import numpy as np
import concourse.bass as bass
from concourse import mybir

F32, F32R, BF16, F16, U32 = mybir.dt.float32, mybir.dt.float32r, mybir.dt.bfloat16, mybir.dt.float16, mybir.dt.uint32
ACT, ALU, AX = mybir.ActivationFunctionType, mybir.AluOpType, mybir.AxisListType

P = 128
D = 1024
KT = D // P
SEQ = 512
QT = SEQ // P
META = 16
L2 = SEQ + META
T2 = QT + 1
CH2 = L2 // 2
HD = 64
PAIRS = 8
D_FF = 4096
FF_PARTS = 4
FF_TILES = D_FF // FF_PARTS // P
SPLITS = 4
SPLITS2 = 2
EPS1, EPS2 = 1e-5, 1e-6
RING = 8
CAUSAL_COLS = [QT * P - P * i for i in range(QT)]
CAUSAL_AT = [sum(CAUSAL_COLS[:i]) for i in range(QT)]
CAUSAL = sum(CAUSAL_COLS)
GROUPS = 4
BRANCHES = 3
UNITS = 4 * BRANCHES
CMP_LEN, CMP_STRIDE, CMP_HID = 32, 16, 256
N_CMP = (SEQ - CMP_LEN) // CMP_STRIDE + 1
CMP_KT = CMP_LEN * HD // P
N_GATES = 48
SCORE_AT = [(1, 384), (2, 0), (1, 0), (0, 0)]
PROB_AT = [0, P, 3 * P, 6 * P]
PT_AT = [(3, 0, 0), (4, 0, SEQ), (5, 0, 2 * SEQ), (4, 384, SEQ + 384)]
GELU_C, GELU_K = 0.044715, (2.0 / np.pi) ** 0.5


HEADS2 = 8
KV2 = 2
Q_PER_KV = HEADS2 // KV2
USES = 8 + 6 * Q_PER_KV
LAM_INIT = 0.8 - 0.6
O_TAIL = 128
MS_TAIL = O_TAIL + META
EXPERTS, CAP, EXPERT_FF = 16, 2 * L2 // 16, 512
FT = EXPERT_FF // P
W_IN = {"qa": 0, "ka": 8, "va": 16, "qb": 24, "kb": 32, "vb": 34, "ga": 36, "gb": 44}


LN_EXP = "natural_log_exp_and_others"


def rows_of(t):
    return P if t < QT else META


class Tally:

    def __init__(self, sem):
        self.sem, self.n, self.turn, self.per, self.start = sem, 0, None, 0, 0

    def inc(self, ins):
        ins.then_inc(self.sem, 1)
        self.n += 1

    def value(self):
        return self.n if self.turn is None else self.turn * self.per + self.n


@contextmanager
def loop(eng, count, **per):
    tallies = per.pop("tallies", [])
    with eng.Fori(0, count) as turn:
        for t, k in tallies:
            t.turn, t.per, t.start = turn, k, t.n
        yield turn
        for t, k in tallies:
            assert t.n - t.start == k, (t.n - t.start, k)
            t.n, t.turn = t.start + k * count, None


class Ring:

    def __init__(self, tile, loaded, free):
        self.tile, self.loaded, self.free = tile, loaded, free
        self.at, self.loads, self.plan = 0, [0] * RING, {}

    def load(self, sp, name, sources, turns=1):
        n = len(sources)
        assert turns == 1 or n % RING == 0, (name, n)
        per = [0] * RING
        waits = []
        for j, s in enumerate(sources):
            slot = (self.at + j) % RING
            waits.append((slot, self.loads[slot], per[slot] + 1))
            per[slot] += s is not None
        self.plan[name] = [(slot, base, k, per[slot]) for slot, base, k in waits]

        def turn_loads(turn):
            for j, s in enumerate(sources):
                if s is None:
                    continue
                slot = (self.at + j) % RING
                sp.wait_ge(self.free, self.at + turn * n + j + 1)
                dst, src = s(self.tile[:, slot, :], turn)
                sp.dma_start(dst, src).then_inc(self.loaded[slot], 16)

        if turns == 1:
            turn_loads(0)
        else:
            with sp.Fori(0, turns) as turn:
                turn_loads(turn)
        self.at += n * turns
        for slot in range(RING):
            self.loads[slot] += per[slot] * turns

    def wait(self, pe, name, j, turn=0):
        slot, base, k, per = self.plan[name][j]
        pe.wait_ge(self.loaded[slot], (turn * per + base + k) * 16)
        return self.tile[:, slot, :]


def cols_tile(w, n_tile):
    def source(slot, turn):
        return (slot.rearrange("p (k n) -> p k n", n=P),
                w[:, bass.ds(n_tile(turn) * P, P)].rearrange("(k p) n -> p k n", p=P))
    return source


def rows_tiles(w, row_tile, col, width=512):
    k = D // width

    def source(slot, turn):
        return (slot.rearrange("p (k n) -> p k n", n=width),
                w[bass.ds(row_tile(turn) * P, k * P), bass.ds(col(turn), width)].rearrange("(k p) n -> p k n", p=P))
    return source


def build_program(nc, A, C, out):
    ctx = ExitStack()
    with ctx:
        def sb(name, shape, dt=F32, stack=ctx):
            return stack.enter_context(nc.sbuf_tensor(name, shape, dt))

        def sb_split(name, shape, stack=ctx):
            with ExitStack() as same:
                whole = sb(name, shape, stack=same)
            return whole, sb(name + "_lo", shape, F32R, stack=stack)

        def sem(name):
            return ctx.enter_context(nc.semaphore(name))

        h = sb("h", [P, T2, D])
        xT = sb("xT", [P, KT, L2])
        ring_tile, ring_lo = sb_split("ring_tile", [P, RING, D])
        ident = sb("ident", [P, P])
        ident_bf = sb("ident_bf", [P, P], BF16)
        gain_rows = sb("gain_rows", [7 * KT, P])
        gains = sb("gains", [P, 7, KT])
        ssq = sb("ssq", [P, T2])
        rstd = sb("rstd", [P, T2])
        xn = sb("xn", [P, 2, D])
        oT, oT_lo = sb_split("oT", [P, KT, L2])

        one = sb("one", [P, 1])
        neg_half = sb("neg_half", [P, 1])
        eps_col = sb("eps_col", [P, 1])
        gain_bc = sb("gain_bc", [P, D])

        psum = ctx.enter_context(nc.psum_tensor("psum", [P, 8, 512], F32))
        bank = [psum[:, k, :] for k in range(8)]

        st = ExitStack()
        x_hi = sb("x_hi", [P, KT, SEQ], F32R, stack=st)
        x_lo = sb("x_lo", [P, KT, SEQ], F32R, stack=st)
        w_hi = sb("w_hi", [P, SPLITS, D], F32R, stack=st)
        with ExitStack() as sticks:
            qT = sb("qT", [P, 2, SEQ], stack=sticks)
            kT = sb("kT", [P, 2, SEQ], stack=sticks)
            vN = sb("vN", [P, 2, QT, P], stack=sticks)
            absz = sb("absz", [P, CAUSAL], stack=sticks)
            softp = sb("softp", [P, CAUSAL], stack=sticks)
            stick = sb("stick", [P, CAUSAL], stack=sticks)
            tri_neg = sb("tri_neg", [P, P], stack=sticks)
            ones_neg = sb("ones_neg", [P, P], stack=sticks)
            past01 = sb("past01", [P, P], stack=sticks)
            past_neg = sb("past_neg", [P, P], stack=sticks)
            past_neg_bf = sb("past_neg_bf", [P, P], BF16, stack=sticks)
            sb_o_hi = sb("sb_o_hi", [P, KT, SEQ], F32R, stack=sticks)
        with ExitStack() as feed_forward:
            w_lo = sb("w_lo", [P, SPLITS, D], F32R, stack=feed_forward)
            hid_hi = sb("hid_hi", [P, FF_TILES, SEQ], F32R, stack=feed_forward)
            hid_lo = sb("hid_lo", [P, FF_TILES, SEQ], F32R, stack=feed_forward)
            relu = sb("relu", [P, 2, SEQ], stack=feed_forward)
            hid_sq = sb("hid_sq", [P, 2, SEQ], stack=feed_forward)
        st.close()

        st = ExitStack()
        k_cmp = sb("k_cmp", [P, GROUPS, N_CMP], stack=st)
        v_cmp = sb("v_cmp", [N_CMP, GROUPS, HD], stack=st)
        k_all = sb("k_all", [P, 2, GROUPS, SEQ], stack=st)
        v_all = sb("v_all", [P, 2, QT, GROUPS, HD], stack=st)
        q_raw = sb("q_raw", [P, 2, SEQ], stack=st)
        rope_a = sb("rope_a", [P, SEQ], stack=st)
        rope_b = sb("rope_b", [P, SEQ], stack=st)
        cos1 = sb("cos1", [P, SEQ], stack=st)
        sin1 = sb("sin1", [P, SEQ], stack=st)
        rot1 = sb("rot1", [P, P], stack=st)
        gate_w = sb("gate_w", [P, KT, N_GATES], stack=st)
        gate_b = sb("gate_b", [P, N_GATES], stack=st)
        gates = sb("gates", [P, QT, N_GATES], stack=st)
        future_neg = sb("future_neg", [P, P], stack=st)
        future_neg_bf = sb("future_neg_bf", [P, P], BF16, stack=st)
        cmp_neg = sb("cmp_neg", [P, QT, N_CMP], stack=st)
        cmp_any = sb("cmp_any", [P, QT], stack=st)
        with ExitStack() as shared_kv:
            kv_pairs = sb("kv_pairs", [P, 2, GROUPS, SEQ], stack=shared_kv)
            blocks = sb("blocks", [P, 2, CMP_KT, GROUPS * N_CMP], stack=shared_kv)
            pos_rows = sb("pos_rows", [2 * CMP_KT, P], stack=shared_kv)
            pos_off = sb("pos_off", [P, 2 * CMP_KT], stack=shared_kv)
            cmp_w2 = sb("cmp_out_w", [P, 2, 2, HD], stack=shared_kv)
            cmp_x = sb("cmp_x", [P, 2, GROUPS * N_CMP], stack=shared_kv)
            cmp_u = sb("cmp_u", [P, 2, GROUPS * N_CMP], stack=shared_kv)
            cmp_h = sb("cmp_h", [P, 2, 2, GROUPS * N_CMP], stack=shared_kv)
        with ExitStack() as groups:
            k_grp = sb("k_grp", [P, 2, SEQ], stack=groups)
            v_grp = sb("v_grp", [P, 2, QT, HD], stack=groups)
            kc_grp = sb("kc_grp", [P, N_CMP], stack=groups)
            vc_grp = sb("vc_grp", [N_CMP, HD], stack=groups)
            q_rot = sb("q_rot", [P, 2, SEQ], stack=groups)
            probs = sb("probs", [P, 2, CAUSAL], stack=groups)
            probs_T = sb("probs_T", [P, 2, CAUSAL], stack=groups)
            top = sb("top", [P, 2, QT], stack=groups)
            rsum = sb("rsum", [P, 2, QT], stack=groups)
            factor = sb("factor", [P, 2, QT], stack=groups)
            ns_o_hi = sb("ns_o_hi", [P, KT, SEQ], F32R, stack=groups)
            ns_w_hi = sb("ns_w_hi", [P, SPLITS2, D], F32R, stack=groups)
        st.close()
        st = ExitStack()
        merged, merged_lo = sb_split("merged", [P, KT, L2], st)
        x2_hi = sb("x2_hi", [P, KT, L2], F32R, stack=st)
        x2_lo = sb("x2_lo", [P, KT, L2], F32R, stack=st)
        w2_hi = sb("w2_hi", [P, SPLITS2, D], F32R, stack=st)
        lam_prod = sb("lam_prod", [P, HD], stack=st)
        lam = sb("lam", [P, 2], stack=st)
        neg_lam = sb("neg_lam", [P, 1], stack=st)
        head_gain_rows = sb("head_gain_rows", [3, P], stack=st)
        head_gain = sb("head_gain", [P, 3], stack=st)
        mean_w = sb("mean_w", [P, P], stack=st)
        cos2 = sb("cos2", [P, L2], stack=st)
        sin2 = sb("sin2", [P, L2], stack=st)
        rot2 = sb("rot2", [P, P], stack=st)
        top2 = sb("top2", [P, 2], stack=st)
        rsum2 = sb("rsum2", [P, 2], stack=st)
        rinv2 = sb("rinv2", [P, 2], stack=st)
        with ExitStack() as heads:
            q2 = sb("q2", [P, 2, L2], stack=heads)
            k2 = sb("k2", [P, 2, L2], stack=heads)
            v2 = sb("v2", [P, 2, T2, P], stack=heads)
            prob_a = sb("prob_a", [P, 2, L2], stack=heads)
            w_T = sb("w_T", [P, 2, T2, P], stack=heads)
            sq2 = sb("sq2", [P, 2, L2], stack=heads)
            var2 = sb("var2", [P, 2, L2], stack=heads)
            with ExitStack() as differential:
                prob_b = sb("prob_b", [P, 2, L2], stack=differential)
                dist = sb("dist", [P, T2, L2], F16, stack=differential)
                slope = sb("slope", [P, 2, P], F16, stack=differential)
                lam_in = sb("lam_in", [P, 4, HD], stack=differential)
            with ExitStack() as grouped:
                raw2 = sb("raw2", [P, 2, L2], stack=grouped)
                norm2 = sb("norm2", [P, 2, L2], stack=grouped)
                rope_c = sb("rope_c", [P, L2], stack=grouped)
        with ExitStack() as branches:
            sig = sb("sig", [P, 2, L2], stack=branches)
            o_hi = sb("o_hi", [P, KT, L2], F32R, stack=branches)
            merged_hi = sb("merged_hi", [P, KT, L2], F32R, stack=branches)
        st.close()
        st = ExitStack()
        u_rows = sb("u_rows", [P, T2, D], stack=st)
        router_w = sb("router_w", [P, KT, EXPERTS], stack=st)
        logits = sb("logits", [P, T2, EXPERTS], stack=st)
        lmax = sb("lmax", [P, T2], stack=st)
        token_aff = sb("token_aff", [P, T2, EXPERTS, 2], stack=st)
        aff_T = sb("aff_T", [EXPERTS, L2], stack=st)
        work = sb("work", [EXPERTS, L2], stack=st)
        best8 = sb("best8", [EXPERTS, 8], stack=st)
        above = sb("above", [EXPERTS, L2], stack=st)
        equal = sb("equal", [EXPERTS, L2], stack=st)
        count = sb("count", [EXPERTS, L2], stack=st)
        ones_row = sb("ones_row", [EXPERTS, L2], stack=st)
        n_above = sb("n_above", [EXPERTS, 2], stack=st)
        slot_T = sb("slot_T", [P, T2, EXPERTS], stack=st)
        slot_no = sb("slot_no", [P, CAP], stack=st)
        token_no = sb("token_no", [P, T2], stack=st)
        one_hot = sb("one_hot", [P, 4, T2, CAP], stack=st)
        pick = sb("pick", [CAP, EXPERTS, 2], stack=st)
        pick_no = sb("pick_no", [CAP, EXPERTS], U32, stack=st)
        no_get = sb("no_get", [CAP, 2, 1], U32, stack=st)
        no_put = sb("no_put", [CAP, 2, 1], U32, stack=st)
        aff_now = sb("aff_now", [CAP, 2, 1], stack=st)
        xs = sb("xs", [CAP, 2, D], stack=st)
        xs_T = sb("xs_T", [P, 2, KT, CAP], stack=st)
        act_sig = sb("act_sig", [CAP, EXPERT_FF], stack=st)
        act_hid = sb("act_hid", [CAP, 2, EXPERT_FF], stack=st)
        hid_T = sb("hid_T", [P, 2, FT, CAP], stack=st)
        ys = sb("ys", [CAP, 2, D], stack=st)
        st.close()
        u_dram = nc.dram_tensor("u_dram", [L2, D], F32).ap()
        y_dram = nc.dram_tensor("y_dram", [L2, D], F32).ap()

        one_in, ff_freed = sem("one_in"), sem("ff_freed")
        const_in, gains_T, gains_in = sem("const_in"), sem("gains_T"), sem("gains_in")
        loaded = [sem(f"slot{k}_loaded") for k in range(RING)]
        slot_free = sem("slot_free")
        h_upd = sem("h_upd")
        dve_step, act_step = sem("dve_step"), sem("act_step")
        norm_sq, norm_ms, norm_sd, norm_xn, norm_tp, norm_ev = (sem(f"norm_{s}") for s in ("sq", "ms", "sd", "xn", "tp", "ev"))
        sb_pj, sb_pe, sb_z, sb_l, sb_sp, sb_zi, sb_a, sb_o, sb_oe = (
            sem(f"sb_{s}") for s in ("pj", "pe", "z", "l", "sp", "zi", "a", "o", "oe"))
        acc_done = sem("acc_done")
        ff_mm, ff_relu, ff_hid, ff_w2 = sem("ff_mm"), sem("ff_relu"), sem("ff_hid"), sem("ff_w2")
        split_x_hi, split_x, split_w_hi, split_w = sem("split_x_hi"), sem("split_x"), sem("split_w_hi"), sem("split_w")
        out_sem = sem("out_sem")
        nsa_in, gain_in = sem("nsa_in"), sem("gain_in")
        kv_mm, kv_ev, kv_rot, kv_k, pos_T, pos_in = (sem(s) for s in ("kv_mm", "kv_ev", "kv_rot", "kv_k", "pos_T", "pos_in"))
        cmp_blk, cmp_mm, cmp_uu, cmp_ee, cmp_hh, cmp_kv, cmp_out = (
            sem(f"cmp_{s}") for s in ("blk", "mm", "uu", "ee", "hh", "kv", "out"))
        gate_mm, gate_x, gate_in = (sem(f"gate_{s}") for s in ("mm", "x", "in"))
        ns_grp, ns_q, ns_qe, ns_s, ns_m, ns_p, ns_f, ns_tt, ns_t, ns_o, ns_oe = (
            sem(f"ns_{s}") for s in ("grp", "q", "qe", "s", "m", "p", "f", "tt", "t", "o", "oe"))

        b2_in, b2_T, b2_ready = sem("b2_in"), sem("b2_T"), sem("b2_ready")
        lam_d, lam_e = sem("lam_d"), sem("lam_e")
        df_pj, df_pe, df_s, df_m, df_p, df_f, df_tt, df_t, df_o, df_sq, df_ms, df_v, df_sd, df_oe = (
            sem(f"df_{s}") for s in ("pj", "pe", "s", "m", "p", "f", "tt", "t", "o", "sq", "ms", "v", "sd", "oe"))
        br_mm, br_sig, br_m, br_o_hi, br_o = (sem(f"br_{s}") for s in ("mm", "sig", "m", "o_hi", "o"))
        split2_hi, split2, out_used = sem("split2_hi"), sem("split2"), sem("out_used")
        gq_b, gq_br, gq_x, gq_sd, gq_s, gq_m, gq_p, gq_f, gq_tt, gq_t, gq_o, gq_oe = (
            sem(f"gq_{s}") for s in ("b", "br", "x", "sd", "s", "m", "p", "f", "tt", "t", "o", "oe"))
        moe_in, u_row, h_out, y_in = (sem(s) for s in ("moe_in", "u_row", "h_out", "y_in"))
        ex_done = sem("ex_done")
        u_scaled, u_out = sem("u_scaled"), sem("u_out")
        ex_x = [sem(f"ex_x{k}") for k in range(2)]
        rt_l, rt_x, rt_e, rt_a, rt_at, rt_s, rt_st, rt_oh, rt_pk, rt_in = (
            sem(f"rt_{s}") for s in ("l", "x", "e", "a", "at", "s", "st", "oh", "pk", "in"))
        ex_no, ex_xt, ex_xe, ex_gu, ex_sg, ex_h, ex_ht, ex_he, ex_y, ex_ye, ex_out = (
            sem(f"ex_{s}") for s in ("no", "xt", "xe", "gu", "sg", "h", "ht", "he", "y", "ye", "out"))

        ring = Ring(ring_tile, loaded, slot_free)
        NSA_CONST = 16 * 10
        B2_CONST, MOE_CONST = 16 * 12, 16 * 3
        NORM_TILES = [QT] * 6 + [T2] * 2 + [QT]
        PLAIN = (5, 8)
        GAIN = {**{u: u for u in range(5)}, 6: 5, 7: 6}
        EPS = [EPS1] * 6 + [EPS2] * 3
        UPD = 2 * QT
        FF_UPD = FF_PARTS * UPD
        H_BEFORE = [0, UPD, UPD + FF_UPD, UPD + FF_UPD, 2 * UPD + FF_UPD]
        H_ALL = 2 * UPD + 2 * FF_UPD
        H_X2 = H_ALL + QT
        H_FFN = H_X2 + 2 * T2

        block = ctx.enter_context(nc.Block())

        def load_ff(sp, m):
            w1, w2 = A["mlp_w1"][m], A["mlp_w2"][m]
            ring.load(sp, f"ff{m}",
                      [cols_tile(w1, lambda t, j=j: t * FF_TILES + j) for j in range(FF_TILES)]
                      + [rows_tiles(w2, lambda t, k=k: t * FF_TILES + 2 * k, lambda t, n=n: 512 * n)
                         for n in range(2) for k in range(FF_TILES // 2)], FF_PARTS)

        def finish(sp):
            sp.wait_ge(h_upd, H_FFN + QT)
            sp.dma_start(out[0].rearrange("(t p) d -> p t d", p=P), h[:, 0:QT, :]).then_inc(out_sem, 16)
            sp.wait_ge(out_sem, 16)

        ALL_CONST = 16 * (QT + 4 + 7)

        @block.sync
        def _(sp):
            n_const = 0
            for t in range(QT):
                sp.dma_start(h[:, t, :], A["x"][0, t * P:(t + 1) * P, :]).then_inc(const_in, 16)
            for dst, src in ((ident, C["ident"]), (tri_neg, C["tri_neg"]), (past01, C["past01"]), (past_neg, C["past_neg"])):
                sp.dma_start(dst[:, :], src[:, :]).then_inc(const_in, 16)
            for k, g in enumerate((A["norm_gain"][0, 0], A["norm_gain"][0, 1], A["kv_norm"], A["norm_gain"][1, 0],
                                   A["norm_gain"][1, 1], A["g_mix_2"][0], A["g_ffn_2"][0])):
                sp.dma_start(gain_rows[k * KT:(k + 1) * KT, :], g.rearrange("(k p) -> k p", p=P)).then_inc(const_in, 16)

            wq = A["sb_w_qkv"][0]

            def pair(p):
                return [cols_tile(wq, lambda t: p(t)), cols_tile(wq, lambda t: KT + p(t)),
                        cols_tile(wq, lambda t: 2 * KT + p(t)), None]
            ring.load(sp, "sb_first", pair(lambda t: 0))
            ring.load(sp, "sb_loop", pair(lambda t: t * 2 + 1) + pair(lambda t: t * 2 + 2), PAIRS // 2 - 1)
            ring.load(sp, "sb_last", pair(lambda t: PAIRS - 1))
            ring.load(sp, "sb_o", [rows_tiles(A["sb_w_o"][0], lambda t, k=k: 2 * k, lambda t, n=n: 512 * n)
                                   for n in range(2) for k in range(KT // 2)])
            load_ff(sp, 0)

            sp.wait_ge(h_upd, H_BEFORE[2])
            for dst, src in ((pos_rows[:, :], A["cmp_pos"].rearrange("c (k l) d -> (c k) (l d)", l=2)),
                             (cmp_w2[:, :, :, :], A["cmp_w2"].rearrange("c (e p) d -> p c e d", p=P)),
                             (gate_w[:, :, :], A["nsa_w_q"][0][:, D:D + N_GATES].rearrange("(k p) n -> p k n", p=P)),
                             (gate_b[:, :], A["nsa_gate_b"][0].partition_broadcast(P)),
                             (cos1[:, :], C["cos1"]), (sin1[:, :], C["sin1"]), (rot1[:, :], C["rot1"]),
                             (future_neg[:, :], C["future_neg"]), (cmp_neg[:, :, :], C["cmp_neg"]), (cmp_any[:, :], C["cmp_any"])):
                sp.dma_start(dst, src).then_inc(nsa_in, 16)
            sp.dma_start(gain_bc[:, :], A["final_norm"].partition_broadcast(P)).then_inc(gain_in, 16)
            ring.load(sp, "kv", [cols_tile(A["nsa_w_kv"], lambda t, j=j: j) for j in range(12)])
            ring.load(sp, "cmp", [rows_tiles(A["cmp_w1"][c], lambda t, k=k: 4 * k, lambda t: 0, CMP_HID)
                                  for c in range(2) for k in range(CMP_KT // 4)])
            wq = A["nsa_w_q"][0]
            ring.load(sp, "nsa", [cols_tile(wq, lambda t: t * 2), None, None, None,
                                  cols_tile(wq, lambda t: t * 2 + 1), None, None, None], GROUPS)
            ring.load(sp, "nsa_o", [rows_tiles(A["nsa_w_o"][0], lambda t, k=k: 2 * k, lambda t, n=n: 512 * n)
                                    for n in range(2) for k in range(KT // 2)])
            load_ff(sp, 1)

            sp.dma_start(h[0:META, QT, :], A["meta_tokens_2"][:, :]).then_inc(b2_in, 16)
            sp.wait_ge(h_upd, H_ALL)
            for dst, src in ((dist[:, :, :], C["dist"]), (cos2[:, :], C["cos2"]), (sin2[:, :], C["sin2"]), (rot2[:, :], C["rot2"]),
                             (head_gain_rows[0:1, :], A["g_subln_2"]), (head_gain_rows[1:2, :], A["g_qnorm_2"]),
                             (head_gain_rows[2:3, :], A["g_knorm_2"]),
                             (lam_in[:, 0, :], A["lambda_q1_2"][0].partition_broadcast(P)),
                             (lam_in[:, 1, :], A["lambda_k1_2"][0].partition_broadcast(P)),
                             (lam_in[:, 2, :], A["lambda_q2_2"][0].partition_broadcast(P)),
                             (lam_in[:, 3, :], A["lambda_k2_2"][0].partition_broadcast(P))):
                sp.dma_start(dst, src).then_inc(b2_in, 16)
            w = A["w_in_2"][0]

            def head(p):
                return [cols_tile(w, lambda t, c=c: c + p(t)) for c in (W_IN["qa"], W_IN["ka"], W_IN["va"])] + [None]

            def branch(name, gate, out_w):
                pairs = [(cols_tile(w, lambda t, n=n: gate + t * 4 + n), cols_tile(out_w, lambda t, n=n: t * 4 + n)) for n in range(4)]
                ring.load(sp, name, [s for p in pairs for s in p], 2)

            ring.load(sp, "df_first", head(lambda t: 0))
            ring.load(sp, "df_loop", head(lambda t: t * 2 + 1) + head(lambda t: t * 2 + 2), HEADS2 // 2 - 1)
            ring.load(sp, "df_last", head(lambda t: HEADS2 - 1))
            branch("br0", W_IN["ga"], A["w_branch_a_2"][0])
            queries = [cols_tile(w, lambda t, j=j: W_IN["qb"] + t * Q_PER_KV + j) for j in range(Q_PER_KV)]
            ring.load(sp, "gqa", [cols_tile(w, lambda t: W_IN["kb"] + t), queries[0], cols_tile(w, lambda t: W_IN["vb"] + t)]
                      + queries[1:] + [None, None], KV2)
            branch("br1", W_IN["gb"], A["w_branch_b_2"][0])
            ring.load(sp, "w_out", [rows_tiles(A["w_out_2"][0], lambda t, k=k: 2 * k, lambda t, n=n: 512 * n)
                                    for n in range(2) for k in range(KT // 2)])

            sp.wait_ge(h_upd, H_FFN)
            for dst, src in ((router_w[:, :, :], A["w_router_2"][0].rearrange("(k p) n -> p k n", p=P)),
                             (slot_no[:, :], C["slot_no"]), (token_no[:, :], C["token_no"])):
                sp.dma_start(dst, src).then_inc(moe_in, 16)
            sp.wait_ge(gain_in, 16)
            sp.dma_start(gain_bc[:, :], A["g_ffn_2"][0].partition_broadcast(P)).then_inc(gain_in, 16)
            wg, wu, wd = (A[n][0].rearrange("e r c -> (e r) c") for n in ("w_gate_2", "w_up_2", "w_down_2"))

            def gate_up(e):
                return [rows_tiles(m, lambda t, k=k: e(t) * KT + 2 * k, lambda t: 0) for m in (wg, wu) for k in range(KT // 2)]

            def down(e):
                return [rows_tiles(wd, lambda t, k=k: e(t) * FT + k, lambda t: 0, D) for k in range(FT)]

            ring.load(sp, "ex_first", gate_up(lambda t: 0))
            ring.load(sp, "ex_loop", gate_up(lambda t: t * 2 + 1) + down(lambda t: t * 2)
                      + gate_up(lambda t: t * 2 + 2) + down(lambda t: t * 2 + 1), EXPERTS // 2 - 1)
            ring.load(sp, "ex_last", gate_up(lambda t: EXPERTS - 1) + down(lambda t: EXPERTS - 2) + down(lambda t: EXPERTS - 1))
            sp.wait_ge(u_row, T2)
            sp.dma_start(gain_bc[:, :], A["g_final_2"].partition_broadcast(P)).then_inc(gain_in, 16)
            finish(sp)

        def take_o(dve, hi, rows, pair, src, taken):
            upper, rest = (x[rows, bass.ds(pair, 1), 0:SEQ].rearrange("p a n -> p (a n)") for x in (hi, oT_lo))
            step(dve, dve.tensor_copy(upper, src[0:HD, :]))
            dve.tensor_tensor(rest, src[0:HD, :], upper.bitcast(F32), ALU.subtract).then_inc(taken, 1)

        def norm_base(u):
            return sum(n for v, n in enumerate(NORM_TILES[:u]) if v not in PLAIN)

        SHARED = 1

        def stat(u):
            return u - (SHARED if u >= 3 else 0)

        def norm_act(act, u, updated=None):
            act.preload_act_table_set(LN_EXP)
            for t in range(NORM_TILES[u]):
                r = P if t < QT else META
                if updated is not None:
                    act.wait_ge(h_upd, updated + t + 1)
                last = act.activation(sq_junk(r), h[0:r, t, :], ACT.Square, scale=D ** -0.5, accum_out=ssq[0:r, t:t + 1])
                if t < NORM_TILES[u] - 1:
                    act_t.inc(last)
                    act.wait_ge(act_step, act_t.value())
            last.then_inc(norm_sq, 1)

        def norm_pool(pool, u):
            pool.wait_ge(norm_sq, stat(u) + 1)
            pool.tensor_scalar(rstd[:, :], ssq[:, :], EPS[u], None, ALU.add).then_inc(norm_ms, 1)
            pool.wait_ge(norm_ms, stat(u) + 1)
            pool.tensor_tensor(rstd[:, :], rstd[:, :], neg_half[:, :].broadcast_to([P, T2]), ALU.pow).then_inc(norm_sd, 1)

        def sq_junk(r):
            return xn[0:r, 1, :]

        def norm_dve(dve, u):
            base = norm_base(u)
            dve.wait_ge(norm_sd, stat(u) + 1)

            def scale(t):
                r = P if t < QT else META
                if t >= 2:
                    dve.wait_ge(norm_tp, 2 * (base + t - 1))
                dve.tensor_scalar(xn[0:r, t % 2, :], h[0:r, t, :], rstd[0:r, t:t + 1], None, ALU.mult).then_inc(norm_xn, 1)

            scale(0)
            for t in range(NORM_TILES[u]):
                if t + 1 < NORM_TILES[u]:
                    scale(t + 1)
                r = P if t < QT else META
                for c in range(2):
                    dve.wait_ge(norm_tp, 2 * (base + t) + c + 1)
                    src = bank[2 * (t % 2) + c][:, :].rearrange("p (k n) -> p k n", k=4)[:, :, 0:r]
                    dve.tensor_tensor(xT[:, 4 * c:4 * c + 4, t * P:t * P + r], src,
                                      gains[:, GAIN[u], 4 * c:4 * c + 4].unsqueeze(2).broadcast_to([P, 4, r]), ALU.mult).then_inc(norm_ev, 1)
                if u in SPLIT_NORMS and t:
                    split_x_dve(dve, u, t - 1)
            if u in SPLIT_NORMS:
                split_x_dve(dve, u, NORM_TILES[u] - 1)

        SPLIT_NORMS = (0, 1, 4, 6)
        FF_NORMS = (1, 4)

        def x_part(x, t, c):
            return x[:, 4 * c:4 * c + 4, t * P:t * P + rows_of(t)]

        def split_base(u):
            return sum(2 * NORM_TILES[v] for v in SPLIT_NORMS if v < u)

        def split_of(u):
            return (x2_hi, x2_lo) if u == 6 else (x_hi, x_lo)

        def split_x_act(act, u):
            for t in range(NORM_TILES[u]):
                for c in range(2):
                    act.wait_ge(norm_ev, 2 * (norm_base(u) + t) + c + 1)
                    act.activation(x_part(split_of(u)[0], t, c), x_part(xT, t, c), ACT.Copy).then_inc(split_x_hi, 1)

        def split_x_dve(dve, u, t):
            for c in range(2):
                dve.wait_ge(norm_ev, 2 * (norm_base(u) + t) + c + 1)
                dve.wait_ge(split_x_hi, split_base(u) + 2 * t + c + 1)
                hi, lo = split_of(u)
                dve.tensor_tensor(x_part(lo, t, c), x_part(xT, t, c), x_part(hi, t, c).bitcast(F32), ALU.subtract).then_inc(split_x, 1)

        def norm_pe(pe, u):
            base = norm_base(u)
            for t in range(NORM_TILES[u]):
                r = P if t < QT else META
                pe.wait_ge(norm_xn, base + t + 1)
                if t >= 2:
                    pe.wait_ge(norm_ev, 2 * (base + t - 1))
                for c in range(2):
                    for k in range(4):
                        last = pe.transpose(bank[2 * (t % 2) + c][:, k * P:k * P + r],
                                            xn[0:r, t % 2, (4 * c + k) * P:(4 * c + k + 1) * P], ident[0:r, 0:r])
                    last.then_inc(norm_tp, 1)
            pe.wait_ge(norm_ev, 2 * (base + NORM_TILES[u]))

        def plain_norm_dve(dve, u, tiles):
            dve.wait_ge(norm_sd, stat(u) + 1)
            for t in range(tiles):
                dve.scalar_tensor_tensor(h[:, t, :], h[:, t, :], rstd[:, t:t + 1], gain_bc[:, :], ALU.mult, ALU.mult).then_inc(h_upd, 1)

        BR_SPLITS, GQ_SPLITS = 2 * KT, Q_PER_KV + 1
        SPLIT_COUNTS = (("sb", 2 * PAIRS), ("sb_o", KT), ("nsa_o", KT), ("df", 2 * HEADS2), ("br0", BR_SPLITS),
                        ("gqa", KV2 * GQ_SPLITS), ("br1", BR_SPLITS), ("w_out", KT))
        SPLIT_BASE = {name: sum(n for _, n in SPLIT_COUNTS[:i]) for i, (name, _) in enumerate(SPLIT_COUNTS)}

        def split2_pool(pool, name, j, turn, no, hi):
            raw = ring.wait(pool, name, j, turn)
            lo = ring_lo[:, ring.plan[name][j][0], :]
            pool.tensor_tensor(hi, raw, one[:, :].broadcast_to([P, D]), ALU.mult).then_inc(split2_hi, 1)
            pool.wait_ge(split2_hi, no + 1)
            pool.tensor_tensor(lo, raw, hi.bitcast(F32), ALU.subtract).then_inc(split2, 1)

        def split2_wait(pe, name, j, turn, no, hi, width=P):
            pe.wait_ge(split2, no + 1)
            lo = ring_lo[:, ring.plan[name][j][0], :]
            return [w.rearrange("p (k n) -> p k n", n=width) for w in (hi, lo)]

        def mm3_T(pe, dst, w, x_hi, x_lo, c):
            return mm3_K(pe, dst, w, x_hi[:, :, half(c)], x_lo[:, :, half(c)])

        def mm3_K(pe, dst, w, x_hi, x_lo, k0=0, k1=KT):
            hi, lo = w
            for k in range(k0, k1):
                last = mm3(pe, dst, hi[:, k, :], lo[:, k, :], x_hi[:, k, :], x_lo[:, k, :], k == 0, k == KT - 1)
            return last

        def split_heads_pool(pool, kind, first, rest, last, heads, used, per, hi):
            each = per // 3

            def head(name, j, turn, hd, again=True):
                for n in range(2):
                    if again:
                        pool.wait_ge(used, hd * per + ((n + 1) * each - per))
                    split2_pool(pool, name, j + n, turn, hd * 2 + (SPLIT_BASE[kind] + n), hi[:, n, :])

            head(first, 0, 0, 0, False)
            with loop(pool, heads // 2 - 1) as turn:
                head(rest, 0, turn, turn * 2 + 1)
                head(rest, 4, turn, turn * 2 + 2)
            head(last, 0, 0, heads - 1)
            pool.wait_ge(used, (heads - 1) * per + 2 * each)

        OUT_NAMES = ("sb_o", "nsa_o", "w_out")

        def output_pool(pool, name, hi):
            for j in range(KT):
                if j >= SPLITS2:
                    pool.wait_ge(out_used, OUT_NAMES.index(name) * (KT - 1) + j - SPLITS2 + 1)
                split2_pool(pool, name, j, 0, SPLIT_BASE[name] + j, hi[:, j % SPLITS2, :])

        def output_pe(pe, name, a_hi, a_lo, w_hi, tiles, bank_of, done, again=None):
            for n in range(2):
                for k in range(KT):
                    j = n * (KT // 2) + k // 2
                    if k % 2 == 0:
                        hi, lo = split2_wait(pe, name, j, 0, SPLIT_BASE[name] + j, w_hi[:, j % SPLITS2, :], 512)
                    for t in range(tiles):
                        r = rows_of(t)
                        rows = slice(t * P, t * P + r)
                        if k == 0 and again:
                            again(n, t)
                        dst = bank[bank_of(n, t)][0:r, :]
                        first = pe.matmul(dst, a_hi[:, k, rows], lo[:, k % 2, :], start=(k == 0), stop=False)
                        if j and t == 0 and k % 2 == 0:
                            first.then_inc(out_used, 1)
                        pe.matmul(dst, a_lo[:, k, rows], hi[:, k % 2, :], start=False, stop=False)
                        last = pe.matmul(dst, a_hi[:, k, rows], hi[:, k % 2, :], start=False, stop=(k == KT - 1))
                        if k == KT - 1:
                            last.then_inc(acc_done, 1)
                    if k == KT - 1:
                        pe.wait_ge(acc_done, done + (n + 1) * tiles)
                        pe.sem_inc(slot_free, 1)
                    elif k % 2:
                        last.then_inc(slot_free, 1)

        def half_banks(n, t):
            return 4 * (1 - n) + t

        KV_ROT = {4: 0, 5: 1, 8: 2, 9: 3}

        def kv_pe(pe):
            pe.wait_ge(nsa_in, NSA_CONST)
            pe.transpose(bank[7][:, 0:2 * CMP_KT], pos_rows[:, :], ident[0:2 * CMP_KT, 0:2 * CMP_KT]).then_inc(pos_T, 1)

            def tile(n):
                slot = ring.wait(pe, "kv", n)
                if n >= 4:
                    pe.wait_ge(kv_ev, n - 3)
                if n in (6, 7, 10, 11):
                    for t in range(QT):
                        last = mm_N(pe, bank[n % 4][:, t * P:(t + 1) * P], slot, t)
                else:
                    last = mm_T(pe, bank[n % 4][:, :], slot, xT[:, :, 0:SEQ])
                last.then_inc(kv_mm, 1)
                pe.wait_ge(kv_mm, n + 1)
                pe.sem_inc(slot_free, 1)

            def rotate(n):
                pe.wait_ge(kv_ev, n + 1)
                pe.matmul(bank[4 + n % 2][:, :], rot1[:, :], (rope_a if n % 2 == 0 else rope_b)[:, :],
                          start=True, stop=True).then_inc(kv_rot, 1)

            for n in range(4):
                tile(n)
            for n in (4, 8):
                tile(n)
                tile(n + 1)
                rotate(n)
                tile(n + 2)
                rotate(n + 1)
                tile(n + 3)
            pe.wait_ge(kv_k, 4)
            for c in range(2):
                for k in range(CMP_KT):
                    w = ring.wait(pe, "cmp", c * 4 + k // 4).rearrange("p (k n) -> p k n", n=CMP_HID)
                    if k == 0:
                        pe.wait_ge(cmp_blk, c + 1)
                    for e in range(2):
                        last = pe.matmul(bank[4 + 2 * c + e][:, 0:GROUPS * N_CMP], w[:, k % 4, e * P:(e + 1) * P], blocks[:, c, k, :],
                                         start=(k == 0), stop=(k == CMP_KT - 1))
                    if k == CMP_KT - 1:
                        last.then_inc(cmp_mm, 1)
                        pe.wait_ge(cmp_mm, c + 1)
                        pe.sem_inc(slot_free, 1)
                    elif k % 4 == 3:
                        last.then_inc(slot_free, 1)
            pe.wait_ge(cmp_hh, 2)
            for half in range(2):
                for e in range(2):
                    pe.matmul(bank[0][HD * half:HD * half + HD, 0:GROUPS * N_CMP], cmp_w2[:, 0, e, :], cmp_h[:, 0, e, :],
                              start=(e == 0), stop=(e == 1))
            for g in range(GROUPS):
                for e in range(2):
                    last = pe.matmul(bank[1][0:N_CMP, g * HD:(g + 1) * HD], cmp_h[:, 1, e, g * N_CMP:(g + 1) * N_CMP],
                                     cmp_w2[:, 1, e, :], start=(e == 0), stop=(e == 1))
            last.then_inc(cmp_kv, 1)

        def kv_dve(dve):
            dve.wait_ge(nsa_in, NSA_CONST)
            dve.tensor_copy(future_neg_bf[:, :], future_neg[:, :])
            dve.wait_ge(pos_T, 1)
            step(dve, dve.tensor_copy(pos_off[:, :], bank[7][:, 0:2 * CMP_KT]))
            for n in range(4):
                c, gp = n // 2, n % 2
                dve.wait_ge(kv_mm, n + 1)
                for gi in range(2):
                    src = bank[n % 4][HD * gi:HD * gi + HD, :]
                    dve.tensor_copy(kv_pairs[0:HD, c, 2 * gp + gi, :], src)
                    last = dve.tensor_copy(kv_pairs[HD:P, c, 2 * gp + gi, 0:SEQ - 1], src[:, 1:SEQ])
                last.then_inc(kv_ev, 1)
            def take_blocks(c, k0, k1):
                dve.wait_ge(kv_ev, 2 * c + 2)
                for k in range(k0, k1):
                    last = dve.tensor_scalar(blocks[:, c, k, :].rearrange("p (g n) -> p g n", g=GROUPS),
                                             kv_pairs[:, c, :, bass.ds(2 * k, N_CMP, CMP_STRIDE)],
                                             pos_off[:, c * CMP_KT + k:c * CMP_KT + k + 1], None, ALU.add)
                if k1 == CMP_KT:
                    last.then_inc(cmp_blk, 1)

            for br, n0 in ((0, 4), (1, 8)):
                for n in (n0, n0 + 1):
                    dve.wait_ge(kv_mm, n + 1)
                    raw = (rope_a if n % 2 == 0 else rope_b)
                    dve.tensor_copy(raw[:, :], bank[n % 4][:, :]).then_inc(kv_ev, 1)
                for n in (n0, n0 + 1):
                    raw = (rope_a if n % 2 == 0 else rope_b)
                    dve.wait_ge(kv_rot, KV_ROT[n] + 1)
                    dve_t.inc(dve.tensor_tensor(q_raw[:, 0, :], raw[:, :], cos1[:, :], ALU.mult))
                    step(dve, dve.tensor_tensor(q_raw[:, 1, :], bank[4 + n % 2][:, :], sin1[:, :], ALU.mult))
                    for gi in range(2):
                        r = slice(HD * gi, HD * gi + HD)
                        for half in range(2):
                            last = dve.tensor_tensor(k_all[HD * half:HD * half + HD, br, 2 * (n - n0) + gi, :],
                                                     q_raw[r, 0, :], q_raw[r, 1, :], ALU.add)
                    last.then_inc(kv_k, 1)
                    dve.wait_ge(kv_k, KV_ROT[n] + 1)
                    dve.wait_ge(kv_mm, n + 3)
                    dve.tensor_copy(v_all[:, br, :, 2 * (n - n0):2 * (n - n0) + 2, :],
                                    bank[(n + 2) % 4][:, :].rearrange("p (t g d) -> p t g d", t=QT, g=2)).then_inc(kv_ev, 1)
                take_blocks(br, 0, CMP_KT)
            for c in range(2):
                dve.wait_ge(cmp_mm, c + 1)
                for e in range(2):
                    last = dve.tensor_copy(cmp_x[:, e, :], bank[4 + 2 * c + e][:, 0:GROUPS * N_CMP])
                step(dve, last)
                step(dve, dve.tensor_tensor(cmp_u[:, :, :], cmp_x[:, :, :], cmp_x[:, :, :], ALU.mult))
                step(dve, dve.tensor_scalar(cmp_u[:, :, :], cmp_u[:, :, :], GELU_C, 1.0, ALU.mult, ALU.add))
                dve.tensor_tensor(cmp_u[:, :, :], cmp_u[:, :, :], cmp_x[:, :, :], ALU.mult).then_inc(cmp_uu, 1)
                dve.wait_ge(cmp_ee, c + 1)
                step(dve, dve.tensor_scalar(cmp_u[:, :, :], cmp_u[:, :, :], 0.5, 0.5, ALU.mult, ALU.add))
                dve.tensor_tensor(cmp_h[:, c, :, :], cmp_u[:, :, :], cmp_x[:, :, :], ALU.mult).then_inc(cmp_hh, 1)
                dve.wait_ge(cmp_hh, c + 1)
            dve.wait_ge(cmp_kv, 1)
            dve.tensor_copy(k_cmp[:, :, :].rearrange("p g n -> p (g n)"), bank[0][:, 0:GROUPS * N_CMP])
            dve.tensor_copy(v_cmp[:, :, :].rearrange("p g d -> p (g d)"), bank[1][0:N_CMP, 0:GROUPS * HD]).then_inc(cmp_out, 1)

        def kv_act(act):
            for c in range(2):
                act.wait_ge(cmp_uu, c + 1)
                act.activation(cmp_u[:, :, :], cmp_u[:, :, :], ACT.Tanh, scale=GELU_K).then_inc(cmp_ee, 1)

        def gates_pe(pe):
            for t in range(QT):
                for k in range(KT):
                    last = pe.matmul(bank[4][:, t * N_GATES:(t + 1) * N_GATES], xT[:, k, t * P:(t + 1) * P], gate_w[:, k, :],
                                     start=(k == 0), stop=(k == KT - 1))
            last.then_inc(gate_mm, 1)

        def gates_dve(dve):
            dve.wait_ge(gate_mm, 1)
            dve.tensor_tensor(gates[:, :, :], bank[4][:, 0:QT * N_GATES].rearrange("p (t n) -> p t n", t=QT),
                              gate_b[:, :].unsqueeze(1).broadcast_to([P, QT, N_GATES]), ALU.add).then_inc(gate_x, 1)
            dve.wait_ge(gate_in, 1)

        def gates_act(act):
            act.wait_ge(gate_x, 1)
            act.activation(gates[:, :, :], gates[:, :, :], ACT.Sigmoid).then_inc(gate_in, 1)

        def unit(n):
            head, br = n // BRANCHES, n % BRANCHES
            return head // 2, slice(HD * (head % 2), HD * (head % 2) + HD), br

        PIECES = ((3,), (2, 0), (1,))
        PER_HEAD = 1 + 2 * len(PIECES)

        def piece(n, k):
            head, br = n // BRANCHES, n % BRANCHES
            return head * PER_HEAD + (3 * br - 2 + k if br else 0)

        def piece_before(n, k):
            head, br = n // BRANCHES, n % BRANCHES
            return piece(n, 0) + (-1, (-4, -3, -1)[k], k - 3)[br]

        PER_GROUP = 4 * PER_HEAD

        def pieces(br):
            return PIECES if br else (range(QT),)

        def score_bank(i, br):
            if br == 0:
                return bank[2][:, 256 + 32 * i:256 + 32 * i + N_CMP]
            b, at = SCORE_AT[i]
            return bank[b][:, at:at + P * (i + 1)]

        def nsa_pe(pe, g):
            def project(u):
                slot = ring.wait(pe, "nsa", 4 * u, g)
                mm_T(pe, bank[7 - u][:, :], slot, xT[:, :, 0:SEQ]).then_inc(ns_q, 1)
                pe.wait_ge(ns_q, g * 4 + u + 1)
                pe.sem_inc(slot_free, 4)

            def rotate(u):
                pe.wait_ge(ns_qe, g * 4 + u + 1)
                pe.matmul(bank[7 - u][:, :], rot1[:, :], q_raw[:, u, :], start=True, stop=True).then_inc(ns_q, 1)

            def scores(n):
                u, r, br = unit(n)
                if n == 0:
                    pe.wait_ge(ns_grp, g + 1)
                if n in (1, 7):
                    pe.wait_ge(ns_qe, g * 4 + 3 + u)
                for k, tiles in enumerate(pieces(br)):
                    pe.wait_ge(ns_p, g * PER_GROUP + piece_before(n, k) + 4)
                    for i in tiles:
                        q, dst = slice(i * P, (i + 1) * P), score_bank(i, br)
                        if br == 0:
                            last = pe.matmul(dst, q_raw[r, u, q], kc_grp[r, :], start=True, stop=True)
                            continue
                        pe.matmul(dst, q_rot[r, u, q], k_grp[r, br - 1, 0:P * (i + 1)], start=True, stop=False, skip_group_check=True)
                        last = pe.matmul(dst[:, i * P:(i + 1) * P], ident_bf[:, :], future_neg_bf[:, :], start=False, stop=True,
                                         skip_group_check=True)
                    last.then_inc(ns_s, 1)

            def transposes(n):
                _, _, br = unit(n)
                pe.wait_ge(ns_f, g * UNITS + n + 1)
                pe.wait_ge(ns_t, g * UNITS + n + 1)
                if br == 0:
                    for i in range(QT):
                        last = pe.transpose(bank[3][0:N_CMP, i * P:(i + 1) * P], probs[:, n % 2, i * N_CMP:(i + 1) * N_CMP], ident[:, :])
                else:
                    for j in range(QT):
                        b, at, _ = PT_AT[j]
                        for i in range(j, QT):
                            last = pe.transpose(bank[b][:, at + (i - j) * P:at + (i - j + 1) * P],
                                                probs[:, n % 2, PROB_AT[i] + j * P:PROB_AT[i] + (j + 1) * P], ident[:, :])
                last.then_inc(ns_tt, 1)

            def weigh(n):
                u, r, br = unit(n)
                pe.wait_ge(ns_t, g * UNITS + n + 2)
                if br == 0:
                    pe.wait_ge(ns_oe, g * 4 + n // BRANCHES + 1)
                    pe.matmul(bank[6][0:HD, :], vc_grp[:, :], probs_T[0:N_CMP, n % 2, 0:SEQ], start=True, stop=False, skip_group_check=True)
                    return
                for j in range(QT):
                    at = PT_AT[j][2]
                    last = pe.matmul(bank[6][0:HD, j * P:SEQ], v_grp[:, br - 1, j, :], probs_T[:, n % 2, at:at + CAUSAL_COLS[j]],
                                     start=False, stop=(br == 2 and j == QT - 1), skip_group_check=True)
                if br == 2:
                    last.then_inc(ns_o, 1)

            pe.wait_ge(ns_oe, g * 4 + 1)
            project(0)
            project(1)
            rotate(0)
            rotate(1)
            scores(0)
            for n in range(UNITS):
                if n + 1 < UNITS:
                    scores(n + 1)
                if n:
                    weigh(n - 1)
                transposes(n)
            weigh(UNITS - 1)

        def nsa_act(act, g):
            def exps(n):
                _, _, br = unit(n)
                for k, tiles in enumerate(pieces(br)):
                    act.wait_ge(ns_m, g * PER_GROUP + piece(n, k) + 1)
                    if br == 0:
                        act.activation(probs[:, n % 2, 0:QT * N_CMP], probs[:, n % 2, 0:QT * N_CMP], ACT.Exp).then_inc(ns_p, 1)
                        return
                    for i in tiles:
                        last = act.activation(probs[:, n % 2, PROB_AT[i]:PROB_AT[i] + P * (i + 1)], score_bank(i, br), ACT.Exp,
                                              bias=top[:, n % 2, i:i + 1], accum_out=rsum[:, n % 2, i:i + 1])
                    last.then_inc(ns_p, 1)

            def take(n):
                _, _, br = unit(n)
                act.wait_ge(ns_tt, g * UNITS + n + 1)
                if br == 0:
                    act.activation(probs_T[0:N_CMP, n % 2, 0:SEQ], bank[3][0:N_CMP, :], ACT.Copy).then_inc(ns_t, 1)
                    return
                act.activation(probs_T[:, n % 2, 0:SEQ], bank[3][:, :], ACT.Copy)
                act.activation(probs_T[:, n % 2, SEQ:2 * SEQ], bank[4][:, :], ACT.Copy)
                act.activation(probs_T[:, n % 2, 2 * SEQ:CAUSAL], bank[5][:, 0:256], ACT.Copy).then_inc(ns_t, 1)

            exps(0)
            for n in range(UNITS):
                if n + 1 < UNITS:
                    exps(n + 1)
                take(n)

        def nsa_dve(dve, g):
            def one(ap):
                return ap.rearrange("p a n -> p (a n)")

            for br in range(2):
                dve.tensor_copy(k_grp[:, br, :], one(k_all[:, br, bass.ds(g, 1), :]))
                dve.tensor_copy(v_grp[:, br, :, :], v_all[:, br, :, bass.ds(g, 1), :].rearrange("p t a d -> p t (a d)"))
            dve.tensor_copy(kc_grp[:, :], one(k_cmp[:, bass.ds(g, 1), :]))
            dve.tensor_copy(vc_grp[:, :], one(v_cmp[:, bass.ds(g, 1), :])).then_inc(ns_grp, 1)
            for u in range(2):
                dve.wait_ge(ns_q, g * 4 + u + 1)
                dve.tensor_scalar(q_raw[:, u, :], bank[7 - u][:, :], HD ** -0.5, None, ALU.mult).then_inc(ns_qe, 1)
            for u in range(2):
                dve.wait_ge(ns_q, g * 4 + 3 + u)
                dve_t.inc(dve.tensor_tensor(rope_a[:, :], q_raw[:, u, :], cos1[:, :], ALU.mult))
                step(dve, dve.tensor_tensor(rope_b[:, :], bank[7 - u][:, :], sin1[:, :], ALU.mult))
                dve.tensor_tensor(q_rot[:, u, :], rope_a[:, :], rope_b[:, :], ALU.add).then_inc(ns_qe, 1)
                dve.wait_ge(ns_qe, g * 4 + 3 + u)
            def cmp_probs(n):
                return probs[:, n % 2, 0:QT * N_CMP].rearrange("p (t n) -> p t n", t=QT)

            def maxima(n):
                br, p = n % BRANCHES, cmp_probs(n)
                for k, tiles in enumerate(pieces(br)):
                    dve.wait_ge(ns_s, g * PER_GROUP + piece(n, k) + 1)
                    if br == 0:
                        s = bank[2][:, 256:384].rearrange("p (t n) -> p t n", t=QT)[:, :, 0:N_CMP]
                        step(dve, dve.tensor_tensor(p, s, cmp_neg[:, :, :], ALU.add))
                        step(dve, dve.reduce_max(top[:, n % 2, :], p, AX.X))
                        dve.tensor_tensor(p, p, top[:, n % 2, :].unsqueeze(2).broadcast_to([P, QT, N_CMP]), ALU.subtract).then_inc(ns_m, 1)
                        return
                    for i in tiles:
                        last = dve.reduce_max(top[:, n % 2, i:i + 1], score_bank(i, br), AX.X, negate=True)
                    last.then_inc(ns_m, 1)

            maxima(0)
            for n in range(UNITS):
                head, br = n // BRANCHES, n % BRANCHES
                p = cmp_probs(n)
                if n + 1 < UNITS:
                    maxima(n + 1)
                dve.wait_ge(ns_p, g * PER_GROUP + piece(n, len(pieces(br)) - 1) + 4)
                sums = rsum[:, n % 2, :]
                if br == 0:
                    step(dve, dve.reduce_sum(sums, p, AX.X))
                step(dve, dve.reciprocal(factor[:, n % 2, :], sums))
                gate = gates[:, :, bass.ds(g * 4 + (br * 16 + head), 1)].rearrange("p t a -> p (t a)")
                step(dve, dve.tensor_tensor(factor[:, n % 2, :], factor[:, n % 2, :], gate, ALU.mult))
                if br == 0:
                    step(dve, dve.tensor_tensor(factor[:, n % 2, :], factor[:, n % 2, :], cmp_any[:, :], ALU.mult))
                    dve.tensor_tensor(p, p, factor[:, n % 2, :].unsqueeze(2).broadcast_to([P, QT, N_CMP]), ALU.mult).then_inc(ns_f, 1)
                else:
                    for i in range(QT):
                        rows = probs[:, n % 2, PROB_AT[i]:PROB_AT[i] + P * (i + 1)]
                        last = dve.tensor_scalar(rows, rows, factor[:, n % 2, i:i + 1], None, ALU.mult)
                    last.then_inc(ns_f, 1)
                if br == 0 and head:
                    nsa_out(dve, g, head - 1)
            nsa_out(dve, g, 3)

        def nsa_out(dve, g, head):
            dve.wait_ge(ns_o, g * 4 + head + 1)
            r = slice(HD * (head % 2), HD * (head % 2) + HD)
            take_o(dve, ns_o_hi, r, g * 2 + head // 2, bank[6], ns_oe)

        def two(b, r=P):
            return psum[0:r, b:b + 2, 0:CH2]

        def halves(ap):
            return ap.rearrange("p (c n) -> p c n", c=2)

        def half(c):
            return slice(c * CH2, (c + 1) * CH2)

        def project2(pe, name, j, turn, made, taken, no, split, hi):
            w = split2_wait(pe, name, j, turn, split, hi)
            for c in range(2):
                pe.wait_ge(taken, no + c + 1)
                mm3_T(pe, bank[7][:, 0:CH2], w, x2_hi, x2_lo, c).then_inc(made, 1)
                if c:
                    pe.wait_ge(made, no + 2)
                    pe.sem_inc(slot_free, 1)
                yield

        def project_v2(pe, name, j, turn, made, taken, no, slots):
            slot = ring.wait(pe, name, j, turn)
            pe.wait_ge(taken, no + 1)
            for t in range(QT):
                last = mm_N(pe, bank[7][:, t * P:(t + 1) * P], slot, t)
            last.then_inc(made, 1)
            yield
            pe.wait_ge(taken, no + 2)
            mm_N(pe, bank[7][0:META, 0:P], slot, QT, META).then_inc(made, 1)
            pe.wait_ge(made, no + 2)
            pe.sem_inc(slot_free, slots)
            yield

        def take2(dve, dst, c, taken):
            dve.tensor_copy(dst[:, half(c)], bank[7][:, 0:CH2]).then_inc(taken, 1)

        def take_v2(dve, u, c, taken):
            if c == 0:
                dve.tensor_copy(v2[:, u, 0:QT, :], bank[7][:, :].rearrange("p (t n) -> p t n", n=P)).then_inc(taken, 1)
            else:
                dve.tensor_copy(v2[0:META, u, QT, :], bank[7][0:META, 0:P]).then_inc(taken, 1)

        def transposes2(pe, src):
            for j in range(QT):
                pe.transpose(bank[4][:, j * P:(j + 1) * P], src[:, j * P:(j + 1) * P], ident[:, :])
            return pe.transpose(bank[5][0:META, 0:P], src[:, SEQ:L2], ident[:, :])

        def take_T2(act, n, r):
            act.activation(w_T[:, n % 2, 0:QT, 0:r], bank[4][:, :].rearrange("p (j q) -> p j q", q=P)[:, :, 0:r], ACT.Copy)
            return act.activation(w_T[0:META, n % 2, QT, 0:r], bank[5][0:META, 0:r], ACT.Copy)

        def weigh2(pe, n, t, u):
            r = rows_of(t)
            dst = bank[6][:, t * P:(t + 1) * P] if t < QT else bank[5][:, O_TAIL:O_TAIL + META]
            for j in range(T2):
                k = rows_of(j)
                last = pe.matmul(dst, v2[0:k, u, j, :], w_T[0:k, n % 2, j, 0:r], start=(j == 0), stop=(j == T2 - 1))
            return last

        def df_parts(pe, name, j, turn, hd):
            for n in range(2):
                yield from project2(pe, name, j + n, turn, df_pj, df_pe, hd * 6 + 2 * n, hd * 2 + (SPLIT_BASE["df"] + n), w2_hi[:, n, :])
            yield from project_v2(pe, name, j + 2, turn, df_pj, df_pe, hd * 6 + 4, 2)

        def df_scores(pe, hd, u, t):
            r = rows_of(t)
            if t < QT:
                pe.wait_ge(df_p, hd * T2 + t + 1)
            if t == 0:
                pe.wait_ge(df_pe, hd * 6 + 5)
            for m in range(2):
                f = slice(HD * m, HD * m + HD)
                for c in range(2):
                    dst, k = bank[2 * m + c][0:r, 0:CH2], slice(c * CH2, (c + 1) * CH2)
                    last = pe.matmul(dst, q2[f, u, t * P:t * P + r], k2[f, u, k], start=True, stop=(t == QT), skip_group_check=True)
                    if t < QT:
                        last = pe.matmul(dst, slope[:, u, :], dist[:, t, k], start=False, stop=True, skip_group_check=True)
            last.then_inc(df_s, 1)

        def df_pe_head(pe, hd, u, parts):
            more = bool(parts)
            parts = iter(parts)
            for t in range(T2):
                if t < QT - 1:
                    df_scores(pe, hd, u, t + 1)
                if t:
                    df_weigh(pe, hd, u, t - 1)
                if t == QT - 1:
                    df_scores(pe, hd, u, QT)
                if t == 0:
                    pe.wait_ge(df_v, hd + 1)
                next(parts, None)
                pe.wait_ge(df_f, hd * T2 + t + 1)
                pe.wait_ge(df_t, hd * T2 + t + 1)
                if t == 0:
                    pe.wait_ge(df_oe, hd + 1)
                transposes2(pe, prob_a[:, t % 2, :]).then_inc(df_tt, 1)
            if more:
                df_scores(pe, hd + 1, 1 - u, 0)
            df_weigh(pe, hd, u, QT)
            for _ in parts:
                pass
            if more:
                pe.wait_ge(df_pe, hd * 6 + 13)
            pe.wait_ge(df_sq, hd + 1)
            pe.matmul(bank[7][:, :], mean_w[:, :], sq2[:, 0, 0:SEQ], start=True, stop=True)
            pe.matmul(bank[5][:, MS_TAIL:MS_TAIL + META], mean_w[:, :], sq2[:, 0, SEQ:L2], start=True, stop=True).then_inc(df_ms, 1)

        def df_weigh(pe, hd, u, t):
            pe.wait_ge(df_t, hd * T2 + t + 2)
            if t == 0:
                pe.wait_ge(df_pe, hd * 6 + 7)
            last = weigh2(pe, t, t, u)
            if t == QT:
                last.then_inc(df_o, 1)

        def df_exps(act, hd, t):
            r = rows_of(t)
            act.wait_ge(df_m, hd * T2 + t + 1)
            for m, dst in enumerate((prob_a, prob_b)):
                last = act.activation(halves(dst[0:r, t % 2, :]), two(2 * m, r), ACT.Exp, bias=top2[0:r, m:m + 1],
                                      scale=HD ** -0.5, accum_out=rsum2[0:r, m:m + 1])
            last.then_inc(df_p, 1)

        def df_act_head(act, hd, more):
            for t in range(T2):
                if t < QT:
                    df_exps(act, hd, t + 1)
                act.wait_ge(df_tt, hd * T2 + t + 1)
                take_T2(act, t, rows_of(t)).then_inc(df_t, 1)
            if more:
                df_exps(act, hd + 1, 0)
            act.wait_ge(df_o, hd + 1)
            act.activation(sq2[:, 0, 0:SEQ], bank[6][:, :], ACT.Square)
            act.activation(sq2[:, 0, SEQ:L2], bank[5][:, O_TAIL:O_TAIL + META], ACT.Square).then_inc(df_sq, 1)
            act.wait_ge(df_ms, hd + 1)
            act.activation(var2[:, 0, 0:SEQ], bank[7][:, :], ACT.Ln, bias=eps_col[:, :])
            act.activation(var2[:, 0, SEQ:L2], bank[5][:, MS_TAIL:MS_TAIL + META], ACT.Ln, bias=eps_col[:, :]).then_inc(df_v, 1)
            act.wait_ge(df_v, hd + 2)
            act.activation(var2[:, 0, :], var2[:, 0, :], ACT.Exp, scale=-0.5).then_inc(df_sd, 1)

        def df_maxima(dve, hd, t):
            r = rows_of(t)
            dve.wait_ge(df_s, hd * T2 + t + 1)
            for m in range(2):
                last = dve.reduce_max(top2[0:r, m:m + 1], two(2 * m, r), AX.XY)
            step(dve, last)
            dve.tensor_scalar(top2[0:r, :], top2[0:r, :], -HD ** -0.5, None, ALU.mult).then_inc(df_m, 1)

        def df_dve_head(dve, hd, u, take):
            for t in range(T2):
                r = rows_of(t)
                dve.wait_ge(df_p, hd * T2 + t + 2)
                step(dve, dve.reciprocal(rinv2[0:r, :], rsum2[0:r, :]))
                dve_t.inc(dve.tensor_tensor(rinv2[0:r, 1:2], rinv2[0:r, 1:2], neg_lam[0:r, :], ALU.mult))
                a, b = prob_a[0:r, t % 2, :], prob_b[0:r, t % 2, :]
                step(dve, dve.tensor_scalar(a, a, rinv2[0:r, 0:1], None, ALU.mult))
                dve.scalar_tensor_tensor(a, b, rinv2[0:r, 1:2], a, ALU.mult, ALU.add).then_inc(df_f, 1)
                if t < QT:
                    df_maxima(dve, hd, t + 1)
                if take:
                    df_take(dve, t, hd + 1, 1 - u)
            if take:
                df_maxima(dve, hd + 1, 0)
                df_take(dve, T2, hd + 1, 1 - u)
            step(dve, dve.tensor_scalar(slope[:, u, :], slope[:, u, :], 0.25, None, ALU.mult))
            dve.wait_ge(df_sd, hd + 1)
            o = oT[:, bass.ds(hd, 1), :].rearrange("p a n -> p (a n)")
            dve.scalar_tensor_tensor(o[:, 0:SEQ], bank[6][:, :], head_gain[:, 0:1], var2[:, 0, 0:SEQ], ALU.mult, ALU.mult)
            dve.scalar_tensor_tensor(o[:, SEQ:L2], bank[5][:, O_TAIL:O_TAIL + META], head_gain[:, 0:1], var2[:, 0, SEQ:L2],
                                     ALU.mult, ALU.mult).then_inc(df_oe, 1)

        def ready2_dve(dve):
            dve.wait_ge(b2_T, 1)
            dve.tensor_scalar(head_gain[:, 0:1], bank[7][:, 0:1], 1.0 - LAM_INIT, None, ALU.mult)
            dve.tensor_copy(head_gain[:, 1:3], bank[7][:, 1:3])
            dve.memset(mean_w[:, :], 1.0 / P)
            for u in range(2):
                dve_t.inc(dve.tensor_scalar(slope[:, u, :], ident[:, :], -(HD ** 0.5) * 0.5 ** (u + 1), None, ALU.mult))
            for m in range(2):
                step(dve, dve.tensor_tensor(lam_prod[:, :], lam_in[:, 2 * m, :], lam_in[:, 2 * m + 1, :], ALU.mult))
                last = dve.reduce_sum(lam[:, m:m + 1], lam_prod[:, :], AX.X)
                if m:
                    last.then_inc(lam_d, 1)
                else:
                    step(dve, last)
            dve.wait_ge(lam_e, 1)
            step(dve, dve.tensor_tensor(neg_lam[:, :], lam[:, 1:2], lam[:, 0:1], ALU.subtract))
            dve.tensor_scalar(neg_lam[:, :], neg_lam[:, :], -LAM_INIT, None, ALU.add).then_inc(b2_ready, 1)
            dve.wait_ge(b2_ready, 1)

        def df_take(dve, n, hd, u):
            dve.wait_ge(df_pj, hd * 6 + n + 1)
            if n >= 4:
                take_v2(dve, u, n % 2, df_pe)
            else:
                take2(dve, (q2, k2)[n // 2][:, u, :], n % 2, df_pe)

        def branch_pool(pool, b):
            with loop(pool, 2) as turn:
                for j in range(KT):
                    n = turn * KT + (b * BR_SPLITS + j)
                    pool.wait_ge(br_mm, n + 1)
                    split2_pool(pool, f"br{b}", j, turn, turn * KT + (SPLIT_BASE[f"br{b}"] + j), w2_hi[:, j % SPLITS2, :])

        def branch_pe(pe, b):
            with loop(pe, 2) as turn:
                for n in range(4):
                    i = turn * 4 + (b * KT + n)
                    for m, src in enumerate(((x2_hi, x2_lo), (o_hi, oT_lo))):
                        j = 2 * n + m
                        w = split2_wait(pe, f"br{b}", j, turn, turn * KT + (SPLIT_BASE[f"br{b}"] + j), w2_hi[:, j % SPLITS2, :])
                        if m == 0:
                            pe.wait_ge(br_m, i + 1)
                        elif n == 0:
                            pe.wait_ge(br_o, KT * (b + 1))
                        for c in range(2):
                            last = mm3_T(pe, bank[4 * (n % 2) + 2 * m + c][:, 0:CH2], w, *src, c)
                        last.then_inc(br_mm, 1)
                        pe.wait_ge(br_mm, i * 2 + m + 3)
                        pe.sem_inc(slot_free, 1)

        def split_o_act(act, b, done):
            act.wait_ge(done, HEADS2 + 1)
            for k in range(KT):
                act.activation(o_hi[:, k, :], oT[:, k, :], ACT.Copy).then_inc(br_o_hi, 1)

        def split_o_dve(dve, b):
            for k in range(KT):
                dve.wait_ge(br_o_hi, b * KT + k + 1)
                dve.tensor_tensor(oT_lo[:, k, :], oT[:, k, :], o_hi[:, k, :].bitcast(F32), ALU.subtract).then_inc(br_o, 1)

        def branch_act(act, b):
            with loop(act, 2) as turn:
                for n in range(4):
                    i = turn * 4 + (b * KT + n)
                    act.wait_ge(br_mm, i * 2 + 3)
                    act.wait_ge(br_m, i + 1)
                    act.activation(halves(sig[:, n % 2, :]), two(4 * (n % 2)), ACT.Sigmoid).then_inc(br_sig, 1)

        def branch_dve(dve, b, per):
            with loop(dve, 2, tallies=[(dve_t, per)]) as turn:
                for n in range(4):
                    i = turn * 4 + (b * KT + n)
                    dve.wait_ge(br_mm, i * 2 + 4)
                    dve.wait_ge(br_sig, i + 1)
                    m = merged[:, bass.ds(turn * 4 + n, 1), :].rearrange("p a n -> p (a n)")
                    if b == 0:
                        dve.tensor_tensor(halves(m), halves(sig[:, n % 2, :]), two(4 * (n % 2) + 2), ALU.mult).then_inc(br_m, 1)
                    else:
                        gated = sig[:, n % 2, :]
                        step(dve, dve.tensor_tensor(halves(gated), halves(gated), two(4 * (n % 2) + 2), ALU.mult))
                        step(dve, dve.tensor_tensor(m, m, gated, ALU.add))
                        hi = merged_hi[:, bass.ds(turn * 4 + n, 1), :].rearrange("p a n -> p (a n)")
                        step(dve, dve.tensor_copy(hi, m))
                        lo = merged_lo[:, bass.ds(turn * 4 + n, 1), :].rearrange("p a n -> p (a n)")
                        dve.tensor_tensor(lo, m, hi.bitcast(F32), ALU.subtract).then_inc(br_m, 1)

        def piece_no(tile, what, c=0):
            if what == "value":
                return (6, 9)[c]
            k = ("proj", "mean", "rot").index(what)
            return c + (((0, 4, 10), (2, 7, 12))[tile][k] if tile < 2 else 14 + 6 * (tile - 2) + 2 * k)

        def piece_bank(tile, c):
            return bank[2 * tile + c if tile < 2 else 7][:, 0:CH2]

        def x_no(tile, k):
            return 2 * (k - 1) + tile + 1 if tile < 2 else 6 + 3 * (tile - 2) + k

        XS = 3 * (Q_PER_KV + 1)
        UN = Q_PER_KV * T2

        def gq_pool(pool):
            pool.wait_ge(br_mm, BR_SPLITS + 2)
            for kv in range(KV2):
                for tile in range(GQ_SPLITS):
                    before = (kv, tile - SPLITS2) if tile >= SPLITS2 else (kv - 1, (4, 3)[tile])
                    if before[0] >= 0:
                        pool.wait_ge(gq_b, before[0] * USES + piece_no(before[1], "proj", 1) + 1)
                    split2_pool(pool, "gqa", tile + (tile > 1), kv, SPLIT_BASE["gqa"] + kv * GQ_SPLITS + tile, w2_hi[:, tile % SPLITS2, :])
            pool.wait_ge(gq_b, KV2 * USES)

        def gq_pe_turn(pe, kv):
            def taken(no):
                pe.wait_ge(gq_br, kv * USES + no + 2)

            def project(tile):
                w = split2_wait(pe, "gqa", tile + (tile > 1), kv, kv * GQ_SPLITS + (SPLIT_BASE["gqa"] + tile), w2_hi[:, tile % SPLITS2, :])
                no = piece_no(tile, "proj")
                for c in range(2):
                    if tile >= 2:
                        taken(no + c - 1)
                    elif c == 0:
                        pe.wait_ge(gq_p, kv * UN + 2)
                    mm3_T(pe, piece_bank(tile, c), w, x2_hi, x2_lo, c).then_inc(gq_b, 1)
                pe.wait_ge(gq_b, kv * USES + no + 2)
                pe.sem_inc(slot_free, 1)

            def small(tile, what, weight, src):
                pe.wait_ge(gq_x, kv * XS + x_no(tile, 1 if what == "mean" else 2))
                for c in range(2):
                    no = piece_no(tile, what, c)
                    taken(piece_no(tile, "proj" if what == "mean" else "mean", c) if tile < 2 else no - 1)
                    pe.matmul(piece_bank(tile, c), weight[:, :], src[:, tile % 2, half(c)], start=True, stop=True).then_inc(gq_b, 1)

            def mean(tile):
                small(tile, "mean", mean_w, sq2)

            def rotate(tile):
                small(tile, "rot", rot2, norm2)

            def values(c):
                slot = ring.wait(pe, "gqa", 2, kv)
                if c == 0:
                    pe.wait_ge(gq_br, kv * USES + 1)
                    for t in range(QT):
                        last = mm_N(pe, bank[7][:, t * P:(t + 1) * P], slot, t)
                    last.then_inc(gq_b, 1)
                else:
                    taken(piece_no(0, "value", 0))
                    mm_N(pe, bank[7][0:META, 0:P], slot, QT, META).then_inc(gq_b, 1)
                    pe.wait_ge(gq_b, kv * USES + piece_no(0, "value", 1) + 1)
                    pe.sem_inc(slot_free, 1)

            def prepare(tile):
                project(tile)
                yield
                mean(tile)
                yield
                yield
                rotate(tile)
                yield

            def scores(n):
                j, t = n // T2, n % T2
                r = rows_of(t)
                pe.wait_ge(gq_p, kv * UN + n + 1)
                if t == 0:
                    pe.wait_ge(gq_x, kv * XS + x_no(j + 1, 3))
                for c in range(2):
                    last = pe.matmul(bank[2 * (n % 2) + c][0:r, 0:CH2], q2[:, j % 2, t * P:t * P + r], k2[:, 0, c * CH2:(c + 1) * CH2],
                                     start=True, stop=True)
                last.then_inc(gq_s, 1)

            def weigh(n):
                j, t = n // T2, n % T2
                pe.wait_ge(gq_t, kv * UN + n + 2)
                if t == 0:
                    pe.wait_ge(gq_oe, kv * Q_PER_KV + j + 1)
                last = weigh2(pe, n, t, 0)
                if t == QT:
                    last.then_inc(gq_o, 1)

            project(0)
            project(1)
            mean(0)
            values(0)
            mean(1)
            values(1)
            rotate(0)
            rotate(1)
            scores(0)
            parts = iter(())
            for n in range(UN):
                j, t = n // T2, n % T2
                if t == 0:
                    parts = prepare(j + 2) if j + 1 < Q_PER_KV else iter(())
                if n + 1 < UN:
                    scores(n + 1)
                if n:
                    weigh(n - 1)
                next(parts, None)
                pe.wait_ge(gq_f, kv * UN + n + 1)
                pe.wait_ge(gq_t, kv * UN + n + 1)
                if t == 0:
                    pe.wait_ge(gq_oe, kv * Q_PER_KV + j + 1)
                transposes2(pe, prob_a[:, n % 2, :]).then_inc(gq_tt, 1)
            weigh(UN - 1)
            pe.sem_inc(slot_free, 2)

        def gq_act_turn(act, kv):
            def root(tile):
                act.wait_ge(gq_br, kv * USES + piece_no(tile, "mean", 1) + 2)
                var = var2[:, tile % 2, :]
                act_t.inc(act.activation(var, var, ACT.Ln))
                act.wait_ge(act_step, act_t.value())
                act.activation(var, var, ACT.Exp, scale=-0.5).then_inc(gq_sd, 1)

            def exps(n):
                r = rows_of(n % T2)
                act.wait_ge(gq_m, kv * UN + n + 1)
                act.activation(halves(prob_a[0:r, n % 2, :]), two(2 * (n % 2), r), ACT.Exp, bias=top2[0:r, n % 2:n % 2 + 1],
                               scale=P ** -0.5, accum_out=rsum2[0:r, n % 2:n % 2 + 1]).then_inc(gq_p, 1)

            root(0)
            root(1)
            exps(0)
            for n in range(UN):
                j, t = n // T2, n % T2
                if n + 1 < UN:
                    exps(n + 1)
                act.wait_ge(gq_tt, kv * UN + n + 1)
                take_T2(act, n, rows_of(t)).then_inc(gq_t, 1)
                if t == 1 and j + 1 < Q_PER_KV:
                    root(j + 2)

        def gq_dve_turn(dve, kv):
            def piece(tile, what, c):
                dve.wait_ge(gq_b, kv * USES + piece_no(tile, what, c) + 1)

            def square(tile, c):
                piece(tile, "proj", c)
                raw = raw2[:, tile % 2, :]
                dve.tensor_copy(raw[:, half(c)], piece_bank(tile, c)).then_inc(gq_br, 1)
                if c:
                    dve.wait_ge(gq_br, kv * USES + piece_no(tile, "proj", 1) + 2)
                    dve.tensor_tensor(sq2[:, tile % 2, :], raw, raw, ALU.mult).then_inc(gq_x, 1)

            def variance(tile, c):
                piece(tile, "mean", c)
                dve.tensor_scalar(var2[:, tile % 2, half(c)], piece_bank(tile, c), EPS2, None, ALU.add).then_inc(gq_br, 1)

            def normalise(tile):
                dve.wait_ge(gq_sd, kv * (Q_PER_KV + 1) + tile + 1)
                g = 2 if tile == 0 else 1
                raw, norm = raw2[:, tile % 2, :], norm2[:, tile % 2, :]
                dve.scalar_tensor_tensor(norm, raw, head_gain[:, g:g + 1], var2[:, tile % 2, :], ALU.mult, ALU.mult).then_inc(gq_x, 1)
                dve.wait_ge(gq_x, kv * XS + x_no(tile, 2))
                dve_t.inc(dve.tensor_tensor(raw, norm, cos2[:, :], ALU.mult))

            def rotated(tile, c):
                piece(tile, "rot", c)
                dve.tensor_tensor(rope_c[:, half(c)], piece_bank(tile, c), sin2[:, half(c)], ALU.mult).then_inc(gq_br, 1)
                dve.wait_ge(gq_br, kv * USES + piece_no(tile, "rot", c) + 2)
                dve.wait_ge(dve_step, dve_t.value())
                dst = k2[:, 0, half(c)] if tile == 0 else q2[:, (tile - 1) % 2, half(c)]
                last = dve.tensor_tensor(dst, raw2[:, tile % 2, half(c)], rope_c[:, half(c)], ALU.add)
                if c:
                    last.then_inc(gq_x, 1)
                    dve.wait_ge(gq_x, kv * XS + x_no(tile, 3))

            def values(c):
                piece(0, "value", c)
                take_v2(dve, 0, c, gq_br)

            for stage, tile in ((square, 0), (square, 1), (variance, 0)):
                for c in range(2):
                    stage(tile, c)
            normalise(0)
            values(0)
            for c in range(2):
                variance(1, c)
            values(1)
            normalise(1)
            for tile in range(2):
                for c in range(2):
                    rotated(tile, c)

            def maxima(n):
                r, c = rows_of(n % T2), n % 2
                dve.wait_ge(gq_s, kv * UN + n + 1)
                step(dve, dve.reduce_max(top2[0:r, c:c + 1], two(2 * c, r), AX.XY))
                dve.tensor_scalar(top2[0:r, c:c + 1], top2[0:r, c:c + 1], -P ** -0.5, None, ALU.mult).then_inc(gq_m, 1)

            maxima(0)
            for n in range(UN):
                j, t = n // T2, n % T2
                r, more = rows_of(t), j + 1 < Q_PER_KV
                c = n % 2
                stage = {0: square, 1: variance, 3: rotated}.get(t) if more else None
                if stage:
                    stage(j + 2, 0)
                dve.wait_ge(gq_p, kv * UN + n + 3)
                step(dve, dve.reciprocal(rinv2[0:r, c:c + 1], rsum2[0:r, c:c + 1]))
                a = prob_a[0:r, c, :]
                dve.tensor_scalar(a, a, rinv2[0:r, c:c + 1], None, ALU.mult).then_inc(gq_f, 1)
                if n + 1 < UN:
                    maxima(n + 1)
                if t == 0 and j:
                    gq_out(dve, kv, j - 1)
                if stage:
                    stage(j + 2, 1)
                if more and t == 2:
                    normalise(j + 2)
            gq_out(dve, kv, Q_PER_KV - 1)

        def gq_out(dve, kv, j):
            dve.wait_ge(gq_o, kv * Q_PER_KV + j + 1)
            o = oT[:, bass.ds(kv * Q_PER_KV + j, 1), :].rearrange("p a n -> p (a n)")
            dve.tensor_copy(o[:, 0:SEQ], bank[6][:, :])
            dve.tensor_copy(o[:, SEQ:L2], bank[5][:, O_TAIL:O_TAIL + META]).then_inc(gq_oe, 1)

        def route_pe(pe):
            pe.wait_ge(moe_in, MOE_CONST)
            for t in range(T2):
                r = rows_of(t)
                for k in range(KT):
                    last = pe.matmul(bank[0][0:r, t * EXPERTS:(t + 1) * EXPERTS], xT[:, k, t * P:t * P + r], router_w[:, k, :],
                                     start=(k == 0), stop=(k == KT - 1))
            last.then_inc(rt_l, 1)
            pe.wait_ge(rt_a, 1)
            for t in range(T2):
                r = rows_of(t)
                dst = bank[1][0:EXPERTS, t * P:(t + 1) * P] if t < QT else bank[2][0:EXPERTS, 0:META]
                last = pe.transpose(dst, logits[0:r, t, :], ident[0:r, 0:r])
            last.then_inc(rt_at, 1)
            pe.wait_ge(rt_s, 1)
            for t in range(T2):
                r = rows_of(t)
                at = META + t * P if t < QT else 0
                last = pe.transpose(bank[3][0:r, t * EXPERTS:(t + 1) * EXPERTS], work[:, at:at + r], ident[0:EXPERTS, 0:EXPERTS])
            last.then_inc(rt_st, 1)
            for e in range(EXPERTS):
                pe.wait_ge(rt_oh, e + 1)
                for t in range(T2):
                    r = rows_of(t)
                    last = pe.matmul(bank[4][0:CAP, 2 * e:2 * e + 2], one_hot[0:r, e % 4, t, :], token_aff[0:r, t, e, :],
                                     start=(t == 0), stop=(t == QT))
                last.then_inc(rt_pk, 1)

        def route_act(act):
            act.wait_ge(rt_x, 1)
            act.activation(logits[:, :, :], logits[:, :, :], ACT.Exp).then_inc(rt_e, 1)

        def route_dve(dve):
            dve.wait_ge(moe_in, MOE_CONST)
            dve_t.inc(dve.memset(logits[:, :, :], 0.0))
            dve_t.inc(dve.memset(slot_T[:, :, :], -1.0))
            dve_t.inc(dve.memset(ones_row[:, :], 1.0))
            step(dve, dve.tensor_copy(token_aff[:, :, :, 0], token_no[:, :].unsqueeze(2).broadcast_to([P, T2, EXPERTS])))
            dve.wait_ge(rt_l, 1)
            dve_t.inc(dve.tensor_copy(logits[:, 0:QT, :], bank[0][:, 0:QT * EXPERTS].rearrange("p (t n) -> p t n", n=EXPERTS)))
            step(dve, dve.tensor_copy(logits[0:META, QT, :], bank[0][0:META, QT * EXPERTS:T2 * EXPERTS]))

            def wide(ap):
                return ap.unsqueeze(2).broadcast_to([P, T2, EXPERTS])

            step(dve, dve.reduce_max(lmax[:, :], logits[:, :, :], AX.X))
            dve.tensor_tensor(logits[:, :, :], logits[:, :, :], wide(lmax[:, :]), ALU.subtract).then_inc(rt_x, 1)
            dve.wait_ge(rt_e, 1)
            step(dve, dve.reduce_sum(lmax[:, :], logits[:, :, :], AX.X))
            step(dve, dve.reciprocal(lmax[:, :], lmax[:, :]))
            dve.tensor_tensor(logits[:, :, :], logits[:, :, :], wide(lmax[:, :]), ALU.mult).then_inc(rt_a, 1)
            dve.wait_ge(rt_a, 1)
            dve_t.inc(dve.tensor_copy(token_aff[:, :, :, 1], logits[:, :, :]))
            dve.wait_ge(rt_at, 1)
            dve_t.inc(dve.tensor_copy(aff_T[:, META:L2], bank[1][0:EXPERTS, :]))
            step(dve, dve.tensor_copy(aff_T[:, 0:META], bank[2][0:EXPERTS, 0:META]))
            src = aff_T
            for k in range((CAP - 1) // 8 + 1):
                step(dve, dve.max(best8[:, :], src[:, :]))
                if k < (CAP - 1) // 8:
                    step(dve, dve.match_replace(work[:, :], best8[:, :], src[:, :], -1.0))
                    src = work
            least = best8[:, (CAP - 1) % 8:(CAP - 1) % 8 + 1]
            step(dve, dve.tensor_scalar(above[:, :], aff_T[:, :], least, None, ALU.is_gt))
            dve_t.inc(dve.reduce_sum(n_above[:, 0:1], above[:, :], AX.X))
            step(dve, dve.tensor_scalar(equal[:, :], aff_T[:, :], least, None, ALU.is_equal))
            dve_t.inc(dve.tensor_scalar(n_above[:, 1:2], n_above[:, 0:1], -1.0, float(CAP), ALU.mult, ALU.add))
            step(dve, dve.tensor_tensor_scan(count[:, :], ones_row[:, :], equal[:, :], 0.0, ALU.mult, ALU.add))
            step(dve, dve.scalar_tensor_tensor(equal[:, :], count[:, :], n_above[:, 1:2], equal[:, :], ALU.is_le, ALU.mult))
            step(dve, dve.tensor_tensor(above[:, :], above[:, :], equal[:, :], ALU.add))
            step(dve, dve.tensor_tensor_scan(count[:, :], ones_row[:, :], above[:, :], 0.0, ALU.mult, ALU.add))
            step(dve, dve.tensor_tensor(work[:, :], count[:, :], above[:, :], ALU.mult))
            dve.tensor_scalar(work[:, :], work[:, :], -1.0, None, ALU.add).then_inc(rt_s, 1)
            dve.wait_ge(rt_st, 1)
            dve_t.inc(dve.tensor_copy(slot_T[:, 0:QT, :], bank[3][:, 0:QT * EXPERTS].rearrange("p (t n) -> p t n", n=EXPERTS)))
            step(dve, dve.tensor_copy(slot_T[0:META, QT, :], bank[3][0:META, QT * EXPERTS:T2 * EXPERTS]))
            for e in range(EXPERTS):
                if e >= 4:
                    dve.wait_ge(rt_pk, e - 3)
                dve.tensor_tensor(one_hot[:, e % 4, :, :], slot_no[:, :].unsqueeze(1).broadcast_to([P, T2, CAP]),
                                  slot_T[:, :, e:e + 1].broadcast_to([P, T2, CAP]), ALU.is_equal).then_inc(rt_oh, 1)
            dve.wait_ge(rt_pk, EXPERTS)
            step(dve, dve.tensor_copy(pick[:, :, :].rearrange("p e c -> p (e c)"), bank[4][0:CAP, 0:2 * EXPERTS]))
            dve.tensor_copy(pick_no[:, :], pick[:, :, 0]).then_inc(ex_no, 1)

        def tokens_act(act):
            act.wait_ge(norm_sd, 8 - SHARED)
            for t in range(T2):
                r = rows_of(t)
                act.activation(u_rows[0:r, t, :], h[0:r, t, :], ACT.Copy, scale=rstd[0:r, t:t + 1]).then_inc(u_scaled, 1)

        def tokens_pool(pool):
            pool.wait_ge(gain_in, 32)
            for t in range(T2):
                r = rows_of(t)
                pool.wait_ge(u_scaled, t + 1)
                pool.tensor_tensor(u_rows[0:r, t, :], u_rows[0:r, t, :], gain_bc[0:r, :], ALU.mult).then_inc(u_row, 1)
                pool.wait_ge(u_row, t + 1)
                pool.dma_start(u_dram[t * P:t * P + r, :], u_rows[0:r, t, :]).then_inc(u_out, 16)

        def ex_tokens_pe(pe, i, u):
            e = i * 2 + u
            pe.wait_ge(ex_x[u], i * 16 + 16)
            pe.wait_ge(ex_xe, e + 1)
            for k in range(KT):
                last = pe.transpose(bank[k // 4][:, (k % 4) * CAP:(k % 4 + 1) * CAP], xs[:, u, k * P:(k + 1) * P], ident[0:CAP, 0:CAP])
            last.then_inc(ex_xt, 1)

        def ex_gate_up_pe(pe, name, j, turn, i, u, m):
            e = i * 2 + u
            if m == 0:
                pe.wait_ge(ex_xe, e + 2)
                pe.wait_ge(ex_h, e + 1)
            for k in range(KT):
                n = m * (KT // 2) + k // 2
                w = ring.wait(pe, name, j + n, turn).rearrange("p (k n) -> p k n", n=512)
                last = pe.matmul(bank[2 + m][0:CAP, :], xs_T[:, u, k, :], w[:, k % 2, :], start=(k == 0), stop=(k == KT - 1))
                if k % 2 and not (m == 1 and k == KT - 1):
                    last.then_inc(slot_free, 1)
            if m == 1:
                last.then_inc(ex_gu, 1)

        def ex_up_done_pe(pe, i, u):
            pe.wait_ge(ex_gu, i * 2 + (u + 1))
            pe.sem_inc(slot_free, 1)

        def ex_hidden_pe(pe, i, u):
            e = i * 2 + u
            pe.wait_ge(ex_h, e + 2)
            pe.wait_ge(ex_he, e + 1)
            for k in range(FT):
                last = pe.transpose(bank[4][:, k * CAP:(k + 1) * CAP], act_hid[:, u, k * P:(k + 1) * P], ident[0:CAP, 0:CAP])
            last.then_inc(ex_ht, 1)

        def ex_down_pe(pe, name, j, turn, i, u):
            e = i * 2 + u
            pe.wait_ge(ex_he, e + 2)
            pe.wait_ge(ex_ye, e + 1)
            for k in range(FT):
                w = ring.wait(pe, name, j + k, turn)
                for n in range(2):
                    last = pe.matmul(bank[5 + n][0:CAP, :], hid_T[:, u, k, :], w[:, 512 * n:512 * n + 512], start=(k == 0), stop=(k == FT - 1))
                if k < FT - 1:
                    last.then_inc(slot_free, 1)
            last.then_inc(ex_y, 1)
            pe.wait_ge(ex_y, e + 1)
            pe.sem_inc(slot_free, 1)

        def ex_tokens_act(act, i, u):
            e = i * 2 + u
            act.wait_ge(ex_xt, e + 3)
            for c in range(2):
                last = act.activation(xs_T[:, u, 4 * c:4 * c + 4, :], bank[c][:, 0:4 * CAP].rearrange("p (k n) -> p k n", n=CAP), ACT.Copy)
            last.then_inc(ex_xe, 1)

        def ex_act(act, i, u):
            e = i * 2 + u
            act.wait_ge(ex_gu, e + 1)
            act.wait_ge(ex_h, e + 1)
            act.activation(act_sig[:, :], bank[2][0:CAP, :], ACT.Sigmoid).then_inc(ex_sg, 1)

        def ex_hid_dve(dve, i, u):
            e = i * 2 + u
            dve.wait_ge(ex_sg, e + 1)
            step(dve, dve.tensor_tensor(act_hid[:, u, :], act_sig[:, :], bank[2][0:CAP, :], ALU.mult))
            dve.tensor_tensor(act_hid[:, u, :], act_hid[:, u, :], bank[3][0:CAP, :], ALU.mult).then_inc(ex_h, 1)

        def ex_hidden_dve(dve, i, u):
            e = i * 2 + u
            dve.wait_ge(ex_ht, e + 1)
            dve.tensor_copy(hid_T[:, u, :, :], bank[4][:, 0:FT * CAP].rearrange("p (k n) -> p k n", n=CAP)).then_inc(ex_he, 1)

        def ex_out_dve(dve, i, u):
            e = i * 2 + u
            dve.wait_ge(ex_done, e + 1)
            step(dve, dve.tensor_copy(aff_now[:, u, :], pick[:, bass.ds(e, 1), 1]))
            dve.wait_ge(ex_y, e + 1)
            for n in range(2):
                last = dve.tensor_scalar(ys[:, u, 512 * n:512 * n + 512], bank[5 + n][0:CAP, :], aff_now[:, u, :], None, ALU.mult)
            last.then_inc(ex_ye, 1)

        def ex_put(pool, i, u):
            e = i * 2 + u
            pool.wait_ge(ex_ye, e + 2)
            pool.tensor_copy(no_put[:, u, :], pick_no[:, bass.ds(e, 1)])
            pool.drain()
            pool.indirect_dma_start(y_dram[:, :], bass.IndirectOffsetOnAxis(ap=no_put[:, u, :], axis=0), ys[:, u, :], None,
                                    compute_op=ALU.add).then_inc(ex_out, 16)
            pool.wait_ge(ex_out, e * 16 + 16)
            pool.sem_inc(ex_done, 1)
        def ex_get(pool, i, u):
            e = i * 2 + u
            pool.wait_ge(ex_xt, e + 1)
            pool.tensor_copy(no_get[:, u, :], pick_no[:, bass.ds(e, 1)])
            pool.drain()
            pool.indirect_dma_start(xs[:, u, :], None, u_dram[:, :], bass.IndirectOffsetOnAxis(ap=no_get[:, u, :], axis=0)).then_inc(ex_x[u], 16)

        def mm_T(pe, dst, slot, src, k0=0, k1=KT):
            w = slot.rearrange("p (k n) -> p k n", n=P)
            for k in range(k0, k1):
                last = pe.matmul(dst, w[:, k, :], src[:, k, :], start=(k == 0), stop=(k == KT - 1))
            return last

        def mm_N(pe, dst, slot, t, r=P):
            w = slot.rearrange("p (k n) -> p k n", n=P)
            for k in range(KT):
                last = pe.matmul(dst, xT[:, k, t * P:t * P + r], w[:, k, :], start=(k == 0), stop=(k == KT - 1))
            return last

        def sb_project(pe, name, j, turn, p):
            for n, b in ((0, 5), (1, 6)):
                for half in range(2):
                    if half == 0:
                        w = split2_wait(pe, name, j + n, turn, p * 2 + (SPLIT_BASE["sb"] + n), w_hi[:, n, :])
                        pe.wait_ge(sb_pe, p * 3 + n + 1)
                    last = mm3_K(pe, bank[b][:, :], w, x_hi, x_lo, half * 4, half * 4 + 4)
                    if half:
                        last.then_inc(sb_pj, 1)
                        pe.wait_ge(sb_pj, p * 3 + n + 1)
                        pe.sem_inc(slot_free, 1)
                    yield
            slot = ring.wait(pe, name, j + 2, turn)
            pe.wait_ge(sb_pe, p * 3 + 3)
            for half in range(2):
                for t in (2 * half, 2 * half + 1):
                    last = mm_N(pe, bank[7][:, t * P:(t + 1) * P], slot, t)
                if half:
                    last.then_inc(sb_pj, 1)
                    pe.wait_ge(sb_pj, p * 3 + 3)
                    pe.sem_inc(slot_free, 2)
                yield

        def sb_pair_pe(pe, p, u, project):
            parts = iter(project)

            def fill(n):
                for _ in range(n):
                    next(parts, None)

            pe.wait_ge(sb_pe, p * 3 + 6)
            for hh in range(2):
                hd = p * 2 + hh
                r = slice(HD * hh, HD * hh + HD)
                for i in range(QT):
                    pe.matmul(bank[i][:, 0:CAUSAL_COLS[i]], kT[r, u, i * P:(i + 1) * P], qT[r, u, i * P:SEQ],
                              start=True, stop=True).then_inc(sb_z, 1)
                fill(2)
                pe.wait_ge(sb_sp, hd + 1)
                for i in range(QT):
                    n = CAUSAL_COLS[i]
                    for j in range(i, QT):
                        pe.matmul(bank[i][:, n - CAUSAL_COLS[j]:n], (tri_neg if j == i else ones_neg)[:, :],
                                  softp[:, CAUSAL_AT[j]:CAUSAL_AT[j] + CAUSAL_COLS[j]], start=False, stop=False,
                                  skip_group_check=True)
                    pe.matmul(bank[i][:, 0:P], ident_bf[:, :], past_neg_bf[:, :], start=False, stop=True,
                              skip_group_check=True).then_inc(sb_zi, 1)
                fill(1)
                pe.wait_ge(sb_oe, hd + 1)
                for i in range(QT):
                    pe.wait_ge(sb_a, hd * QT + i + 1)
                    last = pe.matmul(bank[4][0:HD, i * P:SEQ], vN[:, u, i, r], stick[:, CAUSAL_AT[i]:CAUSAL_AT[i] + CAUSAL_COLS[i]],
                                     start=(i == 0), stop=(i == QT - 1))
                last.then_inc(sb_o, 1)
            fill(6)

        def w_out_pe(pe):
            def again(n, t):
                i = n * T2 + t
                if i >= 8:
                    pe.wait_ge(h_upd, H_X2 + i - 7)
            output_pe(pe, "w_out", merged_hi, merged_lo, w2_hi, T2, lambda n, t: (n * T2 + t) % 8, H_ALL, again)

        def mm3(pe, dst, a_hi, a_lo, b_hi, b_lo, first, final):
            pe.matmul(dst, a_hi, b_hi, start=first, stop=False)
            pe.matmul(dst, a_hi, b_lo, start=False, stop=False)
            return pe.matmul(dst, a_lo, b_hi, start=False, stop=final)

        FF_SLOTS = 2 * FF_TILES

        def ff_pe(pe, m, upd):
            def weights(f, j, width):
                pe.wait_ge(split_w, f * FF_SLOTS + (m * FF_PARTS * FF_SLOTS + j + 1))
                return [w[:, j % SPLITS, :].rearrange("p (k n) -> p k n", n=width) for w in (w_hi, w_lo)]

            pe.wait_ge(split_x, split_base(FF_NORMS[m]) + 2 * QT)
            with loop(pe, FF_PARTS) as f:
                for j in range(FF_TILES):
                    n = f * FF_TILES + (m * FF_PARTS * FF_TILES + j)
                    hi, lo = weights(f, j, P)
                    pe.wait_ge(ff_relu, n + 1)
                    if j < QT:
                        pe.wait_ge(h_upd, f * UPD + (upd - UPD + QT + j + 1))
                    for k in range(KT):
                        last = mm3(pe, bank[j % 4][:, :], hi[:, k, :], lo[:, k, :], x_hi[:, k, :], x_lo[:, k, :], k == 0, k == KT - 1)
                    last.then_inc(ff_mm, 1)
                pe.wait_ge(ff_hid, f * FF_TILES + ((m * FF_PARTS + 1) * FF_TILES + 2))
                for n in range(2):
                    for k in range(FF_TILES):
                        if k % 2 == 0:
                            hi, lo = weights(f, FF_TILES + n * (FF_TILES // 2) + k // 2, 512)
                        for t in range(QT):
                            rows = slice(t * P, (t + 1) * P)
                            last = mm3(pe, bank[4 * (1 - n) + t][:, :], hid_hi[:, k, rows], hid_lo[:, k, rows],
                                       hi[:, k % 2, :], lo[:, k % 2, :], k == 0, k == FF_TILES - 1)
                            if k == FF_TILES - 1:
                                last.then_inc(acc_done, 1)
                        if k % 2 and k < FF_TILES - 1:
                            last.then_inc(ff_w2, 1)

        def ff_pool(pool, m, upd):
            w2_frees = FF_TILES // 2 - 1
            with loop(pool, FF_PARTS) as f:
                for j in range(FF_SLOTS):
                    n = f * FF_SLOTS + (m * FF_PARTS * FF_SLOTS + j)
                    was = (j - SPLITS) % FF_SLOTS
                    half, k = (was - FF_TILES) // (FF_TILES // 2), (was - FF_TILES) % (FF_TILES // 2)
                    part = 0 if j < SPLITS else 1
                    if was < FF_TILES:
                        pool.wait_ge(ff_mm, f * FF_TILES + (m * FF_PARTS * FF_TILES + was + 1))
                    elif k < w2_frees:
                        pool.wait_ge(ff_w2, f * (2 * w2_frees) + ((m * FF_PARTS + part) * 2 * w2_frees + half * w2_frees + k + 1))
                    else:
                        pool.wait_ge(acc_done, f * UPD + (upd + (part - 1) * UPD + (half + 1) * QT))
                    raw = ring.wait(pool, f"ff{m}", j, f)
                    hi, lo = w_hi[:, j % SPLITS, :], w_lo[:, j % SPLITS, :]
                    pool.tensor_tensor(hi, raw, one[:, :].broadcast_to([P, D]), ALU.mult).then_inc(split_w_hi, 1)
                    pool.wait_ge(split_w_hi, n + 1)
                    pool.tensor_tensor(lo, raw, hi.bitcast(F32), ALU.subtract).then_inc(split_w, 1)
                    pool.wait_ge(split_w, n + 1)
                    pool.sem_inc(slot_free, 1)

        @block.tensor
        def _(pe):
            pe.sem_inc(slot_free, RING)
            pe.sem_inc(ex_xt, 2)
            pe.sem_inc(br_mm, 2)
            pe.wait_ge(const_in, ALL_CONST)
            pe.transpose(bank[0][:, 0:7 * KT], gain_rows[:, :], ident[0:7 * KT, 0:7 * KT]).then_inc(gains_T, 1)
            pe.wait_ge(gains_in, 1)
            norm_pe(pe, 0)
            pe.wait_ge(split_x, split_base(1))
            for _ in sb_project(pe, "sb_first", 0, 0, 0):
                pass
            with loop(pe, PAIRS // 2 - 1) as turn:
                sb_pair_pe(pe, turn * 2, 0, sb_project(pe, "sb_loop", 0, turn, turn * 2 + 1))
                sb_pair_pe(pe, turn * 2 + 1, 1, sb_project(pe, "sb_loop", 4, turn, turn * 2 + 2))
            sb_pair_pe(pe, PAIRS - 2, 0, sb_project(pe, "sb_last", 0, 0, PAIRS - 1))
            sb_pair_pe(pe, PAIRS - 1, 1, ())
            pe.wait_ge(sb_oe, 2 * PAIRS + 1)
            output_pe(pe, "sb_o", sb_o_hi, oT_lo, w_hi, QT, half_banks, 0)
            norm_pe(pe, 1)
            ff_pe(pe, 0, UPD)
            norm_pe(pe, 2)
            pe.wait_ge(ff_freed, 1)
            ring.wait(pe, "kv", RING - 1)
            kv_pe(pe)
            norm_pe(pe, 3)
            gates_pe(pe)
            pe.wait_ge(gate_in, 1)
            with loop(pe, GROUPS) as g:
                nsa_pe(pe, g)
            pe.wait_ge(ns_oe, 4 * GROUPS + 1)
            output_pe(pe, "nsa_o", ns_o_hi, oT_lo, ns_w_hi, QT, half_banks, H_BEFORE[3])
            norm_pe(pe, 4)
            ff_pe(pe, 1, H_BEFORE[4])

            pe.wait_ge(b2_in, B2_CONST)
            pe.transpose(bank[7][:, 0:3], head_gain_rows[:, :], ident[0:3, 0:3]).then_inc(b2_T, 1)
            pe.wait_ge(b2_ready, 1)
            norm_pe(pe, 6)
            pe.wait_ge(ff_freed, 2)
            ring.wait(pe, "df_loop", 2)
            pe.wait_ge(split_x, split_base(7))
            for _ in df_parts(pe, "df_first", 0, 0, 0):
                pass
            df_scores(pe, 0, 0, 0)
            with loop(pe, HEADS2 // 2 - 1) as turn:
                df_pe_head(pe, turn * 2, 0, df_parts(pe, "df_loop", 0, turn, turn * 2 + 1))
                df_pe_head(pe, turn * 2 + 1, 1, df_parts(pe, "df_loop", 4, turn, turn * 2 + 2))
            df_pe_head(pe, HEADS2 - 2, 0, df_parts(pe, "df_last", 0, 0, HEADS2 - 1))
            df_pe_head(pe, HEADS2 - 1, 1, ())
            pe.wait_ge(df_oe, HEADS2 + 1)
            branch_pe(pe, 0)
            pe.wait_ge(br_m, KT + 2)
            with loop(pe, KV2) as kv:
                gq_pe_turn(pe, kv)
            pe.wait_ge(gq_oe, HEADS2 + 1)
            branch_pe(pe, 1)
            pe.wait_ge(br_m, 2 * KT + 2)
            w_out_pe(pe)
            norm_pe(pe, 7)
            route_pe(pe)
            ex_tokens_pe(pe, 0, 0)
            ex_gate_up_pe(pe, "ex_first", 0, 0, 0, 0, 0)
            ex_gate_up_pe(pe, "ex_first", 0, 0, 0, 0, 1)
            ex_tokens_pe(pe, 0, 1)
            ex_up_done_pe(pe, 0, 0)
            with loop(pe, EXPERTS // 2 - 1) as turn:
                ex_gate_up_pe(pe, "ex_loop", 0, turn, turn, 1, 0)
                ex_hidden_pe(pe, turn, 0)
                ex_gate_up_pe(pe, "ex_loop", 0, turn, turn, 1, 1)
                ex_tokens_pe(pe, turn + 1, 0)
                ex_up_done_pe(pe, turn, 1)
                ex_down_pe(pe, "ex_loop", 8, turn, turn, 0)
                ex_gate_up_pe(pe, "ex_loop", 12, turn, turn + 1, 0, 0)
                ex_hidden_pe(pe, turn, 1)
                ex_gate_up_pe(pe, "ex_loop", 12, turn, turn + 1, 0, 1)
                ex_tokens_pe(pe, turn + 1, 1)
                ex_up_done_pe(pe, turn + 1, 0)
                ex_down_pe(pe, "ex_loop", 20, turn, turn, 1)
            last = EXPERTS // 2 - 1
            ex_gate_up_pe(pe, "ex_last", 0, 0, last, 1, 0)
            ex_hidden_pe(pe, last, 0)
            ex_gate_up_pe(pe, "ex_last", 0, 0, last, 1, 1)
            ex_up_done_pe(pe, last, 1)
            ex_down_pe(pe, "ex_last", 8, 0, last, 0)
            ex_hidden_pe(pe, last, 1)
            ex_down_pe(pe, "ex_last", 12, 0, last, 1)

        def sb_pair_act(act, p):
            for hh in range(2):
                hd = p * 2 + hh
                for i in range(QT):
                    act.wait_ge(sb_z, hd * QT + i + 1)
                    act_t.inc(act.activation(absz[:, CAUSAL_AT[i]:CAUSAL_AT[i] + CAUSAL_COLS[i]], bank[i][:, 0:CAUSAL_COLS[i]], ACT.Abs))
                act.wait_ge(act_step, act_t.value())
                act_t.inc(act.activation(absz[:, :], absz[:, :], ACT.Exp, scale=-1.0))
                act.wait_ge(act_step, act_t.value())
                act.activation(absz[:, :], absz[:, :], ACT.Ln, bias=1.0).then_inc(sb_l, 1)
                for i in range(QT):
                    act.wait_ge(sb_zi, hd * QT + i + 1)
                    act.activation(stick[:, CAUSAL_AT[i]:CAUSAL_AT[i] + CAUSAL_COLS[i]], bank[i][:, 0:CAUSAL_COLS[i]], ACT.Exp).then_inc(sb_a, 1)

        def ff_act(act, m):
            with loop(act, FF_PARTS) as f:
                for j in range(FF_TILES):
                    n = f * FF_TILES + (m * FF_PARTS * FF_TILES + j)
                    act.wait_ge(ff_mm, n + 1)
                    act.wait_ge(ff_hid, n + 1)
                    act.activation(relu[:, j % 2, :], bank[j % 4][:, :], ACT.Relu).then_inc(ff_relu, 1)

        act_t, dve_t = Tally(act_step), Tally(dve_step)

        @block.scalar
        def _(act):
            act.sem_inc(ff_relu, 4)
            act.sem_inc(ns_p, 3)
            act.sem_inc(ns_t, 1)
            act.sem_inc(df_p, 1)
            act.sem_inc(df_t, 1)
            act.sem_inc(df_v, 1)
            act.sem_inc(gq_p, 2)
            act.sem_inc(gq_t, 1)
            act.sem_inc(ex_xe, 1)
            act.wait_ge(const_in, ALL_CONST)
            act.wait_ge(gains_in, 1)
            act.wait_ge(one_in, 1)
            norm_act(act, 0)
            split_x_act(act, 0)
            with loop(act, PAIRS // 2 - 1, tallies=[(act_t, 4 * (QT + 1))]) as turn:
                sb_pair_act(act, turn * 2)
                sb_pair_act(act, turn * 2 + 1)
            sb_pair_act(act, PAIRS - 2)
            sb_pair_act(act, PAIRS - 1)
            norm_act(act, 1, H_BEFORE[1] - QT)
            split_x_act(act, 1)
            ff_act(act, 0)
            norm_act(act, 2, H_BEFORE[2] - QT)
            kv_act(act)
            gates_act(act)
            act.preload_act_table_set(LN_EXP)
            with loop(act, GROUPS) as g:
                nsa_act(act, g)
            norm_act(act, 4, H_BEFORE[4] - QT)
            split_x_act(act, 4)
            ff_act(act, 1)
            norm_act(act, 5, H_ALL - QT)

            act.wait_ge(lam_d, 1)
            act.activation(lam[:, :], lam[:, :], ACT.Exp).then_inc(lam_e, 1)
            act.wait_ge(b2_in, B2_CONST)
            act.wait_ge(h_upd, H_X2)
            norm_act(act, 6)
            split_x_act(act, 6)
            df_exps(act, 0, 0)
            with loop(act, HEADS2 - 1) as hd:
                df_act_head(act, hd, True)
            df_act_head(act, HEADS2 - 1, False)
            split_o_act(act, 0, df_oe)
            branch_act(act, 0)
            act.preload_act_table_set(LN_EXP)
            with loop(act, KV2, tallies=[(act_t, Q_PER_KV + 1)]) as kv:
                gq_act_turn(act, kv)
            split_o_act(act, 1, gq_oe)
            branch_act(act, 1)
            norm_act(act, 7, H_FFN - T2)
            tokens_act(act)
            route_act(act)
            ex_tokens_act(act, 0, 0)
            ex_tokens_act(act, 0, 1)
            ex_act(act, 0, 0)
            with loop(act, EXPERTS // 2 - 1) as turn:
                ex_tokens_act(act, turn + 1, 0)
                ex_act(act, turn, 1)
                ex_tokens_act(act, turn + 1, 1)
                ex_act(act, turn + 1, 0)
            ex_act(act, EXPERTS // 2 - 1, 1)
            act.wait_ge(y_in, 16)
            norm_act(act, 8)

        def step(dve, ins):
            dve_t.inc(ins)
            dve.wait_ge(dve_step, dve_t.value())

        def sb_take(dve, n, p, u):
            dve.wait_ge(sb_pj, p * 3 + n + 1)
            if n == 0:
                dve.tensor_scalar(qT[:, u, :], bank[5][:, :], HD ** -0.5, None, ALU.mult).then_inc(sb_pe, 1)
            elif n == 1:
                dve.tensor_copy(kT[:, u, :], bank[6][:, :]).then_inc(sb_pe, 1)
            else:
                dve.tensor_copy(vN[:, u, :, :], bank[7][:, :].rearrange("p (t n) -> p t n", n=P)).then_inc(sb_pe, 1)

        def sb_pair_dve(dve, p, u, take):
            for hh in range(2):
                hd = p * 2 + hh
                dve.wait_ge(sb_l, hd + 1)
                for i in range(QT):
                    s = slice(CAUSAL_AT[i], CAUSAL_AT[i] + CAUSAL_COLS[i])
                    dve_t.inc(dve.scalar_tensor_tensor(softp[:, s], bank[i][:, 0:CAUSAL_COLS[i]], 0.0, absz[:, s], ALU.max, ALU.add))
                dve.wait_ge(dve_step, dve_t.value())
                for i in range(QT):
                    d = softp[:, CAUSAL_AT[i]:CAUSAL_AT[i] + P]
                    last = dve.tensor_tensor(d, d, past01[:, :], ALU.mult)
                    if i == QT - 1:
                        last.then_inc(sb_sp, 1)
                if take and hh == 0:
                    sb_take(dve, 0, p + 1, 1 - u)
                if take and hh == 1:
                    sb_take(dve, 1, p + 1, 1 - u)
                    sb_take(dve, 2, p + 1, 1 - u)
                dve.wait_ge(sb_o, hd + 1)
                take_o(dve, sb_o_hi, slice(HD * hh, HD * hh + HD), p, bank[4], sb_oe)

        def w_out_dve(dve):
            for n in range(2):
                for t in range(T2):
                    r = rows_of(t)
                    dve.wait_ge(acc_done, H_ALL + n * T2 + t + 1)
                    hs = h[0:r, t, 512 * n:512 * n + 512]
                    dve.tensor_tensor(hs, bank[(n * T2 + t) % 8][0:r, :], hs, ALU.add).then_inc(h_upd, 1)

        def residual_dve(dve, done):
            for n in range(2):
                for t in range(QT):
                    dve.wait_ge(acc_done, done + n * QT + t + 1)
                    hs = h[:, t, 512 * n:512 * n + 512]
                    dve.tensor_tensor(hs, bank[4 * (1 - n) + t][:, :], hs, ALU.add).then_inc(h_upd, 1)

        def ff_dve(dve, m, upd):
            with loop(dve, FF_PARTS, tallies=[(dve_t, 2 * FF_TILES)]) as f:
                for j in range(FF_TILES):
                    n = f * FF_TILES + (m * FF_PARTS * FF_TILES + j)
                    dve.wait_ge(ff_relu, n + 5)
                    r, sq = relu[:, j % 2, :], hid_sq[:, j % 2, :]
                    dve_t.inc(dve.tensor_tensor(sq, r, r, ALU.mult))
                    step(dve, dve.tensor_tensor(hid_hi[:, j, :], r, r, ALU.mult))
                    dve.tensor_tensor(hid_lo[:, j, :], sq, hid_hi[:, j, :].bitcast(F32), ALU.subtract).then_inc(ff_hid, 1)
                residual_dve(dve, f * UPD + upd)

        @block.vector
        def _(dve):
            dve.sem_inc(sb_pe, 3)
            dve.sem_inc(sb_oe, 1)
            dve.sem_inc(ff_hid, 2)
            dve.sem_inc(ns_oe, 1)
            dve.sem_inc(df_pe, 1)
            dve.sem_inc(df_oe, 1)
            dve.sem_inc(br_m, 2)
            dve.sem_inc(gq_br, 1)
            dve.sem_inc(gq_oe, 1)
            dve.sem_inc(ex_h, 1)
            dve.sem_inc(ex_he, 1)
            dve.sem_inc(ex_ye, 1)
            dve.sem_inc(ex_done, 2)
            dve_t.inc(dve.memset(ssq[:, :], 0.0))
            dve.memset(ones_neg[:, :], -1.0)
            dve.wait_ge(const_in, ALL_CONST)
            dve.tensor_copy(ident_bf[:, :], ident[:, :])
            dve.tensor_copy(past_neg_bf[:, :], past_neg[:, :])
            dve.wait_ge(gains_T, 1)
            dve.tensor_copy(gains[:, :, :].rearrange("p g k -> p (g k)"), bank[0][:, 0:7 * KT]).then_inc(gains_in, 1)
            norm_dve(dve, 0)
            for n in range(3):
                sb_take(dve, n, 0, 0)
            with loop(dve, PAIRS // 2 - 1, tallies=[(dve_t, 4 * QT + 4)]) as turn:
                sb_pair_dve(dve, turn * 2, 0, True)
                sb_pair_dve(dve, turn * 2 + 1, 1, True)
            sb_pair_dve(dve, PAIRS - 2, 0, True)
            sb_pair_dve(dve, PAIRS - 1, 1, False)
            residual_dve(dve, 0)
            norm_dve(dve, 1)
            ff_dve(dve, 0, UPD)
            norm_dve(dve, 2)
            kv_dve(dve)
            norm_dve(dve, 3)
            gates_dve(dve)
            with loop(dve, GROUPS, tallies=[(dve_t, 48)]) as g:
                nsa_dve(dve, g)
            residual_dve(dve, H_BEFORE[3])
            norm_dve(dve, 4)
            ff_dve(dve, 1, H_BEFORE[4])
            dve.wait_ge(gain_in, 16)
            plain_norm_dve(dve, 5, QT)

            ready2_dve(dve)
            norm_dve(dve, 6)
            for n in range(6):
                df_take(dve, n, 0, 0)
            df_maxima(dve, 0, 0)
            with loop(dve, HEADS2 // 2 - 1, tallies=[(dve_t, 2 * (4 * T2 + 1))]) as turn:
                df_dve_head(dve, turn * 2, 0, True)
                df_dve_head(dve, turn * 2 + 1, 1, True)
            df_dve_head(dve, HEADS2 - 2, 0, True)
            df_dve_head(dve, HEADS2 - 1, 1, False)
            split_o_dve(dve, 0)
            branch_dve(dve, 0, 0)
            with loop(dve, KV2, tallies=[(dve_t, 45)]) as kv:
                gq_dve_turn(dve, kv)
            split_o_dve(dve, 1)
            branch_dve(dve, 1, 12)
            w_out_dve(dve)
            norm_dve(dve, 7)
            route_dve(dve)
            ex_hid_dve(dve, 0, 0)
            with loop(dve, EXPERTS // 2 - 1, tallies=[(dve_t, 4)]) as turn:
                ex_hidden_dve(dve, turn, 0)
                ex_hid_dve(dve, turn, 1)
                ex_out_dve(dve, turn, 0)
                ex_hidden_dve(dve, turn, 1)
                ex_hid_dve(dve, turn + 1, 0)
                ex_out_dve(dve, turn, 1)
            ex_hidden_dve(dve, EXPERTS // 2 - 1, 0)
            ex_hid_dve(dve, EXPERTS // 2 - 1, 1)
            ex_out_dve(dve, EXPERTS // 2 - 1, 0)
            ex_hidden_dve(dve, EXPERTS // 2 - 1, 1)
            ex_out_dve(dve, EXPERTS // 2 - 1, 1)
            dve.wait_ge(gain_in, 48)
            plain_norm_dve(dve, 8, QT)

        @block.gpsimd
        def _(pool):
            pool.sem_inc(ff_w2, 2 * (FF_TILES // 2 - 1))
            pool.memset(eps_col[:, :], EPS2)
            pool.memset(neg_half[:, :], -0.5)
            pool.memset(one[:, :], 1.0).then_inc(one_in, 1)
            pool.wait_ge(one_in, 1)
            norm_pool(pool, 0)
            split_heads_pool(pool, "sb", "sb_first", "sb_loop", "sb_last", PAIRS, sb_pj, 3, w_hi)
            output_pool(pool, "sb_o", w_hi)
            norm_pool(pool, 1)
            for m in range(2):
                pool.wait_ge(norm_tp, 2 * norm_base(FF_NORMS[m]) + 1)
                ff_pool(pool, m, UPD if m == 0 else H_BEFORE[4])
                pool.sem_inc(ff_freed, 1)
                if m == 0:
                    norm_pool(pool, 2)
                    pool.wait_ge(ns_grp, 1)
                    output_pool(pool, "nsa_o", ns_w_hi)
                    norm_pool(pool, 4)
            norm_pool(pool, 5)
            norm_pool(pool, 6)
            split_heads_pool(pool, "df", "df_first", "df_loop", "df_last", HEADS2, df_pj, 6, w2_hi)
            branch_pool(pool, 0)
            gq_pool(pool)
            branch_pool(pool, 1)
            pool.wait_ge(br_mm, 2 * BR_SPLITS + 2)
            output_pool(pool, "w_out", w2_hi)
            norm_pool(pool, 7)
            pool.wait_ge(h_upd, H_FFN)
            pool.dma_start(y_dram[0:SEQ, :].rearrange("(t p) d -> p t d", p=P), h[:, 0:QT, :]).then_inc(h_out, 16)
            pool.dma_start(y_dram[SEQ:L2, :], h[0:META, QT, :]).then_inc(h_out, 16)
            tokens_pool(pool)
            pool.wait_ge(ex_no, 1)
            pool.wait_ge(h_out, 32)
            pool.wait_ge(u_out, 16 * T2)
            ex_get(pool, 0, 0)
            ex_get(pool, 0, 1)
            with loop(pool, EXPERTS // 2 - 1) as turn:
                ex_get(pool, turn + 1, 0)
                ex_put(pool, turn, 0)
                ex_get(pool, turn + 1, 1)
                ex_put(pool, turn, 1)
            ex_put(pool, EXPERTS // 2 - 1, 0)
            ex_put(pool, EXPERTS // 2 - 1, 1)
            pool.dma_start(h[:, 0:QT, :], y_dram[0:SEQ, :].rearrange("(t p) d -> p t d", p=P)).then_inc(y_in, 16)
            norm_pool(pool, 8)


def rope_tables_1():
    f, half = np.float32, 8
    inv = f(500000.0) ** (-np.arange(half, dtype=f) * f(2.0) / f(16))
    ang = np.arange(SEQ, dtype=f)[None, :] * inv[:, None]
    cos, sin, rot = np.ones((P, SEQ), f), np.zeros((P, SEQ), f), np.zeros((P, P), f)
    for base in (0, HD):
        for d in range(half):
            for x, y, sign in ((d, d + half, -1), (d + half, d, 1)):
                cos[base + x], sin[base + x] = np.cos(ang[d]), np.sin(ang[d])
                rot[base + y, base + x] = sign
    return cos, sin, rot


def rope_tables_2():
    f, half, grid_w = np.float32, HD // 2, 64
    inv = f(10000.0) ** (-np.arange(0, HD, 2, dtype=f) / f(HD))
    i = np.arange(SEQ)
    cos, sin, rot = np.ones((P, L2), f), np.zeros((P, L2), f), np.zeros((P, P), f)
    for base, place in ((0, i // grid_w), (HD, i % grid_w)):
        ang = place.astype(f)[None, :] * inv[:, None]
        for d in range(half):
            for x, y, sign in ((d, d + half, -1), (d + half, d, 1)):
                cos[base + x, 0:SEQ], sin[base + x, 0:SEQ] = np.cos(ang[d]), np.sin(ang[d])
                rot[base + y, base + x] = sign
    return cos, sin, rot


def distances():
    pos = np.arange(T2 * P)
    d = np.abs(pos[:, None] - pos[None, :L2])
    d[(pos >= SEQ), :] = 0
    d[:, SEQ:] = 0
    return np.ascontiguousarray(d.reshape(T2, P, L2).transpose(1, 0, 2)).astype(np.float16)


def constants():
    f = np.float32
    i = np.arange(P)
    tok = i[:, None] + P * np.arange(QT)[None, :]
    cmp_ok = (CMP_STRIDE * np.arange(N_CMP) + CMP_LEN - 1)[None, None, :] <= tok[:, :, None]
    cos1, sin1, rot1 = rope_tables_1()
    cos2, sin2, rot2 = rope_tables_2()
    return {
        "ident": np.eye(P, dtype=f),
        "tri_neg": -(i[:, None] >= i[None, :]).astype(f),
        "past01": (i[:, None] < i[None, :]).astype(f),
        "future_neg": np.where(i[:, None] >= i[None, :], f(0), f(-1e30)).astype(f),
        "cmp_neg": np.where(cmp_ok, f(0), f(-1e30)).astype(f),
        "cmp_any": cmp_ok.any(-1).astype(f),
        "cos1": cos1, "sin1": sin1, "rot1": rot1,
        "cos2": cos2, "sin2": sin2, "rot2": rot2, "dist": distances(),
        "slot_no": np.tile(np.arange(CAP, dtype=f), (P, 1)),
        "token_no": (i[:, None] + P * np.arange(T2)[None, :]).astype(f),
        "past_neg": np.where(i[:, None] < i[None, :], f(0), f(-1e30)).astype(f),
    }


def kernel(**inputs):
    import concourse.bacc as _bacc
    from concourse.bass_utils import run_bass_kernel_spmd as _run

    nc = _bacc.Bacc("TRN2", target_bir_lowering=False, num_devices=1)
    arrays, A, C = {}, {}, {}
    for kind, into, values in (("in", A, inputs), ("c", C, constants())):
        for name, value in values.items():
            a = np.ascontiguousarray(value)
            arrays[f"{kind}_{name}"] = a
            into[name] = nc.dram_tensor(f"{kind}_{name}", a.shape, mybir.dt.from_np(a.dtype), kind="ExternalInput").ap()
    out = nc.dram_tensor("out", (1, SEQ, D), F32, kind="ExternalOutput").ap()
    build_program(nc, A, C, out)
    return _run(nc, [arrays], core_ids=[0]).results[0]["out"]
```

```python
from contextlib import ExitStack, contextmanager

import numpy as np
import concourse.bass as bass
from concourse import mybir

F32, F32R, BF16, F16, U32 = mybir.dt.float32, mybir.dt.float32r, mybir.dt.bfloat16, mybir.dt.float16, mybir.dt.uint32
ACT, ALU, AX = mybir.ActivationFunctionType, mybir.AluOpType, mybir.AxisListType

P = 128
D = 1024
KT = D // P
SEQ = 512
QT = SEQ // P
META = 16
L2 = SEQ + META
T2 = QT + 1
CH2 = L2 // 2
HD = 64
PAIRS = 8
D_FF = 4096
FF_PARTS = 4
FF_TILES = D_FF // FF_PARTS // P
SPLITS = 4
SPLITS2 = 2
EPS1, EPS2 = 1e-5, 1e-6
RING = 8
CAUSAL_COLS = [QT * P - P * i for i in range(QT)]
CAUSAL_AT = [sum(CAUSAL_COLS[:i]) for i in range(QT)]
CAUSAL = sum(CAUSAL_COLS)
GROUPS = 4
BRANCHES = 3
UNITS = 4 * BRANCHES
CMP_LEN, CMP_STRIDE, CMP_HID = 32, 16, 256
N_CMP = (SEQ - CMP_LEN) // CMP_STRIDE + 1
CMP_KT = CMP_LEN * HD // P
N_GATES = 48
SCORE_AT = [(1, 384), (2, 0), (1, 0), (0, 0)]
PROB_AT = [0, P, 3 * P, 6 * P]
PT_AT = [(3, 0, 0), (4, 0, SEQ), (5, 0, 2 * SEQ), (4, 384, SEQ + 384)]
GELU_C, GELU_K = 0.044715, (2.0 / np.pi) ** 0.5


HEADS2 = 8
KV2 = 2
Q_PER_KV = HEADS2 // KV2
USES = 8 + 6 * Q_PER_KV
LAM_INIT = 0.8 - 0.6
O_TAIL = 128
MS_TAIL = O_TAIL + META
EXPERTS, CAP, EXPERT_FF = 16, 2 * L2 // 16, 512
FT = EXPERT_FF // P
PICKS = 5
EARLY_SPLITS = 2
EARLY = 4
W_IN = {"qa": 0, "ka": 8, "va": 16, "qb": 24, "kb": 32, "vb": 34, "ga": 36, "gb": 44}


LN_EXP = "natural_log_exp_and_others"


def rows_of(t):
    return P if t < QT else META


class Tally:

    def __init__(self, sem):
        self.sem, self.n, self.turn, self.per, self.start = sem, 0, None, 0, 0

    def inc(self, ins):
        ins.then_inc(self.sem, 1)
        self.n += 1

    def value(self):
        return self.n if self.turn is None else self.turn * self.per + self.n


@contextmanager
def loop(eng, count, **per):
    tallies = per.pop("tallies", [])
    with eng.Fori(0, count) as turn:
        for t, k in tallies:
            t.turn, t.per, t.start = turn, k, t.n
        yield turn
        for t, k in tallies:
            assert t.n - t.start == k, (t.n - t.start, k)
            t.n, t.turn = t.start + k * count, None


class Ring:

    def __init__(self, tile, loaded, free):
        self.tile, self.loaded, self.free = tile, loaded, free
        self.at, self.loads, self.plan = 0, [0] * RING, {}

    def load(self, sp, name, sources, turns=1):
        n = len(sources)
        assert turns == 1 or n % RING == 0, (name, n)
        per = [0] * RING
        waits = []
        for j, s in enumerate(sources):
            slot = (self.at + j) % RING
            waits.append((slot, self.loads[slot], per[slot] + 1))
            per[slot] += s is not None
        self.plan[name] = [(slot, base, k, per[slot]) for slot, base, k in waits]

        def turn_loads(turn):
            for j, s in enumerate(sources):
                if s is None:
                    continue
                slot = (self.at + j) % RING
                sp.wait_ge(self.free, self.at + turn * n + j + 1)
                dst, src = s(self.tile[:, slot, :], turn)
                sp.dma_start(dst, src).then_inc(self.loaded[slot], 16)

        if turns == 1:
            turn_loads(0)
        else:
            with sp.Fori(0, turns) as turn:
                turn_loads(turn)
        self.at += n * turns
        for slot in range(RING):
            self.loads[slot] += per[slot] * turns

    def wait(self, pe, name, j, turn=0):
        slot, base, k, per = self.plan[name][j]
        pe.wait_ge(self.loaded[slot], (turn * per + base + k) * 16)
        return self.tile[:, slot, :]


def cols_tile(w, n_tile):
    def source(slot, turn):
        return (slot.rearrange("p (k n) -> p k n", n=P),
                w[:, bass.ds(n_tile(turn) * P, P)].rearrange("(k p) n -> p k n", p=P))
    return source


def rows_tiles(w, row_tile, col, width=512):
    k = D // width

    def source(slot, turn):
        return (slot.rearrange("p (k n) -> p k n", n=width),
                w[bass.ds(row_tile(turn) * P, k * P), bass.ds(col(turn), width)].rearrange("(k p) n -> p k n", p=P))
    return source


def build_program(nc, A, C, out):
    ctx = ExitStack()
    with ctx:
        def sb(name, shape, dt=F32, stack=ctx):
            return stack.enter_context(nc.sbuf_tensor(name, shape, dt))

        def sb_split(name, shape, stack=ctx):
            with ExitStack() as same:
                whole = sb(name, shape, stack=same)
            return whole, sb(name + "_lo", shape, F32R, stack=stack)

        def sem(name):
            return ctx.enter_context(nc.semaphore(name))

        h = sb("h", [P, T2, D])
        xT = sb("xT", [P, KT, L2])
        ring_tile, ring_lo = sb_split("ring_tile", [P, RING, D])
        ident = sb("ident", [P, P])
        ident_bf = sb("ident_bf", [P, P], BF16)
        gain_rows = sb("gain_rows", [7 * KT, P])
        gains = sb("gains", [P, 7, KT])
        ssq = sb("ssq", [P, 2, T2])
        rstd = sb("rstd", [P, T2])
        xn = sb("xn", [P, 2, D])
        oT, oT_lo = sb_split("oT", [P, KT, L2])

        one = sb("one", [P, 1])
        neg_half = sb("neg_half", [P, 1])
        eps_col = sb("eps_col", [P, 1])
        gain_bc = sb("gain_bc", [P, D])

        psum = ctx.enter_context(nc.psum_tensor("psum", [P, 8, 512], F32))
        bank = [psum[:, k, :] for k in range(8)]

        st = ExitStack()
        x_hi = sb("x_hi", [P, KT, SEQ], F32R, stack=st)
        x_lo = sb("x_lo", [P, KT, SEQ], F32R, stack=st)
        w_hi = sb("w_hi", [P, SPLITS, D], F32R, stack=st)
        with ExitStack() as sticks:
            qT = sb("qT", [P, 2, SEQ], stack=sticks)
            kT = sb("kT", [P, 2, SEQ], stack=sticks)
            vN = sb("vN", [P, 2, QT, P], stack=sticks)
            absz = sb("absz", [P, CAUSAL], stack=sticks)
            softp = sb("softp", [P, CAUSAL], stack=sticks)
            stick = sb("stick", [P, CAUSAL], stack=sticks)
            tri_neg = sb("tri_neg", [P, P], stack=sticks)
            ones_neg = sb("ones_neg", [P, P], stack=sticks)
            past01 = sb("past01", [P, P], stack=sticks)
            past_neg = sb("past_neg", [P, P], stack=sticks)
            past_neg_bf = sb("past_neg_bf", [P, P], BF16, stack=sticks)
            sb_o_hi = sb("sb_o_hi", [P, KT, SEQ], F32R, stack=sticks)
        with ExitStack() as feed_forward:
            w_lo = sb("w_lo", [P, SPLITS, D], F32R, stack=feed_forward)
            hid_hi = sb("hid_hi", [P, FF_TILES, SEQ], F32R, stack=feed_forward)
            hid_lo = sb("hid_lo", [P, FF_TILES, SEQ], F32R, stack=feed_forward)
            relu = sb("relu", [P, 2, SEQ], stack=feed_forward)
            hid_sq = sb("hid_sq", [P, 2, SEQ], stack=feed_forward)
        st.close()

        st = ExitStack()
        k_cmp = sb("k_cmp", [P, GROUPS, N_CMP], stack=st)
        v_cmp = sb("v_cmp", [N_CMP, GROUPS, HD], stack=st)
        k_all = sb("k_all", [P, 2, GROUPS, SEQ], stack=st)
        v_all = sb("v_all", [P, 2, QT, GROUPS, HD], stack=st)
        q_raw = sb("q_raw", [P, 2, SEQ], stack=st)
        rope_a = sb("rope_a", [P, SEQ], stack=st)
        rope_b = sb("rope_b", [P, SEQ], stack=st)
        cos1 = sb("cos1", [P, SEQ], stack=st)
        sin1 = sb("sin1", [P, SEQ], stack=st)
        rot1 = sb("rot1", [P, P], stack=st)
        gate_w = sb("gate_w", [P, KT, N_GATES], stack=st)
        gate_b = sb("gate_b", [P, N_GATES], stack=st)
        gates = sb("gates", [P, QT, N_GATES], stack=st)
        future_neg = sb("future_neg", [P, P], stack=st)
        future_neg_bf = sb("future_neg_bf", [P, P], BF16, stack=st)
        cmp_neg = sb("cmp_neg", [P, QT, N_CMP], stack=st)
        cmp_any = sb("cmp_any", [P, QT], stack=st)
        with ExitStack() as shared_kv:
            kv_pairs = sb("kv_pairs", [P, 2, GROUPS, SEQ], stack=shared_kv)
            blocks = sb("blocks", [P, 2, CMP_KT, GROUPS * N_CMP], stack=shared_kv)
            pos_rows = sb("pos_rows", [2 * CMP_KT, P], stack=shared_kv)
            pos_off = sb("pos_off", [P, 2 * CMP_KT], stack=shared_kv)
            cmp_w2 = sb("cmp_out_w", [P, 2, 2, HD], stack=shared_kv)
            cmp_x = sb("cmp_x", [P, 2, GROUPS * N_CMP], stack=shared_kv)
            cmp_u = sb("cmp_u", [P, 2, GROUPS * N_CMP], stack=shared_kv)
            cmp_h = sb("cmp_h", [P, 2, 2, GROUPS * N_CMP], stack=shared_kv)
        with ExitStack() as groups:
            k_grp = sb("k_grp", [P, 2, SEQ], stack=groups)
            v_grp = sb("v_grp", [P, 2, QT, HD], stack=groups)
            kc_grp = sb("kc_grp", [P, N_CMP], stack=groups)
            vc_grp = sb("vc_grp", [N_CMP, HD], stack=groups)
            q_rot = sb("q_rot", [P, 2, SEQ], stack=groups)
            probs = sb("probs", [P, 2, CAUSAL], stack=groups)
            probs_T = sb("probs_T", [P, 2, CAUSAL], stack=groups)
            top = sb("top", [P, 2, QT], stack=groups)
            rsum = sb("rsum", [P, 2, QT], stack=groups)
            factor = sb("factor", [P, 2, QT], stack=groups)
            ns_o_hi = sb("ns_o_hi", [P, KT, SEQ], F32R, stack=groups)
            ns_w_hi = sb("ns_w_hi", [P, SPLITS2, D], F32R, stack=groups)
        st.close()
        st = ExitStack()
        merged, merged_lo = sb_split("merged", [P, KT, L2], st)
        x2_hi = sb("x2_hi", [P, KT, L2], F32R, stack=st)
        x2_lo = sb("x2_lo", [P, KT, L2], F32R, stack=st)
        w2_hi = sb("w2_hi", [P, SPLITS2, D], F32R, stack=st)
        lam_prod = sb("lam_prod", [P, HD], stack=st)
        lam = sb("lam", [P, 2], stack=st)
        neg_lam = sb("neg_lam", [P, 1], stack=st)
        head_gain_rows = sb("head_gain_rows", [3, P], stack=st)
        head_gain = sb("head_gain", [P, 3], stack=st)
        mean_w = sb("mean_w", [P, P], stack=st)
        cos2 = sb("cos2", [P, L2], stack=st)
        sin2 = sb("sin2", [P, L2], stack=st)
        rot2 = sb("rot2", [P, P], stack=st)
        top2 = sb("top2", [P, 2], stack=st)
        rsum2 = sb("rsum2", [P, 2], stack=st)
        rinv2 = sb("rinv2", [P, 2], stack=st)
        with ExitStack() as heads:
            q2 = sb("q2", [P, 2, L2], stack=heads)
            k2 = sb("k2", [P, 2, L2], stack=heads)
            v2 = sb("v2", [P, 2, T2, P], stack=heads)
            prob_a = sb("prob_a", [P, 2, L2], stack=heads)
            w_T = sb("w_T", [P, 2, T2, P], stack=heads)
            sq2 = sb("sq2", [P, 2, L2], stack=heads)
            var2 = sb("var2", [P, 2, L2], stack=heads)
            with ExitStack() as differential:
                prob_b = sb("prob_b", [P, 2, L2], stack=differential)
                dist = sb("dist", [P, T2, L2], F16, stack=differential)
                slope = sb("slope", [P, 2, P], F16, stack=differential)
                lam_in = sb("lam_in", [P, 4, HD], stack=differential)
            with ExitStack() as grouped:
                raw2 = sb("raw2", [P, 2, L2], stack=grouped)
                norm2 = sb("norm2", [P, 2, L2], stack=grouped)
                rope_c = sb("rope_c", [P, L2], stack=grouped)
        with ExitStack() as branches:
            sig = sb("sig", [P, 2, L2], stack=branches)
            o_hi = sb("o_hi", [P, KT, L2], F32R, stack=branches)
            merged_hi = sb("merged_hi", [P, KT, L2], F32R, stack=branches)
        st.close()
        st = ExitStack()
        u_rows = sb("u_rows", [P, T2, D], stack=st)
        router_w = sb("router_w", [P, KT, EXPERTS], stack=st)
        logits = sb("logits", [P, T2, EXPERTS], stack=st)
        lmax = sb("lmax", [P, T2], stack=st)
        token_aff = sb("token_aff", [P, T2, EXPERTS, PICKS], BF16, stack=st)
        aff_rest = sb("aff_rest", [P, T2, EXPERTS], stack=st)
        aff_T = sb("aff_T", [EXPERTS, L2], stack=st)
        work = sb("work", [EXPERTS, L2], stack=st)
        best8 = sb("best8", [EXPERTS, 8], stack=st)
        above = sb("above", [EXPERTS, L2], stack=st)
        equal = sb("equal", [EXPERTS, L2], stack=st)
        count = sb("count", [EXPERTS, L2], stack=st)
        ones_row = sb("ones_row", [EXPERTS, L2], stack=st)
        n_above = sb("n_above", [EXPERTS, 2], stack=st)
        slot_T = sb("slot_T", [P, T2, EXPERTS], stack=st)
        slot_no = sb("slot_no", [P, CAP], stack=st)
        token_no = sb("token_no", [P, 2, T2], stack=st)
        one_hot = sb("one_hot", [P, 4, T2, CAP], BF16, stack=st)
        pick = sb("pick", [CAP, EXPERTS, PICKS], stack=st)
        pick_no = sb("pick_no", [CAP, EXPERTS], U32, stack=st)
        no_get = sb("no_get", [CAP, 2, 1], U32, stack=st)
        no_put = sb("no_put", [CAP, 2, 1], U32, stack=st)
        aff_now = sb("aff_now", [CAP, 2, 1], stack=st)
        xs = sb("xs", [CAP, 2, D], stack=st)
        xs_hi = sb("xs_hi", [P, 2, KT, CAP], F32R, stack=st)
        xs_lo = sb("xs_lo", [P, 2, KT, CAP], F32R, stack=st)
        ex_w_hi = sb("ex_w_hi", [P, KT, D], F32R, stack=st)
        act_sig = sb("act_sig", [CAP, EXPERT_FF], stack=st)
        act_hid = sb("act_hid", [CAP, 2, EXPERT_FF], stack=st)
        hid_T = sb("hid_T", [P, 2, FT, CAP], stack=st)
        ys = sb("ys", [CAP, 2, D], stack=st)
        st.close()
        u_dram = nc.dram_tensor("u_dram", [L2, D], F32).ap()
        y_dram = nc.dram_tensor("y_dram", [L2, D], F32).ap()

        one_in, cleared, ff_freed = (sem(s) for s in ("one_in", "cleared", "ff_freed"))
        tile_in = [sem(f"tile{t}_in") for t in range(QT)]
        const_in, gains_T, gains_in = sem("const_in"), sem("gains_T"), sem("gains_in")
        loaded = [sem(f"slot{k}_loaded") for k in range(RING)]
        slot_free = sem("slot_free")
        h_upd = sem("h_upd")
        dve_step, act_step = sem("dve_step"), sem("act_step")
        norm_sq, norm_ms, norm_sd, norm_xn, norm_tp, norm_ev = (sem(f"norm_{s}") for s in ("sq", "ms", "sd", "xn", "tp", "ev"))
        sb_pj, sb_pe, sb_z, sb_l, sb_sp, sb_zi, sb_a, sb_o, sb_oe = (
            sem(f"sb_{s}") for s in ("pj", "pe", "z", "l", "sp", "zi", "a", "o", "oe"))
        acc_done = sem("acc_done")
        ff_mm, ff_relu, ff_hid, ff_w2 = sem("ff_mm"), sem("ff_relu"), sem("ff_hid"), sem("ff_w2")
        split_x_hi, split_x, split_w_hi, split_w = sem("split_x_hi"), sem("split_x"), sem("split_w_hi"), sem("split_w")
        out_sem = sem("out_sem")
        nsa_in, gain_in = sem("nsa_in"), sem("gain_in")
        kv_mm, kv_ev, kv_rot, kv_k, pos_T = (sem(s) for s in ("kv_mm", "kv_ev", "kv_rot", "kv_k", "pos_T"))
        cmp_blk, cmp_mm, cmp_uu, cmp_ee, cmp_hh, cmp_kv, cmp_out = (
            sem(f"cmp_{s}") for s in ("blk", "mm", "uu", "ee", "hh", "kv", "out"))
        gate_mm, gate_x, gate_in = (sem(f"gate_{s}") for s in ("mm", "x", "in"))
        ns_grp, ns_q, ns_qe, ns_s, ns_m, ns_p, ns_f, ns_tt, ns_t, ns_o, ns_oe = (
            sem(f"ns_{s}") for s in ("grp", "q", "qe", "s", "m", "p", "f", "tt", "t", "o", "oe"))

        b2_in, b2_T, b2_ready = sem("b2_in"), sem("b2_T"), sem("b2_ready")
        lam_d, lam_e = sem("lam_d"), sem("lam_e")
        df_pj, df_pe, df_s, df_m, df_p, df_f, df_tt, df_t, df_o, df_sq, df_ms, df_v, df_sd, df_oe = (
            sem(f"df_{s}") for s in ("pj", "pe", "s", "m", "p", "f", "tt", "t", "o", "sq", "ms", "v", "sd", "oe"))
        br_mm, br_sig, br_m, br_o_hi, br_o = (sem(f"br_{s}") for s in ("mm", "sig", "m", "o_hi", "o"))
        split2_hi, split2, out_used = sem("split2_hi"), sem("split2"), sem("out_used")
        gq_b, gq_br, gq_x, gq_sd, gq_s, gq_m, gq_p, gq_f, gq_tt, gq_t, gq_o, gq_oe = (
            sem(f"gq_{s}") for s in ("b", "br", "x", "sd", "s", "m", "p", "f", "tt", "t", "o", "oe"))
        moe_in, u_row, h_out = (sem(s) for s in ("moe_in", "u_row", "h_out"))
        fin_sq, fin_ms, fin_sd, fin_h = (sem(f"fin_{s}") for s in ("sq", "ms", "sd", "h"))
        ex_done = sem("ex_done")
        ex_xh, ex_gate, ex_wh, ex_ws = (sem(f"ex_{s}") for s in ("xh", "gate", "wh", "ws"))
        u_scaled, u_out = sem("u_scaled"), sem("u_out")
        ex_x = [sem(f"ex_x{k}") for k in range(2)]
        rt_l, rt_x, rt_e, rt_a, rt_at, rt_s, rt_st, rt_oh, rt_pk = (
            sem(f"rt_{s}") for s in ("l", "x", "e", "a", "at", "s", "st", "oh", "pk"))
        ex_no, ex_xt, ex_xe, ex_gu, ex_sg, ex_h, ex_ht, ex_he, ex_y, ex_ye, ex_out = (
            sem(f"ex_{s}") for s in ("no", "xt", "xe", "gu", "sg", "h", "ht", "he", "y", "ye", "out"))

        ring = Ring(ring_tile, loaded, slot_free)
        NSA_CONST = 16 * 10
        B2_CONST, MOE_CONST = 16 * 12, 16 * 3
        NORM_TILES = [QT] * 6 + [T2] * 2
        PLAIN = (5,)
        GAIN = {**{u: u for u in range(5)}, 6: 5, 7: 6}
        EPS = [EPS1] * 6 + [EPS2] * 2
        UPD = 2 * QT
        FF_UPD = FF_PARTS * UPD
        H_BEFORE = [0, UPD, UPD + FF_UPD, UPD + FF_UPD, 2 * UPD + FF_UPD]
        H_ALL = 2 * UPD + 2 * FF_UPD
        H_X2 = H_ALL + QT
        H_FFN = H_X2 + 2 * T2

        block = ctx.enter_context(nc.Block())

        def load_ff(sp, m):
            w1, w2 = A["mlp_w1"][m], A["mlp_w2"][m]
            ring.load(sp, f"ff{m}",
                      [cols_tile(w1, lambda t, j=j: t * FF_TILES + j) for j in range(FF_TILES)]
                      + [rows_tiles(w2, lambda t, k=k: t * FF_TILES + 2 * k, lambda t, n=n: 512 * n)
                         for n in range(2) for k in range(FF_TILES // 2)], FF_PARTS)

        def finish(sp):
            sp.wait_ge(ex_out, EXPERTS * 16)
            for t in range(QT):
                sp.dma_start(h[:, t, :], y_dram[t * P:(t + 1) * P, :]).then_inc(tile_in[t], 16)
            for t in range(QT):
                sp.wait_ge(fin_h, t + 1)
                sp.dma_start(out[0, t * P:(t + 1) * P, :], h[:, t, :]).then_inc(out_sem, 16)
            sp.wait_ge(out_sem, 16 * QT)

        ALL_CONST = 16 * (4 + 7)

        @block.sync
        def _(sp):
            for t in range(QT):
                sp.dma_start(h[:, t, :], A["x"][0, t * P:(t + 1) * P, :]).then_inc(tile_in[t], 16)
            for dst, src in ((ident, C["ident"]), (tri_neg, C["tri_neg"]), (past01, C["past01"]), (past_neg, C["past_neg"])):
                sp.dma_start(dst[:, :], src[:, :]).then_inc(const_in, 16)
            for k, g in enumerate((A["norm_gain"][0, 0], A["norm_gain"][0, 1], A["kv_norm"], A["norm_gain"][1, 0],
                                   A["norm_gain"][1, 1], A["g_mix_2"][0], A["g_ffn_2"][0])):
                sp.dma_start(gain_rows[k * KT:(k + 1) * KT, :], g.rearrange("(k p) -> k p", p=P)).then_inc(const_in, 16)

            wq = A["sb_w_qkv"][0]

            def pair(p):
                return [cols_tile(wq, lambda t: p(t)), cols_tile(wq, lambda t: KT + p(t)),
                        cols_tile(wq, lambda t: 2 * KT + p(t)), None]
            ring.load(sp, "sb_first", pair(lambda t: 0))
            ring.load(sp, "sb_loop", pair(lambda t: t * 2 + 1) + pair(lambda t: t * 2 + 2), PAIRS // 2 - 1)
            ring.load(sp, "sb_last", pair(lambda t: PAIRS - 1))
            ring.load(sp, "sb_o", [rows_tiles(A["sb_w_o"][0], lambda t, k=k: 2 * k, lambda t, n=n: 512 * n)
                                   for n in range(2) for k in range(KT // 2)])
            load_ff(sp, 0)

            ring.load(sp, "kv_first", [cols_tile(A["nsa_w_kv"], lambda t, j=j: j) for j in range(RING)])
            sp.wait_ge(h_upd, H_BEFORE[2])
            for dst, src in ((pos_rows[:, :], A["cmp_pos"].rearrange("c (k l) d -> (c k) (l d)", l=2)),
                             (cmp_w2[:, :, :, :], A["cmp_w2"].rearrange("c (e p) d -> p c e d", p=P)),
                             (gate_w[:, :, :], A["nsa_w_q"][0][:, D:D + N_GATES].rearrange("(k p) n -> p k n", p=P)),
                             (gate_b[:, :], A["nsa_gate_b"][0].partition_broadcast(P)),
                             (cos1[:, :], C["cos1"]), (sin1[:, :], C["sin1"]), (rot1[:, :], C["rot1"]),
                             (future_neg[:, :], C["future_neg"]), (cmp_neg[:, :, :], C["cmp_neg"]), (cmp_any[:, :], C["cmp_any"])):
                sp.dma_start(dst, src).then_inc(nsa_in, 16)
            sp.dma_start(gain_bc[:, :], A["final_norm"].partition_broadcast(P)).then_inc(gain_in, 16)
            ring.load(sp, "kv_last", [cols_tile(A["nsa_w_kv"], lambda t, j=j: j) for j in range(RING, 12)])
            ring.load(sp, "cmp", [rows_tiles(A["cmp_w1"][c], lambda t, k=k: 4 * k, lambda t: 0, CMP_HID)
                                  for c in range(2) for k in range(CMP_KT // 4)])
            wq = A["nsa_w_q"][0]
            ring.load(sp, "nsa", [cols_tile(wq, lambda t: t * 2), None, None, None,
                                  cols_tile(wq, lambda t: t * 2 + 1), None, None, None], GROUPS)
            ring.load(sp, "nsa_o", [rows_tiles(A["nsa_w_o"][0], lambda t, k=k: 2 * k, lambda t, n=n: 512 * n)
                                    for n in range(2) for k in range(KT // 2)])
            load_ff(sp, 1)

            sp.dma_start(h[0:META, QT, :], A["meta_tokens_2"][:, :]).then_inc(b2_in, 16)
            sp.wait_ge(h_upd, H_ALL)
            for dst, src in ((dist[:, :, :], C["dist"]), (cos2[:, :], C["cos2"]), (sin2[:, :], C["sin2"]), (rot2[:, :], C["rot2"]),
                             (head_gain_rows[0:1, :], A["g_subln_2"]), (head_gain_rows[1:2, :], A["g_qnorm_2"]),
                             (head_gain_rows[2:3, :], A["g_knorm_2"]),
                             (lam_in[:, 0, :], A["lambda_q1_2"][0].partition_broadcast(P)),
                             (lam_in[:, 1, :], A["lambda_k1_2"][0].partition_broadcast(P)),
                             (lam_in[:, 2, :], A["lambda_q2_2"][0].partition_broadcast(P)),
                             (lam_in[:, 3, :], A["lambda_k2_2"][0].partition_broadcast(P))):
                sp.dma_start(dst, src).then_inc(b2_in, 16)
            w = A["w_in_2"][0]

            def head(p):
                return [cols_tile(w, lambda t, c=c: c + p(t)) for c in (W_IN["qa"], W_IN["ka"], W_IN["va"])] + [None]

            def branch(name, gate, out_w):
                pairs = [(cols_tile(w, lambda t, n=n: gate + t * 4 + n), cols_tile(out_w, lambda t, n=n: t * 4 + n)) for n in range(4)]
                ring.load(sp, name, [s for p in pairs for s in p], 2)

            ring.load(sp, "df_first", head(lambda t: 0))
            ring.load(sp, "df_loop", head(lambda t: t * 2 + 1) + head(lambda t: t * 2 + 2), HEADS2 // 2 - 1)
            ring.load(sp, "df_last", head(lambda t: HEADS2 - 1))
            branch("br0", W_IN["ga"], A["w_branch_a_2"][0])
            queries = [cols_tile(w, lambda t, j=j: W_IN["qb"] + t * Q_PER_KV + j) for j in range(Q_PER_KV)]
            ring.load(sp, "gqa", [cols_tile(w, lambda t: W_IN["kb"] + t), queries[0], cols_tile(w, lambda t: W_IN["vb"] + t)]
                      + queries[1:] + [None, None], KV2)
            branch("br1", W_IN["gb"], A["w_branch_b_2"][0])
            ring.load(sp, "w_out", [rows_tiles(A["w_out_2"][0], lambda t, k=k: 2 * k, lambda t, n=n: 512 * n)
                                    for n in range(2) for k in range(KT // 2)])

            sp.wait_ge(h_upd, H_FFN)
            for dst, src in ((router_w[:, :, :], A["w_router_2"][0].rearrange("(k p) n -> p k n", p=P)),
                             (slot_no[:, :], C["slot_no"]), (token_no[:, :, :], C["token_no"])):
                sp.dma_start(dst, src).then_inc(moe_in, 16)
            sp.wait_ge(gain_in, 16)
            sp.dma_start(gain_bc[:, :], A["g_ffn_2"][0].partition_broadcast(P)).then_inc(gain_in, 16)
            wg, wu, wd = (A[n][0].rearrange("e r c -> (e r) c") for n in ("w_gate_2", "w_up_2", "w_down_2"))

            def gate_up(e):
                return [rows_tiles(m, lambda t, k=k: e(t) * KT + 2 * k, lambda t: 0) for m in (wg, wu) for k in range(KT // 2)]

            def down(e):
                return [rows_tiles(wd, lambda t, k=k: e(t) * FT + k, lambda t: 0, D) for k in range(FT)]

            ring.load(sp, "ex_first", gate_up(lambda t: 0))
            ring.load(sp, "ex_loop", gate_up(lambda t: t * 2 + 1) + down(lambda t: t * 2)
                      + gate_up(lambda t: t * 2 + 2) + down(lambda t: t * 2 + 1), EXPERTS // 2 - 1)
            ring.load(sp, "ex_last", gate_up(lambda t: EXPERTS - 1) + down(lambda t: EXPERTS - 2) + down(lambda t: EXPERTS - 1))
            sp.wait_ge(u_row, T2)
            sp.dma_start(gain_bc[:, :], A["g_final_2"].partition_broadcast(P)).then_inc(gain_in, 16)
            finish(sp)

        def take_o(dve, hi, rows, pair, src, taken):
            upper, rest = (x[rows, bass.ds(pair, 1), 0:SEQ].rearrange("p a n -> p (a n)") for x in (hi, oT_lo))
            step(dve, dve.tensor_copy(upper, src[0:HD, :]))
            dve.tensor_tensor(rest, src[0:HD, :], upper.bitcast(F32), ALU.subtract).then_inc(taken, 1)

        def norm_base(u):
            return sum(n for v, n in enumerate(NORM_TILES[:u]) if v not in PLAIN)

        SHARED = 1

        def stat(u):
            return u - (SHARED if u >= 3 else 0)

        HALVED = (1, 2, 4, 5, 7)

        def norm_act(act, u, updated=None):
            if u != 6:
                act.preload_act_table_set(LN_EXP)
            tiles, parts = NORM_TILES[u], 2 if u in HALVED else 1
            for c in range(parts):
                cols = slice(c * D // parts, (c + 1) * D // parts)
                for t in range(tiles):
                    r = rows_of(t)
                    if u == 0:
                        act.wait_ge(tile_in[t], 16)
                    if updated is not None and not (u == 6 and t == QT):
                        act.wait_ge(h_upd, updated - (parts - 1 - c) * tiles + t + 1)
                    last = act.activation(sq_junk(r)[:, cols], h[0:r, t, cols], ACT.Square, scale=D ** -0.5, accum_out=ssq[0:r, c, t:t + 1])
                    if c < parts - 1 or t < tiles - 1:
                        act_t.inc(last)
                        act.wait_ge(act_step, act_t.value())
            last.then_inc(norm_sq, 1)

        def norm_pool(pool, u):
            pool.wait_ge(norm_sq, stat(u) + 1)
            total = ssq[:, 0, :]
            if u in HALVED:
                pool_t.inc(pool.tensor_tensor(rstd[:, :], total, ssq[:, 1, :], ALU.add))
                pool.wait_ge(norm_ms, pool_t.value())
                total = rstd[:, :]
            pool_t.inc(pool.tensor_scalar(rstd[:, :], total, EPS[u], None, ALU.add))
            pool.wait_ge(norm_ms, pool_t.value())
            pool.tensor_tensor(rstd[:, :], rstd[:, :], neg_half[:, :].broadcast_to([P, T2]), ALU.pow).then_inc(norm_sd, 1)

        def sq_junk(r):
            return xn[0:r, 1, :]

        def scale_act(act, u):
            base = norm_base(u)
            act.wait_ge(norm_sd, stat(u) + 1)
            for t in range(NORM_TILES[u]):
                r = rows_of(t)
                if t >= 2:
                    act.wait_ge(norm_tp, 2 * (base + t - 1))
                act.activation(xn[0:r, t % 2, :], h[0:r, t, :], ACT.Copy, scale=rstd[0:r, t:t + 1]).then_inc(norm_xn, 1)
                if u in SPLIT_NORMS and t:
                    split_x_act(act, u, t - 1)
            if u in SPLIT_NORMS:
                split_x_act(act, u, NORM_TILES[u] - 1)

        def norm_dve(dve, u):
            base = norm_base(u)
            for t in range(NORM_TILES[u]):
                r = rows_of(t)
                for c in range(2):
                    dve.wait_ge(norm_tp, 2 * (base + t) + c + 1)
                    src = bank[2 * (t % 2) + c][:, :].rearrange("p (k n) -> p k n", k=4)[:, :, 0:r]
                    dve.tensor_tensor(xT[:, 4 * c:4 * c + 4, t * P:t * P + r], src,
                                      gains[:, GAIN[u], 4 * c:4 * c + 4].unsqueeze(2).broadcast_to([P, 4, r]), ALU.mult).then_inc(norm_ev, 1)
                if u in SPLIT_NORMS and t:
                    split_x_dve(dve, u, t - 1)
            if u in SPLIT_NORMS:
                split_x_dve(dve, u, NORM_TILES[u] - 1)

        SPLIT_NORMS = (0, 1, 4, 6)
        FF_NORMS = (1, 4)

        def x_part(x, t, c):
            return x[:, 4 * c:4 * c + 4, t * P:t * P + rows_of(t)]

        def split_base(u):
            return sum(2 * NORM_TILES[v] for v in SPLIT_NORMS if v < u)

        def split_of(u):
            return (x2_hi, x2_lo) if u == 6 else (x_hi, x_lo)

        def split_x_act(act, u, t):
            for c in range(2):
                act.wait_ge(norm_ev, 2 * (norm_base(u) + t) + c + 1)
                act.activation(x_part(split_of(u)[0], t, c), x_part(xT, t, c), ACT.Copy).then_inc(split_x_hi, 1)

        def split_x_dve(dve, u, t):
            for c in range(2):
                dve.wait_ge(norm_ev, 2 * (norm_base(u) + t) + c + 1)
                dve.wait_ge(split_x_hi, split_base(u) + 2 * t + c + 1)
                hi, lo = split_of(u)
                dve.tensor_tensor(x_part(lo, t, c), x_part(xT, t, c), x_part(hi, t, c).bitcast(F32), ALU.subtract).then_inc(split_x, 1)

        def norm_pe(pe, u, then=None):
            base = norm_base(u)
            for t in range(NORM_TILES[u]):
                r = P if t < QT else META
                pe.wait_ge(norm_xn, base + t + 1)
                if t >= 2:
                    pe.wait_ge(norm_ev, 2 * (base + t - 1))
                for c in range(2):
                    for k in range(4):
                        last = pe.transpose(bank[2 * (t % 2) + c][:, k * P:k * P + r],
                                            xn[0:r, t % 2, (4 * c + k) * P:(4 * c + k + 1) * P], ident[0:r, 0:r])
                    last.then_inc(norm_tp, 1)
                if then and t:
                    pe.wait_ge(norm_ev, 2 * (base + t))
                    then(t - 1)
            pe.wait_ge(norm_ev, 2 * (base + NORM_TILES[u]))
            if then:
                then(NORM_TILES[u] - 1)

        def plain_norm_dve(dve, u, tiles):
            dve.wait_ge(norm_sd, stat(u) + 1)
            for t in range(tiles):
                dve.scalar_tensor_tensor(h[:, t, :], h[:, t, :], rstd[:, t:t + 1], gain_bc[:, :], ALU.mult, ALU.mult).then_inc(h_upd, 1)

        BR_SPLITS, GQ_SPLITS = 2 * KT, Q_PER_KV + 1
        SPLIT_COUNTS = (("sb", 2 * PAIRS), ("sb_o", KT), ("nsa_o", KT), ("df", 2 * HEADS2), ("br0", BR_SPLITS),
                        ("gqa", KV2 * GQ_SPLITS), ("br1", BR_SPLITS), ("w_out", KT))
        SPLIT_BASE = {name: sum(n for _, n in SPLIT_COUNTS[:i]) for i, (name, _) in enumerate(SPLIT_COUNTS)}

        def split2_pool(pool, name, j, turn, no, hi):
            raw = ring.wait(pool, name, j, turn)
            lo = ring_lo[:, ring.plan[name][j][0], :]
            pool.tensor_tensor(hi, raw, one[:, :].broadcast_to([P, D]), ALU.mult).then_inc(split2_hi, 1)
            pool.wait_ge(split2_hi, no + 1)
            pool.tensor_tensor(lo, raw, hi.bitcast(F32), ALU.subtract).then_inc(split2, 1)

        def split2_wait(pe, name, j, turn, no, hi, width=P):
            pe.wait_ge(split2, no + 1)
            lo = ring_lo[:, ring.plan[name][j][0], :]
            return [w.rearrange("p (k n) -> p k n", n=width) for w in (hi, lo)]

        def mm3_T(pe, dst, w, x_hi, x_lo, c, begun=None):
            return mm3_K(pe, dst, w, x_hi[:, :, half(c)], x_lo[:, :, half(c)], begun=begun)

        def mm3_K(pe, dst, w, x_hi, x_lo, k0=0, k1=KT, begun=None):
            hi, lo = w
            for k in range(k0, k1):
                last = mm3(pe, dst, hi[:, k, :], lo[:, k, :], x_hi[:, k, :], x_lo[:, k, :], k == 0, k == KT - 1, begun if k == k0 else None)
            return last

        def split_heads_pool(pool, kind, first, rest, last, heads, used, per, hi):
            each = per // 3

            def head(name, j, turn, hd, again=True):
                for n in range(2):
                    if again:
                        pool.wait_ge(used, hd * per + ((n + 1) * each - per))
                    split2_pool(pool, name, j + n, turn, hd * 2 + (SPLIT_BASE[kind] + n), hi[:, n, :])

            head(first, 0, 0, 0, False)
            with loop(pool, heads // 2 - 1) as turn:
                head(rest, 0, turn, turn * 2 + 1)
                head(rest, 4, turn, turn * 2 + 2)
            head(last, 0, 0, heads - 1)
            pool.wait_ge(used, (heads - 1) * per + 2 * each)

        OUT_NAMES = ("sb_o", "nsa_o", "w_out")

        def output_pool(pool, name, hi, depth=SPLITS2, free=None):
            for j in range(KT):
                if j < depth and free:
                    free(j)
                if j >= depth:
                    pool.wait_ge(out_used, OUT_NAMES.index(name) * (KT - 1) + j - depth + 1)
                split2_pool(pool, name, j, 0, SPLIT_BASE[name] + j, hi[:, j % depth, :])

        def output_weights(pe, name, j, w_hi, depth=SPLITS2):
            return split2_wait(pe, name, j, 0, SPLIT_BASE[name] + j, w_hi[:, j % depth, :], 512)

        def output_mm(pe, dst, a, w, k, t):
            (a_hi, a_lo), (hi, lo), rows = a, w, slice(t * P, t * P + rows_of(t))
            first = pe.matmul(dst, a_hi[:, k, rows], lo[:, k % 2, :], start=(k == 0), stop=False)
            pe.matmul(dst, a_lo[:, k, rows], hi[:, k % 2, :], start=False, stop=False)
            return first, pe.matmul(dst, a_hi[:, k, rows], hi[:, k % 2, :], start=False, stop=(k == KT - 1))

        def output_half_pe(pe, n, name, a, w_hi, tiles, bank_of, done, again=None, depth=SPLITS2):
            for k in range(KT):
                j = n * (KT // 2) + k // 2
                if k % 2 == 0:
                    w = output_weights(pe, name, j, w_hi, depth)
                for t in range(tiles):
                    if k == 0 and again:
                        again(n, t)
                    first, last = output_mm(pe, bank[bank_of(n, t)][0:rows_of(t), :], a, w, k, t)
                    if j and t == 0 and k % 2 == 0:
                        first.then_inc(out_used, 1)
                    if k == KT - 1:
                        last.then_inc(acc_done, 1)
                if k == KT - 1:
                    pe.wait_ge(acc_done, done + (n + 1) * tiles)
                    pe.sem_inc(slot_free, 1)
                elif k % 2:
                    last.then_inc(slot_free, 1)

        def output_pe(pe, name, a_hi, a_lo, w_hi, tiles, bank_of, done, again=None):
            for n in range(2):
                output_half_pe(pe, n, name, (a_hi, a_lo), w_hi, tiles, bank_of, done, again)

        def sb_out_banks(n, t):
            return 4 * (1 - n) + (t + 1 - n) % QT

        def sb_out_early(pe):
            for k in range(KT - 1):
                w = output_weights(pe, "sb_o", k // 2, w_hi, SPLITS)
                pe.wait_ge(sb_oe, 2 * (k + 1) + 1)
                for t in range(QT - 1):
                    output_mm(pe, bank[sb_out_banks(0, t)], (sb_o_hi, oT_lo), w, k, t)
                yield

        def sb_out_pe(pe):
            a, k_last = (sb_o_hi, oT_lo), KT - 1
            pe.wait_ge(sb_oe, 2 * PAIRS + 1)
            w = output_weights(pe, "sb_o", k_last // 2, w_hi, SPLITS)
            for t in range(QT - 1):
                output_mm(pe, bank[sb_out_banks(0, t)], a, w, k_last, t)[1].then_inc(acc_done, 1)
            for k in range(KT):
                w = output_weights(pe, "sb_o", k // 2, w_hi, SPLITS)
                first, last = output_mm(pe, bank[sb_out_banks(0, QT - 1)], a, w, k, QT - 1)
                if k and k % 2 == 0:
                    first.then_inc(out_used, 1)
                if k < k_last and k % 2:
                    last.then_inc(slot_free, 1)
            last.then_inc(acc_done, 1)
            pe.wait_ge(acc_done, QT)
            pe.sem_inc(slot_free, 1)
            output_half_pe(pe, 1, "sb_o", a, w_hi, QT, sb_out_banks, 0, depth=SPLITS)

        def half_banks(n, t):
            return 4 * (1 - n) + t

        KV_ROT = {4: 0, 5: 1, 8: 2, 9: 3}

        def kv_pe(pe):
            def tile(n):
                slot = ring.wait(pe, "kv_first", n) if n < RING else ring.wait(pe, "kv_last", n - RING)
                if n >= 4:
                    pe.wait_ge(kv_ev, n - 3)
                begun = slot_free if n else None
                if n in (6, 7, 10, 11):
                    for t in range(QT):
                        last = mm_N(pe, bank[n % 4][:, t * P:(t + 1) * P], slot, t, begun=begun if t == 0 else None)
                else:
                    last = mm_T(pe, bank[n % 4][:, :], slot, xT[:, :, 0:SEQ], begun=begun)
                last.then_inc(kv_mm, 1)

            def rotate(n):
                pe.wait_ge(kv_ev, n + 1)
                pe.matmul(bank[4 + n % 2][:, :], rot1[:, :], (rope_a if n % 2 == 0 else rope_b)[:, :],
                          start=True, stop=True).then_inc(kv_rot, 1)

            for n in range(4):
                tile(n)
            pe.wait_ge(nsa_in, NSA_CONST)
            pe.transpose(bank[7][:, 0:2 * CMP_KT], pos_rows[:, :], ident[0:2 * CMP_KT, 0:2 * CMP_KT]).then_inc(pos_T, 1)
            for n in (4, 8):
                tile(n)
                tile(n + 1)
                rotate(n)
                tile(n + 2)
                rotate(n + 1)
                tile(n + 3)
            pe.wait_ge(kv_k, 4)
            for c in range(2):
                for k in range(CMP_KT):
                    w = ring.wait(pe, "cmp", c * 4 + k // 4).rearrange("p (k n) -> p k n", n=CMP_HID)
                    if k == 0:
                        pe.wait_ge(cmp_blk, c + 1)
                    for e in range(2):
                        last = pe.matmul(bank[4 + 2 * c + e][:, 0:GROUPS * N_CMP], w[:, k % 4, e * P:(e + 1) * P], blocks[:, c, k, :],
                                         start=(k == 0), stop=(k == CMP_KT - 1))
                        if k == 0 and e == 0:
                            last.then_inc(slot_free, 1)
                    if k == CMP_KT - 1:
                        last.then_inc(cmp_mm, 1)
                        if c:
                            pe.wait_ge(cmp_mm, c + 1)
                            pe.sem_inc(slot_free, 1)
                    elif k % 4 == 3:
                        last.then_inc(slot_free, 1)
            pe.wait_ge(cmp_hh, 2)
            for half in range(2):
                for e in range(2):
                    pe.matmul(bank[0][HD * half:HD * half + HD, 0:GROUPS * N_CMP], cmp_w2[:, 0, e, :], cmp_h[:, 0, e, :],
                              start=(e == 0), stop=(e == 1))
            for g in range(GROUPS):
                for e in range(2):
                    last = pe.matmul(bank[1][0:N_CMP, g * HD:(g + 1) * HD], cmp_h[:, 1, e, g * N_CMP:(g + 1) * N_CMP],
                                     cmp_w2[:, 1, e, :], start=(e == 0), stop=(e == 1))
            last.then_inc(cmp_kv, 1)

        def kv_dve(dve):
            for n in range(4):
                c, gp = n // 2, n % 2
                dve.wait_ge(kv_mm, n + 1)
                for gi in range(2):
                    src = bank[n % 4][HD * gi:HD * gi + HD, :]
                    dve.tensor_copy(kv_pairs[0:HD, c, 2 * gp + gi, :], src)
                    last = dve.tensor_copy(kv_pairs[HD:P, c, 2 * gp + gi, 0:SEQ - 1], src[:, 1:SEQ])
                last.then_inc(kv_ev, 1)
            dve.wait_ge(nsa_in, NSA_CONST)
            dve.tensor_copy(future_neg_bf[:, :], future_neg[:, :])
            dve.wait_ge(pos_T, 1)
            step(dve, dve.tensor_copy(pos_off[:, :], bank[7][:, 0:2 * CMP_KT]))

            def take_blocks(c, k0, k1):
                dve.wait_ge(kv_ev, 2 * c + 2)
                for k in range(k0, k1):
                    last = dve.tensor_scalar(blocks[:, c, k, :].rearrange("p (g n) -> p g n", g=GROUPS),
                                             kv_pairs[:, c, :, bass.ds(2 * k, N_CMP, CMP_STRIDE)],
                                             pos_off[:, c * CMP_KT + k:c * CMP_KT + k + 1], None, ALU.add)
                if k1 == CMP_KT:
                    last.then_inc(cmp_blk, 1)

            for br, n0 in ((0, 4), (1, 8)):
                for n in (n0, n0 + 1):
                    dve.wait_ge(kv_mm, n + 1)
                    raw = (rope_a if n % 2 == 0 else rope_b)
                    dve.tensor_copy(raw[:, :], bank[n % 4][:, :]).then_inc(kv_ev, 1)
                for n in (n0, n0 + 1):
                    raw = (rope_a if n % 2 == 0 else rope_b)
                    dve.wait_ge(kv_rot, KV_ROT[n] + 1)
                    dve_t.inc(dve.tensor_tensor(q_raw[:, 0, :], raw[:, :], cos1[:, :], ALU.mult))
                    step(dve, dve.tensor_tensor(q_raw[:, 1, :], bank[4 + n % 2][:, :], sin1[:, :], ALU.mult))
                    for gi in range(2):
                        r = slice(HD * gi, HD * gi + HD)
                        for half in range(2):
                            last = dve.tensor_tensor(k_all[HD * half:HD * half + HD, br, 2 * (n - n0) + gi, :],
                                                     q_raw[r, 0, :], q_raw[r, 1, :], ALU.add)
                    last.then_inc(kv_k, 1)
                    dve.wait_ge(kv_k, KV_ROT[n] + 1)
                    dve.wait_ge(kv_mm, n + 3)
                    dve.tensor_copy(v_all[:, br, :, 2 * (n - n0):2 * (n - n0) + 2, :],
                                    bank[(n + 2) % 4][:, :].rearrange("p (t g d) -> p t g d", t=QT, g=2)).then_inc(kv_ev, 1)
                take_blocks(br, 0, CMP_KT)
            for c in range(2):
                dve.wait_ge(cmp_mm, c + 1)
                for e in range(2):
                    last = dve.tensor_copy(cmp_x[:, e, :], bank[4 + 2 * c + e][:, 0:GROUPS * N_CMP])
                step(dve, last)
                step(dve, dve.tensor_tensor(cmp_u[:, :, :], cmp_x[:, :, :], cmp_x[:, :, :], ALU.mult))
                step(dve, dve.tensor_scalar(cmp_u[:, :, :], cmp_u[:, :, :], GELU_C, 1.0, ALU.mult, ALU.add))
                dve.tensor_tensor(cmp_u[:, :, :], cmp_u[:, :, :], cmp_x[:, :, :], ALU.mult).then_inc(cmp_uu, 1)
                dve.wait_ge(cmp_ee, c + 1)
                step(dve, dve.tensor_scalar(cmp_u[:, :, :], cmp_u[:, :, :], 0.5, 0.5, ALU.mult, ALU.add))
                dve.tensor_tensor(cmp_h[:, c, :, :], cmp_u[:, :, :], cmp_x[:, :, :], ALU.mult).then_inc(cmp_hh, 1)
                dve.wait_ge(cmp_hh, c + 1)
            dve.wait_ge(cmp_kv, 1)
            dve.tensor_copy(k_cmp[:, :, :].rearrange("p g n -> p (g n)"), bank[0][:, 0:GROUPS * N_CMP])
            dve.tensor_copy(v_cmp[:, :, :].rearrange("p g d -> p (g d)"), bank[1][0:N_CMP, 0:GROUPS * HD]).then_inc(cmp_out, 1)

        def kv_act(act):
            for c in range(2):
                act.wait_ge(cmp_uu, c + 1)
                act.activation(cmp_u[:, :, :], cmp_u[:, :, :], ACT.Tanh, scale=GELU_K).then_inc(cmp_ee, 1)

        def gates_pe(pe):
            for t in range(QT):
                for k in range(KT):
                    last = pe.matmul(bank[4][:, t * N_GATES:(t + 1) * N_GATES], xT[:, k, t * P:(t + 1) * P], gate_w[:, k, :],
                                     start=(k == 0), stop=(k == KT - 1))
            last.then_inc(gate_mm, 1)

        def gates_dve(dve):
            dve.wait_ge(gate_mm, 1)
            dve.tensor_tensor(gates[:, :, :], bank[4][:, 0:QT * N_GATES].rearrange("p (t n) -> p t n", t=QT),
                              gate_b[:, :].unsqueeze(1).broadcast_to([P, QT, N_GATES]), ALU.add).then_inc(gate_x, 1)
            dve.wait_ge(gate_in, 1)

        def gates_act(act):
            act.wait_ge(gate_x, 1)
            act.activation(gates[:, :, :], gates[:, :, :], ACT.Sigmoid).then_inc(gate_in, 1)

        def unit(n):
            head, br = n // BRANCHES, n % BRANCHES
            return head // 2, slice(HD * (head % 2), HD * (head % 2) + HD), br

        PIECES = ((3,), (2, 0), (1,))
        PER_HEAD = 1 + 2 * len(PIECES)

        def piece(n, k):
            head, br = n // BRANCHES, n % BRANCHES
            return head * PER_HEAD + (3 * br - 2 + k if br else 0)

        def piece_before(n, k):
            head, br = n // BRANCHES, n % BRANCHES
            return piece(n, 0) + (-1, (-4, -3, -1)[k], k - 3)[br]

        PER_GROUP = 4 * PER_HEAD

        def pieces(br):
            return PIECES if br else (range(QT),)

        def score_bank(i, br):
            if br == 0:
                return bank[2][:, 256 + 32 * i:256 + 32 * i + N_CMP]
            b, at = SCORE_AT[i]
            return bank[b][:, at:at + P * (i + 1)]

        QUERY_UNITS = (0, 1, 3)
        NEXT_UNITS = (6, 7, 9)
        GROUP_PARTS = 6

        def nsa_queries_pe(pe, g, u, first=False):
            done = g * 4 + 2 * u
            if not first:
                pe.wait_ge(ns_qe, done)
            slot = ring.wait(pe, "nsa", 4 * u, g)
            mm_T(pe, bank[7][:, :], slot, xT[:, :, 0:SEQ], 0, KT // 2)
            yield
            mm_T(pe, bank[7][:, :], slot, xT[:, :, 0:SEQ], KT // 2, KT).then_inc(ns_q, 1)
            yield
            pe.wait_ge(ns_q, done + 1)
            pe.sem_inc(slot_free, 4)
            pe.wait_ge(ns_qe, done + 1)
            pe.matmul(bank[7][:, :], rot1[:, :], q_raw[:, u, :], start=True, stop=True).then_inc(ns_q, 1)
            yield

        def nsa_scores(pe, g, n):
            u, r, br = unit(n)
            if n < BRANCHES:
                pe.wait_ge(ns_grp, g * GROUP_PARTS + (n + 1))
            if n % 6 < 2:
                pe.wait_ge(ns_qe, g * 4 + (2 * u + n % 6 + 1))
            for k, tiles in enumerate(pieces(br)):
                pe.wait_ge(ns_p, g * PER_GROUP + piece_before(n, k) + 4)
                for i in tiles:
                    q, dst = slice(i * P, (i + 1) * P), score_bank(i, br)
                    if br == 0:
                        last = pe.matmul(dst, q_raw[r, u, q], kc_grp[r, :], start=True, stop=True)
                        continue
                    pe.matmul(dst, q_rot[r, u, q], k_grp[r, br - 1, 0:P * (i + 1)], start=True, stop=False, skip_group_check=True)
                    last = pe.matmul(dst[:, i * P:(i + 1) * P], ident_bf[:, :], future_neg_bf[:, :], start=False, stop=True,
                                     skip_group_check=True)
                last.then_inc(ns_s, 1)

        def nsa_pe(pe, g, more):
            def transposes(n):
                _, _, br = unit(n)
                pe.wait_ge(ns_f, g * UNITS + n + 1)
                pe.wait_ge(ns_t, g * UNITS + n + 1)
                if br == 0:
                    for i in range(QT):
                        last = pe.transpose(bank[3][0:N_CMP, i * P:(i + 1) * P], probs[:, n % 2, i * N_CMP:(i + 1) * N_CMP], ident[:, :])
                else:
                    for j in range(QT):
                        b, at, _ = PT_AT[j]
                        for i in range(j, QT):
                            last = pe.transpose(bank[b][:, at + (i - j) * P:at + (i - j + 1) * P],
                                                probs[:, n % 2, PROB_AT[i] + j * P:PROB_AT[i] + (j + 1) * P], ident[:, :])
                last.then_inc(ns_tt, 1)

            def weigh(n):
                u, r, br = unit(n)
                pe.wait_ge(ns_t, g * UNITS + n + 2)
                if n < BRANCHES:
                    pe.wait_ge(ns_grp, g * GROUP_PARTS + (BRANCHES + n + 1))
                if br == 0:
                    pe.wait_ge(ns_oe, g * 4 + n // BRANCHES + 1)
                    pe.matmul(bank[6][0:HD, :], vc_grp[:, :], probs_T[0:N_CMP, n % 2, 0:SEQ], start=True, stop=False, skip_group_check=True)
                    return
                for j in range(QT):
                    at = PT_AT[j][2]
                    last = pe.matmul(bank[6][0:HD, j * P:SEQ], v_grp[:, br - 1, j, :], probs_T[:, n % 2, at:at + CAUSAL_COLS[j]],
                                     start=False, stop=(br == 2 and j == QT - 1), skip_group_check=True)
                if br == 2:
                    last.then_inc(ns_o, 1)

            second = nsa_queries_pe(pe, g, 1)
            following = nsa_queries_pe(pe, g + 1, 0) if more else iter(())
            for n in range(UNITS):
                if n + 1 < UNITS:
                    nsa_scores(pe, g, n + 1)
                elif more:
                    nsa_scores(pe, g + 1, 0)
                if n:
                    weigh(n - 1)
                if n in QUERY_UNITS:
                    next(second)
                elif n in NEXT_UNITS:
                    next(following, None)
                transposes(n)
            weigh(UNITS - 1)

        def nsa_pool(pool):
            def one(ap):
                return ap.rearrange("p a n -> p (a n)")

            def keys_and_values(g, free):
                k_of = [(kc_grp[:, :], one(k_cmp[:, bass.ds(g, 1), :]))]
                k_of += [(k_grp[:, br, :], one(k_all[:, br, bass.ds(g, 1), :])) for br in range(2)]
                v_of = [(vc_grp[:, :], one(v_cmp[:, bass.ds(g, 1), :]))]
                v_of += [(v_grp[:, br, :, :], v_all[:, br, :, bass.ds(g, 1), :].rearrange("p t a d -> p t (a d)")) for br in range(2)]
                for i, (dst, src) in enumerate(k_of + v_of):
                    free(i)
                    pool.tensor_copy(dst, src).then_inc(ns_grp, 1)

            pool.wait_ge(cmp_out, 1)
            keys_and_values(0, lambda i: None)
            with loop(pool, GROUPS - 1) as g:
                def free(i):
                    if i < BRANCHES:
                        n = UNITS - BRANCHES + i
                        pool.wait_ge(ns_s, g * PER_GROUP + (piece(n, len(pieces(i)) - 1) + 1))
                    elif i == BRANCHES:
                        pool.wait_ge(ns_o, g * 4 + 4)
                keys_and_values(g + 1, free)

        def nsa_exps(act, g, n):
            _, _, br = unit(n)
            for k, tiles in enumerate(pieces(br)):
                act.wait_ge(ns_m, g * PER_GROUP + piece(n, k) + 1)
                if br == 0:
                    act.activation(probs[:, n % 2, 0:QT * N_CMP], probs[:, n % 2, 0:QT * N_CMP], ACT.Exp).then_inc(ns_p, 1)
                    return
                for i in tiles:
                    last = act.activation(probs[:, n % 2, PROB_AT[i]:PROB_AT[i] + P * (i + 1)], score_bank(i, br), ACT.Exp,
                                          bias=top[:, n % 2, i:i + 1], accum_out=rsum[:, n % 2, i:i + 1])
                last.then_inc(ns_p, 1)

        def nsa_act(act, g, more):
            def take(n):
                _, _, br = unit(n)
                act.wait_ge(ns_tt, g * UNITS + n + 1)
                if br == 0:
                    act.activation(probs_T[0:N_CMP, n % 2, 0:SEQ], bank[3][0:N_CMP, :], ACT.Copy).then_inc(ns_t, 1)
                    return
                act.activation(probs_T[:, n % 2, 0:SEQ], bank[3][:, :], ACT.Copy)
                act.activation(probs_T[:, n % 2, SEQ:2 * SEQ], bank[4][:, :], ACT.Copy)
                act.activation(probs_T[:, n % 2, 2 * SEQ:CAUSAL], bank[5][:, 0:256], ACT.Copy).then_inc(ns_t, 1)

            for n in range(UNITS):
                if n + 1 < UNITS:
                    nsa_exps(act, g, n + 1)
                elif more:
                    nsa_exps(act, g + 1, 0)
                take(n)

        def nsa_raw_dve(dve, g, u):
            dve.wait_ge(ns_q, g * 4 + (2 * u + 1))
            dve.tensor_scalar(q_raw[:, u, :], bank[7][:, :], HD ** -0.5, None, ALU.mult).then_inc(ns_qe, 1)

        def nsa_rot_dve(dve, g, u):
            dve.wait_ge(ns_qe, g * 4 + (2 * u + 1))
            dve_t.inc(dve.tensor_tensor(rope_a[:, :], q_raw[:, u, :], cos1[:, :], ALU.mult))
            dve.wait_ge(ns_q, g * 4 + (2 * u + 2))
            step(dve, dve.tensor_tensor(rope_b[:, :], bank[7][:, :], sin1[:, :], ALU.mult))
            dve.tensor_tensor(q_rot[:, u, :], rope_a[:, :], rope_b[:, :], ALU.add).then_inc(ns_qe, 1)

        def cmp_probs(n):
            return probs[:, n % 2, 0:QT * N_CMP].rearrange("p (t n) -> p t n", t=QT)

        def nsa_maxima(dve, g, n):
            br, p = n % BRANCHES, cmp_probs(n)
            for k, tiles in enumerate(pieces(br)):
                dve.wait_ge(ns_s, g * PER_GROUP + piece(n, k) + 1)
                if br == 0:
                    s = bank[2][:, 256:384].rearrange("p (t n) -> p t n", t=QT)[:, :, 0:N_CMP]
                    step(dve, dve.tensor_tensor(p, s, cmp_neg[:, :, :], ALU.add))
                    step(dve, dve.reduce_max(top[:, n % 2, :], p, AX.X))
                    dve.tensor_tensor(p, p, top[:, n % 2, :].unsqueeze(2).broadcast_to([P, QT, N_CMP]), ALU.subtract).then_inc(ns_m, 1)
                    return
                for i in tiles:
                    last = dve.reduce_max(top[:, n % 2, i:i + 1], score_bank(i, br), AX.X, negate=True)
                last.then_inc(ns_m, 1)

        def nsa_dve(dve, g, more):
            for n in range(UNITS):
                head, br = n // BRANCHES, n % BRANCHES
                p = cmp_probs(n)
                if n + 1 < UNITS:
                    nsa_maxima(dve, g, n + 1)
                elif more:
                    nsa_maxima(dve, g + 1, 0)
                dve.wait_ge(ns_p, g * PER_GROUP + piece(n, len(pieces(br)) - 1) + 4)
                sums = rsum[:, n % 2, :]
                if br == 0:
                    step(dve, dve.reduce_sum(sums, p, AX.X))
                step(dve, dve.reciprocal(factor[:, n % 2, :], sums))
                gate = gates[:, :, bass.ds(g * 4 + (br * 16 + head), 1)].rearrange("p t a -> p (t a)")
                step(dve, dve.tensor_tensor(factor[:, n % 2, :], factor[:, n % 2, :], gate, ALU.mult))
                if br == 0:
                    step(dve, dve.tensor_tensor(factor[:, n % 2, :], factor[:, n % 2, :], cmp_any[:, :], ALU.mult))
                    dve.tensor_tensor(p, p, factor[:, n % 2, :].unsqueeze(2).broadcast_to([P, QT, N_CMP]), ALU.mult).then_inc(ns_f, 1)
                else:
                    for i in range(QT):
                        rows = probs[:, n % 2, PROB_AT[i]:PROB_AT[i] + P * (i + 1)]
                        last = dve.tensor_scalar(rows, rows, factor[:, n % 2, i:i + 1], None, ALU.mult)
                    last.then_inc(ns_f, 1)
                if br == 0 and head:
                    nsa_out(dve, g, head - 1)
                for tile, units, there in (((g, 1), QUERY_UNITS, True), ((g + 1, 0), NEXT_UNITS, more)):
                    if there and n == units[1]:
                        nsa_raw_dve(dve, *tile)
                    if there and n == units[2]:
                        nsa_rot_dve(dve, *tile)
            nsa_out(dve, g, 3)

        def nsa_out(dve, g, head):
            dve.wait_ge(ns_o, g * 4 + head + 1)
            r = slice(HD * (head % 2), HD * (head % 2) + HD)
            take_o(dve, ns_o_hi, r, g * 2 + head // 2, bank[6], ns_oe)

        def two(b, r=P):
            return psum[0:r, b:b + 2, 0:CH2]

        def halves(ap):
            return ap.rearrange("p (c n) -> p c n", c=2)

        def half(c):
            return slice(c * CH2, (c + 1) * CH2)

        def project2(pe, name, j, turn, made, taken, no, split, hi, later):
            w = split2_wait(pe, name, j, turn, split, hi)
            for c in range(2):
                pe.wait_ge(taken, no + c + 1)
                mm3_T(pe, bank[7][:, 0:CH2], w, x2_hi, x2_lo, c, slot_free if later and c == 0 else None).then_inc(made, 1)
                yield

        def project_v2(pe, name, j, turn, made, taken, no, slots):
            slot = ring.wait(pe, name, j, turn)
            pe.wait_ge(taken, no + 1)
            for t in range(QT):
                last = mm_N(pe, bank[7][:, t * P:(t + 1) * P], slot, t, begun=slot_free if t == 0 else None)
            last.then_inc(made, 1)
            yield
            pe.wait_ge(taken, no + 2)
            mm_N(pe, bank[7][0:META, 0:P], slot, QT, META).then_inc(made, 1)
            pe.wait_ge(made, no + 2)
            pe.sem_inc(slot_free, slots)
            yield

        def take_v2(dve, u, c, taken):
            if c == 0:
                dve.tensor_copy(v2[:, u, 0:QT, :], bank[7][:, :].rearrange("p (t n) -> p t n", n=P)).then_inc(taken, 1)
            else:
                dve.tensor_copy(v2[0:META, u, QT, :], bank[7][0:META, 0:P]).then_inc(taken, 1)

        def transposes2(pe, src):
            for j in range(QT):
                pe.transpose(bank[4][:, j * P:(j + 1) * P], src[:, j * P:(j + 1) * P], ident[:, :])
            return pe.transpose(bank[5][0:META, 0:P], src[:, SEQ:L2], ident[:, :])

        def take_T2(act, n, r):
            act.activation(w_T[:, n % 2, 0:QT, 0:r], bank[4][:, :].rearrange("p (j q) -> p j q", q=P)[:, :, 0:r], ACT.Copy)
            return act.activation(w_T[0:META, n % 2, QT, 0:r], bank[5][0:META, 0:r], ACT.Copy)

        def weigh2(pe, n, t, u):
            r = rows_of(t)
            dst = bank[6][:, t * P:(t + 1) * P] if t < QT else bank[5][:, O_TAIL:O_TAIL + META]
            for j in range(T2):
                k = rows_of(j)
                last = pe.matmul(dst, v2[0:k, u, j, :], w_T[0:k, n % 2, j, 0:r], start=(j == 0), stop=(j == T2 - 1))
            return last

        def df_parts(pe, name, j, turn, hd):
            for n in range(2):
                yield from project2(pe, name, j + n, turn, df_pj, df_pe, hd * 6 + 2 * n, hd * 2 + (SPLIT_BASE["df"] + n), w2_hi[:, n, :], n > 0)
            yield from project_v2(pe, name, j + 2, turn, df_pj, df_pe, hd * 6 + 4, 2)

        def df_scores(pe, hd, u, t):
            r = rows_of(t)
            if t < QT:
                pe.wait_ge(df_p, hd * T2 + t + 1)
            if t == 0:
                pe.wait_ge(df_pe, hd * 6 + 5)
            for m in range(2):
                f = slice(HD * m, HD * m + HD)
                for c in range(2):
                    dst, k = bank[2 * m + c][0:r, 0:CH2], slice(c * CH2, (c + 1) * CH2)
                    last = pe.matmul(dst, q2[f, u, t * P:t * P + r], k2[f, u, k], start=True, stop=(t == QT), skip_group_check=True)
                    if t < QT:
                        last = pe.matmul(dst, slope[:, u, :], dist[:, t, k], start=False, stop=True, skip_group_check=True)
            last.then_inc(df_s, 1)

        def df_pe_head(pe, hd, u, parts):
            more = bool(parts)
            parts = iter(parts)
            for t in range(T2):
                if t < QT - 1:
                    df_scores(pe, hd, u, t + 1)
                if t:
                    df_weigh(pe, hd, u, t - 1)
                if t == QT - 1:
                    df_scores(pe, hd, u, QT)
                if t == 0:
                    pe.wait_ge(df_v, hd + 1)
                next(parts, None)
                pe.wait_ge(df_f, hd * T2 + t + 1)
                pe.wait_ge(df_t, hd * T2 + t + 1)
                if t == 0:
                    pe.wait_ge(df_oe, hd + 1)
                transposes2(pe, prob_a[:, t % 2, :]).then_inc(df_tt, 1)
            if more:
                df_scores(pe, hd + 1, 1 - u, 0)
            df_weigh(pe, hd, u, QT)
            for _ in parts:
                pass
            if more:
                pe.wait_ge(df_pe, hd * 6 + 13)
            pe.wait_ge(df_sq, hd + 1)
            pe.matmul(bank[7][:, :], mean_w[:, :], sq2[:, 0, 0:SEQ], start=True, stop=True)
            pe.matmul(bank[5][:, MS_TAIL:MS_TAIL + META], mean_w[:, :], sq2[:, 0, SEQ:L2], start=True, stop=True).then_inc(df_ms, 1)

        def df_weigh(pe, hd, u, t):
            pe.wait_ge(df_t, hd * T2 + t + 2)
            if t == 0:
                pe.wait_ge(df_pe, hd * 6 + 7)
            last = weigh2(pe, t, t, u)
            if t == QT:
                last.then_inc(df_o, 1)

        def df_exps(act, hd, t):
            r = rows_of(t)
            act.wait_ge(df_m, hd * T2 + t + 1)
            for m, dst in enumerate((prob_a, prob_b)):
                last = act.activation(halves(dst[0:r, t % 2, :]), two(2 * m, r), ACT.Exp, bias=top2[0:r, m:m + 1],
                                      accum_out=rsum2[0:r, m:m + 1])
            last.then_inc(df_p, 1)

        def df_act_head(act, hd, more):
            for t in range(T2):
                if t < QT:
                    df_exps(act, hd, t + 1)
                act.wait_ge(df_tt, hd * T2 + t + 1)
                take_T2(act, t, rows_of(t)).then_inc(df_t, 1)
            if more:
                df_exps(act, hd + 1, 0)
            act.wait_ge(df_o, hd + 1)
            act.activation(sq2[:, 0, 0:SEQ], bank[6][:, :], ACT.Square)
            act.activation(sq2[:, 0, SEQ:L2], bank[5][:, O_TAIL:O_TAIL + META], ACT.Square).then_inc(df_sq, 1)
            act.wait_ge(df_ms, hd + 1)
            act.activation(var2[:, 0, 0:SEQ], bank[7][:, :], ACT.Ln, bias=eps_col[:, :])
            act.activation(var2[:, 0, SEQ:L2], bank[5][:, MS_TAIL:MS_TAIL + META], ACT.Ln, bias=eps_col[:, :]).then_inc(df_v, 1)
            act.wait_ge(df_v, hd + 2)
            act.activation(var2[:, 0, :], var2[:, 0, :], ACT.Exp, scale=-0.5).then_inc(df_sd, 1)

        def df_maxima(dve, hd, t):
            r = rows_of(t)
            dve.wait_ge(df_s, hd * T2 + t + 1)
            dve.reduce_max(top2[0:r, :], psum[0:r, 0:4, 0:CH2].rearrange("p (m c) n -> p m c n", m=2), AX.XY, negate=True).then_inc(df_m, 1)

        def df_dve_head(dve, hd, u, take):
            for t in range(T2):
                r = rows_of(t)
                dve.wait_ge(df_p, hd * T2 + t + 2)
                step(dve, dve.reciprocal(rinv2[0:r, :], rsum2[0:r, :]))
                dve_t.inc(dve.tensor_tensor(rinv2[0:r, 1:2], rinv2[0:r, 1:2], neg_lam[0:r, :], ALU.mult))
                a, b = prob_a[0:r, t % 2, :], prob_b[0:r, t % 2, :]
                step(dve, dve.tensor_scalar(a, a, rinv2[0:r, 0:1], None, ALU.mult))
                dve.scalar_tensor_tensor(a, b, rinv2[0:r, 1:2], a, ALU.mult, ALU.add).then_inc(df_f, 1)
                if t < QT:
                    df_maxima(dve, hd, t + 1)
                if take:
                    df_take(dve, t, hd + 1, 1 - u)
            if take:
                df_maxima(dve, hd + 1, 0)
                df_take(dve, T2, hd + 1, 1 - u)
            step(dve, dve.tensor_scalar(slope[:, u, :], slope[:, u, :], 0.25, None, ALU.mult))
            dve.wait_ge(df_sd, hd + 1)
            o = oT[:, bass.ds(hd, 1), :].rearrange("p a n -> p (a n)")
            dve.scalar_tensor_tensor(o[:, 0:SEQ], bank[6][:, :], head_gain[:, 0:1], var2[:, 0, 0:SEQ], ALU.mult, ALU.mult)
            dve.scalar_tensor_tensor(o[:, SEQ:L2], bank[5][:, O_TAIL:O_TAIL + META], head_gain[:, 0:1], var2[:, 0, SEQ:L2],
                                     ALU.mult, ALU.mult).then_inc(df_oe, 1)

        def ready2_dve(dve):
            dve.wait_ge(b2_T, 1)
            dve.tensor_scalar(head_gain[:, 0:1], bank[7][:, 0:1], 1.0 - LAM_INIT, None, ALU.mult)
            dve.tensor_copy(head_gain[:, 1:3], bank[7][:, 1:3])
            dve.memset(mean_w[:, :], 1.0 / P)
            for u in range(2):
                dve_t.inc(dve.tensor_scalar(slope[:, u, :], ident[:, :], -0.5 ** (u + 1), None, ALU.mult))
            for m in range(2):
                step(dve, dve.tensor_tensor(lam_prod[:, :], lam_in[:, 2 * m, :], lam_in[:, 2 * m + 1, :], ALU.mult))
                last = dve.reduce_sum(lam[:, m:m + 1], lam_prod[:, :], AX.X)
                if m:
                    last.then_inc(lam_d, 1)
                else:
                    step(dve, last)
            dve.wait_ge(lam_e, 1)
            step(dve, dve.tensor_tensor(neg_lam[:, :], lam[:, 1:2], lam[:, 0:1], ALU.subtract))
            dve.tensor_scalar(neg_lam[:, :], neg_lam[:, :], -LAM_INIT, None, ALU.add).then_inc(b2_ready, 1)
            dve.wait_ge(b2_ready, 1)

        def df_take(dve, n, hd, u):
            dve.wait_ge(df_pj, hd * 6 + n + 1)
            if n >= 4:
                take_v2(dve, u, n % 2, df_pe)
            else:
                dve.tensor_scalar((q2, k2)[n // 2][:, u, half(n % 2)], bank[7][:, 0:CH2], 1.0 if n >= 2 else HD ** -0.5, None,
                                  ALU.mult).then_inc(df_pe, 1)

        def branch_pool(pool, b):
            with loop(pool, 2) as turn:
                for j in range(KT):
                    n = turn * KT + (b * BR_SPLITS + j)
                    pool.wait_ge(br_mm, n + 1)
                    split2_pool(pool, f"br{b}", j, turn, turn * KT + (SPLIT_BASE[f"br{b}"] + j), w2_hi[:, j % SPLITS2, :])

        def branch_pe(pe, b):
            with loop(pe, 2) as turn:
                for n in range(4):
                    i = turn * 4 + (b * KT + n)
                    for m, src in enumerate(((x2_hi, x2_lo), (o_hi, oT_lo))):
                        j = 2 * n + m
                        w = split2_wait(pe, f"br{b}", j, turn, turn * KT + (SPLIT_BASE[f"br{b}"] + j), w2_hi[:, j % SPLITS2, :])
                        if m == 0:
                            pe.wait_ge(br_m, i + 1)
                        elif n == 0:
                            pe.wait_ge(br_o, KT * (b + 1))
                        for c in range(2):
                            last = mm3_T(pe, bank[4 * (n % 2) + 2 * m + c][:, 0:CH2], w, *src, c, slot_free if j and c == 0 else None)
                        last.then_inc(br_mm, 1)
                        if j == 7:
                            pe.wait_ge(br_mm, i * 2 + m + 3)
                            pe.sem_inc(slot_free, 1)

        def split_o_act(act, b, done):
            act.wait_ge(done, HEADS2 + 1)
            for k in range(KT):
                act.activation(o_hi[:, k, :], oT[:, k, :], ACT.Copy).then_inc(br_o_hi, 1)

        def split_o_dve(dve, b):
            for k in range(KT):
                dve.wait_ge(br_o_hi, b * KT + k + 1)
                dve.tensor_tensor(oT_lo[:, k, :], oT[:, k, :], o_hi[:, k, :].bitcast(F32), ALU.subtract).then_inc(br_o, 1)

        def branch_act(act, b):
            with loop(act, 2) as turn:
                for n in range(4):
                    i = turn * 4 + (b * KT + n)
                    act.wait_ge(br_mm, i * 2 + 3)
                    act.wait_ge(br_m, i + 1)
                    act.activation(halves(sig[:, n % 2, :]), two(4 * (n % 2)), ACT.Sigmoid).then_inc(br_sig, 1)

        def branch_dve(dve, b, per):
            with loop(dve, 2, tallies=[(dve_t, per)]) as turn:
                for n in range(4):
                    i = turn * 4 + (b * KT + n)
                    dve.wait_ge(br_mm, i * 2 + 4)
                    dve.wait_ge(br_sig, i + 1)
                    m = merged[:, bass.ds(turn * 4 + n, 1), :].rearrange("p a n -> p (a n)")
                    if b == 0:
                        dve.tensor_tensor(halves(m), halves(sig[:, n % 2, :]), two(4 * (n % 2) + 2), ALU.mult).then_inc(br_m, 1)
                    else:
                        gated = sig[:, n % 2, :]
                        step(dve, dve.tensor_tensor(halves(gated), halves(gated), two(4 * (n % 2) + 2), ALU.mult))
                        step(dve, dve.tensor_tensor(m, m, gated, ALU.add))
                        hi = merged_hi[:, bass.ds(turn * 4 + n, 1), :].rearrange("p a n -> p (a n)")
                        step(dve, dve.tensor_copy(hi, m))
                        lo = merged_lo[:, bass.ds(turn * 4 + n, 1), :].rearrange("p a n -> p (a n)")
                        dve.tensor_tensor(lo, m, hi.bitcast(F32), ALU.subtract).then_inc(br_m, 1)

        def piece_no(tile, what, c=0):
            if what == "value":
                return (9, 6)[c]
            k = ("proj", "mean", "rot").index(what)
            return c + (((0, 4, 10), (2, 7, 12))[tile][k] if tile < 2 else 14 + 6 * (tile - 2) + 2 * k)

        def piece_bank(tile, c):
            return bank[2 * tile + c if tile < 2 else 7][:, 0:CH2]

        def x_no(tile, k):
            return 2 * (k - 1) + tile + 1 if tile < 2 else 6 + 3 * (tile - 2) + k

        XS = 3 * (Q_PER_KV + 1)
        UN = Q_PER_KV * T2

        def gq_pool(pool):
            for kv in range(KV2):
                for tile in range(GQ_SPLITS):
                    if kv == 0 and tile < SPLITS2:
                        pool.wait_ge(br_mm, BR_SPLITS - SPLITS2 + tile + 3)
                    before = (kv, tile - SPLITS2) if tile >= SPLITS2 else (kv - 1, (4, 3)[tile])
                    if before[0] >= 0:
                        pool.wait_ge(gq_b, before[0] * USES + piece_no(before[1], "proj", 1) + 1)
                    split2_pool(pool, "gqa", tile + (tile > 1), kv, SPLIT_BASE["gqa"] + kv * GQ_SPLITS + tile, w2_hi[:, tile % SPLITS2, :])
            pool.wait_ge(gq_b, KV2 * USES)

        def gq_pe_turn(pe, kv):
            def taken(no):
                pe.wait_ge(gq_br, kv * USES + no + 2)

            def project(tile, halves):
                w = split2_wait(pe, "gqa", tile + (tile > 1), kv, kv * GQ_SPLITS + (SPLIT_BASE["gqa"] + tile), w2_hi[:, tile % SPLITS2, :])
                no = piece_no(tile, "proj")
                for c in halves:
                    if tile >= 2:
                        taken(no + c - 1)
                    elif c == 0:
                        pe.wait_ge(gq_p, kv * UN + 2)
                    mm3_T(pe, piece_bank(tile, c), w, x2_hi, x2_lo, c).then_inc(gq_b, 1)

            def projected(tile):
                pe.wait_ge(gq_b, kv * USES + piece_no(tile, "proj", 1) + 1)
                pe.sem_inc(slot_free, 1)

            def small(tile, what, weight, src):
                pe.wait_ge(gq_x, kv * XS + x_no(tile, 1 if what == "mean" else 2))
                for c in range(2):
                    no = piece_no(tile, what, c)
                    taken(piece_no(tile, "proj" if what == "mean" else "mean", c) if tile < 2 else no - 1)
                    pe.matmul(piece_bank(tile, c), weight[:, :], src[:, tile % 2, half(c)], start=True, stop=True).then_inc(gq_b, 1)

            def mean(tile):
                projected(tile)
                small(tile, "mean", mean_w, sq2)

            def rotate(tile):
                small(tile, "rot", rot2, norm2)

            def values(c):
                slot = ring.wait(pe, "gqa", 2, kv)
                if c:
                    pe.wait_ge(gq_br, kv * USES + 1)
                    mm_N(pe, bank[7][0:META, 0:P], slot, QT, META).then_inc(gq_b, 1)
                else:
                    taken(piece_no(0, "value", 1))
                    for t in range(QT):
                        last = mm_N(pe, bank[7][:, t * P:(t + 1) * P], slot, t)
                    last.then_inc(gq_b, 1)

            def valued():
                pe.wait_ge(gq_b, kv * USES + piece_no(0, "value", 0) + 1)
                pe.sem_inc(slot_free, 1)

            def scores(n):
                j, t = n // T2, n % T2
                r = rows_of(t)
                pe.wait_ge(gq_p, kv * UN + n + 1)
                if t == 0:
                    pe.wait_ge(gq_x, kv * XS + x_no(j + 1, 3))
                for c in range(2):
                    last = pe.matmul(bank[2 * (n % 2) + c][0:r, 0:CH2], q2[:, j % 2, t * P:t * P + r], k2[:, 0, c * CH2:(c + 1) * CH2],
                                     start=True, stop=True)
                last.then_inc(gq_s, 1)

            def weigh(n):
                j, t = n // T2, n % T2
                pe.wait_ge(gq_t, kv * UN + n + 2)
                if t == 0:
                    pe.wait_ge(gq_oe, kv * Q_PER_KV + j + 1)
                last = weigh2(pe, n, t, 0)
                if t == QT:
                    last.then_inc(gq_o, 1)

            project(0, range(2))
            project(1, range(2))
            pe.wait_ge(br_m, KT + 2)
            mean(0)
            values(1)
            mean(1)
            values(0)
            rotate(0)
            valued()
            rotate(1)
            scores(0)
            scores(1)
            project(2, range(2))
            for n in range(UN):
                j, t = n // T2, n % T2
                if n and t == 0:
                    weigh(n - 1)
                if t == 0 and j + 2 <= Q_PER_KV:
                    mean(j + 2)
                elif t == 4 and j + 3 <= Q_PER_KV:
                    project(j + 3, (1,))
                pe.wait_ge(gq_f, kv * UN + n + 1)
                pe.wait_ge(gq_t, kv * UN + n + 1)
                if t == 0:
                    pe.wait_ge(gq_oe, kv * Q_PER_KV + j + 1)
                transposes2(pe, prob_a[:, n % 2, :]).then_inc(gq_tt, 1)
                if t == 3 and j + 3 <= Q_PER_KV:
                    project(j + 3, (0,))
                if n + 2 < UN:
                    scores(n + 2)
                if t:
                    weigh(n - 1)
                if t == 2 and j + 2 <= Q_PER_KV:
                    rotate(j + 2)
            weigh(UN - 1)
            pe.sem_inc(slot_free, 2)

        def gq_act_turn(act, kv):
            def root(tile):
                act.wait_ge(gq_br, kv * USES + piece_no(tile, "mean", 1) + 2)
                var = var2[:, tile % 2, :]
                act_t.inc(act.activation(var, var, ACT.Ln))
                act.wait_ge(act_step, act_t.value())
                act.activation(var, var, ACT.Exp, scale=-0.5).then_inc(gq_sd, 1)

            def exps(n):
                r = rows_of(n % T2)
                act.wait_ge(gq_m, kv * UN + n + 1)
                act.activation(halves(prob_a[0:r, n % 2, :]), two(2 * (n % 2), r), ACT.Exp, bias=top2[0:r, n % 2:n % 2 + 1],
                               scale=P ** -0.5, accum_out=rsum2[0:r, n % 2:n % 2 + 1]).then_inc(gq_p, 1)

            root(0)
            root(1)
            exps(0)
            exps(1)
            for n in range(UN):
                j, t = n // T2, n % T2
                act.wait_ge(gq_tt, kv * UN + n + 1)
                take_T2(act, n, rows_of(t)).then_inc(gq_t, 1)
                if n + 2 < UN:
                    exps(n + 2)
                if t == 0 and j + 2 <= Q_PER_KV:
                    root(j + 2)

        def gq_dve_turn(dve, kv):
            def piece(tile, what, c):
                dve.wait_ge(gq_b, kv * USES + piece_no(tile, what, c) + 1)

            def square(tile, c):
                piece(tile, "proj", c)
                raw = raw2[:, tile % 2, :]
                dve.tensor_copy(raw[:, half(c)], piece_bank(tile, c)).then_inc(gq_br, 1)
                if c:
                    dve.wait_ge(gq_br, kv * USES + piece_no(tile, "proj", 1) + 2)
                    dve.tensor_tensor(sq2[:, tile % 2, :], raw, raw, ALU.mult).then_inc(gq_x, 1)

            def variance(tile, c):
                piece(tile, "mean", c)
                dve.tensor_scalar(var2[:, tile % 2, half(c)], piece_bank(tile, c), EPS2, None, ALU.add).then_inc(gq_br, 1)

            def normalise(tile):
                dve.wait_ge(gq_sd, kv * (Q_PER_KV + 1) + tile + 1)
                g = 2 if tile == 0 else 1
                raw, norm = raw2[:, tile % 2, :], norm2[:, tile % 2, :]
                dve.scalar_tensor_tensor(norm, raw, head_gain[:, g:g + 1], var2[:, tile % 2, :], ALU.mult, ALU.mult).then_inc(gq_x, 1)
                dve.wait_ge(gq_x, kv * XS + x_no(tile, 2))
                dve_t.inc(dve.tensor_tensor(raw, norm, cos2[:, :], ALU.mult))

            def rotated(tile, c):
                piece(tile, "rot", c)
                dve.tensor_tensor(rope_c[:, half(c)], piece_bank(tile, c), sin2[:, half(c)], ALU.mult).then_inc(gq_br, 1)
                dve.wait_ge(gq_br, kv * USES + piece_no(tile, "rot", c) + 2)
                dve.wait_ge(dve_step, dve_t.value())
                dst = k2[:, 0, half(c)] if tile == 0 else q2[:, (tile - 1) % 2, half(c)]
                last = dve.tensor_tensor(dst, raw2[:, tile % 2, half(c)], rope_c[:, half(c)], ALU.add)
                if c:
                    last.then_inc(gq_x, 1)
                    dve.wait_ge(gq_x, kv * XS + x_no(tile, 3))

            def values(c):
                piece(0, "value", c)
                take_v2(dve, 0, c, gq_br)

            for stage, tile in ((square, 0), (square, 1), (variance, 0)):
                for c in range(2):
                    stage(tile, c)
            normalise(0)
            values(1)
            for c in range(2):
                variance(1, c)
            normalise(1)
            values(0)
            for tile in range(2):
                for c in range(2):
                    rotated(tile, c)

            def maxima(n):
                r, c = rows_of(n % T2), n % 2
                dve.wait_ge(gq_s, kv * UN + n + 1)
                step(dve, dve.reduce_max(top2[0:r, c:c + 1], two(2 * c, r), AX.XY))
                dve.tensor_scalar(top2[0:r, c:c + 1], top2[0:r, c:c + 1], -P ** -0.5, None, ALU.mult).then_inc(gq_m, 1)

            maxima(0)
            maxima(1)
            for c in range(2):
                square(2, c)
            def weights(n):
                r, c = rows_of(n % T2), n % 2
                dve.wait_ge(gq_p, kv * UN + n + 3)
                step(dve, dve.reciprocal(rinv2[0:r, c:c + 1], rsum2[0:r, c:c + 1]))
                a = prob_a[0:r, c, :]
                dve.tensor_scalar(a, a, rinv2[0:r, c:c + 1], None, ALU.mult).then_inc(gq_f, 1)

            weights(0)
            for n in range(UN):
                j, t = n // T2, n % T2
                if t == 0 and j:
                    gq_out(dve, kv, j - 1)
                more = j + 2 <= Q_PER_KV
                if t == 0 and more:
                    variance(j + 2, 0)
                elif t >= 3 and j + 3 <= Q_PER_KV:
                    square(j + 3, t - 3)
                if n + 1 < UN:
                    weights(n + 1)
                if n + 2 < UN:
                    maxima(n + 2)
                if t == 0 and more:
                    variance(j + 2, 1)
                if t == 2 and more:
                    for c in range(2):
                        rotated(j + 2, c)
                if t == 1 and j + 2 <= Q_PER_KV:
                    normalise(j + 2)
            gq_out(dve, kv, Q_PER_KV - 1)

        def gq_out(dve, kv, j):
            dve.wait_ge(gq_o, kv * Q_PER_KV + j + 1)
            o = oT[:, bass.ds(kv * Q_PER_KV + j, 1), :].rearrange("p a n -> p (a n)")
            dve.tensor_copy(o[:, 0:SEQ], bank[6][:, :])
            dve.tensor_copy(o[:, SEQ:L2], bank[5][:, O_TAIL:O_TAIL + META]).then_inc(gq_oe, 1)

        def logits_pe(pe, t):
            r = rows_of(t)
            if t == 0:
                pe.wait_ge(moe_in, MOE_CONST)
            for k in range(KT):
                last = pe.matmul(bank[5][0:r, t * EXPERTS:(t + 1) * EXPERTS], xT[:, k, t * P:t * P + r], router_w[:, k, :],
                                 start=(k == 0), stop=(k == KT - 1))
            if t == QT:
                last.then_inc(rt_l, 1)

        def route_pe(pe):
            pe.wait_ge(rt_a, 1)
            for t in range(T2):
                r = rows_of(t)
                dst = bank[1][0:EXPERTS, t * P:(t + 1) * P] if t < QT else bank[2][0:EXPERTS, 0:META]
                last = pe.transpose(dst, logits[0:r, t, :], ident[0:r, 0:r])
            last.then_inc(rt_at, 1)
            pe.wait_ge(rt_s, 1)
            for t in range(T2):
                r = rows_of(t)
                at = META + t * P if t < QT else 0
                last = pe.transpose(bank[3][0:r, t * EXPERTS:(t + 1) * EXPERTS], work[:, at:at + r], ident[0:EXPERTS, 0:EXPERTS])
            last.then_inc(rt_st, 1)
            for e in range(EXPERTS):
                pe.wait_ge(rt_oh, e + 1)
                for t in range(T2):
                    r = rows_of(t)
                    last = pe.matmul(bank[4 if e < EARLY else 6][0:CAP, PICKS * e:PICKS * (e + 1)], one_hot[0:r, e % 4, t, :], token_aff[0:r, t, e, :],
                                     start=(t == 0), stop=(t == QT))
                last.then_inc(rt_pk, 1)

        def route_act(act):
            act.wait_ge(rt_x, 1)
            act.activation(logits[:, :, :], logits[:, :, :], ACT.Exp).then_inc(rt_e, 1)

        def route_dve(dve):
            dve.wait_ge(moe_in, MOE_CONST)
            dve_t.inc(dve.memset(logits[:, :, :], 0.0))
            dve_t.inc(dve.memset(slot_T[:, :, :], -1.0))
            dve_t.inc(dve.memset(ones_row[:, :], 1.0))
            for i in range(2):
                step(dve, dve.tensor_copy(token_aff[:, :, :, i], token_no[:, i, :].unsqueeze(2).broadcast_to([P, T2, EXPERTS])))
            dve.wait_ge(rt_l, 1)
            dve_t.inc(dve.tensor_copy(logits[:, 0:QT, :], bank[5][:, 0:QT * EXPERTS].rearrange("p (t n) -> p t n", n=EXPERTS)))
            step(dve, dve.tensor_copy(logits[0:META, QT, :], bank[5][0:META, QT * EXPERTS:T2 * EXPERTS]))

            def wide(ap):
                return ap.unsqueeze(2).broadcast_to([P, T2, EXPERTS])

            step(dve, dve.reduce_max(lmax[:, :], logits[:, :, :], AX.X))
            dve.tensor_tensor(logits[:, :, :], logits[:, :, :], wide(lmax[:, :]), ALU.subtract).then_inc(rt_x, 1)
            dve.wait_ge(rt_e, 1)
            step(dve, dve.reduce_sum(lmax[:, :], logits[:, :, :], AX.X))
            step(dve, dve.reciprocal(lmax[:, :], lmax[:, :]))
            dve.tensor_tensor(logits[:, :, :], logits[:, :, :], wide(lmax[:, :]), ALU.mult).then_inc(rt_a, 1)
            dve.wait_ge(rt_a, 1)
            rest = logits[:, :, :]
            for i in range(2, PICKS):
                step(dve, dve.tensor_copy(token_aff[:, :, :, i], rest))
                if i < PICKS - 1:
                    step(dve, dve.tensor_tensor(aff_rest[:, :, :], rest, token_aff[:, :, :, i], ALU.subtract))
                    rest = aff_rest[:, :, :]
            dve.wait_ge(rt_at, 1)
            dve_t.inc(dve.tensor_copy(aff_T[:, META:L2], bank[1][0:EXPERTS, :]))
            step(dve, dve.tensor_copy(aff_T[:, 0:META], bank[2][0:EXPERTS, 0:META]))
            src = aff_T
            for k in range((CAP - 1) // 8 + 1):
                step(dve, dve.max(best8[:, :], src[:, :]))
                if k < (CAP - 1) // 8:
                    step(dve, dve.match_replace(work[:, :], best8[:, :], src[:, :], -1.0))
                    src = work
            least = best8[:, (CAP - 1) % 8:(CAP - 1) % 8 + 1]
            step(dve, dve.tensor_scalar(above[:, :], aff_T[:, :], least, None, ALU.is_gt))
            dve_t.inc(dve.reduce_sum(n_above[:, 0:1], above[:, :], AX.X))
            step(dve, dve.tensor_scalar(equal[:, :], aff_T[:, :], least, None, ALU.is_equal))
            dve_t.inc(dve.tensor_scalar(n_above[:, 1:2], n_above[:, 0:1], -1.0, float(CAP), ALU.mult, ALU.add))
            step(dve, dve.tensor_tensor_scan(count[:, :], ones_row[:, :], equal[:, :], 0.0, ALU.mult, ALU.add))
            step(dve, dve.scalar_tensor_tensor(equal[:, :], count[:, :], n_above[:, 1:2], equal[:, :], ALU.is_le, ALU.mult))
            step(dve, dve.tensor_tensor(above[:, :], above[:, :], equal[:, :], ALU.add))
            step(dve, dve.tensor_tensor_scan(count[:, :], ones_row[:, :], above[:, :], 0.0, ALU.mult, ALU.add))
            step(dve, dve.tensor_tensor(work[:, :], count[:, :], above[:, :], ALU.mult))
            dve.tensor_scalar(work[:, :], work[:, :], -1.0, None, ALU.add).then_inc(rt_s, 1)
            dve.wait_ge(rt_st, 1)
            dve_t.inc(dve.tensor_copy(slot_T[:, 0:QT, :], bank[3][:, 0:QT * EXPERTS].rearrange("p (t n) -> p t n", n=EXPERTS)))
            step(dve, dve.tensor_copy(slot_T[0:META, QT, :], bank[3][0:META, QT * EXPERTS:T2 * EXPERTS]))

            def picked(src, e0, e1):
                dve.wait_ge(rt_pk, e1)
                p = pick[:, e0:e1, :]
                step(dve, dve.tensor_copy(p.rearrange("p e c -> p (e c)"), src[0:CAP, PICKS * e0:PICKS * e1]))
                step(dve, dve.scalar_tensor_tensor(p[:, :, 0], p[:, :, 0], float(P), p[:, :, 1], ALU.mult, ALU.add))
                dve.tensor_copy(pick_no[:, e0:e1], p[:, :, 0]).then_inc(ex_no, 1)

            for e in range(EXPERTS):
                if e >= 4:
                    dve.wait_ge(rt_pk, e - 3)
                dve.tensor_tensor(one_hot[:, e % 4, :, :], slot_no[:, :].unsqueeze(1).broadcast_to([P, T2, CAP]),
                                  slot_T[:, :, e:e + 1].broadcast_to([P, T2, CAP]), ALU.is_equal).then_inc(rt_oh, 1)
                if e == EARLY + 1:
                    picked(bank[4], 0, EARLY)
            picked(bank[6], EARLY, EXPERTS)
            for i in range(3, PICKS):
                step(dve, dve.tensor_tensor(pick[:, :, 2], pick[:, :, 2], pick[:, :, i], ALU.add))

        def tokens_act(act):
            act.wait_ge(norm_sd, 8 - SHARED)
            for t in range(T2):
                r = rows_of(t)
                act.activation(u_rows[0:r, t, :], h[0:r, t, :], ACT.Copy, scale=rstd[0:r, t:t + 1]).then_inc(u_scaled, 1)

        def tokens_pool(pool):
            pool.wait_ge(gain_in, 32)
            for t in range(T2):
                r = rows_of(t)
                pool.wait_ge(u_scaled, t + 1)
                pool.tensor_tensor(u_rows[0:r, t, :], u_rows[0:r, t, :], gain_bc[0:r, :], ALU.mult).then_inc(u_row, 1)
                pool.wait_ge(u_row, t + 1)
                pool.dma_start(u_dram[t * P:t * P + r, :], u_rows[0:r, t, :]).then_inc(u_out, 16)

        def ex_tokens_pe(pe, i, u):
            e = i * 2 + u
            pe.wait_ge(ex_x[u], i * 16 + 16)
            pe.wait_ge(ex_xe, e + 1)
            for k in range(KT):
                last = pe.transpose(bank[k // 4][:, (k % 4) * CAP:(k % 4 + 1) * CAP], xs[:, u, k * P:(k + 1) * P], ident[0:CAP, 0:CAP])
            last.then_inc(ex_xt, 1)

        def ex_gate_up_pe(pe, name, j, turn, i, u, m):
            e = i * 2 + u
            if m == 0:
                pe.wait_ge(ex_xe, e + 2)
                pe.wait_ge(ex_h, e + 1)
            for k in range(KT):
                n = m * (KT // 2) + k // 2
                if k % 2 == 0:
                    pe.wait_ge(ex_ws, e * KT + (n + 1))
                    hi, lo = (w.rearrange("p (k n) -> p k n", n=512)
                              for w in (ex_w_hi[:, n, :], ring_lo[:, ring.plan[name][j + n][0], :]))
                dst = bank[2 + m][0:CAP, :]
                first = pe.matmul(dst, xs_hi[:, u, k, :], lo[:, k % 2, :], start=(k == 0), stop=False)
                if m == 1 and k == 0:
                    first.then_inc(ex_gate, 1)
                elif k == 0 and name != "ex_first":
                    first.then_inc(slot_free, 1)
                pe.matmul(dst, xs_lo[:, u, k, :], hi[:, k % 2, :], start=False, stop=False)
                last = pe.matmul(dst, xs_hi[:, u, k, :], hi[:, k % 2, :], start=False, stop=(k == KT - 1))
                if k % 2 and not (m == 1 and k == KT - 1):
                    last.then_inc(slot_free, 1)
            if m == 1:
                last.then_inc(ex_gu, 1)

        def ex_split_act(act, name, j, turn, i, u, m):
            e = i * 2 + u
            if name != "ex_first":
                act.wait_ge(ex_gate if m == 0 else ex_gu, e)
            for n in range(m * (KT // 2), (m + 1) * (KT // 2)):
                act.activation(ex_w_hi[:, n, :], ring.wait(act, name, j + n, turn), ACT.Copy).then_inc(ex_wh, 1)

        def ex_split_dve(dve, name, j, turn, i, u, m, tiles=None):
            for n in range(m * (KT // 2), (m + 1) * (KT // 2)) if tiles is None else tiles:
                slot = ring.plan[name][j + n][0]
                dve.wait_ge(ex_wh, i * (2 * KT) + (u * KT + n + 1))
                dve.tensor_tensor(ring_lo[:, slot, :], ring_tile[:, slot, :], ex_w_hi[:, n, :].bitcast(F32), ALU.subtract).then_inc(ex_ws, 1)

        def ex_hidden_pe(pe, i, u):
            e = i * 2 + u
            pe.wait_ge(ex_h, e + 2)
            pe.wait_ge(ex_he, e + 1)
            for k in range(FT):
                last = pe.transpose(bank[4][:, k * CAP:(k + 1) * CAP], act_hid[:, u, k * P:(k + 1) * P], ident[0:CAP, 0:CAP])
            last.then_inc(ex_ht, 1)

        def ex_down_pe(pe, name, j, turn, i, u, after_up=True):
            e = i * 2 + u
            pe.wait_ge(ex_he, e + 2)
            pe.wait_ge(ex_ye, e + 1)
            for k in range(FT):
                w = ring.wait(pe, name, j + k, turn)
                for n in range(2):
                    last = pe.matmul(bank[5 + n][0:CAP, :], hid_T[:, u, k, :], w[:, 512 * n:512 * n + 512], start=(k == 0), stop=(k == FT - 1))
                    if k == 0 and n == 0 and after_up:
                        last.then_inc(slot_free, 1)
                if k < FT - 1:
                    last.then_inc(slot_free, 1)
            last.then_inc(ex_y, 1)

        def ex_tokens_act(act, i, u):
            act.wait_ge(ex_xt, i * 2 + (u + 3))
            for c in range(2):
                act.activation(xs_hi[:, u, 4 * c:4 * c + 4, :], bank[c][:, 0:4 * CAP].rearrange("p (k n) -> p k n", n=CAP), ACT.Copy).then_inc(ex_xh, 1)

        def ex_tokens_dve(dve, i, u):
            for c in range(2):
                dve.wait_ge(ex_xh, i * 4 + (2 * u + c + 1))
                k = slice(4 * c, 4 * c + 4)
                last = dve.tensor_tensor(xs_lo[:, u, k, :], bank[c][:, 0:4 * CAP].rearrange("p (k n) -> p k n", n=CAP),
                                         xs_hi[:, u, k, :].bitcast(F32), ALU.subtract)
            last.then_inc(ex_xe, 1)

        def ex_act(act, i, u):
            e = i * 2 + u
            act.wait_ge(ex_gu, e + 1)
            act.wait_ge(ex_h, e + 1)
            act.activation(act_sig[:, :], bank[2][0:CAP, :], ACT.Sigmoid).then_inc(ex_sg, 1)

        def ex_hid_dve(dve, i, u):
            e = i * 2 + u
            dve.wait_ge(ex_sg, e + 1)
            step(dve, dve.tensor_tensor(act_hid[:, u, :], act_sig[:, :], bank[2][0:CAP, :], ALU.mult))
            dve.tensor_tensor(act_hid[:, u, :], act_hid[:, u, :], bank[3][0:CAP, :], ALU.mult).then_inc(ex_h, 1)

        def ex_hidden_dve(dve, i, u):
            e = i * 2 + u
            dve.wait_ge(ex_ht, e + 1)
            dve.tensor_copy(hid_T[:, u, :, :], bank[4][:, 0:FT * CAP].rearrange("p (k n) -> p k n", n=CAP)).then_inc(ex_he, 1)

        def ex_out_dve(dve, i, u):
            e = i * 2 + u
            dve.wait_ge(ex_done, e + 1)
            step(dve, dve.tensor_copy(aff_now[:, u, :], pick[:, bass.ds(e, 1), 2]))
            dve.wait_ge(ex_y, e + 1)
            for n in range(2):
                last = dve.tensor_scalar(ys[:, u, 512 * n:512 * n + 512], bank[5 + n][0:CAP, :], aff_now[:, u, :], None, ALU.mult)
            last.then_inc(ex_ye, 1)

        def ex_put(pool, i, u):
            e = i * 2 + u
            pool.wait_ge(ex_ye, e + 2)
            pool.tensor_copy(no_put[:, u, :], pick_no[:, bass.ds(e, 1)])
            pool.drain()
            pool.indirect_dma_start(y_dram[:, :], bass.IndirectOffsetOnAxis(ap=no_put[:, u, :], axis=0), ys[:, u, :], None,
                                    compute_op=ALU.add).then_inc(ex_out, 16)

        def ex_put_next(pool, i, u):
            pool.wait_ge(ex_out, i * 32 + u * 16)
            pool.sem_inc(ex_done, 1)
            ex_put(pool, i, u)

        def ex_get(pool, i, u):
            e = i * 2 + u
            pool.wait_ge(ex_xt, e + 1)
            pool.tensor_copy(no_get[:, u, :], pick_no[:, bass.ds(e, 1)])
            pool.drain()
            pool.indirect_dma_start(xs[:, u, :], None, u_dram[:, :], bass.IndirectOffsetOnAxis(ap=no_get[:, u, :], axis=0)).then_inc(ex_x[u], 16)

        def mm_T(pe, dst, slot, src, k0=0, k1=KT, begun=None):
            w = slot.rearrange("p (k n) -> p k n", n=P)
            for k in range(k0, k1):
                last = pe.matmul(dst, w[:, k, :], src[:, k, :], start=(k == 0), stop=(k == KT - 1))
                if k == k0 and begun is not None:
                    last.then_inc(begun, 1)
            return last

        def mm_N(pe, dst, slot, t, r=P, begun=None):
            w = slot.rearrange("p (k n) -> p k n", n=P)
            for k in range(KT):
                last = pe.matmul(dst, xT[:, k, t * P:t * P + r], w[:, k, :], start=(k == 0), stop=(k == KT - 1))
                if k == 0 and begun is not None:
                    last.then_inc(begun, 1)
            return last

        def sb_project(pe, name, j, turn, p):
            for n, b in ((0, 5), (1, 6)):
                for half in range(2):
                    if half == 0:
                        w = split2_wait(pe, name, j + n, turn, p * 2 + (SPLIT_BASE["sb"] + n), w_hi[:, n, :])
                        pe.wait_ge(sb_pe, p * 3 + n + 1)
                    last = mm3_K(pe, bank[b][:, :], w, x_hi, x_lo, half * 4, half * 4 + 4, slot_free if n and half == 0 else None)
                    if half:
                        last.then_inc(sb_pj, 1)
                    yield
            slot = ring.wait(pe, name, j + 2, turn)
            pe.wait_ge(sb_pe, p * 3 + 3)
            for half in range(2):
                for t in (2 * half, 2 * half + 1):
                    last = mm_N(pe, bank[7][:, t * P:(t + 1) * P], slot, t, begun=slot_free if t == 0 else None)
                if half:
                    last.then_inc(sb_pj, 1)
                    pe.wait_ge(sb_pj, p * 3 + 3)
                    pe.sem_inc(slot_free, 2)
                yield

        def sb_pair_pe(pe, p, u, project):
            parts = iter(project)

            def fill(n):
                for _ in range(n):
                    next(parts, None)

            pe.wait_ge(sb_pe, p * 3 + 6)
            for hh in range(2):
                hd = p * 2 + hh
                r = slice(HD * hh, HD * hh + HD)
                for i in range(QT):
                    pe.matmul(bank[i][:, 0:CAUSAL_COLS[i]], kT[r, u, i * P:(i + 1) * P], qT[r, u, i * P:SEQ],
                              start=True, stop=True).then_inc(sb_z, 1)
                fill(2)
                pe.wait_ge(sb_sp, hd + 1)
                for i in range(QT):
                    n = CAUSAL_COLS[i]
                    for j in range(i, QT):
                        pe.matmul(bank[i][:, n - CAUSAL_COLS[j]:n], (tri_neg if j == i else ones_neg)[:, :],
                                  softp[:, CAUSAL_AT[j]:CAUSAL_AT[j] + CAUSAL_COLS[j]], start=False, stop=False,
                                  skip_group_check=True)
                    pe.matmul(bank[i][:, 0:P], ident_bf[:, :], past_neg_bf[:, :], start=False, stop=True,
                              skip_group_check=True).then_inc(sb_zi, 1)
                fill(1)
                pe.wait_ge(sb_oe, hd + 1)
                for i in range(QT):
                    pe.wait_ge(sb_a, hd * QT + i + 1)
                    last = pe.matmul(bank[4][0:HD, i * P:SEQ], vN[:, u, i, r], stick[:, CAUSAL_AT[i]:CAUSAL_AT[i] + CAUSAL_COLS[i]],
                                     start=(i == 0), stop=(i == QT - 1))
                last.then_inc(sb_o, 1)
            fill(6)

        def w_out_pe(pe):
            def again(n, t):
                if n == 0 and t in (0, QT):
                    pe.wait_ge(br_m, 2 * KT + 1 + t // QT)
                i = n * T2 + t
                if i >= 8:
                    pe.wait_ge(h_upd, H_X2 + i - 7)
            output_pe(pe, "w_out", merged_hi, merged_lo, w2_hi, T2, lambda n, t: (n * T2 + t) % 8, H_ALL, again)

        def mm3(pe, dst, a_hi, a_lo, b_hi, b_lo, first, final, begun=None):
            upper = pe.matmul(dst, a_hi, b_hi, start=first, stop=False)
            if begun is not None:
                upper.then_inc(begun, 1)
            pe.matmul(dst, a_hi, b_lo, start=False, stop=False)
            return pe.matmul(dst, a_lo, b_hi, start=False, stop=final)

        FF_SLOTS = 2 * FF_TILES

        def ff_pe(pe, m, upd):
            def weights(f, j, width):
                pe.wait_ge(split_w, f * FF_SLOTS + (m * FF_PARTS * FF_SLOTS + j + 1))
                return [w[:, j % SPLITS, :].rearrange("p (k n) -> p k n", n=width) for w in (w_hi, w_lo)]

            pe.wait_ge(split_x, split_base(FF_NORMS[m]) + 2 * QT)
            with loop(pe, FF_PARTS) as f:
                for j in range(FF_TILES):
                    n = f * FF_TILES + (m * FF_PARTS * FF_TILES + j)
                    hi, lo = weights(f, j, P)
                    pe.wait_ge(ff_relu, n + 1)
                    if j < QT:
                        pe.wait_ge(h_upd, f * UPD + (upd - UPD + QT + j + 1))
                    for k in range(KT):
                        last = mm3(pe, bank[j % 4][:, :], hi[:, k, :], lo[:, k, :], x_hi[:, k, :], x_lo[:, k, :], k == 0, k == KT - 1)
                    last.then_inc(ff_mm, 1)
                for n in range(2):
                    for k in range(FF_TILES):
                        if k % 2 == 0:
                            hi, lo = weights(f, FF_TILES + n * (FF_TILES // 2) + k // 2, 512)
                        if n == 0:
                            pe.wait_ge(ff_hid, f * FF_TILES + (m * FF_PARTS * FF_TILES + k + 3))
                        for t in range(QT):
                            rows = slice(t * P, (t + 1) * P)
                            last = mm3(pe, bank[4 * (1 - n) + t][:, :], hid_hi[:, k, rows], hid_lo[:, k, rows],
                                       hi[:, k % 2, :], lo[:, k % 2, :], k == 0, k == FF_TILES - 1)
                            if k == FF_TILES - 1:
                                last.then_inc(acc_done, 1)
                        if k % 2 and k < FF_TILES - 1:
                            last.then_inc(ff_w2, 1)

        def ff_pool(pool, m, upd):
            w2_frees = FF_TILES // 2 - 1
            with loop(pool, FF_PARTS) as f:
                for j in range(FF_SLOTS):
                    n = f * FF_SLOTS + (m * FF_PARTS * FF_SLOTS + j)
                    was = (j - SPLITS) % FF_SLOTS
                    half, k = (was - FF_TILES) // (FF_TILES // 2), (was - FF_TILES) % (FF_TILES // 2)
                    part = 0 if j < SPLITS else 1
                    if was < FF_TILES:
                        pool.wait_ge(ff_mm, f * FF_TILES + (m * FF_PARTS * FF_TILES + was + 1))
                    elif k < w2_frees:
                        pool.wait_ge(ff_w2, f * (2 * w2_frees) + ((m * FF_PARTS + part) * 2 * w2_frees + half * w2_frees + k + 1))
                    else:
                        pool.wait_ge(acc_done, f * UPD + (upd + (part - 1) * UPD + (half + 1) * QT))
                    raw = ring.wait(pool, f"ff{m}", j, f)
                    hi, lo = w_hi[:, j % SPLITS, :], w_lo[:, j % SPLITS, :]
                    pool.tensor_tensor(hi, raw, one[:, :].broadcast_to([P, D]), ALU.mult).then_inc(split_w_hi, 1)
                    pool.wait_ge(split_w_hi, n + 1)
                    pool.tensor_tensor(lo, raw, hi.bitcast(F32), ALU.subtract).then_inc(split_w, 1)
                    pool.wait_ge(split_w, n + 1)
                    pool.sem_inc(slot_free, 1)

        @block.tensor
        def _(pe):
            pe.sem_inc(slot_free, RING)
            pe.sem_inc(ex_xt, 2)
            pe.sem_inc(br_mm, 2)
            pe.wait_ge(const_in, ALL_CONST)
            pe.transpose(bank[0][:, 0:7 * KT], gain_rows[:, :], ident[0:7 * KT, 0:7 * KT]).then_inc(gains_T, 1)
            pe.wait_ge(gains_in, 1)
            norm_pe(pe, 0)
            pe.wait_ge(split_x, split_base(1))
            for _ in sb_project(pe, "sb_first", 0, 0, 0):
                pass
            with loop(pe, PAIRS // 2 - 1) as turn:
                sb_pair_pe(pe, turn * 2, 0, sb_project(pe, "sb_loop", 0, turn, turn * 2 + 1))
                sb_pair_pe(pe, turn * 2 + 1, 1, sb_project(pe, "sb_loop", 4, turn, turn * 2 + 2))
            sb_pair_pe(pe, PAIRS - 2, 0, sb_project(pe, "sb_last", 0, 0, PAIRS - 1))
            sb_pair_pe(pe, PAIRS - 1, 1, sb_out_early(pe))
            sb_out_pe(pe)
            norm_pe(pe, 1)
            ff_pe(pe, 0, UPD)
            norm_pe(pe, 2)
            pe.wait_ge(ff_freed, 1)
            ring.wait(pe, "kv_first", RING - 1)
            kv_pe(pe)
            pe.wait_ge(cmp_out, 1)
            norm_pe(pe, 3)
            gates_pe(pe)
            pe.wait_ge(gate_in, 1)
            for _ in nsa_queries_pe(pe, 0, 0, True):
                pass
            nsa_scores(pe, 0, 0)
            with loop(pe, GROUPS - 1) as g:
                nsa_pe(pe, g, True)
            nsa_pe(pe, GROUPS - 1, False)
            pe.wait_ge(ns_oe, 4 * GROUPS + 1)
            output_pe(pe, "nsa_o", ns_o_hi, oT_lo, ns_w_hi, QT, half_banks, H_BEFORE[3])
            norm_pe(pe, 4)
            ff_pe(pe, 1, H_BEFORE[4])

            pe.wait_ge(b2_in, B2_CONST)
            pe.transpose(bank[7][:, 0:3], head_gain_rows[:, :], ident[0:3, 0:3]).then_inc(b2_T, 1)
            pe.wait_ge(b2_ready, 1)
            norm_pe(pe, 6)
            pe.wait_ge(ff_freed, 2)
            ring.wait(pe, "df_loop", 2)
            pe.wait_ge(split_x, split_base(7))
            for _ in df_parts(pe, "df_first", 0, 0, 0):
                pass
            df_scores(pe, 0, 0, 0)
            with loop(pe, HEADS2 // 2 - 1) as turn:
                df_pe_head(pe, turn * 2, 0, df_parts(pe, "df_loop", 0, turn, turn * 2 + 1))
                df_pe_head(pe, turn * 2 + 1, 1, df_parts(pe, "df_loop", 4, turn, turn * 2 + 2))
            df_pe_head(pe, HEADS2 - 2, 0, df_parts(pe, "df_last", 0, 0, HEADS2 - 1))
            df_pe_head(pe, HEADS2 - 1, 1, ())
            pe.wait_ge(df_p, HEADS2 * T2 + 1)
            branch_pe(pe, 0)
            pe.wait_ge(br_m, KT + 1)
            with loop(pe, KV2) as kv:
                gq_pe_turn(pe, kv)
            pe.wait_ge(gq_p, KV2 * UN + 2)
            branch_pe(pe, 1)
            w_out_pe(pe)
            norm_pe(pe, 7, lambda t: logits_pe(pe, t))
            route_pe(pe)
            ex_tokens_pe(pe, 0, 0)
            ex_gate_up_pe(pe, "ex_first", 0, 0, 0, 0, 0)
            ex_gate_up_pe(pe, "ex_first", 0, 0, 0, 0, 1)
            ex_tokens_pe(pe, 0, 1)
            with loop(pe, EXPERTS // 2 - 1) as turn:
                ex_gate_up_pe(pe, "ex_loop", 0, turn, turn, 1, 0)
                ex_hidden_pe(pe, turn, 0)
                ex_gate_up_pe(pe, "ex_loop", 0, turn, turn, 1, 1)
                ex_tokens_pe(pe, turn + 1, 0)
                ex_down_pe(pe, "ex_loop", 8, turn, turn, 0)
                ex_gate_up_pe(pe, "ex_loop", 12, turn, turn + 1, 0, 0)
                ex_hidden_pe(pe, turn, 1)
                ex_gate_up_pe(pe, "ex_loop", 12, turn, turn + 1, 0, 1)
                ex_tokens_pe(pe, turn + 1, 1)
                ex_down_pe(pe, "ex_loop", 20, turn, turn, 1)
            last = EXPERTS // 2 - 1
            ex_gate_up_pe(pe, "ex_last", 0, 0, last, 1, 0)
            ex_hidden_pe(pe, last, 0)
            ex_gate_up_pe(pe, "ex_last", 0, 0, last, 1, 1)
            ex_down_pe(pe, "ex_last", 8, 0, last, 0)
            ex_hidden_pe(pe, last, 1)
            ex_down_pe(pe, "ex_last", 12, 0, last, 1, False)

        def sb_pair_act(act, p):
            for hh in range(2):
                hd = p * 2 + hh
                for i in range(QT):
                    act.wait_ge(sb_z, hd * QT + i + 1)
                    act_t.inc(act.activation(absz[:, CAUSAL_AT[i]:CAUSAL_AT[i] + CAUSAL_COLS[i]], bank[i][:, 0:CAUSAL_COLS[i]], ACT.Abs))
                act.wait_ge(act_step, act_t.value())
                act_t.inc(act.activation(absz[:, :], absz[:, :], ACT.Exp, scale=-1.0))
                act.wait_ge(act_step, act_t.value())
                act.activation(absz[:, :], absz[:, :], ACT.Ln, bias=1.0).then_inc(sb_l, 1)
                for i in range(QT):
                    act.wait_ge(sb_zi, hd * QT + i + 1)
                    act.activation(stick[:, CAUSAL_AT[i]:CAUSAL_AT[i] + CAUSAL_COLS[i]], bank[i][:, 0:CAUSAL_COLS[i]], ACT.Exp).then_inc(sb_a, 1)

        def ff_act(act, m):
            with loop(act, FF_PARTS) as f:
                for j in range(FF_TILES):
                    n = f * FF_TILES + (m * FF_PARTS * FF_TILES + j)
                    act.wait_ge(ff_mm, n + 1)
                    act.wait_ge(ff_hid, n + 1)
                    act.activation(relu[:, j % 2, :], bank[j % 4][:, :], ACT.Relu).then_inc(ff_relu, 1)

        act_t, dve_t, pool_t = Tally(act_step), Tally(dve_step), Tally(norm_ms)

        @block.scalar
        def _(act):
            act.sem_inc(ff_relu, 4)
            act.sem_inc(ns_p, 3)
            act.sem_inc(ns_t, 1)
            act.sem_inc(df_p, 1)
            act.sem_inc(df_t, 1)
            act.sem_inc(df_v, 1)
            act.sem_inc(gq_p, 2)
            act.sem_inc(gq_t, 1)
            act.wait_ge(cleared, 1)
            act.wait_ge(one_in, 1)
            norm_act(act, 0)
            scale_act(act, 0)
            with loop(act, PAIRS // 2 - 1, tallies=[(act_t, 4 * (QT + 1))]) as turn:
                sb_pair_act(act, turn * 2)
                sb_pair_act(act, turn * 2 + 1)
            sb_pair_act(act, PAIRS - 2)
            sb_pair_act(act, PAIRS - 1)
            norm_act(act, 1, H_BEFORE[1] - QT)
            scale_act(act, 1)
            ff_act(act, 0)
            norm_act(act, 2, H_BEFORE[2] - QT)
            scale_act(act, 2)
            kv_act(act)
            scale_act(act, 3)
            gates_act(act)
            act.preload_act_table_set(LN_EXP)
            nsa_exps(act, 0, 0)
            with loop(act, GROUPS - 1) as g:
                nsa_act(act, g, True)
            nsa_act(act, GROUPS - 1, False)
            norm_act(act, 4, H_BEFORE[4] - QT)
            scale_act(act, 4)
            ff_act(act, 1)
            norm_act(act, 5, H_ALL - QT)

            act.wait_ge(b2_in, B2_CONST)
            norm_act(act, 6, H_ALL)
            act.wait_ge(lam_d, 1)
            act.activation(lam[:, :], lam[:, :], ACT.Exp).then_inc(lam_e, 1)
            scale_act(act, 6)
            df_exps(act, 0, 0)
            with loop(act, HEADS2 - 1) as hd:
                df_act_head(act, hd, True)
            df_act_head(act, HEADS2 - 1, False)
            split_o_act(act, 0, df_oe)
            branch_act(act, 0)
            act.preload_act_table_set(LN_EXP)
            with loop(act, KV2, tallies=[(act_t, Q_PER_KV + 1)]) as kv:
                gq_act_turn(act, kv)
            split_o_act(act, 1, gq_oe)
            branch_act(act, 1)
            norm_act(act, 7, H_FFN - T2)
            scale_act(act, 7)
            ex_split_act(act, "ex_first", 0, 0, 0, 0, 0)
            route_act(act)
            tokens_act(act)
            ex_split_act(act, "ex_first", 0, 0, 0, 0, 1)
            ex_tokens_act(act, 0, 0)
            ex_tokens_act(act, 0, 1)
            ex_act(act, 0, 0)
            with loop(act, EXPERTS // 2 - 1) as turn:
                for m in range(2):
                    ex_split_act(act, "ex_loop", 0, turn, turn, 1, m)
                ex_tokens_act(act, turn + 1, 0)
                ex_act(act, turn, 1)
                for m in range(2):
                    ex_split_act(act, "ex_loop", 12, turn, turn + 1, 0, m)
                ex_tokens_act(act, turn + 1, 1)
                ex_act(act, turn + 1, 0)
            for m in range(2):
                ex_split_act(act, "ex_last", 0, 0, EXPERTS // 2 - 1, 1, m)
            ex_act(act, EXPERTS // 2 - 1, 1)
            for t in range(QT):
                act.wait_ge(tile_in[t], 32)
                act.activation(u_rows[:, t, :], h[:, t, :], ACT.Square, scale=D ** -0.5, accum_out=ssq[:, 0, t:t + 1]).then_inc(fin_sq, 1)

        def step(dve, ins):
            dve_t.inc(ins)
            dve.wait_ge(dve_step, dve_t.value())

        def sb_take(dve, n, p, u):
            dve.wait_ge(sb_pj, p * 3 + n + 1)
            if n == 0:
                dve.tensor_scalar(qT[:, u, :], bank[5][:, :], HD ** -0.5, None, ALU.mult).then_inc(sb_pe, 1)
            elif n == 1:
                dve.tensor_copy(kT[:, u, :], bank[6][:, :]).then_inc(sb_pe, 1)
            else:
                dve.tensor_copy(vN[:, u, :, :], bank[7][:, :].rearrange("p (t n) -> p t n", n=P)).then_inc(sb_pe, 1)

        def sb_pair_dve(dve, p, u, take):
            for hh in range(2):
                hd = p * 2 + hh
                dve.wait_ge(sb_l, hd + 1)
                for i in range(QT):
                    s = slice(CAUSAL_AT[i], CAUSAL_AT[i] + CAUSAL_COLS[i])
                    dve_t.inc(dve.scalar_tensor_tensor(softp[:, s], bank[i][:, 0:CAUSAL_COLS[i]], 0.0, absz[:, s], ALU.max, ALU.add))
                dve.wait_ge(dve_step, dve_t.value())
                for i in range(QT):
                    d = softp[:, CAUSAL_AT[i]:CAUSAL_AT[i] + P]
                    last = dve.tensor_tensor(d, d, past01[:, :], ALU.mult)
                    if i == QT - 1:
                        last.then_inc(sb_sp, 1)
                if take and hh == 0:
                    sb_take(dve, 0, p + 1, 1 - u)
                if take and hh == 1:
                    sb_take(dve, 1, p + 1, 1 - u)
                    sb_take(dve, 2, p + 1, 1 - u)
                dve.wait_ge(sb_o, hd + 1)
                take_o(dve, sb_o_hi, slice(HD * hh, HD * hh + HD), p, bank[4], sb_oe)

        def w_out_dve(dve):
            for n in range(2):
                for t in range(T2):
                    r = rows_of(t)
                    dve.wait_ge(acc_done, H_ALL + n * T2 + t + 1)
                    hs = h[0:r, t, 512 * n:512 * n + 512]
                    dve.tensor_tensor(hs, bank[(n * T2 + t) % 8][0:r, :], hs, ALU.add).then_inc(h_upd, 1)

        def residual_dve(dve, done, bank_of=half_banks):
            for n in range(2):
                for t in range(QT):
                    dve.wait_ge(acc_done, done + n * QT + t + 1)
                    hs = h[:, t, 512 * n:512 * n + 512]
                    dve.tensor_tensor(hs, bank[bank_of(n, t)][:, :], hs, ALU.add).then_inc(h_upd, 1)

        def ff_dve(dve, m, upd):
            with loop(dve, FF_PARTS, tallies=[(dve_t, 2 * FF_TILES)]) as f:
                for j in range(FF_TILES):
                    n = f * FF_TILES + (m * FF_PARTS * FF_TILES + j)
                    dve.wait_ge(ff_relu, n + 5)
                    r, sq = relu[:, j % 2, :], hid_sq[:, j % 2, :]
                    dve_t.inc(dve.tensor_tensor(sq, r, r, ALU.mult))
                    step(dve, dve.tensor_tensor(hid_hi[:, j, :], r, r, ALU.mult))
                    dve.tensor_tensor(hid_lo[:, j, :], sq, hid_hi[:, j, :].bitcast(F32), ALU.subtract).then_inc(ff_hid, 1)
                residual_dve(dve, f * UPD + upd)

        @block.vector
        def _(dve):
            dve.sem_inc(sb_pe, 3)
            dve.sem_inc(sb_oe, 1)
            dve.sem_inc(ff_hid, 2)
            dve.sem_inc(ns_oe, 1)
            dve.sem_inc(df_pe, 1)
            dve.sem_inc(df_oe, 1)
            dve.sem_inc(br_m, 2)
            dve.sem_inc(gq_br, 1)
            dve.sem_inc(gq_oe, 1)
            dve.sem_inc(ex_xe, 1)
            dve.sem_inc(ex_h, 1)
            dve.sem_inc(ex_he, 1)
            dve.sem_inc(ex_ye, 1)
            dve.sem_inc(ex_done, 2)
            dve.memset(ssq[:, :, :], 0.0).then_inc(cleared, 1)
            dve.memset(ones_neg[:, :], -1.0)
            dve.wait_ge(const_in, ALL_CONST)
            dve.tensor_copy(ident_bf[:, :], ident[:, :])
            dve.tensor_copy(past_neg_bf[:, :], past_neg[:, :])
            dve.wait_ge(gains_T, 1)
            dve.tensor_copy(gains[:, :, :].rearrange("p g k -> p (g k)"), bank[0][:, 0:7 * KT]).then_inc(gains_in, 1)
            norm_dve(dve, 0)
            for n in range(3):
                sb_take(dve, n, 0, 0)
            with loop(dve, PAIRS // 2 - 1, tallies=[(dve_t, 4 * QT + 4)]) as turn:
                sb_pair_dve(dve, turn * 2, 0, True)
                sb_pair_dve(dve, turn * 2 + 1, 1, True)
            sb_pair_dve(dve, PAIRS - 2, 0, True)
            sb_pair_dve(dve, PAIRS - 1, 1, False)
            residual_dve(dve, 0, sb_out_banks)
            norm_dve(dve, 1)
            ff_dve(dve, 0, UPD)
            norm_dve(dve, 2)
            kv_dve(dve)
            norm_dve(dve, 3)
            gates_dve(dve)
            nsa_raw_dve(dve, 0, 0)
            nsa_rot_dve(dve, 0, 0)
            nsa_maxima(dve, 0, 0)
            with loop(dve, GROUPS - 1, tallies=[(dve_t, 48)]) as g:
                nsa_dve(dve, g, True)
            nsa_dve(dve, GROUPS - 1, False)
            residual_dve(dve, H_BEFORE[3])
            norm_dve(dve, 4)
            ff_dve(dve, 1, H_BEFORE[4])
            dve.wait_ge(gain_in, 16)
            plain_norm_dve(dve, 5, QT)

            ready2_dve(dve)
            norm_dve(dve, 6)
            for n in range(6):
                df_take(dve, n, 0, 0)
            df_maxima(dve, 0, 0)
            with loop(dve, HEADS2 // 2 - 1, tallies=[(dve_t, 2 * (3 * T2 + 1))]) as turn:
                df_dve_head(dve, turn * 2, 0, True)
                df_dve_head(dve, turn * 2 + 1, 1, True)
            df_dve_head(dve, HEADS2 - 2, 0, True)
            df_dve_head(dve, HEADS2 - 1, 1, False)
            split_o_dve(dve, 0)
            branch_dve(dve, 0, 0)
            with loop(dve, KV2, tallies=[(dve_t, 45)]) as kv:
                gq_dve_turn(dve, kv)
            split_o_dve(dve, 1)
            branch_dve(dve, 1, 12)
            w_out_dve(dve)
            norm_dve(dve, 7)
            ex_split_dve(dve, "ex_first", 0, 0, 0, 0, 0, range(EARLY_SPLITS))
            route_dve(dve)
            ex_tokens_dve(dve, 0, 0)
            ex_split_dve(dve, "ex_first", 0, 0, 0, 0, 0, range(EARLY_SPLITS, KT // 2))
            ex_split_dve(dve, "ex_first", 0, 0, 0, 0, 1)
            ex_tokens_dve(dve, 0, 1)
            ex_hid_dve(dve, 0, 0)
            ex_split_dve(dve, "ex_loop", 0, 0, 0, 1, 0)
            with loop(dve, EXPERTS // 2 - 1, tallies=[(dve_t, 4)]) as turn:
                ex_split_dve(dve, "ex_loop", 0, turn, turn, 1, 1)
                ex_hidden_dve(dve, turn, 0)
                ex_tokens_dve(dve, turn + 1, 0)
                ex_hid_dve(dve, turn, 1)
                ex_split_dve(dve, "ex_loop", 12, turn, turn + 1, 0, 0)
                ex_split_dve(dve, "ex_loop", 12, turn, turn + 1, 0, 1)
                ex_out_dve(dve, turn, 0)
                ex_hidden_dve(dve, turn, 1)
                ex_tokens_dve(dve, turn + 1, 1)
                ex_hid_dve(dve, turn + 1, 0)
                ex_split_dve(dve, "ex_loop", 0, turn + 1, turn + 1, 1, 0)
                ex_out_dve(dve, turn, 1)
            ex_split_dve(dve, "ex_last", 0, 0, EXPERTS // 2 - 1, 1, 1)
            ex_hidden_dve(dve, EXPERTS // 2 - 1, 0)
            ex_hid_dve(dve, EXPERTS // 2 - 1, 1)
            ex_out_dve(dve, EXPERTS // 2 - 1, 0)
            ex_hidden_dve(dve, EXPERTS // 2 - 1, 1)
            ex_out_dve(dve, EXPERTS // 2 - 1, 1)
            dve.wait_ge(gain_in, 48)
            for t in range(QT):
                dve.wait_ge(fin_sd, t + 1)
                dve.scalar_tensor_tensor(h[:, t, :], h[:, t, :], rstd[:, t:t + 1], gain_bc[:, :], ALU.mult, ALU.mult).then_inc(fin_h, 1)

        @block.gpsimd
        def _(pool):
            pool.sem_inc(ff_w2, 2 * (FF_TILES // 2 - 1))
            pool.memset(eps_col[:, :], EPS2)
            pool.memset(neg_half[:, :], -0.5)
            pool.memset(one[:, :], 1.0).then_inc(one_in, 1)
            pool.wait_ge(one_in, 1)
            norm_pool(pool, 0)
            split_heads_pool(pool, "sb", "sb_first", "sb_loop", "sb_last", PAIRS, sb_pj, 3, w_hi)
            output_pool(pool, "sb_o", w_hi, SPLITS)
            norm_pool(pool, 1)
            for m in range(2):
                pool.wait_ge(norm_tp, 2 * norm_base(FF_NORMS[m]) + 1)
                ff_pool(pool, m, UPD if m == 0 else H_BEFORE[4])
                pool.sem_inc(ff_freed, 1)
                if m == 0:
                    norm_pool(pool, 2)
                    nsa_pool(pool)
                    output_pool(pool, "nsa_o", ns_w_hi)
                    norm_pool(pool, 4)
            norm_pool(pool, 5)
            norm_pool(pool, 6)
            split_heads_pool(pool, "df", "df_first", "df_loop", "df_last", HEADS2, df_pj, 6, w2_hi)
            branch_pool(pool, 0)
            gq_pool(pool)
            branch_pool(pool, 1)
            output_pool(pool, "w_out", w2_hi, free=lambda j: pool.wait_ge(br_mm, 2 * BR_SPLITS - SPLITS2 + j + 3))
            norm_pool(pool, 7)
            pool.wait_ge(h_upd, H_FFN)
            pool.dma_start(y_dram[0:SEQ, :].rearrange("(t p) d -> p t d", p=P), h[:, 0:QT, :]).then_inc(h_out, 16)
            pool.dma_start(y_dram[SEQ:L2, :], h[0:META, QT, :]).then_inc(h_out, 16)
            tokens_pool(pool)
            pool.wait_ge(ex_no, 1)
            pool.wait_ge(h_out, 32)
            pool.wait_ge(u_out, 16 * T2)
            for e in range(EARLY):
                ex_get(pool, e // 2, e % 2)
            pool.wait_ge(ex_no, 2)
            ex_put(pool, 0, 0)
            with loop(pool, EXPERTS // 2 - 2) as turn:
                ex_get(pool, turn + 2, 0)
                ex_put_next(pool, turn, 1)
                ex_get(pool, turn + 2, 1)
                ex_put_next(pool, turn + 1, 0)
            for e in range(EXPERTS - 3, EXPERTS):
                ex_put_next(pool, e // 2, e % 2)
            for t in range(QT):
                mean_sq, root = ssq[:, 0, t:t + 1], rstd[:, t:t + 1]
                pool.wait_ge(fin_sq, t + 1)
                pool.tensor_scalar(root, mean_sq, EPS2, None, ALU.add).then_inc(fin_ms, 1)
                pool.wait_ge(fin_ms, t + 1)
                pool.tensor_tensor(root, root, neg_half[:, :], ALU.pow).then_inc(fin_sd, 1)


def rope_tables_1():
    f, half = np.float32, 8
    inv = f(500000.0) ** (-np.arange(half, dtype=f) * f(2.0) / f(16))
    ang = np.arange(SEQ, dtype=f)[None, :] * inv[:, None]
    cos, sin, rot = np.ones((P, SEQ), f), np.zeros((P, SEQ), f), np.zeros((P, P), f)
    for base in (0, HD):
        for d in range(half):
            for x, y, sign in ((d, d + half, -1), (d + half, d, 1)):
                cos[base + x], sin[base + x] = np.cos(ang[d]), np.sin(ang[d])
                rot[base + y, base + x] = sign
    return cos, sin, rot


def rope_tables_2():
    f, half, grid_w = np.float32, HD // 2, 64
    inv = f(10000.0) ** (-np.arange(0, HD, 2, dtype=f) / f(HD))
    i = np.arange(SEQ)
    cos, sin, rot = np.ones((P, L2), f), np.zeros((P, L2), f), np.zeros((P, P), f)
    for base, place in ((0, i // grid_w), (HD, i % grid_w)):
        ang = place.astype(f)[None, :] * inv[:, None]
        for d in range(half):
            for x, y, sign in ((d, d + half, -1), (d + half, d, 1)):
                cos[base + x, 0:SEQ], sin[base + x, 0:SEQ] = np.cos(ang[d]), np.sin(ang[d])
                rot[base + y, base + x] = sign
    return cos, sin, rot


def distances():
    pos = np.arange(T2 * P)
    d = np.abs(pos[:, None] - pos[None, :L2])
    d[(pos >= SEQ), :] = 0
    d[:, SEQ:] = 0
    return np.ascontiguousarray(d.reshape(T2, P, L2).transpose(1, 0, 2)).astype(np.float16)


def constants():
    f = np.float32
    i = np.arange(P)
    tok = i[:, None] + P * np.arange(QT)[None, :]
    cmp_ok = (CMP_STRIDE * np.arange(N_CMP) + CMP_LEN - 1)[None, None, :] <= tok[:, :, None]
    cos1, sin1, rot1 = rope_tables_1()
    cos2, sin2, rot2 = rope_tables_2()
    return {
        "ident": np.eye(P, dtype=f),
        "tri_neg": -(i[:, None] >= i[None, :]).astype(f),
        "past01": (i[:, None] < i[None, :]).astype(f),
        "future_neg": np.where(i[:, None] >= i[None, :], f(0), f(-1e30)).astype(f),
        "cmp_neg": np.where(cmp_ok, f(0), f(-1e30)).astype(f),
        "cmp_any": cmp_ok.any(-1).astype(f),
        "cos1": cos1, "sin1": sin1, "rot1": rot1,
        "cos2": cos2, "sin2": sin2, "rot2": rot2, "dist": distances(),
        "slot_no": np.tile(np.arange(CAP, dtype=f), (P, 1)),
        "token_no": np.stack(np.broadcast_arrays(np.arange(T2)[None, :], i[:, None]), 1).astype(f),
        "past_neg": np.where(i[:, None] < i[None, :], f(0), f(-1e30)).astype(f),
    }


def kernel(**inputs):
    import concourse.bacc as _bacc
    from concourse.bass_utils import run_bass_kernel_spmd as _run

    nc = _bacc.Bacc("TRN2", target_bir_lowering=False, num_devices=1)
    arrays, A, C = {}, {}, {}
    for kind, into, values in (("in", A, inputs), ("c", C, constants())):
        for name, value in values.items():
            a = np.ascontiguousarray(value)
            arrays[f"{kind}_{name}"] = a
            into[name] = nc.dram_tensor(f"{kind}_{name}", a.shape, mybir.dt.from_np(a.dtype), kind="ExternalInput").ap()
    out = nc.dram_tensor("out", (1, SEQ, D), F32, kind="ExternalOutput").ap()
    build_program(nc, A, C, out)
    return _run(nc, [arrays], core_ids=[0]).results[0]["out"]
```
